# Optimizing a Trainium2 kernel written in Bass

```python
import math
import jax
import jax.numpy as jnp
from jax import lax
import numpy as np

D_MODEL = 1024
BATCH = 1
SEQ = 1024
DEPTH = 1

CTX_LEN = 256
GRID_W = 64
D_MIX = D_MODEL
W_A = D_MIX // 4
W_B = D_MIX // 4
W_C = D_MIX // 4
W_D = D_MIX - W_A - W_B - W_C
MLSTM_HEADS = 4
MLSTM_HD = W_A // MLSTM_HEADS
MLSTM_CHUNK = 64
SGU_GROUPS = 4
SGU_GD = W_B // SGU_GROUPS
SGU_CHUNK = 128
CONV_WIDTH = 31
CONV_PAD = CONV_WIDTH // 2
S5_P = 16
S5_GROUPS = W_D // S5_P
S5_N = 64
D_FF = -(-8 * D_MODEL // (3 * 256)) * 256
ALPHA = (2 * DEPTH) ** 0.25
BETA = (8 * DEPTH) ** -0.25
LN_EPS = 1e-5
OFF_B = 4 * W_A + 4 * MLSTM_HEADS
OFF_C = OFF_B + 2 * W_B
OFF_D = OFF_C + 2 * W_C
P_IN = OFF_D + W_D


def layer_norm(x, w, b):
    xf = x.astype(jnp.float32)
    mu = jnp.mean(xf, -1, keepdims=True)
    var = jnp.mean(jnp.square(xf - mu), -1, keepdims=True)
    return ((xf - mu) * lax.rsqrt(var + LN_EPS) * w + b).astype(x.dtype)

def swiglu(h, w_in, w_out):
    g, u = jnp.split(h @ w_in, 2, axis=-1)
    return (jax.nn.silu(g) * u) @ w_out

def mlstm_split(z, gate_bias):
    bsz, t, _ = z.shape
    heads = lambda a: a.reshape(bsz, t, MLSTM_HEADS, MLSTM_HD).transpose(0, 2, 1, 3)
    q, k, v, o = (z[..., i * W_A:(i + 1) * W_A] for i in range(4))
    g = (z[..., 4 * W_A:] + gate_bias).astype(jnp.float32)
    g = g.reshape(bsz, t, 4, MLSTM_HEADS).transpose(2, 0, 3, 1)
    gates = (g[0], jax.nn.log_sigmoid(g[1]), g[2], jax.nn.log_sigmoid(g[3]))
    return heads(q), heads(k) * MLSTM_HD ** -0.5, heads(v), o, gates

def mlstm_zero_state(bsz):
    return (jnp.zeros((bsz, MLSTM_HEADS, MLSTM_HD, MLSTM_HD), jnp.float32),
            jnp.zeros((bsz, MLSTM_HEADS, MLSTM_HD), jnp.float32),
            jnp.zeros((bsz, MLSTM_HEADS), jnp.float32))

def mlstm_context_state(k, v, ig, lf):
    k, v = k.astype(jnp.float32), v.astype(jnp.float32)
    cum = jnp.cumsum(lf, axis=-1)
    logw = cum[..., -1:] - cum + ig
    m = jnp.max(logw, axis=-1)
    e = jnp.exp(logw - m[..., None])
    C = jnp.einsum('bht,bhtv,bhtk->bhvk', e, v, k)
    n = jnp.einsum('bht,bhtk->bhk', e, k)
    return (C, n, m)

def mlstm_chunkwise(q, k, v, ig, lf, state):
    bsz, nh, t, d = q.shape
    nc = t // MLSTM_CHUNK
    chunks = lambda a: jnp.moveaxis(a.astype(jnp.float32).reshape(bsz, nh, nc, MLSTM_CHUNK, *a.shape[3:]), 2, 0)
    xs = tuple(chunks(a) for a in (q, k, v, ig, lf))
    lower = jnp.tril(jnp.ones((MLSTM_CHUNK, MLSTM_CHUNK), bool))

    def step(carry, inp):
        C, n, m = carry
        qc, kc, vc, ic, fc = inp
        b = jnp.cumsum(fc, axis=-1)
        logw = jnp.where(lower, b[..., :, None] - b[..., None, :] + ic[..., None, :], -jnp.inf)
        inter = b + m[..., None]
        m_t = jnp.maximum(inter, jnp.max(logw, axis=-1))
        w_inter = jnp.exp(inter - m_t)
        s = jnp.einsum('bhtd,bhsd->bhts', qc, kc) * jnp.exp(logw - m_t[..., None])
        num = jnp.einsum('bhts,bhsd->bhtd', s, vc) + w_inter[..., None] * jnp.einsum('bhvk,bhtk->bhtv', C, qc)
        den = jnp.sum(s, axis=-1) + w_inter * jnp.einsum('bhk,bhtk->bht', n, qc)
        h = num / jnp.maximum(jnp.abs(den), jnp.exp(-m_t))[..., None]
        b_end = b[..., -1]
        logu = b_end[..., None] - b + ic
        m_new = jnp.maximum(b_end + m, jnp.max(logu, axis=-1))
        e = jnp.exp(logu - m_new[..., None])
        decay = jnp.exp(b_end + m - m_new)
        C = decay[..., None, None] * C + jnp.einsum('bhs,bhsv,bhsk->bhvk', e, vc, kc)
        n = decay[..., None] * n + jnp.einsum('bhs,bhsk->bhk', e, kc)
        return (C, n, m_new), h

    state, h = lax.scan(step, state, xs)
    return jnp.moveaxis(h, 0, 2).reshape(bsz, nh, t, d), state

def mlstm_readout(h, o, norm_w):
    bsz, _, t, _ = h.shape
    h = h.transpose(0, 2, 1, 3)
    mu = jnp.mean(h, -1, keepdims=True)
    var = jnp.mean(jnp.square(h - mu), -1, keepdims=True)
    hn = (h - mu) * lax.rsqrt(var + LN_EPS) * norm_w.reshape(MLSTM_HEADS, MLSTM_HD)
    return (hn.reshape(bsz, t, W_A) * jax.nn.sigmoid(o.astype(jnp.float32))).astype(o.dtype)

def mlstm_mixer(zl, zc, gate_bias, norm_w, need_ctx):
    ql, kl, vl, ol, gl = mlstm_split(zl, gate_bias)
    qc, kc, vc, oc, gc = mlstm_split(zc, gate_bias)
    hl_dirs, hc_dirs = [], []
    for d in range(2):
        orient = (lambda a: jnp.flip(a, axis=2)) if d else (lambda a: a)
        if need_ctx:
            hc, state = mlstm_chunkwise(orient(qc), orient(kc), orient(vc), orient(gc[2 * d]),
                                        orient(gc[2 * d + 1]), mlstm_zero_state(zc.shape[0]))
            hc_dirs.append(orient(hc))
        else:
            state = mlstm_context_state(orient(kc), orient(vc), orient(gc[2 * d]), orient(gc[2 * d + 1]))
        hl, _ = mlstm_chunkwise(orient(ql), orient(kl), orient(vl), orient(gl[2 * d]), orient(gl[2 * d + 1]), state)
        hl_dirs.append(orient(hl))
    yl = mlstm_readout(hl_dirs[0] + hl_dirs[1], ol, norm_w)
    yc = mlstm_readout(hc_dirs[0] + hc_dirs[1], oc, norm_w) if need_ctx else None
    return yl, yc

def sgu_mixer(z, ln_w, ln_b, w_s, b_s):
    bsz, t, _ = z.shape
    u = jax.nn.gelu(z[..., :W_B])
    v = layer_norm(jax.nn.gelu(z[..., W_B:]), ln_w, ln_b)
    v = v.reshape(bsz, t // SGU_CHUNK, SGU_CHUNK, SGU_GROUPS, SGU_GD)
    v = jnp.einsum('gts,bnsgc->bntgc', w_s, v) + b_s.T[:, :, None]
    return u * v.reshape(bsz, t, W_B)

def conv_mixer(z, w, b, ln_w, ln_b, rows):
    a = z[..., :W_C] * jax.nn.sigmoid(z[..., W_C:])
    bsz, t, ch = a.shape
    a = a.reshape(bsz * rows, t // rows, ch)
    a = lax.conv_general_dilated(a, w[:, None, :], window_strides=(1,), padding=[(CONV_PAD, CONV_PAD)],
                                 dimension_numbers=('NWC', 'WIO', 'NWC'), feature_group_count=ch)
    a = a.reshape(bsz, t, ch) + b
    return jax.nn.silu(layer_norm(a, ln_w, ln_b))

def s5_discretize(a_re, a_im, log_dt, b_re, b_im):
    lam = lax.complex(a_re.astype(jnp.float32), a_im.astype(jnp.float32))
    lam_dt = lam * jnp.exp(log_dt.astype(jnp.float32))[:, None]
    a_bar = jnp.exp(lam_dt)
    b_bar = ((a_bar - 1.0) / lam)[..., None] * lax.complex(b_re.astype(jnp.float32), b_im.astype(jnp.float32))
    return lam_dt, a_bar, b_bar

def s5_scan(bu, a_bar):
    def combine(left, right):
        a_l, b_l = left
        a_r, b_r = right
        return a_r * a_l, a_r * b_l + b_r
    a = jnp.broadcast_to(a_bar, (1,) + bu.shape[1:])
    return lax.associative_scan(combine, (a, bu), axis=1)[1]

def s5_final_state(bu, lam_dt):
    t = bu.shape[1]
    lags = jnp.arange(t - 1, -1, -1, dtype=jnp.float32)
    return jnp.einsum('tgn,btgn->bgn', jnp.exp(lags[:, None, None] * lam_dt), bu)

def s5_mixer(zl, zc, a_re, a_im, log_dt, b_re, b_im, c_re, c_im, d_skip, glu_w, glu_b, need_ctx):
    grouped = lambda z: z.astype(jnp.float32).reshape(z.shape[0], z.shape[1], S5_GROUPS, S5_P)
    ul, uc = grouped(zl), grouped(zc)
    xl_dirs, xc_dirs = [], []
    for d in range(2):
        orient = (lambda a: jnp.flip(a, axis=1)) if d else (lambda a: a)
        lam_dt, a_bar, b_bar = s5_discretize(a_re[d], a_im[d], log_dt[d], b_re, b_im)
        bul = orient(jnp.einsum('btgp,gnp->btgn', ul, b_bar))
        buc = orient(jnp.einsum('btgp,gnp->btgn', uc, b_bar))
        if need_ctx:
            sc = s5_scan(buc, a_bar)
            h0 = sc[:, -1]
            xc_dirs.append(orient(sc))
        else:
            h0 = s5_final_state(buc, lam_dt)
        sl = s5_scan(bul.at[:, 0].add(a_bar * h0), a_bar)
        xl_dirs.append(orient(sl))
    c_mat = lax.complex(c_re.astype(jnp.float32), c_im.astype(jnp.float32))
    d_mat = d_skip.astype(jnp.float32).reshape(S5_GROUPS, S5_P)

    def readout(states, u, dtype):
        y = jnp.real(jnp.einsum('gpn,btgn->btgp', c_mat, states)) + d_mat * u
        y = jax.nn.gelu(y.reshape(u.shape[0], u.shape[1], W_D))
        return (y * jax.nn.sigmoid(y @ glu_w.astype(jnp.float32) + glu_b.astype(jnp.float32))).astype(dtype)

    yl = readout(xl_dirs[0] + xl_dirs[1], ul, zl.dtype)
    yc = readout(xc_dirs[0] + xc_dirs[1], uc, zc.dtype) if need_ctx else None
    return yl, yc

def first_inputs(seed: int = 0) -> dict:
    key = jax.random.key(seed)
    ks = iter(jax.random.split(key, 48))
    f32 = jnp.float32
    nrm = lambda shape, scale: jax.random.normal(next(ks), shape, f32) * scale
    L, D = DEPTH, D_MODEL
    x = nrm((BATCH, SEQ, D), 1.0)
    c = nrm((BATCH, D), 1.0)
    ctx = nrm((BATCH, CTX_LEN, D), 1.0)
    c_ctx = nrm((D,), 1.0)
    w_mod = nrm((L, D, 6 * D), 0.5 * D ** -0.5)
    b_mod = nrm((L, 6 * D), 0.02)
    w_in = nrm((L, D, P_IN), D ** -0.5)
    ig_b = nrm((L, 2, 1, MLSTM_HEADS), 0.1)
    fg_b = jnp.linspace(3.0, 6.0, MLSTM_HEADS, dtype=f32) + nrm((L, 2, 1, MLSTM_HEADS), 0.1)
    mlstm_gate_bias = jnp.concatenate([ig_b, fg_b], axis=2).reshape(L, 4 * MLSTM_HEADS)
    mlstm_norm_w = 1.0 + nrm((L, W_A), 0.02)
    sgu_ln_w = 1.0 + nrm((L, W_B), 0.02)
    sgu_ln_b = nrm((L, W_B), 0.02)
    sgu_w = nrm((L, SGU_GROUPS, SGU_CHUNK, SGU_CHUNK), SGU_CHUNK ** -0.5)
    sgu_b = 1.0 + nrm((L, SGU_GROUPS, SGU_CHUNK), 0.02)
    conv_w = nrm((L, CONV_WIDTH, W_C), CONV_WIDTH ** -0.5)
    conv_b = nrm((L, W_C), 0.02)
    conv_ln_w = 1.0 + nrm((L, W_C), 0.02)
    conv_ln_b = nrm((L, W_C), 0.02)
    s5_a_re = -0.5 + nrm((L, 2, S5_GROUPS, S5_N), 0.01)
    s5_a_im = math.pi * jnp.arange(S5_N, dtype=f32) + nrm((L, 2, S5_GROUPS, S5_N), 0.01)
    s5_log_dt = jax.random.uniform(next(ks), (L, 2, S5_GROUPS), f32, math.log(1e-3), math.log(1e-1))
    s5_b_re = nrm((L, S5_GROUPS, S5_N, S5_P), (2 * S5_P) ** -0.5)
    s5_b_im = nrm((L, S5_GROUPS, S5_N, S5_P), (2 * S5_P) ** -0.5)
    s5_c_re = nrm((L, S5_GROUPS, S5_P, S5_N), (2 * S5_N) ** -0.5)
    s5_c_im = nrm((L, S5_GROUPS, S5_P, S5_N), (2 * S5_N) ** -0.5)
    s5_d = nrm((L, W_D), 1.0)
    s5_glu_w = nrm((L, W_D, W_D), W_D ** -0.5)
    s5_glu_b = nrm((L, W_D), 0.02)
    w_out = nrm((L, D_MIX, D), BETA * D_MIX ** -0.5)
    ln1_w = 1.0 + nrm((L, D), 0.02)
    ln1_b = nrm((L, D), 0.02)
    w_ffn_in = nrm((L, D, 2 * D_FF), D ** -0.5)
    w_ffn_out = nrm((L, D_FF, D), BETA * D_FF ** -0.5)
    ln2_w = 1.0 + nrm((L, D), 0.02)
    ln2_b = nrm((L, D), 0.02)
    return {'x': x, 'c': c, 'ctx': ctx, 'c_ctx': c_ctx, 'w_mod': w_mod, 'b_mod': b_mod, 'w_in': w_in,
            'mlstm_gate_bias': mlstm_gate_bias, 'mlstm_norm_w': mlstm_norm_w,
            'sgu_ln_w': sgu_ln_w, 'sgu_ln_b': sgu_ln_b, 'sgu_w': sgu_w, 'sgu_b': sgu_b,
            'conv_w': conv_w, 'conv_b': conv_b, 'conv_ln_w': conv_ln_w, 'conv_ln_b': conv_ln_b,
            's5_a_re': s5_a_re, 's5_a_im': s5_a_im, 's5_log_dt': s5_log_dt, 's5_b_re': s5_b_re,
            's5_b_im': s5_b_im, 's5_c_re': s5_c_re, 's5_c_im': s5_c_im, 's5_d': s5_d,
            's5_glu_w': s5_glu_w, 's5_glu_b': s5_glu_b, 'w_out': w_out, 'ln1_w': ln1_w, 'ln1_b': ln1_b,
            'w_ffn_in': w_ffn_in, 'w_ffn_out': w_ffn_out, 'ln2_w': ln2_w, 'ln2_b': ln2_b}

def first_block(x, c, ctx, c_ctx, w_mod, b_mod, w_in, mlstm_gate_bias, mlstm_norm_w,
              sgu_ln_w, sgu_ln_b, sgu_w, sgu_b, conv_w, conv_b, conv_ln_w, conv_ln_b,
              s5_a_re, s5_a_im, s5_log_dt, s5_b_re, s5_b_im, s5_c_re, s5_c_im, s5_d,
              s5_glu_w, s5_glu_b, w_out, ln1_w, ln1_b, w_ffn_in, w_ffn_out, ln2_w, ln2_b):
    rows = x.shape[1] // GRID_W
    xc = ctx
    for l in range(DEPTH):
        need_ctx = l < DEPTH - 1
        w_in_l = w_in[l]
        mod = jax.nn.silu(c) @ w_mod[l] + b_mod[l]
        mod_c = jax.nn.silu(c_ctx) @ w_mod[l] + b_mod[l]
        sh1, sc1, g1, sh2, sc2, g2 = jnp.split(mod[:, None, :], 6, axis=-1)
        sh1c, sc1c, g1c, sh2c, sc2c, g2c = jnp.split(mod_c, 6, axis=-1)
        h = x * (1.0 + sc1) + sh1
        hc = xc * (1.0 + sc1c) + sh1c
        z = h @ w_in_l
        zc_a = hc @ w_in_l[:, :OFF_B]
        zc_d = hc @ w_in_l[:, OFF_D:]
        y_a, yc_a = mlstm_mixer(z[..., :OFF_B], zc_a, mlstm_gate_bias[l], mlstm_norm_w[l], need_ctx)
        y_b = sgu_mixer(z[..., OFF_B:OFF_C], sgu_ln_w[l], sgu_ln_b[l], sgu_w[l], sgu_b[l])
        y_c = conv_mixer(z[..., OFF_C:OFF_D], conv_w[l], conv_b[l], conv_ln_w[l], conv_ln_b[l], rows)
        y_d, yc_d = s5_mixer(z[..., OFF_D:], zc_d, s5_a_re[l], s5_a_im[l], s5_log_dt[l], s5_b_re[l], s5_b_im[l],
                             s5_c_re[l], s5_c_im[l], s5_d[l], s5_glu_w[l], s5_glu_b[l], need_ctx)
        y = jnp.concatenate([y_a, y_b, y_c, y_d], axis=-1) @ w_out[l]
        x = layer_norm(ALPHA * x + g1 * y, ln1_w[l], ln1_b[l])
        x = layer_norm(ALPHA * x + g2 * swiglu(x * (1.0 + sc2) + sh2, w_ffn_in[l], w_ffn_out[l]), ln2_w[l], ln2_b[l])
        if need_ctx:
            yc_b = sgu_mixer(hc @ w_in_l[:, OFF_B:OFF_C], sgu_ln_w[l], sgu_ln_b[l], sgu_w[l], sgu_b[l])
            yc_c = conv_mixer(hc @ w_in_l[:, OFF_C:OFF_D], conv_w[l], conv_b[l], conv_ln_w[l], conv_ln_b[l], 1)
            yc = jnp.concatenate([yc_a, yc_b, yc_c, yc_d], axis=-1) @ w_out[l]
            xc = layer_norm(ALPHA * xc + g1c * yc, ln1_w[l], ln1_b[l])
            xc = layer_norm(ALPHA * xc + g2c * swiglu(xc * (1.0 + sc2c) + sh2c, w_ffn_in[l], w_ffn_out[l]),
                            ln2_w[l], ln2_b[l])
    return x


_first_inputs = first_inputs


def first_inputs(seed=0):
    import zlib

    import numpy as np

    out = dict(_first_inputs(seed))
    spreads = {}
    factors = {'ctx': 6.508,
     'c_ctx': 7.612,
     'b_mod': 4.658,
     'mlstm_norm_w': 64.0,
     'sgu_ln_w': 60.145,
     'sgu_ln_b': 59.579,
     'sgu_b': 63.078,
     'conv_b': 8.0,
     'conv_ln_w': 60.666,
     'conv_ln_b': 64.0,
     's5_a_re': 64.0,
     's5_a_im': 64.0,
     's5_log_dt': 64.0,
     's5_b_re': 64.0,
     's5_b_im': 64.0,
     's5_c_re': 64.0,
     's5_c_im': 64.0,
     's5_glu_w': 18.351,
     's5_glu_b': 64.0,
     'ln1_w': 8.152,
     'ln1_b': 7.59,
     'ln2_w': 8.199,
     'ln2_b': 8.095}
    for name, (base, spread) in spreads.items():
        noise = np.random.default_rng([zlib.crc32(name.encode()), seed]).standard_normal(out[name].shape)
        drawn = base * np.exp(spread * noise) if base else spread * noise
        out[name] = jnp.asarray(drawn.astype(out[name].dtype))
    for name, factor in factors.items():
        out[name] = (out[name] * factor).astype(out[name].dtype)
    return out


_narrow_inputs = first_inputs


def first_inputs(seed=0):
    out = dict(_narrow_inputs(seed))
    wider = {'mlstm_norm_w': 6.0,
     'sgu_ln_w': 4.97,
     'sgu_ln_b': 4.92,
     'sgu_b': 5.02,
     'conv_ln_w': 4.89,
     'conv_ln_b': 5.13,
     's5_d': 9.54,
     's5_glu_w': 12.0,
     's5_glu_b': 12.0,
     'ln2_w': 3.32,
     'ln2_b': 3.25}
    for name, times in wider.items():
        mean = out[name].mean()
        out[name] = (mean + times * (out[name] - mean)).astype(out[name].dtype)
    return out


CHUNK = 64
Q_BLOCK = 128
PLE_DIM = 256
EPS = 1e-6
ROPE_THETA = 500000.0

RET_HEADS = 8
RET_DK = 64
RET_DV = 64
RET_THETA = 10000.0
RET_W = RET_HEADS * RET_DV

DSA_HEADS = 8
DSA_HEAD_DIM = 64
DSA_ROPE = DSA_HEAD_DIM // 4
DSA_NOPE = DSA_HEAD_DIM - DSA_ROPE
DSA_LATENT = 128
DSA_VDIM = 64
DSA_W = DSA_HEADS * DSA_VDIM
TOPK_MAX = 256

IDX_HEADS = 8
IDX_DIM = 32
IDX_ROPE = IDX_DIM // 4

MIX_W = RET_W + DSA_W

IN_SPLITS = (RET_HEADS * RET_DK, RET_HEADS * RET_DK, RET_W, RET_W,
             DSA_HEADS * DSA_HEAD_DIM, DSA_LATENT, DSA_ROPE, DSA_W,
             IDX_HEADS * IDX_DIM, IDX_DIM, IDX_HEADS)
IN_WIDTH = sum(IN_SPLITS)


def rms_norm(x, g):
    xf = x.astype(jnp.float32)
    y = xf * lax.rsqrt(jnp.mean(xf * xf, -1, keepdims=True) + EPS)
    return (y * g.astype(jnp.float32)).astype(x.dtype)

def head_group_norm(o, g):
    of = o.astype(jnp.float32)
    mu = jnp.mean(of, -1, keepdims=True)
    var = jnp.mean(jnp.square(of - mu), -1, keepdims=True)
    y = ((of - mu) * lax.rsqrt(var + EPS)).reshape(o.shape[:-2] + (-1,))
    return (y * g.astype(jnp.float32)).astype(o.dtype)

def rotary(x, pos, theta):
    r = x.shape[-1]
    inv = theta ** (-jnp.arange(0, r, 2, dtype=jnp.float32) / r)
    ang = pos.astype(jnp.float32)[:, None] * inv[None, :]
    shape = (ang.shape[0],) + (1,) * (x.ndim - 3) + (r // 2,)
    cos = jnp.cos(ang).reshape(shape)
    sin = jnp.sin(ang).reshape(shape)
    xf = x.astype(jnp.float32)
    x1, x2 = xf[..., : r // 2], xf[..., r // 2:]
    out = jnp.concatenate([x1 * cos - x2 * sin, x2 * cos + x1 * sin], -1)
    return out.astype(x.dtype)

def partial_rotary(x, pos, n_rot, theta):
    return jnp.concatenate([rotary(x[..., :n_rot], pos, theta), x[..., n_rot:]], -1)

def retention(q, k, v):
    B, S, H, dk = q.shape
    dv = v.shape[-1]
    nC = S // CHUNK
    dt = q.dtype
    log_g = jnp.log1p(-jnp.exp2(-5.0 - jnp.arange(H, dtype=jnp.float32)))
    n = jnp.arange(CHUNK, dtype=jnp.float32)
    intra = jnp.exp(log_g[:, None, None] * jnp.abs(n[:, None] - n[None, :]))
    zeta = jnp.exp(log_g[:, None] * (CHUNK - 1 - n)[None, :])
    xi = jnp.exp(log_g[:, None] * (n + 1.0)[None, :])
    chunk_decay = jnp.exp(log_g * CHUNK)[:, None, None]

    qc = q.reshape(B, nC, CHUNK, H, dk) * (dk ** -0.5)
    kc = k.reshape(B, nC, CHUNK, H, dk)
    vc = v.reshape(B, nC, CHUNK, H, dv)

    scores = jnp.einsum('bcnhd,bcmhd->bchnm', qc, kc) * intra.astype(dt)
    o_intra = jnp.einsum('bchnm,bcmhe->bcnhe', scores, vc)

    kv = jnp.einsum('bcmhd,bcmhe,hm->cbhde', kc, vc, zeta.astype(dt)).astype(jnp.float32)

    def step(state, kv_c):
        return chunk_decay * state + kv_c, state

    _, prev = lax.scan(step, jnp.zeros((B, H, dk, dv), jnp.float32), kv)
    o_cross = jnp.einsum('bcnhd,cbhde,hn->bcnhe', qc, prev.astype(dt), xi.astype(dt))
    return (o_intra + o_cross).reshape(B, S, H, dv)

def sparse_attention(q_nope, q_pe, c_kv, k_pe, q_idx, k_idx, w_idx, w_uk, w_uv):
    B, S = c_kv.shape[:2]
    n_sel = min(TOPK_MAX, S // 4)
    n_blk = S // Q_BLOCK
    q_lat = jnp.einsum('bshn,hnc->bshc', q_nope, w_uk)
    key_chunk = jnp.arange(S) // CHUNK
    scale = DSA_HEAD_DIM ** -0.5
    idx_scale = IDX_DIM ** -0.5
    gather = jax.vmap(lambda table, ids: table[ids])

    def to_blocks(a):
        return jnp.moveaxis(a.reshape((B, n_blk, Q_BLOCK) + a.shape[2:]), 1, 0)

    def block(args):
        blk, ql, qp, qi, wi = args
        t = blk * Q_BLOCK + jnp.arange(Q_BLOCK)
        valid = key_chunk[None, :] <= (t // CHUNK)[:, None]
        rel = jax.nn.relu(jnp.einsum('bthd,bsd->bths', qi, k_idx) * idx_scale)
        score = jnp.einsum('bth,bths->bts', wi, rel).astype(jnp.float32)
        score = jnp.where(valid[None], score, -jnp.inf)
        top_val, top_idx = lax.top_k(score, n_sel)
        sel_ok = jnp.isfinite(top_val)
        c_sel = gather(c_kv, top_idx)
        pe_sel = gather(k_pe, top_idx)
        logits = (jnp.einsum('bthc,btkc->bthk', ql, c_sel)
                  + jnp.einsum('bthr,btkr->bthk', qp, pe_sel)).astype(jnp.float32) * scale
        logits = jnp.where(sel_ok[:, :, None, :], logits, -jnp.inf)
        prob = jax.nn.softmax(logits, axis=-1).astype(c_kv.dtype)
        o_lat = jnp.einsum('bthk,btkc->bthc', prob, c_sel)
        return jnp.einsum('bthc,hcd->bthd', o_lat, w_uv)

    out = lax.map(block, (jnp.arange(n_blk), to_blocks(q_lat), to_blocks(q_pe),
                          to_blocks(q_idx), to_blocks(w_idx)))
    return jnp.moveaxis(out, 0, 1).reshape(B, S, DSA_HEADS, DSA_VDIM)

def second_inputs(seed: int = 0) -> dict:
    key = jax.random.key(seed)
    ks = jax.random.split(key, 13)
    f32 = jnp.float32

    def normal(k, shape, scale):
        return jax.random.normal(k, shape, f32) * scale

    def gain(k, shape):
        return 1.0 + 0.01 * jax.random.normal(k, shape, f32)

    return {
        "x": normal(ks[0], (BATCH, SEQ, D_MODEL), 1.0),
        "p": normal(ks[1], (DEPTH, BATCH, SEQ, PLE_DIM), 1.0),
        "positions": jnp.arange(SEQ, dtype=jnp.int32),
        "norm_mix": gain(ks[2], (DEPTH, D_MODEL)),
        "w_in": normal(ks[3], (DEPTH, D_MODEL, IN_WIDTH), D_MODEL ** -0.5),
        "ret_norm": gain(ks[4], (DEPTH, RET_W)),
        "kv_norm": gain(ks[5], (DEPTH, DSA_LATENT)),
        "w_uk": normal(ks[6], (DEPTH, DSA_HEADS, DSA_NOPE, DSA_LATENT), DSA_NOPE ** -0.5),
        "w_uv": normal(ks[7], (DEPTH, DSA_HEADS, DSA_LATENT, DSA_VDIM), DSA_LATENT ** -0.5),
        "w_out": normal(ks[8], (DEPTH, MIX_W, D_MODEL), MIX_W ** -0.5),
        "norm_ple": gain(ks[9], (DEPTH, D_MODEL)),
        "w_ple_gate": normal(ks[10], (DEPTH, D_MODEL, D_MODEL), D_MODEL ** -0.5),
        "w_ple_proj": normal(ks[11], (DEPTH, PLE_DIM, D_MODEL), PLE_DIM ** -0.5),
        "norm_final": gain(ks[12], (D_MODEL,)),
    }

def second_block(x, p, positions, norm_mix, w_in, ret_norm, kv_norm, w_uk, w_uv, w_out,
              norm_ple, w_ple_gate, w_ple_proj, norm_final):
    B, S, _ = x.shape
    split_at = np.cumsum(IN_SPLITS)[:-1].tolist()
    for i in range(DEPTH):
        h = rms_norm(x, norm_mix[i])
        proj = h @ w_in[i]
        (r_q, r_k, r_v, r_g, d_q, d_c, d_pe, d_g,
         i_q, i_k, i_w) = jnp.split(proj, split_at, axis=-1)

        r_q = rotary(r_q.reshape(B, S, RET_HEADS, RET_DK), positions, RET_THETA)
        r_k = rotary(r_k.reshape(B, S, RET_HEADS, RET_DK), positions, RET_THETA)
        r_v = r_v.reshape(B, S, RET_HEADS, RET_DV)
        ret = head_group_norm(retention(r_q, r_k, r_v), ret_norm[i]) * jax.nn.silu(r_g)

        d_q = d_q.reshape(B, S, DSA_HEADS, DSA_HEAD_DIM)
        q_pe = rotary(d_q[..., :DSA_ROPE], positions, ROPE_THETA)
        q_nope = d_q[..., DSA_ROPE:]
        c_kv = rms_norm(d_c, kv_norm[i])
        k_pe = rotary(d_pe, positions, ROPE_THETA)
        q_idx = partial_rotary(i_q.reshape(B, S, IDX_HEADS, IDX_DIM), positions, IDX_ROPE, ROPE_THETA)
        k_idx = partial_rotary(i_k, positions, IDX_ROPE, ROPE_THETA)
        w_idx = i_w * (IDX_HEADS ** -0.5)
        dsa = sparse_attention(q_nope, q_pe, c_kv, k_pe, q_idx, k_idx, w_idx,
                               w_uk[i], w_uv[i]).reshape(B, S, DSA_W) * jax.nn.silu(d_g)

        x = x + jnp.concatenate([ret, dsa], axis=-1) @ w_out[i]

        gate = jax.nn.sigmoid(rms_norm(x, norm_ple[i]) @ w_ple_gate[i])
        x = x + gate * (p[i] @ w_ple_proj[i])
    return rms_norm(x, norm_final)


_first_inputs_2 = second_inputs


def second_inputs(seed=0):
    import zlib

    import numpy as np

    out = dict(_first_inputs_2(seed))
    spreads = {}
    factors = {}
    for name, (base, spread) in spreads.items():
        noise = np.random.default_rng([zlib.crc32(name.encode()), seed]).standard_normal(out[name].shape)
        drawn = base * np.exp(spread * noise) if base else spread * noise
        out[name] = jnp.asarray(drawn.astype(out[name].dtype))
    for name, factor in factors.items():
        out[name] = (out[name] * factor).astype(out[name].dtype)
    return out


_narrow_inputs_2 = second_inputs


def second_inputs(seed=0):

    out = dict(_narrow_inputs_2(seed))
    wider = {'norm_mix': 6.57, 'ret_norm': 12.0, 'kv_norm': 12.0, 'norm_ple': 12.0, 'norm_final': 6.5}
    for name, times in wider.items():
        mean = out[name].mean()
        out[name] = (mean + times * (out[name] - mean)).astype(out[name].dtype)
    return out


def setup_inputs(seed=0):
    out = dict(first_inputs(seed))
    for name, value in second_inputs(seed + 1).items():
        if name != "x":
            out[name + "_2"] = value
    return out


def reference(
    x, c, ctx, c_ctx, w_mod, b_mod, w_in, mlstm_gate_bias, mlstm_norm_w, sgu_ln_w, sgu_ln_b,
    sgu_w, sgu_b, conv_w, conv_b, conv_ln_w, conv_ln_b, s5_a_re, s5_a_im, s5_log_dt, s5_b_re,
    s5_b_im, s5_c_re, s5_c_im, s5_d, s5_glu_w, s5_glu_b, w_out, ln1_w, ln1_b, w_ffn_in,
    w_ffn_out, ln2_w, ln2_b, p_2, positions_2, norm_mix_2, w_in_2, ret_norm_2, kv_norm_2,
    w_uk_2, w_uv_2, w_out_2, norm_ple_2, w_ple_gate_2, w_ple_proj_2, norm_final_2,
):
    x = first_block(
        x, c, ctx, c_ctx, w_mod, b_mod, w_in, mlstm_gate_bias, mlstm_norm_w, sgu_ln_w, sgu_ln_b,
        sgu_w, sgu_b, conv_w, conv_b, conv_ln_w, conv_ln_b, s5_a_re, s5_a_im, s5_log_dt,
        s5_b_re, s5_b_im, s5_c_re, s5_c_im, s5_d, s5_glu_w, s5_glu_b, w_out, ln1_w, ln1_b,
        w_ffn_in, w_ffn_out, ln2_w, ln2_b,
    )
    return second_block(
        x, p_2, positions_2, norm_mix_2, w_in_2, ret_norm_2, kv_norm_2, w_uk_2, w_uv_2, w_out_2,
        norm_ple_2, w_ple_gate_2, w_ple_proj_2, norm_final_2,
    )


_drawn_inputs = setup_inputs


def setup_inputs(seed=0):
    import zlib

    import numpy as np

    out = dict(_drawn_inputs(seed))
    spreads = {}
    factors = {'s5_glu_b': 8.0,
     'norm_mix_2': 7.404,
     'ret_norm_2': 8.0,
     'kv_norm_2': 8.0,
     'w_uk_2': 5.832,
     'norm_ple_2': 64.0,
     'p_2': 3.643,
     'w_ple_gate_2': 5.474,
     'w_ple_proj_2': 3.646}
    for name, (base, spread) in spreads.items():
        noise = np.random.default_rng([zlib.crc32(name.encode()), seed]).standard_normal(out[name].shape)
        drawn = base * np.exp(spread * noise) if base else spread * noise
        out[name] = jnp.asarray(drawn.astype(out[name].dtype))
    for name, factor in factors.items():
        out[name] = (out[name] * factor).astype(out[name].dtype)
    return out
```

```python
import math

import numpy as np

import concourse.bass as bass
from concourse import mybir

F32 = mybir.dt.float32
I32 = mybir.dt.int32
ALU = mybir.AluOpType
ACT = mybir.ActivationFunctionType
AX = mybir.AxisListType

P = 128
T = 1024
TC = 256
D = 1024
KT = D // P
NT = T // P
NCT = TC // P
W = 256
HALF = 512
HEADS, HD = 4, 64
LN_EPS = 1e-5
RMS_EPS = 1e-6
DFF = 2816
NF = DFF // P
ALPHA = 2.0 ** 0.25
OFF_B = 4 * W + 16
OFF_C = OFF_B + 2 * W
OFF_D = OFF_C + 2 * W
CONV, PAD, GRID = 31, 15, 64
ROWS = T // GRID
G16, SP, SN, SC = 16, 16, 64, 8
GP = G16 // 2
NCH, NCC = T // SC, TC // SC
NCA = NCH + NCC
LOW = -1.0e30
MAGIC = 1.5 * 2.0 ** 23
LOG2E = 1.4426950408889634
LN2_HI, LN2_LO = 0.693359375, -2.12194440054690583e-4
INV_2PI = 1.0 / (2.0 * math.pi)
TWO_PI_1 = 6.28125
TWO_PI_2 = float(np.float32(round((2.0 * math.pi - TWO_PI_1) * 2 ** 20) / 2 ** 20))
TWO_PI_3 = 2.0 * math.pi - TWO_PI_1 - TWO_PI_2
PI_IN = 3.1415925


RH, RD = 8, 64
RCHUNK = 64
AH, AD = 8, 64
PE_D, NOPE, LAT = 16, 48, 128
IH, IDIM, IROT = 8, 32, 8
TOPK = 256
FREQ_R, FREQ_A, FREQ_I = RD // 2, PE_D // 2, IROT // 2
NFREQ = FREQ_R + FREQ_A + FREQ_I
C_LAT = 5 * HALF
C_GATE = C_LAT + LAT + PE_D
C_IDX = C_GATE + HALF
N_IDX = IH * IDIM + IDIM + IH
M_PE, M_IQ = LAT, LAT + PE_D
M_IK = M_IQ + IH * IDIM
M_IW = M_IK + IDIM
N_MIX = M_IW + IH


def constants():
    def freq(theta, r):
        return theta ** (-np.arange(0, r, 2, dtype=np.float64) / r)

    log_g = np.log1p(-np.exp2(-5.0 - np.arange(RH)))
    n = np.arange(P)
    gap, chunk = n[None, :] - n[:, None], n // RCHUNK
    seen = chunk[None, :] >= chunk[:, None]
    intra = np.exp(log_g[:, None, None] * np.abs(gap)) * seen * RD ** -0.5
    pair = np.repeat(np.arange(2), RD)
    head = 2 * np.arange(RH // 2)[None, :] + pair[:, None]
    return {
        "freq": np.concatenate([freq(10000.0, RD), freq(500000.0, PE_D), freq(500000.0, IROT)])[None].astype(np.float32),
        "intra": intra.transpose(1, 0, 2).astype(np.float32),
        "xi": (np.exp(log_g[head][:, :, None] * (n + 1.0)) * RD ** -0.5).astype(np.float32),
        "zeta": np.exp(log_g[None, :] * (P - 1.0 - n)[:, None]).astype(np.float32),
        "decay": np.exp(log_g[head] * P).astype(np.float32),
    }


class Kept:

    def __init__(self, nc, I, out):
        self.nc, self.I, self.out = nc, I, out


class Link:

    def __init__(self, eng, sem):
        self.eng, self.sem, self.n = eng, sem, 0

    def __call__(self, ins):
        self.n += 1
        ins.then_inc(self.sem, 1)
        self.eng.wait_ge(self.sem, self.n)


def setup(nc, I, out):
    K = Kept(nc, I, out)
    K.ps = nc.alloc_psum_tensor("ps", [P, 8, HALF], F32)
    K.bank = [K.ps[:, i, :] for i in range(8)]
    K.ident = nc.alloc_sbuf_tensor("ident", [P, P], F32)
    K.ones = nc.alloc_sbuf_tensor("ones", [P, P], F32)
    K.prm = nc.alloc_sbuf_tensor("prm", [P, 1152], F32)
    K.wsT = nc.alloc_sbuf_tensor("wsT", [P, 4, P], F32)
    K.base = 24 * 1024
    K.sems = []

    def at(name, kb, shape, dt=F32):
        return nc.alloc_sbuf_tensor_at(name, shape, dt, offset=K.base + int(kb * 1024))

    def sem(name):
        K.sems.append(nc.alloc_semaphore(name))
        return K.sems[-1]

    K.at, K.sem = at, sem
    K.MOD = at("MOD", 0, [P, 6 * D])
    K.HT = at("HT", 24, [P, KT, TC + T])
    K.ydT = at("ydT", 64, [P, 2, T])
    K.HTP = at("HTP", 64, [P, KT, TC])
    K.yT = [at(f"yT{k}", 24 + 4 * k, [P, T]) for k in range(6)] + [K.ydT[:, k, :] for k in range(2)]
    return K


def stage_modulate(K):
    nc, I = K.nc, K.I
    NS, NCK, NCX = 4, 12, 4
    ring = [K.at(f"mod_w{s}", 72 + 16 * s, [P, KT, HALF]) for s in range(NS)]
    brow = K.at("mod_b", 136, [1, NS, HALF])
    cols = K.at("mod_c", 144, [P, 2, KT])
    cb = K.at("mod_cb", 145, [P, 2, KT, P])
    MODC = K.at("MODC", 153, [P, NCX * HALF])
    xr = [K.at(f"mod_x{s}", 161 + 4 * s, [P, D]) for s in range(3)]
    hb = [K.at(f"mod_h{s}", 173 + 4 * s, [P, D]) for s in range(2)]
    c_in, c_act, c_bc = K.sem("c_in"), K.sem("c_act"), K.sem("c_bc")
    consts = K.sem("consts")
    w_in = [K.sem(f"modw_in{s}") for s in range(NS)]
    mod_mm, mod_ev, ctx_mm, ctx_ev = K.sem("mod_mm"), K.sem("mod_ev"), K.sem("ctx_mm"), K.sem("ctx_ev")
    x_in = [K.sem(f"modx_in{s}") for s in range(3)]
    h_mul, h_rdy, h_tr, h_ev = K.sem("h_mul"), K.sem("h_rdy"), K.sem("h_tr"), K.sem("h_ev")
    w_mod = I["w_mod"][0].rearrange("(p t) n -> p t n", t=KT)
    tiles = NCT + NT

    def src(i):
        return I["ctx"][0][i * P:(i + 1) * P, :] if i < NCT else I["x"][0][(i - NCT) * P:(i - NCT + 1) * P, :]

    with nc.Block() as block:
        @block.sync
        def _(sp):
            sp.dma_start(cols[:, 0, :], I["c"][0].rearrange("(p t) -> p t", t=KT)).then_inc(c_in, 16)
            sp.dma_start(cols[:, 1, :], I["c_ctx"].rearrange("(p t) -> p t", t=KT)).then_inc(c_in, 16)
            for s in range(NS):
                sp.dma_start(ring[s][:], w_mod[:, :, s * HALF:(s + 1) * HALF]).then_inc(w_in[s], 16)
                sp.dma_start(brow[:, s, :], I["b_mod"][:, s * HALF:(s + 1) * HALF]).then_inc(w_in[s], 16)
            with sp.Fori(1, NCK // NS) as r:
                for s in range(NS):
                    sp.wait_ge(mod_mm, NS * r + s - (NS - 1))
                    sp.dma_start(ring[s][:], w_mod[:, :, bass.ds(r * (NS * HALF) + s * HALF, HALF)]).then_inc(w_in[s], 16)
                    sp.dma_start(brow[:, s, :], I["b_mod"][:, bass.ds(r * (NS * HALF) + s * HALF, HALF)]).then_inc(w_in[s], 16)

        @block.gpsimd
        def _(pool):
            nc.gpsimd.memset(K.ident[:], 0.0).then_inc(consts, 1)
            nc.gpsimd.memset(K.ones[:], 1.0).then_inc(consts, 1)
            pool.wait_ge(consts, 2)
            nc.gpsimd.affine_select(out=K.ident[:], in_=K.ident[:], compare_op=ALU.not_equal, fill=1.0, base=0,
                                    pattern=[[-1, P]], channel_multiplier=1).then_inc(consts, 1)
            for i in range(tiles):
                if i >= 3:
                    pool.wait_ge(h_rdy, i - 2)
                pool.dma_start(xr[i % 3][:], src(i)).then_inc(x_in[i % 3], 16)

        @block.scalar
        def _(act):
            act.wait_ge(c_in, 32)
            nc.scalar.activation(cols[:], cols[:], ACT.Silu).then_inc(c_act, 1)

            def evacuate(j, col):
                act.wait_ge(mod_mm, j + 1)
                nc.scalar.activation(K.MOD[:, col], K.bank[j % 2][:], ACT.Copy).then_inc(mod_ev, 1)

            for j in range(NCX):
                act.wait_ge(ctx_mm, j + 1)
                nc.scalar.activation(MODC[:, j * HALF:(j + 1) * HALF], K.bank[2 + j % 2][:], ACT.Copy).then_inc(ctx_ev, 1)
                evacuate(j, slice(j * HALF, (j + 1) * HALF))
            for i in range(tiles):
                act.wait_ge(h_tr, i + 1)
                for b in range(2):
                    nc.scalar.activation(K.HT[:, 4 * b:4 * b + 4, i * P:(i + 1) * P],
                                         K.bank[4 + 2 * (i % 2) + b][:].rearrange("p (k t) -> p k t", k=4),
                                         ACT.Copy).then_inc(h_ev, 1)
                    if i < NCT:
                        nk = P // SC
                        for k in range(4):
                            nc.scalar.activation(K.HTP[:, 4 * b + k, :].rearrange("p (s c) -> p c s", s=SC)[:, i * nk:(i + 1) * nk, :],
                                                 K.bank[4 + 2 * (i % 2) + b][:, k * P:(k + 1) * P].rearrange("p (c s) -> p c s", s=SC),
                                                 ACT.Copy).then_inc(h_ev, 1)
            with act.Fori(1, NCK // NS) as r:
                for s in range(NS):
                    act.wait_ge(mod_mm, NS * r + s + 1)
                    nc.scalar.activation(K.MOD[:, bass.ds(r * (NS * HALF) + s * HALF, HALF)], K.bank[s % 2][:],
                                         ACT.Copy).then_inc(mod_ev, 1)

        @block.vector
        def _(dve):
            dve.wait_ge(c_act, 1)
            nc.vector.tensor_copy(cb[:], cols[:].unsqueeze(3).to_broadcast([P, 2, KT, P])).then_inc(c_bc, 1)
            dve.wait_ge(ctx_ev, NCX)
            dve.wait_ge(mod_ev, NCX)
            for i in range(tiles):
                m = MODC if i < NCT else K.MOD
                dve.wait_ge(x_in[i % 3], 16 * (i // 3 + 1))
                if i >= 2:
                    dve.wait_ge(h_tr, i - 1)
                nc.vector.scalar_tensor_tensor(out=hb[i % 2][:], in0=m[:, D:2 * D], scalar=1.0, in1=xr[i % 3][:],
                                               op0=ALU.add, op1=ALU.mult).then_inc(h_mul, 1)
                dve.wait_ge(h_mul, i + 1)
                nc.vector.tensor_tensor(hb[i % 2][:], hb[i % 2][:], m[:, 0:D], ALU.add).then_inc(h_rdy, 1)

        @block.tensor
        def _(pe):
            pe.wait_ge(c_bc, 1)
            pe.wait_ge(consts, 3)

            def product(bank, which, s, done):
                for k in range(KT):
                    nc.tensor.matmul(bank[:], cb[:, which, k, :], ring[s][:, k, :], start=(k == 0), stop=False)
                nc.tensor.matmul(bank[:], K.ones[0:1, :], brow[:, s, :], start=False, stop=True).then_inc(done, 1)

            for j in range(NCX):
                pe.wait_ge(w_in[j], 32)
                if j >= 2:
                    pe.wait_ge(ctx_ev, j - 1)
                    pe.wait_ge(mod_ev, j - 1)
                product(K.bank[2 + j % 2], 1, j, ctx_mm)
                product(K.bank[j % 2], 0, j, mod_mm)
            for i in range(tiles):
                pe.wait_ge(h_rdy, i + 1)
                if i >= 2:
                    pe.wait_ge(h_ev, 2 * (i - 1) + 8 * min(i - 1, NCT))
                for k in range(KT):
                    tr = nc.tensor.transpose(K.bank[4 + 2 * (i % 2) + k // 4][:, (k % 4) * P:(k % 4 + 1) * P],
                                             hb[i % 2][:, k * P:(k + 1) * P], K.ident[:])
                tr.then_inc(h_tr, 1)
            with pe.Fori(1, NCK // NS) as r:
                for s in range(NS):
                    pe.wait_ge(w_in[s], 32 * r + 32)
                    pe.wait_ge(mod_ev, NS * r + s - 1)
                    product(K.bank[s % 2], 0, s, mod_mm)


def cmul(nc, link, out_r, out_i, a_r, a_i, b_r, b_i, t, u, conj=False):
    v = link.eng
    v.tensor_tensor(t, a_r, b_i, ALU.mult)
    link(v.tensor_tensor(u, a_i, b_i, ALU.mult))
    v.tensor_tensor(out_r, a_r, b_r, ALU.mult)
    link(v.tensor_tensor(out_i, a_i, b_r, ALU.mult))
    v.tensor_tensor(out_r, out_r, u, ALU.add if conj else ALU.subtract)
    link(v.tensor_tensor(out_i, out_i, t, ALU.subtract if conj else ALU.add))


def exp_exact(nc, link, dst, x, k, r, ki):
    v = nc.vector
    link(v.tensor_scalar(x, x, -87.0, 88.0, ALU.max, ALU.min))
    link(v.tensor_scalar(k, x, LOG2E, MAGIC, ALU.mult, ALU.add))
    link(v.tensor_scalar(k, k, MAGIC, None, ALU.subtract))
    link(v.scalar_tensor_tensor(out=r, in0=k, scalar=-LN2_HI, in1=x, op0=ALU.mult, op1=ALU.add))
    link(v.scalar_tensor_tensor(out=r, in0=k, scalar=-LN2_LO, in1=r, op0=ALU.mult, op1=ALU.add))
    link(v.tensor_scalar(dst, r, 1.0 / 5040, None, ALU.mult))
    for c in (1.0 / 720, 1.0 / 120, 1.0 / 24, 1.0 / 6, 0.5, 1.0):
        link(v.scalar_tensor_tensor(out=dst, in0=dst, scalar=c, in1=r, op0=ALU.add, op1=ALU.mult))
    link(v.tensor_scalar(k, k, 127.0, None, ALU.add))
    link(v.tensor_copy(ki, k))
    link(v.tensor_scalar(ki, ki, 23, None, ALU.logical_shift_left))
    link(v.scalar_tensor_tensor(out=dst, in0=dst, scalar=1.0, in1=ki.bitcast(F32), op0=ALU.add, op1=ALU.mult))


def reduce_angle(nc, link, r, quarter, x, k):
    v = nc.vector
    link(v.tensor_scalar(k, x, INV_2PI, MAGIC, ALU.mult, ALU.add))
    link(v.tensor_scalar(k, k, MAGIC, None, ALU.subtract))
    link(v.scalar_tensor_tensor(out=r, in0=k, scalar=-TWO_PI_1, in1=x, op0=ALU.mult, op1=ALU.add))
    for c in (TWO_PI_2, TWO_PI_3):
        link(v.scalar_tensor_tensor(out=r, in0=k, scalar=-c, in1=r, op0=ALU.mult, op1=ALU.add))
    link(v.tensor_scalar(r, r, -PI_IN, PI_IN, ALU.max, ALU.min))
    link(v.scalar_tensor_tensor(out=quarter, in0=r, scalar=-1.0, in1=r, op0=ALU.mult, op1=ALU.max))
    link(v.tensor_scalar(quarter, quarter, -1.0, math.pi / 2, ALU.mult, ALU.add))


def stage_s5(K):
    nc, I = K.nc, K.I
    wd = K.at("s5_wd", 72, [P, KT, W])
    d8 = K.at("s5_d8", 80, [P, G16, SC, SP])
    d8c = K.at("s5_d8c", 166, [NCC, SC, W])
    d8g = K.at("s5_d8g", 88, [NCC, G16, SC, SP])
    HB = K.at("s5_HB", 154, [P, 2, GP, NCH])
    ys = K.at("s5_ys", 146, [P, SC, W])
    dcx = K.at("s5_dcx", 96, [P, 2, W])
    glu = K.at("s5_glu", 96, [P, 2, W])
    U8 = K.at("s5_U8", 98, [P, G16, NCA])
    CA = K.at("s5_CA", 108, [P, 2, 2, GP, 9, SP])
    AB = K.at("s5_AB", 126, [P, 2, 2, GP, SC, SP])
    X = K.at("s5_X", 126, [P, 2, 2 * GP, NCA])
    scr = K.at("s5_scr", 146, [P, 2, GP * 9 * SP])
    TAB = K.at("s5_TAB", 146, [P, 2, 2 * GP, NCA])
    ABT = K.at("s5_ABT", 166, [P, 2, GP, 2, P])
    tmp = K.at("s5_tmp", 166, [P, 2, 2 * GP, NCA])
    ptmp = K.at("s5_ptmp", 186, [P, 2, 2 * GP, NCA // 2 - 16])
    yDT = K.at("s5_yDT", 166, [P, 2, T])
    sg = K.at("s5_sg", 174, [P, 2, T])
    Tz = K.at("s5_T", 186, [P, G16, P])
    Cn = K.at("s5_Cn", 186, [P, 2, 2, 2, SN])
    KL = K.at("s5_KL", 64, [SP, G16, 15 * SP])
    Bm = K.at("s5_B", 194, [P, 2, GP, SP])
    Cm = K.at("s5_C", 195, [P, 2, GP, SP])
    BB = K.at("s5_BB", 196, [P, 2, 2, GP, SP])
    Dr = K.at("s5_D", 198, [P, W])
    araw = K.prm[0:2 * GP, 0:3 * P].rearrange("p (a n) -> p a n", a=3)
    used = [3 * P]

    def columns(n, dt=F32):
        used[0] += n
        c = K.prm[:, used[0] - n:used[0]]
        return c if dt == F32 else c.bitcast(dt)

    N2 = 2 * GP
    par = columns(3 * N2).rearrange("p (a j) -> p a j", a=3)
    ang = columns(2 * N2).rearrange("p (a j) -> p a j", a=2)
    red, quar, kk, sn, cs = (columns(2 * N2).rearrange("p (a j) -> p a j", a=2) for _ in range(5))
    dt_c, er, k1, r1, fr, fi, den, tc, uc = (columns(N2) for _ in range(9))
    ki = columns(N2, I32)
    pw = columns(2 * 9 * N2).rearrange("p (c e j) -> p c e j", c=2, e=9)
    rot = columns(2 * N2).rearrange("p (c j) -> p c j", c=2)
    gb = columns(2)
    ldt = columns(2)
    pt = columns(2 * N2).rearrange("p (c j) -> p c j", c=2)
    s5_in, d_in, g_in = K.sem("s5_in"), K.sem("s5_d_in"), K.sem("s5_glu_in")
    mm, ev = K.sem("s5_mm"), K.sem("s5_ev")
    dg_rdy = K.sem("s5_dg")
    ldt_x, par_t, prm_rdy, c_rdy, sin_in, sin_out = (K.sem(f"s5_{n}") for n in ("ldtx", "part", "prm", "crdy", "sinin", "sinout"))
    ab_rdy, tab_rdy, t_in, h_rdy, y_mm, y_ev, y_act = (K.sem(f"s5_{n}") for n in ("ab", "tab", "tin", "h", "ymm", "yev", "yact"))
    yt_mm, yt_ev, g_mm, g_sg, chain, pchain = (K.sem(f"s5_{n}") for n in ("ytmm", "ytev", "gmm", "gsg", "chain", "pchain"))
    N_D, N_U, N_AB, N_X, N_KL = 5, 8, 8, 16, 8
    at_u, at_ab, at_x, at_kl, at_end = (int(v) for v in np.cumsum([N_D, N_U, N_AB, N_X, N_KL]))
    NB = 6

    def bank(n):
        return K.bank[2 + n % NB]

    with nc.Block() as block:
        @block.sync
        def _(sp):
            sp.dma_start(wd[:], I["w_in"][0].rearrange("(k p) n -> p k n", p=P)[:, :, OFF_D:OFF_D + W]).then_inc(s5_in, 16)
            for a, name in enumerate(("s5_a_re", "s5_a_im")):
                sp.dma_start(araw[:, a, :], I[name][0].rearrange("d (j h) n -> (d j) (h n)", h=2)).then_inc(s5_in, 16)
            sp.dma_start(ldt[0:N2, :], I["s5_log_dt"][0].rearrange("d (j h) -> (d j) h", h=2)).then_inc(s5_in, 16)
            for a, name in enumerate(("s5_b_re", "s5_b_im")):
                sp.dma_start(Bm[:, a], I[name][0].rearrange("(j h) n p -> (h n) j p", h=2)).then_inc(s5_in, 16)
            for a, name in enumerate(("s5_c_re", "s5_c_im")):
                for dup in range(2):
                    sp.dma_start(Cn[:, a, :, dup, :], I[name][0].rearrange("(t g) p n -> (g p) t n", t=2)).then_inc(s5_in, 16)
            sp.dma_start(Dr[:], I["s5_d"].to_broadcast([P, W])).then_inc(s5_in, 16)
            with nc.allow_non_contiguous_dma(reason="a bias as a column"):
                sp.dma_start(gb[:], I["s5_glu_b"][0].rearrange("(k p) -> p k", p=P)).then_inc(s5_in, 16)
            sp.wait_ge(ev, N_D)
            for s in range(SC):
                sp.dma_start(d8c[:, s, :], dcx[(s % 4) * NCC:(s % 4 + 1) * NCC, s // 4, :]).then_inc(d_in, 16)
            sp.wait_ge(d_in, 16 * SC)
            sp.dma_start(glu[:], I["s5_glu_w"][0].rearrange("(k p) n -> p k n", p=P)).then_inc(g_in, 16)
            sp.wait_ge(ev, at_end)
            sp.wait_ge(tab_rdy, 1)
            for s in range(SC):
                sp.dma_start(Tz[s * SP:(s + 1) * SP, :, :], KL[:, :, (7 - s) * SP:(15 - s) * SP]).then_inc(t_in, 16)

        @block.tensor
        def _(pe):
            n = 0

            def load(n):
                if n >= NB:
                    pe.wait_ge(ev, n - NB + 1)

            pe.wait_ge(s5_in, 16 * 12)
            for q in range(4):
                load(n)
                for s in (2 * q, 2 * q + 1):
                    for k in range(KT):
                        last = nc.tensor.matmul(bank(n)[:, (s % 2) * W:(s % 2 + 1) * W], K.HT[:, k, TC + s::SC], wd[:, k, :],
                                                start=(k == 0), stop=(k == KT - 1))
                last.then_inc(mm, 1)
                n += 1
            for h in range(2):
                for k in range(KT):
                    last = nc.tensor.matmul(bank(n)[:, h * W:(h + 1) * W],
                                            K.HTP[:, k, h * P:(h + 1) * P],
                                            wd[:, k, :], start=(k == 0), stop=(k == KT - 1))
            last.then_inc(mm, 1)
            n += 1
            pe.wait_ge(ldt_x, 1)
            for a in range(3):
                last = nc.tensor.transpose(K.bank[0][:, a * N2:(a + 1) * N2], araw[:, a, :], K.ident[0:N2, 0:N2])
            for a in range(2):
                for h in range(2):
                    last = nc.tensor.transpose(K.bank[1][:, (2 * a + h) * P:(2 * a + h + 1) * P],
                                               Cn[:, a, h, :, :], K.ident[:])
            last.then_inc(par_t, 1)
            pe.wait_ge(ev, N_D)
            pe.wait_ge(dg_rdy, 1)
            for q in range(N_U):
                load(n)
                for j in range(2):
                    g = 2 * q + j
                    nc.tensor.transpose(bank(n)[:, j * NCA:j * NCA + NCC], d8g[:, g, :, :], K.ident[0:NCC, 0:NCC])
                    last = nc.tensor.transpose(bank(n)[:, j * NCA + NCC:(j + 1) * NCA], d8[:, g, :, :], K.ident[:])
                last.then_inc(mm, 1)
                n += 1
            pe.wait_ge(ab_rdy, 1)
            for q in range(N_AB):
                load(n)
                for r in range(4):
                    d, j, c = (4 * q + r) // (2 * GP), (4 * q + r) // 2 % GP, r % 2
                    last = nc.tensor.transpose(bank(n)[:, r * P:(r + 1) * P], AB[:, d, c, j, :, :], K.ident[:])
                last.then_inc(mm, 1)
                n += 1
            for q in range(N_X):
                if q == 0:
                    pe.wait_ge(ev, at_ab)
                load(n)
                d, j = q // GP, q % GP
                for c in range(2):
                    for h in range(2):
                        last = nc.tensor.matmul(bank(n)[h * SN:(h + 1) * SN, c * NCA:(c + 1) * NCA],
                                                ABT[:, d, j, c, h * SN:(h + 1) * SN], U8[:, 2 * j + h, :], start=True, stop=True)
                last.then_inc(mm, 1)
                n += 1
            for q in range(N_KL):
                load(n)
                h, row = q % 2, slice(q % 2 * SN, (q % 2 + 1) * SN)
                for i2 in range(2):
                    j = q // 2 * 2 + i2
                    o = bank(n)[0:SP, i2 * 15 * SP:(i2 + 1) * 15 * SP]
                    parts = [(o[:, 7 * SP:8 * SP], [(0, 0), (1, 8)], 1), (o[:, 8 * SP:], [(0, 1)], 7), (o[:, :7 * SP], [(1, 1)], 7)]
                    for dst, terms, ne in parts:
                        for i, (d, e) in enumerate(terms):
                            for c in range(2):
                                last = nc.tensor.matmul(dst, BB[row, d, c, j, :], CA[row, d, c, j, e:e + ne, :],
                                                        start=(i == 0 and c == 0), stop=(i == len(terms) - 1 and c == 1))
                last.then_inc(mm, 1)
                n += 1
            pe.wait_ge(t_in, 16 * SC)
            pe.wait_ge(h_rdy, 1)
            for q in range(4):
                for r in range(4):
                    j, h = q // 2 * 4 + r, q % 2
                    g, row = 2 * j + h, slice(h * SN, (h + 1) * SN)
                    o = K.bank[2 + q][:, r * P:(r + 1) * P]
                    nc.tensor.matmul(o, U8[:, g, NCC:], Tz[:, g, :], start=True, stop=False)
                    for d in range(2):
                        for c in range(2):
                            st = X[row, c, d * GP + j, NCC - 1:NCA - 1] if d == 0 else HB[row, c, j, :]
                            last = nc.tensor.matmul(o, st, CA[row, d, c, j, 1 - d:9 - d, :], start=False, stop=(d == 1 and c == 1))
                last.then_inc(y_mm, 1)
            pe.wait_ge(y_act, 1)
            for q in range(4):
                if q >= 2:
                    pe.wait_ge(yt_ev, q - 1)
                for r in range(4):
                    last = nc.tensor.transpose(K.bank[6 + q % 2][:, r * P:(r + 1) * P],
                                               ys[:, 4 * (q % 2) + r, (q // 2) * P:(q // 2 + 1) * P], K.ident[:])
                last.then_inc(yt_mm, 1)
            pe.wait_ge(yt_ev, 4)
            pe.wait_ge(g_in, 16)
            for m in range(2):
                for h in range(2):
                    for k in range(2):
                        last = nc.tensor.matmul(K.bank[2 + 2 * m + h][:], glu[:, k, m * P:(m + 1) * P], yDT[:, k, h * HALF:(h + 1) * HALF],
                                                start=(k == 0), stop=(k == 1))
                    last.then_inc(g_mm, 1)

        @block.scalar
        def _(act):
            n = 0

            def take(dst, src, last=True):
                ins = nc.scalar.activation(dst, src, ACT.Copy)
                if last:
                    ins.then_inc(ev, 1)

            for q in range(4):
                act.wait_ge(mm, n + 1)
                for s in range(2):
                    take(d8[:, :, 2 * q + s, :], bank(n)[:, s * W:(s + 1) * W].rearrange("p (g o) -> p g o", g=G16), last=(s == 1))
                n += 1
            act.wait_ge(mm, n + 1)
            take(dcx[:], bank(n)[:].rearrange("p (h n) -> p h n", h=2))
            n += 1
            for q in range(N_U):
                act.wait_ge(mm, n + 1)
                take(U8[:, 2 * q:2 * q + 2, :], bank(n)[:, 0:2 * NCA].rearrange("p (g c) -> p g c", g=2))
                n += 1
            act.wait_ge(sin_in, 1)
            nc.scalar.activation(sn[:], red[:], ACT.Sin).then_inc(sin_out, 1)
            nc.scalar.activation(cs[:], quar[:], ACT.Sin).then_inc(sin_out, 1)
            for q in range(N_AB):
                act.wait_ge(mm, n + 1)
                d, j = 4 * q // (2 * GP), 2 * q % GP
                take(ABT[:, d, j:j + 2, :, :], bank(n)[:].rearrange("p (j c n) -> p j c n", j=2, c=2))
                n += 1
            for q in range(N_X):
                act.wait_ge(mm, n + 1)
                src = bank(n)[:, 0:2 * NCA].rearrange("p (c n) -> p c n", c=2)
                if q < GP:
                    take(X[:, :, q, :], src)
                else:
                    take(X[:, :, q, 0:NCC], src[:, :, NCC - 1::-1], last=False)
                    take(X[:, :, q, NCC:], src[:, :, :NCC - 1:-1])
                n += 1
            for q in range(N_KL):
                act.wait_ge(mm, n + 1)
                take(KL[:, q // 2 * 4 + q % 2:q // 2 * 4 + 4:2, :], bank(n)[0:SP, 0:30 * SP].rearrange("p (h l) -> p h l", h=2))
                n += 1
            act.wait_ge(y_ev, 4)
            nc.scalar.activation(ys[:], ys[:], ACT.Gelu_apprx_tanh).then_inc(y_act, 1)
            for q in range(4):
                act.wait_ge(yt_mm, q + 1)
                nc.scalar.activation(yDT[:, q // 2, :].rearrange("p (c s) -> p s c", s=SC)[:, 4 * (q % 2):4 * (q % 2) + 4, :],
                                     K.bank[6 + q % 2][:].rearrange("p (s c) -> p s c", s=4), ACT.Copy).then_inc(yt_ev, 1)
            for q in range(4):
                act.wait_ge(g_mm, q + 1)
                nc.scalar.activation(sg[:, q // 2, (q % 2) * HALF:(q % 2 + 1) * HALF], K.bank[2 + q][:], ACT.Sigmoid,
                                     bias=gb[:, q // 2:q // 2 + 1]).then_inc(g_sg, 1)

        @block.gpsimd
        def _(pool):
            pool.wait_ge(d_in, 16 * SC)
            nc.gpsimd.tensor_copy(d8g[:].rearrange("c g s o -> c s g o"), d8c[:].rearrange("c s (g o) -> c s g o", g=G16)).then_inc(dg_rdy, 1)
            link = Link(nc.gpsimd, pchain)
            pool.wait_ge(ab_rdy, 1)
            link(nc.gpsimd.memset(TAB[:, 0, :, 0:1], 1.0))
            link(nc.gpsimd.memset(TAB[:, 1, :, 0:1], 0.0))
            n = 1
            while n < NCA:
                m = min(n, NCA - n)
                turn = [rot[:, c, :].unsqueeze(2).to_broadcast([P, N2, m]) for c in range(2)]
                t, u = ptmp[:, 0, :, 0:m], ptmp[:, 1, :, 0:m]
                cmul(nc, link, TAB[:, 0, :, n:n + m], TAB[:, 1, :, n:n + m], TAB[:, 0, :, 0:m], TAB[:, 1, :, 0:m],
                     turn[0], turn[1], t, u)
                n += m
                if n < NCA:
                    cmul(nc, link, pt[:, 0, :], pt[:, 1, :], rot[:, 0, :], rot[:, 1, :], rot[:, 0, :], rot[:, 1, :], tc[:], uc[:])
                    link(nc.gpsimd.tensor_copy(rot[:], pt[:]))
            pool.sem_inc(tab_rdy, 1)

        @block.vector
        def _(dve):
            link = Link(nc.vector, chain)
            v = nc.vector
            dve.wait_ge(s5_in, 16 * 12)
            v.tensor_copy(araw[:, 2, :].rearrange("p (h n) -> p h n", h=2),
                          ldt[0:N2, :].unsqueeze(2).to_broadcast([N2, 2, SN])).then_inc(ldt_x, 1)
            dve.wait_ge(par_t, 1)
            link(v.tensor_copy(par[:], K.bank[0][:, 0:3 * N2].rearrange("p (a j) -> p a j", a=3)))
            for h in range(2):
                link(v.tensor_copy(Cm[h * SN:(h + 1) * SN].rearrange("p c (t g) o -> p (c t) g o", t=2),
                                   K.bank[1][h * SN:(h + 1) * SN, :].rearrange("p (a g h o) -> p a g h o", a=4, g=4, h=2)[:, :, :, h, :]))
            a_re, a_im = par[:, 0, :], par[:, 1, :]
            exp_exact(nc, link, dt_c[:], par[:, 2, :], k1[:], r1[:], ki[:])
            link(v.tensor_tensor(ang[:, 0, :], a_im, dt_c[:], ALU.mult))
            link(v.tensor_scalar(ang[:, 1, :], ang[:, 0, :], float(SC), None, ALU.mult))
            reduce_angle(nc, link, red[:], quar[:], ang[:], kk[:])
            link(v.tensor_tensor(dt_c[:], a_re, dt_c[:], ALU.mult))
            dve.sem_inc(sin_in, 1)
            exp_exact(nc, link, er[:], dt_c[:], k1[:], r1[:], ki[:])
            dve.wait_ge(sin_out, 2)
            link(v.memset(pw[:, 0, 0, :], 1.0))
            link(v.memset(pw[:, 1, 0, :], 0.0))
            link(v.tensor_tensor(pw[:, 0, 1, :], er[:], cs[:, 0, :], ALU.mult))
            link(v.tensor_tensor(pw[:, 1, 1, :], er[:], sn[:, 0, :], ALU.mult))
            for lo, n, by in ((2, 1, 1), (3, 2, 2), (5, 4, 4)):
                q = [pw[:, c, by, :].unsqueeze(1).to_broadcast([P, n, N2]) for c in range(2)]
                t, u = (scr[:, i, 0:n * N2].rearrange("p (e j) -> p e j", e=n) for i in range(2))
                cmul(nc, link, pw[:, 0, lo:lo + n, :], pw[:, 1, lo:lo + n, :], pw[:, 0, 1:1 + n, :], pw[:, 1, 1:1 + n, :],
                     q[0], q[1], t, u)
            for _ in range(3):
                link(v.tensor_tensor(er[:], er[:], er[:], ALU.mult))
            link(v.tensor_copy(rot[:, 0, :], cs[:, 1, :]))
            link(v.tensor_copy(rot[:, 1, :], sn[:, 1, :]))
            link(v.tensor_scalar(r1[:], pw[:, 0, 1, :], 1.0, None, ALU.subtract))
            link(v.tensor_tensor(den[:], a_re, a_re, ALU.mult))
            link(v.tensor_tensor(k1[:], a_im, a_im, ALU.mult))
            link(v.tensor_tensor(den[:], den[:], k1[:], ALU.add))
            link(v.reciprocal(den[:], den[:]))
            cmul(nc, link, fr[:], fi[:], r1[:], pw[:, 1, 1, :], a_re, a_im, tc[:], uc[:], conj=True)
            link(v.tensor_tensor(fr[:], fr[:], den[:], ALU.mult))
            link(v.tensor_tensor(fi[:], fi[:], den[:], ALU.mult))
            for d in range(2):
                s = slice(d * GP, (d + 1) * GP)
                f = [c[:, s].unsqueeze(2).to_broadcast([P, GP, SP]) for c in (fr, fi)]
                t, u = (scr[:, i, 0:GP * SP].rearrange("p (j o) -> p j o", j=GP) for i in range(2))
                cmul(nc, link, BB[:, d, 0], BB[:, d, 1], Bm[:, 0], Bm[:, 1], f[0], f[1], t, u)

                def powers(c, exps):
                    p = pw[:, c, exps, s]
                    return p.rearrange("p e j -> p j e").unsqueeze(3).to_broadcast([P, GP, p.shape[1], SP])

                e = slice(7, None, -1) if d == 0 else slice(0, SC)
                b = [BB[:, d, c].unsqueeze(2).to_broadcast([P, GP, SC, SP]) for c in range(2)]
                t, u = (scr[:, i, 0:GP * SC * SP].rearrange("p (j e o) -> p j e o", j=GP, e=SC) for i in range(2))
                cmul(nc, link, AB[:, d, 0], AB[:, d, 1], powers(0, e), powers(1, e), b[0], b[1], t, u)
                e = slice(0, 9) if d == 0 else slice(8, None, -1)
                cm = [Cm[:, c].unsqueeze(2).to_broadcast([P, GP, 9, SP]) for c in range(2)]
                t, u = (scr[:, i, :].rearrange("p (j e o) -> p j e o", j=GP, e=9) for i in range(2))
                cmul(nc, link, CA[:, d, 0], CA[:, d, 1], powers(0, e), powers(1, e), cm[0], cm[1], t, u)
                link(v.tensor_scalar(CA[:, d, 1], CA[:, d, 1], -1.0, None, ALU.mult))
            dve.sem_inc(ab_rdy, 1)
            dve.wait_ge(ev, at_u + N_U)
            for s in range(SC):
                link(v.tensor_tensor(d8[:, :, s, :], d8[:, :, s, :], Dr[:].rearrange("p (g o) -> p g o", g=G16), ALU.mult))
            dve.wait_ge(ev, at_x + N_X)
            dve.wait_ge(tab_rdy, 1)
            xr, xi = X[:, 0], X[:, 1]
            t, u = tmp[:, 0], tmp[:, 1]
            cmul(nc, link, xr, xi, xr, xi, TAB[:, 0], TAB[:, 1], t, u, conj=True)
            link(v.tensor_copy(t, er[:].unsqueeze(2).to_broadcast([P, N2, NCA])))
            link(v.memset(tmp[:, 0, :, 0:1], 0.0))
            for c in range(2):
                flat = X[:, c].rearrange("p j n -> p (j n)")
                link(v.tensor_tensor_scan(flat, tmp[:, 0].rearrange("p j n -> p (j n)"), flat, 0.0, ALU.mult, ALU.add))
            cmul(nc, link, xr, xi, xr, xi, TAB[:, 0], TAB[:, 1], t, u)
            for c in range(2):
                link(v.tensor_copy(HB[:, c], X[:, c, GP:, NCA - 2:NCC - 2:-1]))
            dve.sem_inc(h_rdy, 1)
            for q in range(4):
                dve.wait_ge(y_mm, q + 1)
                for r in range(4):
                    g = 2 * (q // 2 * 4 + r) + q % 2
                    last = v.tensor_tensor(ys[:, :, g * SP:(g + 1) * SP], K.bank[2 + q][:, r * P:(r + 1) * P].rearrange("p (s o) -> p s o", s=SC),
                                           d8[:, g], ALU.add)
                last.then_inc(y_ev, 1)
            for q in range(4):
                dve.wait_ge(g_sg, q + 1)
                o = (slice(None), q // 2, slice((q % 2) * HALF, (q % 2 + 1) * HALF))
                v.tensor_tensor(K.ydT[o], yDT[o], sg[o], ALU.mult).then_inc(chain, 1)


def stage_mixers(K):
    nc, I = K.nc, K.I
    NL = NCT + NT
    qkT = K.at("mx_qkT", 72, [P, 4, T])
    kn = K.at("mx_kn", 88, [P, NL, W])
    vx = K.at("mx_vx", 98, [P, NL, HEADS, HD + 1])
    so = K.at("mx_so", 109, [P, NT, W])
    GT = K.at("mx_GT", 117, [P, NL, 2, 2, HEADS])
    zb = K.at("mx_zb", 118, [P, NT, 2 * W])
    cT = K.at("mx_cT", 134, [P, 4, T])
    acc = K.at("mx_acc", 142, [P, 2, T])
    yc = K.at("mx_yc", 134, [P, NT, W])
    H = K.at("mx_H", 142, [P, NT, HEADS, HD])
    ring = [K.at(f"mx_w{s}", 150 + 16 * s, [P, KT, HALF]) for s in range(2)]
    apad = K.at("mx_apad", 182, [P, 2, ROWS, GRID + 2 * PAD])
    rows = K.at("mx_rows", 194, [P, 5, W])
    wsn = K.at("mx_wsn", 88, [P, 4, P])
    wcn = K.at("mx_wcn", 90, [CONV + 1, W])
    QR = 36
    ig, lf, bc, win, ee, d0m, d0a = (K.at(f"mx_g{n}", 150 + 5 * n + (2 if n == 6 else 0), [QR, NL * P]) for n in range(7))
    COL = K.at("mx_COL", 187, [P, 2, 4, NL, HEADS])
    CS = K.at("mx_CS", 188.5, [P, 2, 2, HD + 1])
    selp = K.at("mx_selp", 189.75, [QR, 2, 2, HD])
    mask = K.at("mx_mask", 190.75, [P, 2, P])
    sel = K.at("mx_sel", 191.75, [QR, HEADS, P])
    arg = [K.at(f"mx_arg{d}", 48 + 2 * d, [P, HEADS, P]) for d in range(2)]
    PT = [K.at(f"mx_PT{d}", 52 + 2 * d, [P, HEADS, P]) for d in range(2)]
    num = [K.at(f"mx_num{d}", 56 + 1.25 * d, [P, HEADS, HD + 1]) for d in range(2)]
    ke = [K.at(f"mx_ke{d}", 58.5 + d, [P, HEADS, HD]) for d in range(2)]
    used = [0]

    def columns(n):
        used[0] += n
        return K.prm[:, used[0] - n:used[0]]

    wcol = columns(2 * (CONV + 1)).rearrange("p (c k) -> p c k", c=2)
    bs = columns(4)
    gbias = columns(16)
    st6 = columns(6)
    mv = columns(2 * NT).rearrange("p (i a) -> p i a", a=2)
    rstd = columns(NT)
    mvc = columns(2 * NT).rearrange("p (i a) -> p i a", a=2)
    rstdc = columns(NT)
    BE, ME, BM, MPc, MEc, DEC = (columns(NL) for _ in range(6))
    MP = columns(NL + 1)
    dcol = columns(2 * 2 * NL).rearrange("p (d j c) -> p d j c", d=2, j=2)
    nd = [columns(HEADS) for _ in range(2)]
    sums = columns(NT * HEADS).rearrange("p (i h) -> p i h", h=HEADS)
    sqs = columns(NT * HEADS).rearrange("p (i h) -> p i h", h=HEADS)
    gt = columns(NL * 2 * HEADS).rearrange("p (i d h) -> p i d h", i=NL, d=2)
    ge = columns(NL * 2 * HEADS).rearrange("p (i d h) -> p i d h", i=NL, d=2)

    w_in = [K.sem(f"mx_win{s}") for s in range(2)]
    names = ("prm mm ev cons sel conv ctmm sgn wst bmm bdone ycn yc_tr yc_ev yb_tr yb_ev "
             "g1 g2 g3 gx gmm gev ga gb colmm colev st argmm argr pr ptr qmm pvmm nr ker umm hr yam yae eps1 eps2 chain pchain").split()
    S = {n: K.sem("mx_" + n) for n in names}
    slabs = [(OFF_C, 512), (OFF_B, 512), (3 * W, W + 16), (0, 512), (W, 512)]
    loads = [8, 8, NL, 8, NL]
    first = np.cumsum([0] + loads)
    total = int(first[-1])
    order = [list(range(NL)), [1, 0] + list(range(NL - 1, NCT - 1, -1))]

    with nc.Block() as block:
        @block.sync
        def _(sp):
            w = I["w_in"][0].rearrange("(k p) n -> p k n", p=P)
            for j, (col, n) in enumerate(slabs):
                if j >= 2:
                    sp.wait_ge(S["mm"], int(first[j - 1]))
                sp.dma_start(ring[j % 2][:, :, 0:n], w[:, :, col:col + n]).then_inc(w_in[j % 2], 16)
                if j == 1:
                    sp.dma_start(wcn[0:CONV, :], I["conv_w"][0]).then_inc(S["prm"], 16)
                    sp.dma_start(wcn[CONV:CONV + 1, :], I["conv_b"]).then_inc(S["prm"], 16)
                    sp.dma_start(wsn[:], I["sgu_w"][0].rearrange("g t s -> t g s")).then_inc(S["prm"], 16)
                    with nc.allow_non_contiguous_dma(reason="a bias as columns"):
                        sp.dma_start(bs[:], I["sgu_b"][0].rearrange("g t -> t g")).then_inc(S["prm"], 16)
                    sp.dma_start(gbias[:], I["mlstm_gate_bias"].to_broadcast([P, 16])).then_inc(S["prm"], 16)
                    for r, name in enumerate(("conv_ln_w", "conv_ln_b", "sgu_ln_w", "sgu_ln_b", "mlstm_norm_w")):
                        sp.dma_start(rows[:, r, :], I[name].to_broadcast([P, W])).then_inc(S["prm"], 16)

        @block.gpsimd
        def _(pool):
            g = nc.gpsimd
            g.memset(apad[:], 0.0).then_inc(S["cons"], 1)
            g.memset(vx[:, :, :, HD:], 1.0).then_inc(S["cons"], 1)
            pool.wait_ge(S["conv"], 1)
            pool.wait_ge(S["mm"], total)
            link = Link(g, S["pchain"])
            for t in (selp, mask, sel, CS, ig, lf, bc, win, ee, d0a):
                link(g.memset(t[:], 0.0))
            link(g.memset(d0m[:], 1.0))
            for r in (0, 32):
                link(g.affine_select(out=selp[r:r + 4], in_=selp[r:r + 4], compare_op=ALU.not_equal, fill=1.0, base=0,
                                     pattern=[[-2, 2], [-1, 2], [0, HD]], channel_multiplier=1))
                link(g.affine_select(out=sel[r:r + 4], in_=sel[r:r + 4], compare_op=ALU.not_equal, fill=-1.0, base=0,
                                     pattern=[[-1, HEADS], [0, P]], channel_multiplier=1))
                start = slice(0, None, P) if r == 0 else slice(P - 1, None, P)
                link(g.memset(d0m[r:r + 4, start], 0.0))
                link(g.memset(d0a[r:r + 4, start], LOW))
            link(g.affine_select(out=mask[:, 0, :], in_=mask[:, 0, :], compare_op=ALU.is_ge, fill=LOW, base=0,
                                 pattern=[[1, P]], channel_multiplier=-1))
            link(g.affine_select(out=mask[:, 1, :], in_=mask[:, 1, :], compare_op=ALU.is_ge, fill=LOW, base=0,
                                 pattern=[[-1, P]], channel_multiplier=1))
            pool.sem_inc(S["sel"], 1)

        @block.tensor
        def _(pe):
            n = 0

            def group(bank, cols, pairs, last):
                for k, (lhs, rhs) in enumerate(pairs):
                    mm = nc.tensor.matmul(bank[:, 0:cols], lhs, rhs, start=(k == 0), stop=(k == KT - 1))
                if last:
                    mm.then_inc(S["mm"], 1)

            for j, (col, cols) in enumerate(slabs):
                pe.wait_ge(w_in[j % 2], 16 * (j // 2 + 1))
                w = ring[j % 2]
                for r in range(loads[j]):
                    if n >= 8:
                        pe.wait_ge(S["ev"], n - 7)
                    if j in (0, 3):
                        m, h = r // 2, r % 2
                        group(K.bank[n % 8], HALF, [(w[:, k, m * P:(m + 1) * P], K.HT[:, k, TC + h * HALF:TC + (h + 1) * HALF]) for k in range(KT)], True)
                    else:
                        i = r + NCT if j == 1 else r
                        group(K.bank[n % 8], cols, [(K.HT[:, k, i * P:(i + 1) * P], w[:, k, 0:cols]) for k in range(KT)], True)
                    n += 1
                if j == 0:
                    pe.wait_ge(S["prm"], 16 * 10)
                    pe.wait_ge(S["ev"], 8)
                    for g in range(4):
                        nc.tensor.transpose(K.bank[1][:, g * P:(g + 1) * P], wsn[:, g, :], K.ident[:])
                    for c in range(2):
                        last = nc.tensor.transpose(K.bank[0][:, c * (CONV + 1):(c + 1) * (CONV + 1)], wcn[:, c * P:(c + 1) * P],
                                                   K.ident[0:CONV + 1, 0:CONV + 1])
                    last.then_inc(S["wst"], 1)
                    pe.wait_ge(S["g1"], 1)

            pe.wait_ge(S["ev"], total)
            pe.wait_ge(S["conv"], 1)
            for q in range(4):
                for r in range(4):
                    i, c = 2 * q + r // 2, r % 2
                    last = nc.tensor.transpose(K.bank[q][:, r * P:(r + 1) * P], acc[:, c, i * P:(i + 1) * P], K.ident[:])
                last.then_inc(S["ctmm"], 1)
            pe.wait_ge(S["sgn"], 1)
            for g in range(4):
                nc.tensor.matmul(K.bank[4 + g][:].rearrange("p (i n) -> p i n", i=NT), K.wsT[:, g, :],
                                 zb[:, :, W + g * HD:W + (g + 1) * HD], start=True, stop=True).then_inc(S["bmm"], 1)
            pe.wait_ge(S["ycn"], 1)
            for q in range(4):
                for r in range(4):
                    last = nc.tensor.transpose(K.bank[q][:, r * P:(r + 1) * P], yc[:, 4 * (q % 2) + r, (q // 2) * P:(q // 2 + 1) * P], K.ident[:])
                last.then_inc(S["yc_tr"], 1)
            pe.wait_ge(S["bdone"], 4)
            for q in range(4):
                for r in range(4):
                    last = nc.tensor.transpose(K.bank[4 + q][:, r * P:(r + 1) * P], zb[:, 4 * (q % 2) + r, (q // 2) * P:(q // 2 + 1) * P], K.ident[:])
                last.then_inc(S["yb_tr"], 1)
            pe.wait_ge(S["yc_ev"], 4)
            pe.wait_ge(S["yb_ev"], 4)
            pe.wait_ge(S["g3"], 1)
            for a in range(2):
                for c in range(NL):
                    for d in range(2):
                        last = nc.tensor.matmul(K.bank[4 * a + c // 4][32 * d:32 * d + HEADS, (c % 4) * P:(c % 4 + 1) * P],
                                                GT[:, c, d, a, :], K.ident[:], start=True, stop=True)
            last.then_inc(S["gmm"], 1)
            pe.wait_ge(S["gb"], 1)
            for d in range(2):
                r = slice(32 * d, 32 * d + HEADS)
                for a, t in enumerate((ig, win, bc, ee)):
                    for c in range(NL):
                        o = (a * NL + c) * HEADS
                        nc.tensor.matmul(K.bank[3 + 4 * d][:, o:o + HEADS], t[r, c * P:(c + 1) * P], K.ident[r, r], start=True, stop=True)
                for j in range(2):
                    o = 4 * NL * HEADS + j * NL
                    last = nc.tensor.matmul(K.bank[3 + 4 * d][:, o:o + NL], selp[r, j, :, :], DEC[r, :], start=True, stop=True)
            last.then_inc(S["colmm"], 1)
            pe.wait_ge(S["colev"], 1)
            nq = 0
            for step in range(NL):
                for d in range(2):
                    c = order[d][step]
                    r = slice(32 * d, 32 * d + HEADS)
                    b = [K.bank[4 * d + m] for m in range(4)]
                    tok = slice((c - NCT) * P, (c - NCT + 1) * P)
                    if c >= NCT:
                        if step > NCT:
                            pe.wait_ge(S["nr"], 2 * (step - NCT) - 1 + d)
                        pe.wait_ge(S["st"], 2 * step - 1 + d)
                        for h in range(HEADS):
                            last = nc.tensor.matmul(b[0][:, h * P:(h + 1) * P], sel[r, h, :], lf[r, c * P:(c + 1) * P], start=True, stop=True)
                        last.then_inc(S["argmm"], 1)
                        for h in range(HEADS):
                            hr = slice((h % 2) * HD, (h % 2 + 1) * HD)
                            last = nc.tensor.matmul(b[1 + h % 2][:, (h // 2) * P:(h // 2 + 1) * P], qkT[hr, 2 + h // 2, tok],
                                                    qkT[hr, h // 2, tok], start=True, stop=True)
                        for h in range(HEADS):
                            hr = slice((h % 2) * HD, (h % 2 + 1) * HD)
                            o = 2 * P + (h // 2) * (HD + 1)
                            last = nc.tensor.matmul(b[1 + h % 2][:, o:o + HD + 1], qkT[hr, h // 2, tok], CS[hr, d, h // 2, :], start=True, stop=True)
                        last.then_inc(S["qmm"], 1)
                    if step < NL - 1:
                        pe.wait_ge(S["ker"], 2 * step + 1 + d)
                        for h in range(HEADS):
                            o = (h // 2) * (HD + 1)
                            last = nc.tensor.matmul(b[0][(h % 2) * HD:(h % 2 + 1) * HD, o:o + HD + 1], ke[d][:, h, :], vx[:, c, h, :],
                                                    start=True, stop=True)
                        last.then_inc(S["umm"], 1)
                    if c >= NCT:
                        pe.wait_ge(S["ptr"], 2 * (step - NCT) + 1 + d)
                        for h in range(HEADS):
                            last = nc.tensor.matmul(b[3][:, h * (HD + 1):(h + 1) * (HD + 1)], PT[d][:, h, :], vx[:, c, h, :], start=True, stop=True)
                        last.then_inc(S["pvmm"], 1)
            pe.wait_ge(S["hr"], 1)
            for q in range(4):
                for r in range(4):
                    last = nc.tensor.transpose(K.bank[q][:, r * P:(r + 1) * P],
                                               H[:, 4 * (q % 2) + r, 2 * (q // 2):2 * (q // 2) + 2, :], K.ident[:])
                last.then_inc(S["yam"], 1)

        @block.scalar
        def _(act):
            n = 0

            def take(dst, src, func=ACT.Copy, last=True):
                ins = nc.scalar.activation(dst, src, func)
                if last:
                    ins.then_inc(S["ev"], 1)

            for j in range(5):
                if j == 4:
                    act.wait_ge(S["cons"], 2)
                for r in range(loads[j]):
                    act.wait_ge(S["mm"], n + 1)
                    b = K.bank[n % 8]
                    if j == 0:
                        take(cT[:, r // 2, (r % 2) * HALF:(r % 2 + 1) * HALF], b[:], ACT.Copy if r < 4 else ACT.Sigmoid)
                    elif j == 1:
                        take(zb[:, r, :], b[:], ACT.Gelu_apprx_tanh)
                    elif j == 2:
                        if r >= NCT:
                            take(so[:, r - NCT, :], b[:, 0:W], ACT.Sigmoid, last=False)
                        take(GT[:, r], b[:, W:W + 16].rearrange("p (d a h) -> p d a h", d=2, a=2))
                    elif j == 3:
                        take(qkT[:, r // 2, (r % 2) * HALF:(r % 2 + 1) * HALF], b[:])
                    else:
                        take(kn[:, r, :], b[:, 0:W], last=False)
                        take(vx[:, r, :, 0:HD], b[:, W:].rearrange("p (h e) -> p h e", h=HEADS))
                    n += 1
            act.wait_ge(S["g2"], 1)
            nc.scalar.activation(ge[:], gt[:], ACT.Exp).then_inc(S["gx"], 1)
            act.wait_ge(S["gx"], 1)
            nc.scalar.activation(ge[:], ge[:], ACT.Ln, bias=1.0).then_inc(S["gx"], 1)
            act.wait_ge(S["eps1"], 1)
            nc.scalar.activation(rstd[:], rstd[:], ACT.Sqrt).then_inc(S["eps1"], 1)
            act.wait_ge(S["eps2"], 1)
            nc.scalar.activation(rstdc[:], rstdc[:], ACT.Sqrt).then_inc(S["eps2"], 1)
            act.wait_ge(S["eps2"], 3)
            nc.scalar.activation(yc[:], yc[:], ACT.Silu).then_inc(S["ycn"], 1)
            for q in range(4):
                act.wait_ge(S["yc_tr"], q + 1)
                nc.scalar.activation(K.yT[4 + q // 2][:, (q % 2) * HALF:(q % 2 + 1) * HALF], K.bank[q][:], ACT.Copy).then_inc(S["yc_ev"], 1)
            for q in range(4):
                act.wait_ge(S["yb_tr"], q + 1)
                nc.scalar.activation(K.yT[2 + q // 2][:, (q % 2) * HALF:(q % 2 + 1) * HALF], K.bank[4 + q][:], ACT.Copy).then_inc(S["yb_ev"], 1)
            act.wait_ge(S["ga"], 1)
            for t in (win[:], ee[:], DEC[0:QR, :]):
                nc.scalar.activation(t, t, ACT.Exp)
            nc.scalar.activation(bc[:], bc[:], ACT.Exp, scale=-1.0).then_inc(S["gb"], 1)
            for m in range(2 * NT):
                act.wait_ge(S["argr"], m + 1)
                nc.scalar.activation(arg[m % 2][:], arg[m % 2][:], ACT.Exp).then_inc(S["pr"], 1)
            act.wait_ge(S["nr"], 2 * NT + 1)
            nc.scalar.activation(sqs[:], sqs[:], ACT.Sqrt).then_inc(S["nr"], 1)
            for q in range(4):
                act.wait_ge(S["yam"], q + 1)
                nc.scalar.activation(K.yT[q // 2][:, (q % 2) * HALF:(q % 2 + 1) * HALF], K.bank[q][:], ACT.Copy).then_inc(S["yae"], 1)

        @block.vector
        def _(dve):
            v = nc.vector
            link = Link(v, S["chain"])
            dve.wait_ge(S["wst"], 1)
            link(v.tensor_copy(K.wsT[:], K.bank[1][:].rearrange("p (g t) -> p g t", g=4)))
            v.tensor_copy(wcol[:], K.bank[0][:, 0:2 * (CONV + 1)].rearrange("p (c k) -> p c k", c=2)).then_inc(S["g1"], 1)
            dve.wait_ge(S["g1"], 1)
            dve.wait_ge(S["cons"], 2)
            dve.wait_ge(S["ev"], 8)
            for c in range(2):
                link(v.tensor_tensor(apad[:, c, :, PAD:PAD + GRID], cT[:, c, :].rearrange("p (r t) -> p r t", r=ROWS),
                                     cT[:, 2 + c, :].rearrange("p (r t) -> p r t", r=ROWS), ALU.mult))
            out = [acc[:, c, :].rearrange("p (r t) -> p r t", r=ROWS) for c in range(2)]
            for c in range(2):
                link(v.tensor_scalar(out[c], apad[:, c, :, 0:GRID], wcol[:, c, 0:1], wcol[:, c, CONV:CONV + 1], ALU.mult, ALU.add))
            for k in range(1, CONV):
                for c in range(2):
                    link(v.scalar_tensor_tensor(out=out[c], in0=apad[:, c, :, k:k + GRID], scalar=wcol[:, c, k:k + 1], in1=out[c],
                                                op0=ALU.mult, op1=ALU.add))
            dve.sem_inc(S["conv"], 1)

            def norm(x, mean_var, inv, i):
                link(v.bn_stats(st6[:], x))
                link(v.bn_aggr(mean_var[:, i, :], st6[:]))

            dve.wait_ge(S["ev"], int(first[2]))
            dve.wait_ge(S["prm"], 16 * 10)
            for i in range(NT):
                norm(zb[:, i, W:], mv, rstd, i)
            link(v.tensor_scalar(rstd[:], mv[:, :, 1], LN_EPS, None, ALU.add))
            dve.sem_inc(S["eps1"], 1)
            dve.wait_ge(S["ev"], int(first[3]))
            flat = GT[:].rearrange("p i d a h -> p i (d a h)")
            link(v.tensor_tensor(flat, flat, gbias[:].unsqueeze(1).to_broadcast([P, NL, 16]), ALU.add))
            for d in range(2):
                link(v.scalar_tensor_tensor(out=gt[:, :, d, :], in0=GT[:, :, d, 1, :], scalar=-1.0, in1=GT[:, :, d, 1, :], op0=ALU.mult, op1=ALU.min))
            dve.sem_inc(S["g2"], 1)
            dve.wait_ge(S["gx"], 2)
            for d in range(2):
                link(v.scalar_tensor_tensor(out=GT[:, :, d, 1, :], in0=GT[:, :, d, 1, :], scalar=0.0, in1=ge[:, :, d, :], op0=ALU.min, op1=ALU.subtract))
            dve.sem_inc(S["g3"], 1)
            dve.wait_ge(S["eps1"], 2)
            link(v.reciprocal(rstd[:], rstd[:]))
            for i in range(NT):
                link(v.tensor_scalar(zb[:, i, W:], zb[:, i, W:], mv[:, i, 0:1], rstd[:, i:i + 1], ALU.subtract, ALU.mult))
            for r, op in ((2, ALU.mult), (3, ALU.add)):
                link(v.tensor_tensor(zb[:, :, W:], zb[:, :, W:], rows[:, r, :].unsqueeze(1).to_broadcast([P, NT, W]), op))
            dve.sem_inc(S["sgn"], 1)
            for i in range(NT):
                dve.wait_ge(S["ctmm"], i // 2 + 1)
                x = K.bank[i // 2][:, (i % 2) * W:(i % 2 + 1) * W]
                norm(x, mvc, rstdc, i)
            link(v.tensor_scalar(rstdc[:], mvc[:, :, 1], LN_EPS, None, ALU.add))
            dve.sem_inc(S["eps2"], 1)
            dve.wait_ge(S["eps2"], 2)
            link(v.reciprocal(rstdc[:], rstdc[:]))
            for i in range(NT):
                x = K.bank[i // 2][:, (i % 2) * W:(i % 2 + 1) * W]
                link(v.tensor_scalar(yc[:, i, :], x, mvc[:, i, 0:1], rstdc[:, i:i + 1], ALU.subtract, ALU.mult))
            for r, op in ((0, ALU.mult), (1, ALU.add)):
                link(v.tensor_tensor(yc[:], yc[:], rows[:, r, :].unsqueeze(1).to_broadcast([P, NT, W]), op))
            dve.sem_inc(S["eps2"], 1)
            for g in range(4):
                dve.wait_ge(S["bmm"], g + 1)
                o = zb[:, :, g * HD:(g + 1) * HD]
                v.scalar_tensor_tensor(out=o, in0=K.bank[4 + g][:].rearrange("p (i n) -> p i n", i=NT), scalar=bs[:, g:g + 1], in1=o,
                                       op0=ALU.add, op1=ALU.mult).then_inc(S["bdone"], 1)
            dve.wait_ge(S["sel"], 1)
            dve.wait_ge(S["gmm"], 1)
            for a, t in enumerate((ig, lf)):
                for d in range(2):
                    r = slice(32 * d, 32 * d + HEADS)
                    for q in range(3):
                        n = min(HALF, NL * P - q * HALF)
                        link(v.tensor_copy(t[r, q * HALF:q * HALF + n], K.bank[4 * a + q][r, 0:n]))
            way = [slice(None), slice(None, None, -1)]
            for d in range(2):
                r = slice(32 * d, 32 * d + HEADS)
                link(v.tensor_tensor_scan(bc[r, way[d]], d0m[r, way[d]], lf[r, way[d]], 0.0, ALU.mult, ALU.add))
            link(v.tensor_tensor(ig[:], ig[:], bc[:], ALU.subtract))
            for d in range(2):
                r = slice(32 * d, 32 * d + HEADS)
                link(v.tensor_tensor_scan(lf[r, way[d]], d0a[r, way[d]], ig[r, way[d]], LOW, ALU.add, ALU.max))
            link(v.memset(BE[0:QR, :], 0.0))
            link(v.memset(ME[0:QR, :], 0.0))
            link(v.memset(MEc[0:QR, :], 0.0))
            link(v.memset(MPc[0:QR, :], 0.0))
            link(v.memset(MP[0:QR, :], LOW))
            for d in range(2):
                r = slice(32 * d, 32 * d + HEADS)
                for dst, src in ((BE, bc), (ME, lf)):
                    e = src[r, P - 1::P] if d == 0 else src[r, 0::P]
                    if d == 0:
                        link(v.tensor_copy(dst[r, :], e))
                    else:
                        link(v.tensor_copy(dst[r, 0:NCT], e[:, NCT - 1::-1]))
                        link(v.tensor_copy(dst[r, NCT:], e[:, :NCT - 1:-1]))
                link(v.tensor_copy(MEc[r, :], lf[r, P - 1::P] if d == 0 else lf[r, 0::P]))
            link(v.tensor_tensor(BM[0:QR, :], BE[0:QR, :], ME[0:QR, :], ALU.add))
            link(v.tensor_tensor_scan(MP[0:QR, 1:], BE[0:QR, :], BM[0:QR, :], LOW, ALU.add, ALU.max))
            link(v.tensor_copy(MPc[0:HEADS, :], MP[0:HEADS, 0:NL]))
            r = slice(32, 32 + HEADS)
            link(v.tensor_copy(MPc[r, 0:NCT], MP[r, NCT - 1::-1]))
            link(v.tensor_copy(MPc[r, NCT:], MP[r, NL - 1:NCT - 1:-1]))
            link(v.tensor_tensor(MEc[0:QR, :], MEc[0:QR, :], MPc[0:QR, :], ALU.max))

            def chunked(t):
                return t[:].rearrange("p (c t) -> p c t", c=NL)

            before, after = (t[0:QR, :].unsqueeze(2).to_broadcast([QR, NL, P]) for t in (MPc, MEc))
            link(v.tensor_tensor(chunked(lf), chunked(lf), before, ALU.max))
            link(v.tensor_tensor(chunked(win), before, chunked(lf), ALU.subtract))
            link(v.tensor_tensor(chunked(ee), chunked(ig), after, ALU.subtract))
            link(v.tensor_tensor(bc[:], bc[:], lf[:], ALU.add))
            link(v.tensor_tensor(DEC[0:QR, :], MPc[0:QR, :], MEc[0:QR, :], ALU.subtract))
            dve.sem_inc(S["ga"], 1)
            link(v.memset(H[:], 0.0))
            dve.wait_ge(S["colmm"], 1)
            for d in range(2):
                n = 4 * NL * HEADS
                link(v.tensor_copy(COL[:, d].rearrange("p a c h -> p (a c h)"), K.bank[3 + 4 * d][:, 0:n]))
                link(v.tensor_copy(dcol[:, d].rearrange("p j c -> p (j c)"), K.bank[3 + 4 * d][:, n:n + 2 * NL]))
            dve.sem_inc(S["colev"], 1)
            lat = 0
            for step in range(NL):
                for d in range(2):
                    c = order[d][step]
                    b = [K.bank[4 * d + m] for m in range(4)]
                    if c >= NCT:
                        dve.wait_ge(S["argmm"], lat + 1)
                        for h in range(HEADS):
                            last = v.scalar_tensor_tensor(out=arg[d][:, h, :], in0=b[0][:, h * P:(h + 1) * P], scalar=COL[:, d, 0, c, h:h + 1],
                                                          in1=mask[:, d, :], op0=ALU.add, op1=ALU.min)
                        last.then_inc(S["argr"], 1)
                    if step < NL - 1:
                        v.scalar_tensor_tensor(out=ke[d][:], in0=kn[:, c, :].rearrange("p (h e) -> p h e", h=HEADS), scalar=HD ** -0.5,
                                               in1=COL[:, d, 3, c, :].unsqueeze(2).to_broadcast([P, HEADS, HD]),
                                               op0=ALU.mult, op1=ALU.mult).then_inc(S["ker"], 1)
                    if c >= NCT:
                        dve.wait_ge(S["pr"], lat + 1)
                        dve.wait_ge(S["qmm"], lat + 1)
                        for m in range(2):
                            last = v.scalar_tensor_tensor(out=PT[d][:, m::2, :], in0=b[1 + m][:, 0:2 * P].rearrange("p (j t) -> p j t", j=2),
                                                          scalar=HD ** -0.5, in1=arg[d][:, m::2, :], op0=ALU.mult, op1=ALU.mult)
                        last.then_inc(S["ptr"], 1)
                        for m in range(2):
                            link(v.tensor_tensor(num[d][:, m::2, :], b[1 + m][:, 2 * P:2 * P + 2 * (HD + 1)].rearrange("p (j e) -> p j e", j=2),
                                                 COL[:, d, 1, c, m::2].unsqueeze(2).to_broadcast([P, 2, HD + 1]), ALU.mult))
                    if step < NL - 1:
                        dve.wait_ge(S["umm"], 2 * step + 1 + d)
                        for j in range(2):
                            o = j * (HD + 1)
                            last = v.scalar_tensor_tensor(out=CS[:, d, j, :], in0=CS[:, d, j, :], scalar=dcol[:, d, j, c:c + 1],
                                                          in1=b[0][:, o:o + HD + 1], op0=ALU.mult, op1=ALU.add)
                        last.then_inc(S["st"], 1)
                    if c >= NCT:
                        dve.wait_ge(S["pvmm"], lat + 1)
                        v.tensor_tensor(num[d][:], num[d][:], b[3][:, 0:HEADS * (HD + 1)].rearrange("p (h e) -> p h e", h=HEADS), ALU.add).then_inc(S["nr"], 1)
                        dve.wait_ge(S["nr"], lat + 1)
                        den = num[d][:, :, HD]
                        link(v.scalar_tensor_tensor(out=nd[d][:], in0=den, scalar=-1.0, in1=den, op0=ALU.mult, op1=ALU.max))
                        link(v.tensor_tensor(nd[d][:], nd[d][:], COL[:, d, 2, c, :], ALU.max))
                        link(v.reciprocal(nd[d][:], nd[d][:]))
                        x = num[d][:, :, 0:HD]
                        link(v.tensor_tensor(x, x, nd[d][:].unsqueeze(2).to_broadcast([P, HEADS, HD]), ALU.mult))
                        link(v.tensor_tensor(H[:, c - NCT], H[:, c - NCT], x, ALU.add))
                        lat += 1
            flat = H[:].rearrange("p i h e -> p (i h) e")
            mean, var = sums[:].rearrange("p i h -> p (i h)"), sqs[:].rearrange("p i h -> p (i h)")
            spare = kn[:, 0:NT, :].rearrange("p i (h e) -> p (i h) e", h=HEADS)
            link(v.tensor_reduce(mean, flat, AX.X, ALU.add))
            link(v.tensor_scalar(mean, mean, 1.0 / HD, None, ALU.mult))
            link(v.tensor_tensor(flat, flat, mean.unsqueeze(2).to_broadcast([P, NT * HEADS, HD]), ALU.subtract))
            link(v.tensor_tensor(spare, flat, flat, ALU.mult))
            link(v.tensor_reduce(var, spare, AX.X, ALU.add))
            v.tensor_scalar(var, var, 1.0 / HD, LN_EPS, ALU.mult, ALU.add).then_inc(S["nr"], 1)
            dve.wait_ge(S["nr"], 2 * NT + 2)
            link(v.reciprocal(var, var))
            link(v.tensor_tensor(flat, flat, var.unsqueeze(2).to_broadcast([P, NT * HEADS, HD]), ALU.mult))
            wide = H[:].rearrange("p i h e -> p i (h e)")
            link(v.tensor_tensor(wide, wide, rows[:, 4, :].unsqueeze(1).to_broadcast([P, NT, W]), ALU.mult))
            v.tensor_tensor(wide, wide, so[:], ALU.mult).then_inc(S["hr"], 1)


def stage_join(K):
    nc, I = K.nc, K.I
    wo = K.at("jn_w", 72, [P, KT, D])
    xr = [K.at(f"jn_x{s}", 104 + 4 * s, [P, D]) for s in range(3)]
    rows = K.at("jn_rows", 116, [P, 2, D])
    t = [K.at(f"jn_t{s}", 124 + 4 * s, [P, D]) for s in range(2)]
    h = [K.at(f"jn_h{s}", 140 + 4 * s, [P, D]) for s in range(2)]
    K.h2T = K.at("h2T", 152, [P, KT, T])
    st, mv, rs = K.prm[:, 0:12].rearrange("p (a b) -> p a b", a=2), K.prm[:, 12:14], K.prm[:, 14:15]
    K.x1 = nc.dram_tensor("x1", (T, D), F32, kind="Internal").ap()
    w_in, x_in, r_in = K.sem("jn_win"), [K.sem(f"jn_xin{s}") for s in range(3)], K.sem("jn_rin")
    mm, mev, sq, x1r, hr, tr, tev, chain = (K.sem("jn_" + n) for n in "mm mev sq x1r hr tr tev chain".split())
    stored = [K.sem(f"jn_st{s}") for s in range(2)]
    with nc.Block() as block:
        @block.sync
        def _(sp):
            w = I["w_out"][0].rearrange("(k p) n -> p k n", p=P)
            for k in range(0, KT, 4):
                sp.dma_start(wo[:, k:k + 4, :], w[:, k:k + 4, :]).then_inc(w_in, 16)
            for r, name in enumerate(("ln1_w", "ln1_b")):
                sp.dma_start(rows[:, r, :], I[name].to_broadcast([P, D])).then_inc(r_in, 16)
            for i in range(NT):
                if i >= 3:
                    sp.wait_ge(x1r, i - 2)
                sp.dma_start(xr[i % 3][:], I["x"][0][i * P:(i + 1) * P, :]).then_inc(x_in[i % 3], 16)

        @block.gpsimd
        def _(pool):
            for i in range(NT):
                pool.wait_ge(x1r, i + 1)
                pool.dma_start(K.x1[i * P:(i + 1) * P, :], t[i % 2][:]).then_inc(stored[i % 2], 16)
            for s in range(2):
                pool.wait_ge(stored[s], 16 * NT // 2)

        @block.tensor
        def _(pe):
            def turn(i):
                pe.wait_ge(hr, i + 1)
                if i >= 2:
                    pe.wait_ge(tev, 2 * (i - 1))
                for k in range(KT):
                    last = nc.tensor.transpose(K.bank[4 + 2 * (i % 2) + k // 4][:, (k % 4) * P:(k % 4 + 1) * P],
                                               h[i % 2][:, k * P:(k + 1) * P], K.ident[:])
                last.then_inc(tr, 1)

            pe.wait_ge(w_in, 32)
            for i in range(NT):
                if i >= 2:
                    pe.wait_ge(mev, i - 1)
                for b in range(2):
                    for k in range(KT):
                        last = nc.tensor.matmul(K.bank[2 * (i % 2) + b][:], K.yT[k][:, i * P:(i + 1) * P], wo[:, k, b * HALF:(b + 1) * HALF],
                                                start=(k == 0), stop=(k == KT - 1))
                last.then_inc(mm, 1)
                if i:
                    turn(i - 1)
            turn(NT - 1)

        @block.scalar
        def _(act):
            def take(i):
                act.wait_ge(tr, i + 1)
                for b in range(2):
                    nc.scalar.activation(K.h2T[:, 4 * b:4 * b + 4, i * P:(i + 1) * P],
                                         K.bank[4 + 2 * (i % 2) + b][:].rearrange("p (k t) -> p k t", k=4), ACT.Copy).then_inc(tev, 1)

            for i in range(NT):
                act.wait_ge(sq, 2 * i + 1)
                nc.scalar.activation(rs, rs, ACT.Sqrt).then_inc(sq, 1)
                if i:
                    take(i - 1)
            take(NT - 1)

        @block.vector
        def _(dve):
            v = nc.vector
            link = Link(v, chain)
            dve.wait_ge(r_in, 32)
            for i in range(NT):
                x, y = xr[i % 3], t[i % 2]
                dve.wait_ge(mm, i + 1)
                if i >= 2:
                    dve.wait_ge(stored[i % 2], 16 * (i // 2))
                for b in range(2):
                    s = slice(b * HALF, (b + 1) * HALF)
                    last = v.tensor_tensor(y[:, s], K.bank[2 * (i % 2) + b][:], K.MOD[:, 2 * D + b * HALF:2 * D + (b + 1) * HALF], ALU.mult)
                last.then_inc(mev, 1)
                dve.wait_ge(mev, i + 1)
                dve.wait_ge(x_in[i % 3], 16 * (i // 3 + 1))
                link(v.scalar_tensor_tensor(out=y[:], in0=x[:], scalar=ALPHA, in1=y[:], op0=ALU.mult, op1=ALU.add))
                norm_rows(K, dve, link, y, st, mv, rs, sq, i)
                for r, op in ((0, ALU.mult), (1, ALU.add)):
                    ins = v.tensor_tensor(y[:], y[:], rows[:, r, :], op)
                    if r == 0:
                        link(ins)
                    else:
                        ins.then_inc(x1r, 1)
                dve.wait_ge(x1r, i + 1)
                if i >= 2:
                    dve.wait_ge(tr, i - 1)
                link(v.scalar_tensor_tensor(out=h[i % 2][:], in0=K.MOD[:, 4 * D:5 * D], scalar=1.0, in1=y[:], op0=ALU.add, op1=ALU.mult))
                v.tensor_tensor(h[i % 2][:], h[i % 2][:], K.MOD[:, 3 * D:4 * D], ALU.add).then_inc(hr, 1)


def norm_rows(K, dve, link, y, st, mv, rs, sq, i):
    v = K.nc.vector
    for b in range(2):
        link(v.bn_stats(st[:, b, :], y[:, b * HALF:(b + 1) * HALF]))
    link(v.bn_aggr(mv, st))
    v.tensor_scalar(rs, mv[:, 1:2], LN_EPS, None, ALU.add).then_inc(sq, 1)
    dve.wait_ge(sq, 2 * i + 2)
    link(v.reciprocal(rs, rs))
    link(v.tensor_scalar(y[:], y[:], mv[:, 0:1], rs, ALU.subtract, ALU.mult))


def stage_ffn(K):
    nc, I = K.nc, K.I
    hid = K.at("ff_hid", 24, [P, NF, T])
    wi = [K.at(f"ff_wi{s}", 112 + 8 * s, [P, KT, 2, P]) for s in range(2)]
    wo = [K.at(f"ff_wo{s}", 128 + 11 * s, [P, NF, P]) for s in range(2)]
    sil = [K.at(f"ff_sil{s}", 184 + 4 * s, [P, T]) for s in range(2)]
    K.ynT = K.at("ynT", 152, [P, KT, T])
    wi_in, wo_in = ([K.sem(f"ff_{n}{s}") for s in range(2)] for n in ("wi", "wo"))
    mm, sr, hr, omm, oev = (K.sem("ff_" + n) for n in "mm sr hr omm oev".split())
    w1 = I["w_ffn_in"][0].rearrange("(k p) (a f) -> p k a f", p=P, a=2)
    w2 = I["w_ffn_out"][0].rearrange("(f p) n -> p f n", p=P)
    with nc.Block() as block:
        @block.sync
        def _(sp):
            def hidden_weights(f, s):
                for a in range(2):
                    sp.dma_start(wi[s][:, :, a, :], w1[:, :, a, f]).then_inc(wi_in[s], 16)

            for s in range(2):
                hidden_weights(slice(s * P, (s + 1) * P), s)
                sp.dma_start(wo[s][:], w2[:, :, s * P:(s + 1) * P]).then_inc(wo_in[s], 16)
            with sp.Fori(1, NF // 2) as r:
                for s in range(2):
                    sp.wait_ge(mm, 2 * r + s - 1)
                    hidden_weights(bass.ds(r * (2 * P) + s * P, P), s)
            with sp.Fori(1, KT // 2) as r:
                for s in range(2):
                    sp.wait_ge(omm, 2 * r + s - 1)
                    sp.dma_start(wo[s][:], w2[:, :, bass.ds(r * (2 * P) + s * P, P)]).then_inc(wo_in[s], 16)

        @block.tensor
        def _(pe):
            def hidden(r, s):
                pe.wait_ge(wi_in[s], 32 * r + 32)
                if not isinstance(r, int):
                    pe.wait_ge(hr, 2 * r + s - 1)
                for a in range(2):
                    for b in range(2):
                        for k in range(KT):
                            last = nc.tensor.matmul(K.bank[4 * s + 2 * a + b][:], wi[s][:, k, a, :], K.h2T[:, k, b * HALF:(b + 1) * HALF],
                                                    start=(k == 0), stop=(k == KT - 1))
                last.then_inc(mm, 1)

            def output(r, s):
                pe.wait_ge(wo_in[s], 16 * r + 16)
                if not isinstance(r, int):
                    pe.wait_ge(oev, 2 * r + s - 1)
                for b in range(2):
                    for f in range(NF):
                        last = nc.tensor.matmul(K.bank[2 * s + b][:], wo[s][:, f, :], hid[:, f, b * HALF:(b + 1) * HALF],
                                                start=(f == 0), stop=(f == NF - 1))
                last.then_inc(omm, 1)

            for s in range(2):
                hidden(0, s)
            with pe.Fori(1, NF // 2) as r:
                for s in range(2):
                    hidden(r, s)
            pe.wait_ge(hr, NF)
            for s in range(2):
                output(0, s)
            with pe.Fori(1, KT // 2) as r:
                for s in range(2):
                    output(r, s)

        @block.scalar
        def _(act):
            def silu(r, s):
                act.wait_ge(mm, 2 * r + s + 1)
                if not isinstance(r, int):
                    act.wait_ge(hr, 2 * r + s - 1)
                for b in range(2):
                    last = nc.scalar.activation(sil[s][:, b * HALF:(b + 1) * HALF], K.bank[4 * s + b][:], ACT.Silu)
                last.then_inc(sr, 1)

            for s in range(2):
                silu(0, s)
            with act.Fori(1, NF // 2) as r:
                for s in range(2):
                    silu(r, s)
            act.wait_ge(mm, NF)
            with act.Fori(0, KT // 2) as r:
                for s in range(2):
                    act.wait_ge(omm, 2 * r + s + 1)
                    for b in range(2):
                        last = nc.scalar.activation(K.ynT[:, bass.ds(2 * r + s, 1), b * HALF:(b + 1) * HALF], K.bank[2 * s + b][:].unsqueeze(1), ACT.Copy)
                    last.then_inc(oev, 1)

        @block.vector
        def _(dve):
            with dve.Fori(0, NF // 2) as r:
                for s in range(2):
                    dve.wait_ge(sr, 2 * r + s + 1)
                    for b in range(2):
                        last = nc.vector.tensor_tensor(hid[:, bass.ds(2 * r + s, 1), b * HALF:(b + 1) * HALF],
                                                       sil[s][:, b * HALF:(b + 1) * HALF].unsqueeze(1), K.bank[4 * s + 2 + b][:].unsqueeze(1), ALU.mult)
                    last.then_inc(hr, 1)


def stage_first_end(K):
    nc, I = K.nc, K.I
    xr = [K.at(f"fe_x{s}", 24 + 4 * s, [P, D]) for s in range(3)]
    rows = K.at("fe_rows", 36, [P, 3, D])
    t = [K.at(f"fe_t{s}", 48 + 4 * s, [P, D]) for s in range(2)]
    h = [K.at(f"fe_h{s}", 56 + 4 * s, [P, D]) for s in range(2)]
    K.h3T = K.at("h3T", 112, [P, KT, T])
    st, mv, rs = K.prm[:, 0:12].rearrange("p (a b) -> p a b", a=2), K.prm[:, 12:14], K.prm[:, 14:15]
    ss = K.prm[:, 16:24]
    K.x2 = nc.dram_tensor("x2", (T, D), F32, kind="Internal").ap()
    x_in, r_in = [K.sem(f"fe_xin{s}") for s in range(3)], K.sem("fe_rin")
    mm, mev, sq, x2r, ssr, hr, tr, tev, chain = (K.sem("fe_" + n) for n in "mm mev sq x2r ssr hr tr tev chain".split())
    stored = [K.sem(f"fe_st{s}") for s in range(2)]
    with nc.Block() as block:
        @block.sync
        def _(sp):
            for r, name in enumerate(("ln2_w", "ln2_b", "norm_mix_2")):
                sp.dma_start(rows[:, r, :], I[name].to_broadcast([P, D])).then_inc(r_in, 16)
            for i in range(NT):
                if i >= 3:
                    sp.wait_ge(x2r, i - 2)
                sp.dma_start(xr[i % 3][:], K.x1[i * P:(i + 1) * P, :]).then_inc(x_in[i % 3], 16)

        @block.gpsimd
        def _(pool):
            for i in range(NT):
                pool.wait_ge(x2r, i + 1)
                pool.dma_start(K.x2[i * P:(i + 1) * P, :], t[i % 2][:]).then_inc(stored[i % 2], 16)
            for s in range(2):
                pool.wait_ge(stored[s], 16 * NT // 2)

        @block.tensor
        def _(pe):
            def back(i):
                if i >= 2:
                    pe.wait_ge(mev, i - 1)
                for k in range(KT):
                    last = nc.tensor.transpose(K.bank[2 * (i % 2) + k // 4][:, (k % 4) * P:(k % 4 + 1) * P],
                                               K.ynT[:, k, i * P:(i + 1) * P], K.ident[:])
                last.then_inc(mm, 1)

            def turn(i):
                pe.wait_ge(hr, i + 1)
                if i >= 2:
                    pe.wait_ge(tev, 2 * (i - 1))
                for k in range(KT):
                    last = nc.tensor.transpose(K.bank[4 + 2 * (i % 2) + k // 4][:, (k % 4) * P:(k % 4 + 1) * P],
                                               h[i % 2][:, k * P:(k + 1) * P], K.ident[:])
                last.then_inc(tr, 1)

            for i in range(NT):
                back(i)
                if i:
                    turn(i - 1)
            turn(NT - 1)

        @block.scalar
        def _(act):
            def take(i):
                act.wait_ge(tr, i + 1)
                for b in range(2):
                    nc.scalar.activation(K.h3T[:, 4 * b:4 * b + 4, i * P:(i + 1) * P],
                                         K.bank[4 + 2 * (i % 2) + b][:].rearrange("p (k t) -> p k t", k=4), ACT.Copy).then_inc(tev, 1)

            for i in range(NT):
                act.wait_ge(sq, 2 * i + 1)
                nc.scalar.activation(rs, rs, ACT.Sqrt).then_inc(sq, 1)
                act.wait_ge(ssr, 2 * i + 1)
                nc.scalar.activation(ss[:, i:i + 1], ss[:, i:i + 1], ACT.Sqrt).then_inc(ssr, 1)
                if i:
                    take(i - 1)
            take(NT - 1)

        @block.vector
        def _(dve):
            v = nc.vector
            link = Link(v, chain)
            dve.wait_ge(r_in, 48)
            for i in range(NT):
                x, y = xr[i % 3], t[i % 2]
                dve.wait_ge(mm, i + 1)
                if i >= 2:
                    dve.wait_ge(stored[i % 2], 16 * (i // 2))
                for b in range(2):
                    s = slice(b * HALF, (b + 1) * HALF)
                    last = v.tensor_tensor(y[:, s], K.bank[2 * (i % 2) + b][:], K.MOD[:, 5 * D + b * HALF:5 * D + (b + 1) * HALF], ALU.mult)
                last.then_inc(mev, 1)
                dve.wait_ge(mev, i + 1)
                dve.wait_ge(x_in[i % 3], 16 * (i // 3 + 1))
                link(v.scalar_tensor_tensor(out=y[:], in0=x[:], scalar=ALPHA, in1=y[:], op0=ALU.mult, op1=ALU.add))
                norm_rows(K, dve, link, y, st, mv, rs, sq, i)
                link(v.tensor_tensor(y[:], y[:], rows[:, 0, :], ALU.mult))
                v.tensor_tensor(y[:], y[:], rows[:, 1, :], ALU.add).then_inc(x2r, 1)
                dve.wait_ge(x2r, i + 1)
                if i >= 2:
                    dve.wait_ge(tr, i - 1)
                rms_rows(K, dve, link, h[i % 2], y, ss[:, i:i + 1], ssr, i)
                v.tensor_tensor(h[i % 2][:], h[i % 2][:], rows[:, 2, :], ALU.mult).then_inc(hr, 1)


def rms_rows(K, dve, link, out, x, ss, ssr, i):
    v = K.nc.vector
    link(v.tensor_tensor_reduce(out=out[:], in0=x[:], in1=x[:], scale=1.0, scalar=0.0, op0=ALU.mult, op1=ALU.add, accum_out=ss))
    v.tensor_scalar(ss, ss, 1.0 / D, RMS_EPS, ALU.mult, ALU.add).then_inc(ssr, 1)
    dve.wait_ge(ssr, 2 * i + 2)
    link(v.reciprocal(ss, ss))
    link(v.tensor_scalar(out[:], x[:], ss, None, ALU.mult))


def packed(i):
    return slice(P * i * (i + 1) // 2, P * (i + 1) * (i + 2) // 2)


def stage_project(K):
    nc, I = K.nc, K.I
    K.PJ = K.at("PJ", 0, [P, 6, NT, HALF])
    K.MS = K.at("MS", 96, [P, NT, N_MIX])
    ring = [K.at(f"pj_w{s}", 144 + 16 * s, [P, KT, HALF]) for s in range(2)]
    K.NM = K.at("NM", 176, [P, P * NT * (NT + 1) // 2])
    iqT = K.at("pj_iqT", 80, [P, 2, T])
    ikT = K.at("pj_ikT", 88, [P, T])
    ikd = K.at("pj_ikd", 92, [P, NT, P])
    ang, red, quar, kk = (K.at(f"pj_ang{n}", 194 + 1.375 * n, [P, NT, NFREQ]) for n in range(4))
    rel = [K.at(f"pj_rel{s}", 194 + 2 * s, [P, HALF]) for s in range(2)]
    run = K.at("pj_run", 194, [P, T])
    flag = K.at("pj_flag", 198, [P, T], mybir.dt.uint8)
    junk = K.at("pj_junk", 194, [P, P * NT * (NT + 1) // 2], mybir.dt.uint8)
    sqr = K.at("pj_sqr", 80, [P, NT, LAT])
    kvr = K.at("pj_kvr", 84, [P, LAT])
    scr = K.at("pj_scr", 86, [P, 2, NT * IH * FREQ_I])
    pscr = K.at("pj_pscr", 112, [P, 2, NT * RH * FREQ_R])
    used = [0]

    def columns(n, dt=F32):
        used[0] += n
        c = K.prm[:, used[0] - n:used[0]]
        return c if dt == F32 else c.bitcast(dt)

    NB = NT - 2
    sin, cos = (columns(NT * NFREQ).rearrange("p (i f) -> p i f", i=NT) for _ in range(2))
    freq, pos = columns(NFREQ), columns(NT)
    posi = columns(NT, I32)
    wq = columns(NT * IH).rearrange("p (i h) -> p i h", i=NT)
    ss = columns(NT)
    key, bit, cand, sign, flip, keep = (columns(NB, I32) for _ in range(6))
    cnt, need = columns(NB), columns(NB)
    w_in = [K.sem(f"pj_win{s}") for s in range(2)]
    names = "prm mm ev angr tab rope rms kvr itr iev smm relr used zero key chain pchain dqr rqr rkr".split()
    S = {n: K.sem("pj_" + n) for n in names}
    R_Q, R_K, R_V, R_G, D_Q, D_G = range(6)
    slabs = [None, D_Q, R_Q, R_K, R_V, R_G, D_G]
    pieces = [(i, h, c) for i in range(NT) for h in range(IH) for c in range(0, P * (i + 1), HALF)]

    def table(t, lo, n, heads):
        return t[:, :, lo:lo + n].unsqueeze(2).to_broadcast([P, NT, heads, n])

    with nc.Block() as block:
        @block.sync
        def _(sp):
            w = I["w_in_2"][0].rearrange("(k p) n -> p k n", p=P)
            sp.dma_start(ring[0][:, :, 0:M_IQ], w[:, :, C_LAT:C_LAT + M_IQ]).then_inc(w_in[0], 16)
            sp.dma_start(ring[0][:, :, M_IQ:N_MIX], w[:, :, C_IDX:C_IDX + N_IDX]).then_inc(w_in[0], 16)
            with nc.allow_non_contiguous_dma(reason="positions as columns"):
                sp.dma_start(posi[:], I["positions_2"].rearrange("(i p) -> p i", p=P)).then_inc(S["prm"], 16)
            sp.dma_start(freq[:], I["freq"].to_broadcast([P, NFREQ])).then_inc(S["prm"], 16)
            sp.dma_start(kvr[:], I["kv_norm_2"].to_broadcast([P, LAT])).then_inc(S["prm"], 16)
            for j in range(1, len(slabs)):
                col = C_GATE if slabs[j] == D_G else slabs[j] * HALF
                if j >= 2:
                    sp.wait_ge(S["mm"], NT * (j - 1))
                sp.dma_start(ring[j % 2][:], w[:, :, col:col + HALF]).then_inc(w_in[j % 2], 16)

        @block.tensor
        def _(pe):
            n = 0

            def slab(j, n):
                pe.wait_ge(w_in[j % 2], (32 if j % 2 == 0 else 16) + 16 * (j // 2))
                cols = N_MIX if j == 0 else HALF
                for i in range(NT):
                    if n >= 4:
                        pe.wait_ge(S["ev"], n - 3)
                    for k in range(KT):
                        last = nc.tensor.matmul(K.bank[n % 4][:, 0:cols], K.h3T[:, k, i * P:(i + 1) * P], ring[j % 2][:, k, 0:cols],
                                                start=(k == 0), stop=(k == KT - 1))
                    last.then_inc(S["mm"], 1)
                    n += 1
                return n

            n = slab(0, n)
            n = slab(1, n)
            pe.wait_ge(S["rope"], 1)
            for i in range(NT):
                if i >= 4:
                    pe.wait_ge(S["iev"], i - 3)
                b = K.bank[4 + i % 4]
                for m in range(2):
                    nc.tensor.transpose(b[:, m * P:(m + 1) * P], K.MS[:, i, M_IQ + m * P:M_IQ + (m + 1) * P], K.ident[:])
                nc.tensor.transpose(b[:, 2 * P:3 * P], ikd[:, i, :], K.ident[:]).then_inc(S["itr"], 1)
            pe.wait_ge(S["iev"], NT)
            for m, (i, h, c) in enumerate(pieces):
                if m >= 4:
                    pe.wait_ge(S["relr"], m - 3)
                r = slice(IDIM * (h % 4), IDIM * (h % 4 + 1))
                e = min(c + HALF, P * (i + 1))
                nc.tensor.matmul(K.bank[4 + m % 4][:, 0:e - c], iqT[r, h // 4, i * P:(i + 1) * P], ikT[r, c:e],
                                 start=True, stop=True).then_inc(S["smm"], 1)
            for j in range(2, len(slabs)):
                n = slab(j, n)

        @block.scalar
        def _(act):
            n = 0

            def slab(j, n):
                for i in range(NT):
                    act.wait_ge(S["mm"], n + 1)
                    dst = K.MS[:, i, :] if j == 0 else K.PJ[:, slabs[j], i, :]
                    func = ACT.Silu if slabs[j] in (R_G, D_G) else ACT.Copy
                    nc.scalar.activation(dst, K.bank[n % 4][:, 0:N_MIX if j == 0 else HALF], func).then_inc(S["ev"], 1)
                    n += 1
                return n

            act.wait_ge(S["angr"], 1)
            nc.scalar.activation(sin[:], red[:], ACT.Sin).then_inc(S["tab"], 1)
            nc.scalar.activation(cos[:], quar[:], ACT.Sin).then_inc(S["tab"], 1)
            n = slab(0, n)
            act.wait_ge(S["rms"], 1)
            nc.scalar.activation(ss[:], ss[:], ACT.Sqrt).then_inc(S["rms"], 1)
            n = slab(1, n)
            for i in range(NT):
                act.wait_ge(S["itr"], i + 1)
                b = K.bank[4 + i % 4]
                nc.scalar.activation(iqT[:, :, i * P:(i + 1) * P], b[:, 0:2 * P].rearrange("p (m t) -> p m t", m=2), ACT.Copy)
                nc.scalar.activation(ikT[:, i * P:(i + 1) * P], b[:, 2 * P:3 * P], ACT.Copy).then_inc(S["iev"], 1)
            for m, (i, h, c) in enumerate(pieces):
                act.wait_ge(S["smm"], m + 1)
                if m >= 2:
                    act.wait_ge(S["used"], m - 1)
                e = min(c + HALF, P * (i + 1))
                nc.scalar.activation(rel[m % 2][:, 0:e - c], K.bank[4 + m % 4][:, 0:e - c], ACT.Relu, scale=IDIM ** -0.5).then_inc(S["relr"], 1)
            for j in range(2, len(slabs)):
                n = slab(j, n)

        @block.gpsimd
        def _(pool):
            g = nc.gpsimd
            link = Link(g, S["pchain"])
            pool.wait_ge(S["tab"], 2)
            pool.wait_ge(S["mm"], NT * len(slabs))
            for wait, slab, lo, n in ((2, D_Q, FREQ_R, FREQ_A), (3, R_Q, 0, FREQ_R), (4, R_K, 0, FREQ_R)):
                pool.wait_ge(S["ev"], NT * wait)
                x = K.PJ[:, slab].rearrange("p i (h e) -> p i h e", h=RH)
                t, u = (pscr[:, a, 0:NT * RH * n].rearrange("p (i h f) -> p i h f", i=NT, h=RH) for a in range(2))
                cmul(nc, link, x[:, :, :, 0:n], x[:, :, :, n:2 * n], x[:, :, :, 0:n], x[:, :, :, n:2 * n],
                     table(cos, lo, n, RH), table(sin, lo, n, RH), t, u)

        @block.vector
        def _(dve):
            v = nc.vector
            link = Link(v, S["chain"])
            dve.wait_ge(S["prm"], 48)
            link(v.tensor_copy(pos[:], posi[:]))
            link(v.tensor_tensor(ang[:], pos[:].unsqueeze(2).to_broadcast([P, NT, NFREQ]), freq[:].unsqueeze(1).to_broadcast([P, NT, NFREQ]), ALU.mult))
            reduce_angle(nc, link, red[:], quar[:], ang[:], kk[:])
            dve.sem_inc(S["angr"], 1)
            dve.wait_ge(S["ev"], NT)
            lat = K.MS[:, :, 0:LAT]
            link(v.tensor_tensor(sqr[:], lat, lat, ALU.mult))
            link(v.tensor_reduce(ss[:], sqr[:], AX.X, ALU.add))
            v.tensor_scalar(ss[:], ss[:], 1.0 / LAT, RMS_EPS, ALU.mult, ALU.add).then_inc(S["rms"], 1)
            dve.wait_ge(S["tab"], 2)
            for at, heads, width, lo, n in ((M_PE, 1, PE_D, FREQ_R, FREQ_A), (M_IK, 1, IDIM, FREQ_R + FREQ_A, FREQ_I),
                                            (M_IQ, IH, IDIM, FREQ_R + FREQ_A, FREQ_I)):
                x = K.MS[:, :, at:at + heads * width].rearrange("p i (h e) -> p i h e", h=heads)
                t, u = (scr[:, a, 0:NT * heads * n].rearrange("p (i h f) -> p i h f", i=NT, h=heads) for a in range(2))
                cmul(nc, link, x[:, :, :, 0:n], x[:, :, :, n:2 * n], x[:, :, :, 0:n], x[:, :, :, n:2 * n],
                     table(cos, lo, n, heads), table(sin, lo, n, heads), t, u)
            dve.wait_ge(S["rms"], 2)
            link(v.reciprocal(ss[:], ss[:]))
            link(v.tensor_tensor(lat, lat, ss[:].unsqueeze(2).to_broadcast([P, NT, LAT]), ALU.mult))
            link(v.tensor_tensor(lat, lat, kvr[:].unsqueeze(1).to_broadcast([P, NT, LAT]), ALU.mult))
            for m in range(4):
                link(v.tensor_copy(ikd[:, :, m * IDIM:(m + 1) * IDIM], K.MS[:, :, M_IK:M_IK + IDIM]))
            link(v.tensor_scalar(wq[:], K.MS[:, :, M_IW:M_IW + IH], IH ** -0.5, None, ALU.mult))
            dve.sem_inc(S["rope"], 1)
            for m, (i, h, c) in enumerate(pieces):
                dve.wait_ge(S["relr"], m + 1)
                e = min(c + HALF, P * (i + 1))
                dst = K.NM[:, packed(i)][:, c:e]
                if h == 0:
                    ins = v.tensor_scalar(dst, rel[m % 2][:, 0:e - c], wq[:, i, h:h + 1], None, ALU.mult)
                else:
                    ins = v.scalar_tensor_tensor(out=dst, in0=rel[m % 2][:, 0:e - c], scalar=wq[:, i, h:h + 1], in1=dst, op0=ALU.mult, op1=ALU.add)
                ins.then_inc(S["used"], 1)
                dve.wait_ge(S["used"], m + 1)
            for i in range(2):
                link(v.memset(K.NM[:, packed(i)], 0.0))
            for i in range(NT):
                link(v.memset(K.NM[0:RCHUNK, packed(i)][:, P * (i + 1) - RCHUNK:], LOW))
            link(v.memset(key[:], 0))
            link(v.memset(bit[:], 1))
            link(v.tensor_scalar(bit[:], bit[:], 31, None, ALU.logical_shift_left))
            with dve.Fori(0, 32) as r:
                per = 8
                v.tensor_tensor(cand[:], key[:], bit[:], ALU.bitwise_or).then_inc(S["key"], 1)
                dve.wait_ge(S["key"], per * r + 1)
                v.tensor_scalar(sign[:], cand[:], 31, None, ALU.arith_shift_right).then_inc(S["key"], 1)
                dve.wait_ge(S["key"], per * r + 2)
                v.tensor_scalar(flip[:], sign[:], -1, -2147483648, ALU.bitwise_xor, ALU.bitwise_or).then_inc(S["key"], 1)
                dve.wait_ge(S["key"], per * r + 3)
                v.tensor_tensor(flip[:], cand[:], flip[:], ALU.bitwise_xor).then_inc(S["key"], 1)
                dve.wait_ge(S["key"], per * r + 4)
                for j in range(NB):
                    i = j + 2
                    last = v.tensor_scalar(junk[:, packed(i)], K.NM[:, packed(i)], flip[:, j:j + 1].bitcast(F32), 0.0, ALU.is_ge, ALU.add,
                                           accum_out=cnt[:, j:j + 1])
                last.then_inc(S["key"], 1)
                dve.wait_ge(S["key"], per * r + 5)
                v.tensor_scalar(keep[:], cnt[:], TOPK - 0.5, None, ALU.is_ge).then_inc(S["key"], 1)
                dve.wait_ge(S["key"], per * r + 6)
                v.tensor_scalar(bit[:], bit[:], 1, None, ALU.logical_shift_right).then_inc(S["key"], 1)
                v.copy_predicated(key[:], keep[:], cand[:]).then_inc(S["key"], 1)
                dve.wait_ge(S["key"], per * r + 8)
            link(v.tensor_scalar(sign[:], key[:], 31, None, ALU.arith_shift_right))
            link(v.tensor_scalar(flip[:], sign[:], -1, -2147483648, ALU.bitwise_xor, ALU.bitwise_or))
            link(v.tensor_tensor(flip[:], key[:], flip[:], ALU.bitwise_xor))
            for j in range(NB):
                i = j + 2
                n = P * (i + 1)
                thr, x = flip[:, j:j + 1].bitcast(F32), K.NM[:, packed(i)]
                link(v.tensor_scalar(flag[:, 0:n], x, thr, 0.0, ALU.is_gt, ALU.add, accum_out=cnt[:, j:j + 1]))
                link(v.tensor_scalar(need[:, j:j + 1], cnt[:, j:j + 1], -1.0, TOPK + 0.5, ALU.mult, ALU.add))
                link(v.tensor_scalar(flag[:, 0:n], x, thr, None, ALU.is_equal))
                link(v.tensor_tensor_scan(run[:, 0:n], flag[:, 0:n], flag[:, 0:n], 0.0, ALU.add, ALU.max))
                link(v.scalar_tensor_tensor(out=run[:, 0:n], in0=run[:, 0:n], scalar=need[:, j:j + 1], in1=flag[:, 0:n], op0=ALU.is_le, op1=ALU.mult))
                link(v.scalar_tensor_tensor(out=x, in0=x, scalar=thr, in1=run[:, 0:n], op0=ALU.is_gt, op1=ALU.add))
                link(v.tensor_scalar(x, x, 1.0, -LOW, ALU.subtract, ALU.mult))


def stage_retention(K):
    nc, I = K.nc, K.I
    J = RH // 2
    qT, kT, xq, rkz = ([K.at(f"rt_{n}{s}", kb + 2 * s, [P, J, P]) for s in range(2)]
                       for n, kb in (("qT", 112), ("kT", 116), ("xq", 120), ("kz", 132)))
    prob = [K.at(f"rt_prob{s}", 124 + 4 * s, [P, J, 2, P]) for s in range(2)]
    state = [K.at(f"rt_state{s}", 136 + s, [P, J, RD]) for s in range(2)]
    intra = K.at("rt_intra", 138, [P, J, 2, P])
    xi = K.at("rt_xi", 142, [P, J, P])
    row = K.at("rt_row", 109.75, [P, HALF])
    sqr = K.at("rt_sqr", 160, [P, RH, RD])
    K.dqT = K.at("dqT", 144, [P, J, T])
    zeta, decay = K.prm[:, 0:RH], K.prm[:, 8:8 + J]
    mu, var = (K.prm[:, 16 + RH * n:16 + RH * (n + 1)] for n in range(2))
    names = "const tr qkr dqr smm prob xqr kzr out oev upd state var gate norm done chain".split()
    S = {n: K.sem("rt_" + n) for n in names}
    R_Q, R_K, R_V, R_G, D_Q, D_G = range(6)

    with nc.Block() as block:
        @block.sync
        def _(sp):
            sp.dma_start(intra[:], I["intra"].rearrange("p (j a) t -> p j a t", a=2)).then_inc(S["const"], 16)
            sp.dma_start(xi[:], I["xi"]).then_inc(S["const"], 16)
            sp.dma_start(zeta, I["zeta"]).then_inc(S["const"], 16)
            sp.dma_start(decay, I["decay"]).then_inc(S["const"], 16)
            sp.dma_start(row[:], I["ret_norm_2"].to_broadcast([P, HALF])).then_inc(S["const"], 16)

        @block.tensor
        def _(pe):
            def turn(i):
                if i:
                    pe.wait_ge(S["qkr"], 2 * i)
                    pe.wait_ge(S["dqr"], i)
                for b, slab in enumerate((R_Q, R_K, D_Q)):
                    for j in range(J):
                        tr = nc.tensor.transpose(K.bank[b][:, j * P:(j + 1) * P], K.PJ[:, slab, i, j * P:(j + 1) * P], K.ident[:])
                    tr.then_inc(S["tr"], 1)

            turn(0)
            for i in range(NT):
                s = i % 2
                pe.wait_ge(S["qkr"], 2 * (i + 1))
                if i:
                    pe.wait_ge(S["prob"], i)
                for h in range(RH):
                    d = slice(RD * (h % 2), RD * (h % 2 + 1))
                    mm = nc.tensor.matmul(K.bank[3 + h % 2][:, (h // 2) * P:(h // 2 + 1) * P], kT[s][d, h // 2, :], qT[s][d, h // 2, :],
                                          start=True, stop=True)
                mm.then_inc(S["smm"], 1)
                if i + 1 < NT:
                    turn(i + 1)
                    pe.wait_ge(S["kzr"], i + 1)
                    if i:
                        pe.wait_ge(S["state"], i)
                    for j in range(J):
                        mm = nc.tensor.matmul(K.bank[7][:, j * P:(j + 1) * P], rkz[s][:, j, :], K.PJ[:, R_V, i, j * P:(j + 1) * P],
                                              start=True, stop=True)
                    mm.then_inc(S["upd"], 1)
                pe.wait_ge(S["prob"], i + 1)
                if i:
                    pe.wait_ge(S["xqr"], i + 1)
                    pe.wait_ge(S["state"], i)
                    pe.wait_ge(S["oev"], i)
                for h in range(RH):
                    o = K.bank[5 + h % 2][:, (h // 2) * RD:(h // 2 + 1) * RD]
                    d = slice(RD * (h % 2), RD * (h % 2 + 1))
                    mm = nc.tensor.matmul(o, prob[s][:, h // 2, h % 2, :], K.PJ[:, R_V, i, h * RD:(h + 1) * RD], start=True, stop=(i == 0))
                    if i:
                        mm = nc.tensor.matmul(o, xq[s][d, h // 2, :], state[s][d, h // 2, :], start=False, stop=True)
                mm.then_inc(S["out"], 1)

        @block.scalar
        def _(act):
            def take(i):
                if i >= 2:
                    act.wait_ge(S["xqr"], i - 1)
                act.wait_ge(S["tr"], 3 * i + 3)
                for b, dst in enumerate((qT[i % 2], kT[i % 2])):
                    nc.scalar.activation(dst[:], K.bank[b][:].rearrange("p (j t) -> p j t", j=J), ACT.Copy).then_inc(S["qkr"], 1)
                nc.scalar.activation(K.dqT[:, :, i * P:(i + 1) * P], K.bank[2][:].rearrange("p (j t) -> p j t", j=J), ACT.Copy).then_inc(S["dqr"], 1)

            take(0)
            for i in range(NT):
                if i + 1 < NT:
                    take(i + 1)
                act.wait_ge(S["out"], i + 1)
                for b in range(2):
                    ev = nc.scalar.activation(K.PJ[:, R_Q, i, :].rearrange("p (j a d) -> p j a d", a=2, d=RD)[:, :, b, :],
                                              K.bank[5 + b][:, 0:J * RD].rearrange("p (j d) -> p j d", j=J), ACT.Copy)
                ev.then_inc(S["oev"], 1)
                act.wait_ge(S["var"], 2 * i + 1)
                nc.scalar.activation(var, var, ACT.Sqrt).then_inc(S["var"], 1)

        @block.gpsimd
        def _(pool):
            g = nc.gpsimd
            pool.wait_ge(S["const"], 80)
            for i in range(NT):
                s = i % 2
                if i + 1 < NT:
                    if i >= 2:
                        pool.wait_ge(S["upd"], i - 1)
                    g.tensor_tensor(rkz[s][:].rearrange("p j (a d) -> p (j a) d", a=2), K.PJ[:, R_K, i, :].rearrange("p (h d) -> p h d", h=RH),
                                    zeta.unsqueeze(2).to_broadcast([P, RH, RD]), ALU.mult).then_inc(S["kzr"], 1)
                pool.wait_ge(S["qkr"], 2 * i + 1)
                if i >= 2:
                    pool.wait_ge(S["out"], i - 1)
                g.tensor_tensor(xq[s][:], qT[s][:], xi[:], ALU.mult).then_inc(S["xqr"], 1)
                g.tensor_tensor(K.PJ[:, R_G, i, :], K.PJ[:, R_G, i, :], row[:], ALU.mult).then_inc(S["gate"], 1)
                if i:
                    pool.wait_ge(S["gate"], i)
                    pool.wait_ge(S["norm"], i)
                    g.tensor_tensor(K.PJ[:, R_Q, i - 1, :], K.PJ[:, R_Q, i - 1, :], K.PJ[:, R_G, i - 1, :], ALU.mult).then_inc(S["done"], 1)
            pool.wait_ge(S["norm"], NT)
            pool.wait_ge(S["gate"], NT)
            g.tensor_tensor(K.PJ[:, R_Q, NT - 1, :], K.PJ[:, R_Q, NT - 1, :], K.PJ[:, R_G, NT - 1, :], ALU.mult).then_inc(S["done"], 1)

        @block.vector
        def _(dve):
            v = nc.vector
            link = Link(v, S["chain"])

            def norm(i):
                o = K.PJ[:, R_Q, i, :].rearrange("p (h d) -> p h d", h=RH)
                dve.wait_ge(S["oev"], i + 1)
                link(v.tensor_reduce(mu, o, AX.X, ALU.add))
                link(v.tensor_scalar(mu, mu, 1.0 / RD, None, ALU.mult))
                link(v.tensor_tensor(o, o, mu.unsqueeze(2).to_broadcast([P, RH, RD]), ALU.subtract))
                link(v.tensor_tensor(sqr[:], o, o, ALU.mult))
                link(v.tensor_reduce(var, sqr[:], AX.X, ALU.add))
                v.tensor_scalar(var, var, 1.0 / RD, RMS_EPS, ALU.mult, ALU.add).then_inc(S["var"], 1)
                dve.wait_ge(S["var"], 2 * i + 2)
                link(v.reciprocal(var, var))
                v.tensor_tensor(o, o, var.unsqueeze(2).to_broadcast([P, RH, RD]), ALU.mult).then_inc(S["norm"], 1)

            dve.wait_ge(S["const"], 80)
            for i in range(NT):
                s = i % 2
                dve.wait_ge(S["smm"], i + 1)
                if i >= 2:
                    dve.wait_ge(S["out"], i - 1)
                for a in range(2):
                    pr = v.tensor_tensor(prob[s][:, :, a, :], K.bank[3 + a][:].rearrange("p (j t) -> p j t", j=J), intra[:, :, a, :], ALU.mult)
                pr.then_inc(S["prob"], 1)
                if i + 1 < NT:
                    new = state[1 - s]
                    if i:
                        link(v.tensor_tensor(new[:], state[s][:], decay.unsqueeze(2).to_broadcast([P, J, RD]), ALU.mult))
                    dve.wait_ge(S["upd"], i + 1)
                    b = K.bank[7][:].rearrange("p (j c) -> p j c", j=J)
                    for a in range(2):
                        d = slice(RD * a, RD * (a + 1))
                        if i:
                            up = v.tensor_tensor(new[d], new[d], b[d, :, d], ALU.add)
                        else:
                            up = v.tensor_copy(new[d], b[d, :, d])
                    up.then_inc(S["state"], 1)
                    dve.wait_ge(S["state"], i + 1)
                if i:
                    norm(i - 1)
            norm(NT - 1)


def stage_attention(K):
    nc, I = K.nc, K.I
    J = AH // 2
    kfT = K.at("at_kT", 112, [P, J, T])
    val = K.at("at_v", 128, [P, NT, AH * AD])
    prob = [K.at(f"at_prob{s}", 160 + 4 * s, [P, T]) for s in range(2)]
    probT = [K.at(f"at_probT{s}", 168 + 4 * s, [P, NT, P]) for s in range(2)]
    latT = K.at("at_latT", 168, [P, T])
    peT = K.at("at_peT", 172, [PE_D, T])
    ukT = K.at("at_ukT", 194, [P, J, P])
    wuv = K.at("at_wuv", 196, [P, AH, AD])
    spread = K.at("at_spread", 198, [PE_D, 2, AD])
    uk = K.wsT
    den = K.prm[:, 0:NT * AH].rearrange("p (i h) -> p i h", i=NT)
    top = K.prm[:, 64:64 + 2]
    K.w_out2 = K.at("w_out2", 48, [P, KT, D])
    K.w_gate = K.at("w_gate", 16, [P, KT, D])
    K.end_in = K.sem("end_in")
    names = "zero uk wuv spread turn ukr latr pre prer lmm logit mx er tr pa pd pv done chain".split()
    S = {n: K.sem("at_" + n) for n in names}
    R_Q, R_K, R_V, R_G, D_Q, D_G = range(6)
    steps = [(i, h) for i in range(NT) for h in range(AH)]
    long_before = lambda n: sum(i >= 4 for i, h in steps[:n])
    n_pre = 2 * J + NT

    with nc.Block() as block:
        @block.sync
        def _(sp):
            sp.wait_ge(S["zero"], 2)
            for h in range(AH):
                sp.dma_start(uk[AD * (h % 2) + PE_D:AD * (h % 2 + 1), h // 2, :], I["w_uk_2"][0, h]).then_inc(S["uk"], 16)
            with nc.allow_non_contiguous_dma(reason="latent to partitions"):
                sp.dma_start(wuv[:], I["w_uv_2"][0].rearrange("h c d -> c h d")).then_inc(S["wuv"], 16)
            sp.dma_start(K.w_out2[:], I["w_out_2"][0].rearrange("(k p) n -> p k n", p=P)).then_inc(K.end_in, 16)
            sp.dma_start(K.w_gate[:], I["w_ple_gate_2"][0].rearrange("(k p) n -> p k n", p=P)).then_inc(K.end_in, 16)

        @block.gpsimd
        def _(pool):
            nc.gpsimd.memset(spread[:], 0.0).then_inc(S["zero"], 1)
            nc.gpsimd.memset(uk[:], 0.0).then_inc(S["zero"], 1)

        @block.tensor
        def _(pe):
            for i in range(NT):
                if i >= 4:
                    pe.wait_ge(S["latr"], i - 3)
                b = K.bank[i % 4]
                nc.tensor.transpose(b[:, 0:P], K.MS[:, i, 0:LAT], K.ident[:])
                nc.tensor.transpose(b[0:PE_D, P:2 * P], K.MS[:, i, M_PE:M_PE + PE_D], K.ident[:]).then_inc(S["turn"], 1)
            pe.wait_ge(S["uk"], 16 * AH)
            for j in range(J):
                tr = nc.tensor.transpose(K.bank[4][:, j * P:(j + 1) * P], uk[:, j, :], K.ident[:])
            tr.then_inc(S["ukr"], 1)
            pe.wait_ge(S["latr"], NT)
            pe.wait_ge(S["wuv"], 16)
            n = 0
            for i in range(NT):
                if n >= 4:
                    pe.wait_ge(S["prer"], n - 3)
                nc.tensor.matmul(K.bank[n % 4][:], latT[:, i * P:(i + 1) * P], wuv[:].rearrange("p h d -> p (h d)"),
                                 start=True, stop=True).then_inc(S["pre"], 1)
                n += 1
            pe.wait_ge(S["ukr"], 2)
            pe.wait_ge(S["spread"], 2)
            for j in range(J):
                for c in range(0, T, HALF):
                    pe.wait_ge(S["prer"], n - 3)
                    nc.tensor.matmul(K.bank[n % 4][:], ukT[:, j, :], latT[:, c:c + HALF], start=True, stop=False)
                    nc.tensor.matmul(K.bank[n % 4][:], spread[:].rearrange("p a d -> p (a d)"), peT[:, c:c + HALF],
                                     start=False, stop=True).then_inc(S["pre"], 1)
                    n += 1
            pe.wait_ge(S["prer"], n_pre)

            def logits(n):
                i, h = steps[n]
                d = slice(AD * (h % 2), AD * (h % 2 + 1))
                if n >= 2:
                    pe.wait_ge(S["logit"], n - 1)
                for c in range(0, P * (i + 1), HALF):
                    e = min(c + HALF, P * (i + 1))
                    mm = nc.tensor.matmul(K.bank[2 * (h % 2) + c // HALF][:, 0:e - c], K.dqT[d, h // 2, i * P:(i + 1) * P], kfT[d, h // 2, c:e],
                                          start=True, stop=True)
                mm.then_inc(S["lmm"], 1)

            def turn(n):
                i, h = steps[n]
                pe.wait_ge(S["er"], n + 1)
                if n:
                    pe.wait_ge(S["pa"], n)
                    if long_before(n):
                        pe.wait_ge(S["pd"], long_before(n))
                for t in range(i + 1):
                    tr = nc.tensor.transpose(K.bank[4 + t // 4][:, (t % 4) * P:(t % 4 + 1) * P], prob[n % 2][:, t * P:(t + 1) * P], K.ident[:])
                tr.then_inc(S["tr"], 1)

            def values(n):
                i, h = steps[n]
                pe.wait_ge(S["pa"], n + 1)
                if i >= 4:
                    pe.wait_ge(S["pd"], long_before(n + 1))
                if h == 0 and i >= 2:
                    pe.wait_ge(S["done"], i - 1)
                for t in range(i + 1):
                    mm = nc.tensor.matmul(K.bank[6 + i % 2][:, h * AD:(h + 1) * AD], probT[n % 2][:, t, :], val[:, t, h * AD:(h + 1) * AD],
                                          start=(t == 0), stop=(t == i))
                mm.then_inc(S["pv"], 1)

            logits(0)
            for n in range(len(steps)):
                if n + 1 < len(steps):
                    logits(n + 1)
                turn(n)
                if n:
                    values(n - 1)
            values(len(steps) - 1)

        @block.scalar
        def _(act):
            for i in range(NT):
                act.wait_ge(S["turn"], i + 1)
                b = K.bank[i % 4]
                nc.scalar.activation(latT[:, i * P:(i + 1) * P], b[:, 0:P], ACT.Copy)
                nc.scalar.activation(peT[:, i * P:(i + 1) * P], b[0:PE_D, P:2 * P], ACT.Copy).then_inc(S["latr"], 1)
            act.wait_ge(S["ukr"], 1)
            nc.scalar.activation(ukT[:], K.bank[4][:].rearrange("p (j r) -> p j r", j=J), ACT.Copy).then_inc(S["ukr"], 1)
            for n in range(n_pre):
                act.wait_ge(S["pre"], n + 1)
                m = n - NT
                dst = val[:, n, :] if n < NT else kfT[:, m // 2, (m % 2) * HALF:(m % 2 + 1) * HALF]
                nc.scalar.activation(dst, K.bank[n % 4][:], ACT.Copy).then_inc(S["prer"], 1)

            def expo(n):
                i, h = steps[n]
                act.wait_ge(S["mx"], n + 1)
                x = prob[n % 2][:, 0:P * (i + 1)]
                nc.scalar.activation(x, x, ACT.Exp, bias=top[:, n % 2:n % 2 + 1], accum_out=den[:, i, h:h + 1]).then_inc(S["er"], 1)

            def take(n):
                i, h = steps[n]
                act.wait_ge(S["tr"], n + 1)
                if n >= 2:
                    act.wait_ge(S["pv"], n - 1)
                c = min(i + 1, 4)
                nc.scalar.activation(probT[n % 2][:, 0:c, :], K.bank[4][:, 0:c * P].rearrange("p (s t) -> p s t", s=c), ACT.Copy).then_inc(S["pa"], 1)

            expo(0)
            for n in range(len(steps)):
                if n + 1 < len(steps):
                    expo(n + 1)
                take(n)

        @block.vector
        def _(dve):
            v = nc.vector
            link = Link(v, S["chain"])
            dve.wait_ge(S["zero"], 1)
            for a in range(2):
                v.tensor_copy(spread[:, a, 0:PE_D], K.ident[0:PE_D, 0:PE_D]).then_inc(S["spread"], 1)

            def logit(n):
                i, h = steps[n]
                w = P * (i + 1)
                dve.wait_ge(S["lmm"], n + 1)
                if n >= 2:
                    dve.wait_ge(S["tr"], n - 1)
                b = K.ps[:, 2 * (h % 2):2 * (h % 2) + 2, :].rearrange("p b c -> p (b c)")
                mx = top[:, n % 2:n % 2 + 1]
                v.tensor_tensor_reduce(out=prob[n % 2][:, 0:w], in0=b[:, 0:w], in1=K.NM[:, packed(i)], scale=AD ** -0.5, scalar=LOW,
                                       op0=ALU.add, op1=ALU.max, accum_out=mx).then_inc(S["logit"], 1)
                dve.wait_ge(S["logit"], n + 1)
                v.tensor_scalar(mx, mx, -1.0, None, ALU.mult).then_inc(S["mx"], 1)

            def take(n):
                i, h = steps[n]
                if i < 4:
                    return
                dve.wait_ge(S["tr"], n + 1)
                dve.wait_ge(S["pv"], n - 1)
                c = i + 1 - 4
                v.tensor_copy(probT[n % 2][:, 4:4 + c, :], K.bank[5][:, 0:c * P].rearrange("p (s t) -> p s t", s=c)).then_inc(S["pd"], 1)

            def finish(i):
                dve.wait_ge(S["pv"], AH * (i + 1))
                g = K.PJ[:, D_G, i, :]
                v.tensor_tensor(g, K.bank[6 + i % 2][:], g, ALU.mult).then_inc(S["done"], 1)
                dve.wait_ge(S["done"], i + 1)
                link(v.reciprocal(den[:, i, :], den[:, i, :]))
                g = g.rearrange("p (h d) -> p h d", h=AH)
                link(v.tensor_tensor(g, g, den[:, i, :].unsqueeze(2).to_broadcast([P, AH, AD]), ALU.mult))

            dve.wait_ge(S["prer"], n_pre)
            logit(0)
            for n in range(len(steps)):
                if n + 1 < len(steps):
                    logit(n + 1)
                take(n)
                if n and steps[n][1] == 0:
                    finish(steps[n - 1][0])
            finish(NT - 1)


def stage_second_end(K):
    nc, I = K.nc, K.I
    MIX = (K.PJ[:, 0], K.PJ[:, 5])
    w_proj = K.at("w_proj", 96, [P, 2, D])
    pn = K.at("se_pn", 104, [P, NT, 2, P])
    mT = [K.at(f"se_mT{s}", 112 + 4 * s, [P, KT, P]) for s in range(2)]
    xr = [K.at(f"se_x2{s}", 120 + 4 * s, [P, D]) for s in range(3)]
    x3 = [K.at(f"se_x3{s}", 132 + 4 * s, [P, D]) for s in range(3)]
    h = [K.at(f"se_h{s}", 144 + 4 * s, [P, D]) for s in range(2)]
    hT = [K.at(f"se_hT{s}", 152 + 4 * s, [P, KT, P]) for s in range(2)]
    gate = [K.at(f"se_gate{s}", 160 + 4 * s, [P, D]) for s in range(2)]
    rows = K.at("se_rows", 168, [P, 2, D])
    y = [K.at(f"se_y{s}", 176 + 4 * s, [P, D]) for s in range(2)]
    pT = K.at("se_pT", 184, [P, 2, T])
    ss, ss2 = K.prm[:, 0:NT], K.prm[:, NT:2 * NT]
    p_in, r_in, wp_in = K.sem("se_pin"), K.sem("se_rin"), K.sem("se_wpin")
    x_in = [K.sem(f"se_xin{s}") for s in range(3)]
    stored = [K.sem(f"se_st{s}") for s in range(2)]
    names = "ptr ptev mtr mtev omm oev ssr hr htr htev gmm gr pmm used x4 ssr2 outr chain".split()
    S = {n: K.sem("se_" + n) for n in names}
    with nc.Block() as block:
        @block.sync
        def _(sp):
            sp.dma_start(pn[:], I["p_2"][0, 0].rearrange("(i p) (k c) -> p i k c", p=P, k=2)).then_inc(p_in, 16)
            for i in range(NT):
                if i >= 3:
                    sp.wait_ge(S["oev"], 2 * (i - 2))
                sp.dma_start(xr[i % 3][:], K.x2[i * P:(i + 1) * P, :]).then_inc(x_in[i % 3], 16)
                if i == 0:
                    for r, name in enumerate(("norm_ple_2", "norm_final_2")):
                        src = I[name] if name == "norm_ple_2" else I[name].unsqueeze(0)
                        sp.dma_start(rows[:, r, :], src.to_broadcast([P, D])).then_inc(r_in, 16)
                    sp.dma_start(w_proj[:], I["w_ple_proj_2"][0].rearrange("(k p) n -> p k n", p=P)).then_inc(wp_in, 16)

        @block.gpsimd
        def _(pool):
            for i in range(NT):
                pool.wait_ge(S["outr"], i + 1)
                pool.dma_start(K.out[0, i * P:(i + 1) * P, :], y[i % 2][:]).then_inc(stored[i % 2], 16)
            for s in range(2):
                pool.wait_ge(stored[s], 16 * NT // 2)

        @block.tensor
        def _(pe):
            pbank = (0, 1, 2, 7)

            def turn_mix(i):
                if i == 0:
                    pe.wait_ge(S["ptev"], 2)
                else:
                    pe.wait_ge(S["mtev"], 2 * i)
                    if i >= 2:
                        pe.wait_ge(S["htev"], 2 * (i - 1))
                for k in range(KT):
                    tr = nc.tensor.transpose(K.bank[k // 4][:, (k % 4) * P:(k % 4 + 1) * P], MIX[k // 4][:, i, (k % 4) * P:(k % 4 + 1) * P], K.ident[:])
                tr.then_inc(S["mtr"], 1)

            def output(i):
                pe.wait_ge(S["mtev"], 2 * (i + 1))
                if i:
                    pe.wait_ge(S["oev"], 2 * i)
                for b in range(2):
                    for k in range(KT):
                        mm = nc.tensor.matmul(K.bank[3 + b][:], mT[i % 2][:, k, :], K.w_out2[:, k, b * HALF:(b + 1) * HALF], start=(k == 0), stop=(k == KT - 1))
                    mm.then_inc(S["omm"], 1)

            def turn_h(i):
                pe.wait_ge(S["hr"], i + 1)
                pe.wait_ge(S["mtev"], 2 * min(i + 2, NT))
                for k in range(KT):
                    tr = nc.tensor.transpose(K.bank[k // 4][:, (k % 4) * P:(k % 4 + 1) * P], h[i % 2][:, k * P:(k + 1) * P], K.ident[:])
                tr.then_inc(S["htr"], 1)

            def project(i):
                if i == 0:
                    pe.wait_ge(wp_in, 16)
                    pe.wait_ge(S["ptev"], 4)
                else:
                    pe.wait_ge(S["used"], 2 * i)
                for b in range(2):
                    for k in range(2):
                        mm = nc.tensor.matmul(K.bank[(2, 7)[b]][:], pT[:, k, i * P:(i + 1) * P], w_proj[:, k, b * HALF:(b + 1) * HALF], start=(k == 0), stop=(k == 1))
                    mm.then_inc(S["pmm"], 1)

            def gates(i):
                pe.wait_ge(S["htev"], 2 * (i + 1))
                if i:
                    pe.wait_ge(S["gr"], 2 * i)
                for b in range(2):
                    for k in range(KT):
                        mm = nc.tensor.matmul(K.bank[5 + b][:], hT[i % 2][:, k, :], K.w_gate[:, k, b * HALF:(b + 1) * HALF], start=(k == 0), stop=(k == KT - 1))
                    mm.then_inc(S["gmm"], 1)

            pe.wait_ge(p_in, 16)
            for b in range(4):
                for m in range(2):
                    for k in range(2):
                        tr = nc.tensor.transpose(K.bank[pbank[b]][:, (2 * k + m) * P:(2 * k + m + 1) * P], pn[:, 2 * b + m, k, :], K.ident[:])
                tr.then_inc(S["ptr"], 1)
            turn_mix(0)
            pe.wait_ge(K.end_in, 32)
            output(0)
            turn_mix(1)
            for i in range(1, NT):
                output(i)
                turn_h(i - 1)
                project(i - 1)
                if i + 1 < NT:
                    turn_mix(i + 1)
                gates(i - 1)
            turn_h(NT - 1)
            project(NT - 1)
            gates(NT - 1)

        @block.scalar
        def _(act):
            def take(dst, done, i, sem):
                act.wait_ge(done, i + 1)
                for b in range(2):
                    nc.scalar.activation(dst[i % 2][:, 4 * b:4 * b + 4, :], K.bank[b][:].rearrange("p (k t) -> p k t", k=4), ACT.Copy).then_inc(sem, 1)

            def take_mix(i):
                if i >= 2:
                    act.wait_ge(S["omm"], 2 * (i - 1))
                take(mT, S["mtr"], i, S["mtev"])

            def take_h(i):
                if i >= 2:
                    act.wait_ge(S["gmm"], 2 * (i - 1))
                take(hT, S["htr"], i, S["htev"])

            def root(col, sem, i):
                act.wait_ge(sem, 2 * i + 1)
                nc.scalar.activation(col[:, i:i + 1], col[:, i:i + 1], ACT.Sqrt).then_inc(sem, 1)

            def sigmoid(i):
                if i >= 2:
                    act.wait_ge(S["x4"], i - 1)
                for b in range(2):
                    act.wait_ge(S["gmm"], 2 * i + b + 1)
                    nc.scalar.activation(gate[i % 2][:, b * HALF:(b + 1) * HALF], K.bank[5 + b][:], ACT.Sigmoid).then_inc(S["gr"], 1)

            for b in range(4):
                act.wait_ge(S["ptr"], b + 1)
                nc.scalar.activation(pT[:, :, 2 * b * P:2 * (b + 1) * P], K.bank[(0, 1, 2, 7)[b]][:].rearrange("p (k t) -> p k t", k=2), ACT.Copy).then_inc(S["ptev"], 1)
            take_mix(0)
            take_mix(1)
            root(ss, S["ssr"], 0)
            for i in range(1, NT):
                root(ss, S["ssr"], i)
                take_h(i - 1)
                if i + 1 < NT:
                    take_mix(i + 1)
                sigmoid(i - 1)
                root(ss2, S["ssr2"], i - 1)
            take_h(NT - 1)
            sigmoid(NT - 1)
            root(ss2, S["ssr2"], NT - 1)

        @block.vector
        def _(dve):
            v = nc.vector
            link = Link(v, S["chain"])

            def residual(i):
                x = x3[i % 3]
                dve.wait_ge(x_in[i % 3], 16 * (i // 3 + 1))
                for b in range(2):
                    s = slice(b * HALF, (b + 1) * HALF)
                    dve.wait_ge(S["omm"], 2 * i + b + 1)
                    v.tensor_tensor(x[:, s], K.bank[3 + b][:], xr[i % 3][:, s], ALU.add).then_inc(S["oev"], 1)
                dve.wait_ge(S["oev"], 2 * (i + 1))
                if i >= 2:
                    dve.wait_ge(S["htr"], i - 1)
                rms_rows(K, dve, link, h[i % 2], x, ss[:, i:i + 1], S["ssr"], i)
                v.tensor_tensor(h[i % 2][:], h[i % 2][:], rows[:, 0, :], ALU.mult).then_inc(S["hr"], 1)

            def finish(i):
                g = gate[i % 2]
                for b in range(2):
                    s = slice(b * HALF, (b + 1) * HALF)
                    dve.wait_ge(S["gr"], 2 * i + b + 1)
                    dve.wait_ge(S["pmm"], 2 * i + b + 1)
                    v.tensor_tensor(g[:, s], K.bank[(2, 7)[b]][:], g[:, s], ALU.mult).then_inc(S["used"], 1)
                dve.wait_ge(S["used"], 2 * (i + 1))
                v.tensor_tensor(x3[i % 3][:], x3[i % 3][:], g[:], ALU.add).then_inc(S["x4"], 1)
                dve.wait_ge(S["x4"], i + 1)
                if i >= 2:
                    dve.wait_ge(stored[i % 2], 16 * (i // 2))
                rms_rows(K, dve, link, y[i % 2], x3[i % 3], ss2[:, i:i + 1], S["ssr2"], i)
                v.tensor_tensor(y[i % 2][:], y[i % 2][:], rows[:, 1, :], ALU.mult).then_inc(S["outr"], 1)

            dve.wait_ge(r_in, 32)
            residual(0)
            for i in range(1, NT):
                residual(i)
                finish(i - 1)
            finish(NT - 1)


def build(nc, I, out):
    K = setup(nc, I, out)
    for stage in (stage_modulate, stage_s5, stage_mixers, stage_join, stage_ffn, stage_first_end,
                  stage_project, stage_retention, stage_attention, stage_second_end):
        stage(K)
        if stage is stage_first_end:
            nc.clear_and_free_semaphores(K.sems)
            nc.all_engine_barrier()


def kernel(**inputs):
    import concourse.bacc as bacc
    from concourse.bass_utils import run_bass_kernel_spmd

    nc = bacc.Bacc("TRN2", target_bir_lowering=False, num_devices=1)
    arrays = {f"in_{name}": np.ascontiguousarray(a) for name, a in {**inputs, **constants()}.items()}
    I = {name[3:]: nc.dram_tensor(name, a.shape, mybir.dt.from_np(a.dtype), kind="ExternalInput").ap() for name, a in arrays.items()}
    out = nc.dram_tensor("out", (1, T, D), F32, kind="ExternalOutput").ap()
    build(nc, I, out)
    return run_bass_kernel_spmd(nc, [arrays], core_ids=[0]).results[0]["out"]
```

```python
import math

import numpy as np

import concourse.bass as bass
from concourse import mybir

F32 = mybir.dt.float32
I32 = mybir.dt.int32
FR = mybir.dt.float32r
ALU = mybir.AluOpType
ACT = mybir.ActivationFunctionType
AX = mybir.AxisListType

P = 128
T = 1024
TC = 256
D = 1024
KT = D // P
NT = T // P
NCT = TC // P
W = 256
HALF = 512
HEADS, HD = 4, 64
LN_EPS = 1e-5
RMS_EPS = 1e-6
DFF = 2816
NF = DFF // P
ALPHA = 2.0 ** 0.25
OFF_B = 4 * W + 16
OFF_C = OFF_B + 2 * W
OFF_D = OFF_C + 2 * W
CONV, PAD, GRID = 31, 15, 64
ROWS = T // GRID
G16, SP, SN, SC = 16, 16, 64, 8
GP = G16 // 2
NCH, NCC = T // SC, TC // SC
NCA = NCH + NCC
LOW = -1.0e30
MAGIC = 1.5 * 2.0 ** 23
LOG2E = 1.4426950408889634
LN2_HI, LN2_LO = 0.693359375, -2.12194440054690583e-4
INV_2PI = 1.0 / (2.0 * math.pi)
TWO_PI_1 = 6.28125
TWO_PI_2 = float(np.float32(round((2.0 * math.pi - TWO_PI_1) * 2 ** 20) / 2 ** 20))
TWO_PI_3 = 2.0 * math.pi - TWO_PI_1 - TWO_PI_2
PI_IN = 3.1415925


RH, RD = 8, 64
RCHUNK = 64
AH, AD = 8, 64
PE_D, NOPE, LAT = 16, 48, 128
IH, IDIM, IROT = 8, 32, 8
TOPK = 256
FREQ_R, FREQ_A, FREQ_I = RD // 2, PE_D // 2, IROT // 2
NFREQ = FREQ_R + FREQ_A + FREQ_I
C_LAT = 5 * HALF
C_GATE = C_LAT + LAT + PE_D
C_IDX = C_GATE + HALF
N_IDX = IH * IDIM + IDIM + IH
M_PE, M_IQ = LAT, LAT + PE_D
M_IK = M_IQ + IH * IDIM
M_IW = M_IK + IDIM
N_MIX = M_IW + IH


def constants():
    def freq(theta, r):
        return theta ** (-np.arange(0, r, 2, dtype=np.float64) / r)

    log_g = np.log1p(-np.exp2(-5.0 - np.arange(RH)))
    n = np.arange(P)
    gap, chunk = n[None, :] - n[:, None], n // RCHUNK
    seen = chunk[None, :] >= chunk[:, None]
    intra = np.exp(log_g[:, None, None] * np.abs(gap)) * seen * RD ** -0.5
    pair = np.repeat(np.arange(2), RD)
    head = 2 * np.arange(RH // 2)[None, :] + pair[:, None]
    return {
        "freq": np.concatenate([freq(10000.0, RD), freq(500000.0, PE_D), freq(500000.0, IROT)])[None].astype(np.float32),
        "intra": intra.transpose(1, 0, 2).astype(np.float32),
        "xi": (np.exp(log_g[head][:, :, None] * (n + 1.0)) * RD ** -0.5).astype(np.float32),
        "zeta": np.exp(log_g[None, :] * (P - 1.0 - n)[:, None]).astype(np.float32),
        "decay": np.exp(log_g[head] * P).astype(np.float32),
    }


class Kept:

    def __init__(self, nc, I, out):
        self.nc, self.I, self.out = nc, I, out


class Link:

    def __init__(self, eng, sem):
        self.eng, self.sem, self.n = eng, sem, 0

    def __call__(self, ins):
        self.n += 1
        ins.then_inc(self.sem, 1)
        self.eng.wait_ge(self.sem, self.n)


def setup(nc, I, out):
    K = Kept(nc, I, out)
    K.ps = nc.alloc_psum_tensor("ps", [P, 8, HALF], F32)
    K.bank = [K.ps[:, i, :] for i in range(8)]
    K.ident = nc.alloc_sbuf_tensor("ident", [P, P], F32)
    K.ones = nc.alloc_sbuf_tensor("ones", [P, P], F32)
    K.prm = nc.alloc_sbuf_tensor("prm", [P, 1152], F32)
    K.eps = nc.alloc_sbuf_tensor("eps", [P, 1], F32)
    K.wsT = nc.alloc_sbuf_tensor("wsT", [P, 4, P], F32)
    K.base = 24 * 1024
    K.sems = []

    def at(name, kb, shape, dt=F32):
        return nc.alloc_sbuf_tensor_at(name, shape, dt, offset=K.base + int(kb * 1024))

    def sem(name):
        K.sems.append(nc.alloc_semaphore(name))
        return K.sems[-1]

    K.at, K.sem = at, sem
    K.MOD = at("MOD", 0, [P, 6 * D])
    K.HT = at("HT", 24, [P, KT, TC + T])
    K.ydT = at("ydT", 64, [P, 2, T])
    K.HTP = at("HTP", 64, [P, KT, TC])
    K.yT = [at(f"yT{k}", 24 + 4 * k, [P, T]) for k in range(6)] + [K.ydT[:, k, :] for k in range(2)]
    return K


def stage_modulate(K):
    nc, I = K.nc, K.I
    NS, NCK, NCX = 4, 12, 4
    ring = [K.at(f"mod_w{s}", 72 + 16 * s, [P, KT, HALF]) for s in range(NS)]
    brow = K.at("mod_b", 136, [1, NS, HALF])
    cols = K.at("mod_c", 144, [P, 2, KT])
    cb = K.at("mod_cb", 145, [P, 2, KT, P])
    MODC = K.at("MODC", 153, [P, NCX * HALF])
    xr = [K.at(f"mod_x{s}", 161 + 4 * s, [P, D]) for s in range(3)]
    hb = [K.at(f"mod_h{s}", 173 + 4 * s, [P, D]) for s in range(2)]
    c_in, c_act, c_bc = K.sem("c_in"), K.sem("c_act"), K.sem("c_bc")
    consts = K.sem("consts")
    w_in = [K.sem(f"modw_in{s}") for s in range(NS)]
    mod_mm, mod_ev, ctx_mm, ctx_ev = K.sem("mod_mm"), K.sem("mod_ev"), K.sem("ctx_mm"), K.sem("ctx_ev")
    x_in = [K.sem(f"modx_in{s}") for s in range(3)]
    h_mul, h_rdy, h_tr, h_ev = K.sem("h_mul"), K.sem("h_rdy"), K.sem("h_tr"), K.sem("h_ev")
    w_mod = I["w_mod"][0].rearrange("(p t) n -> p t n", t=KT)
    tiles = NCT + NT

    def src(i):
        return I["ctx"][0][i * P:(i + 1) * P, :] if i < NCT else I["x"][0][(i - NCT) * P:(i - NCT + 1) * P, :]

    with nc.Block() as block:
        @block.sync
        def _(sp):
            sp.dma_start(cols[:, 0, :], I["c"][0].rearrange("(p t) -> p t", t=KT)).then_inc(c_in, 16)
            sp.dma_start(cols[:, 1, :], I["c_ctx"].rearrange("(p t) -> p t", t=KT)).then_inc(c_in, 16)
            for s in range(NS):
                sp.dma_start(ring[s][:], w_mod[:, :, s * HALF:(s + 1) * HALF]).then_inc(w_in[s], 16)
                sp.dma_start(brow[:, s, :], I["b_mod"][:, s * HALF:(s + 1) * HALF]).then_inc(w_in[s], 16)
            with sp.Fori(1, NCK // NS) as r:
                for s in range(NS):
                    sp.wait_ge(mod_mm, NS * r + s - (NS - 1))
                    sp.dma_start(ring[s][:], w_mod[:, :, bass.ds(r * (NS * HALF) + s * HALF, HALF)]).then_inc(w_in[s], 16)
                    sp.dma_start(brow[:, s, :], I["b_mod"][:, bass.ds(r * (NS * HALF) + s * HALF, HALF)]).then_inc(w_in[s], 16)

        @block.gpsimd
        def _(pool):
            nc.gpsimd.memset(K.eps[:], RMS_EPS)
            nc.gpsimd.memset(K.ident[:], 0.0).then_inc(consts, 1)
            nc.gpsimd.memset(K.ones[:], 1.0).then_inc(consts, 1)
            pool.wait_ge(consts, 2)
            nc.gpsimd.affine_select(out=K.ident[:], in_=K.ident[:], compare_op=ALU.not_equal, fill=1.0, base=0,
                                    pattern=[[-1, P]], channel_multiplier=1).then_inc(consts, 1)
            for i in range(tiles):
                if i >= 3:
                    pool.wait_ge(h_rdy, i - 2)
                pool.dma_start(xr[i % 3][:], src(i)).then_inc(x_in[i % 3], 16)

        @block.scalar
        def _(act):
            act.wait_ge(c_in, 32)
            nc.scalar.activation(cols[:], cols[:], ACT.Silu).then_inc(c_act, 1)

            def evacuate(j, col):
                act.wait_ge(mod_mm, j + 1)
                nc.scalar.activation(K.MOD[:, col], K.bank[j % 2][:], ACT.Copy).then_inc(mod_ev, 1)

            for j in range(NCX):
                act.wait_ge(ctx_mm, j + 1)
                nc.scalar.activation(MODC[:, j * HALF:(j + 1) * HALF], K.bank[2 + j % 2][:], ACT.Copy).then_inc(ctx_ev, 1)
                evacuate(j, slice(j * HALF, (j + 1) * HALF))
            for i in range(tiles):
                act.wait_ge(h_tr, i + 1)
                for b in range(2):
                    nc.scalar.activation(K.HT[:, 4 * b:4 * b + 4, i * P:(i + 1) * P],
                                         K.bank[4 + 2 * (i % 2) + b][:].rearrange("p (k t) -> p k t", k=4),
                                         ACT.Copy).then_inc(h_ev, 1)
                    if i < NCT:
                        nk = P // SC
                        for k in range(4):
                            nc.scalar.activation(K.HTP[:, 4 * b + k, :].rearrange("p (s c) -> p c s", s=SC)[:, i * nk:(i + 1) * nk, :],
                                                 K.bank[4 + 2 * (i % 2) + b][:, k * P:(k + 1) * P].rearrange("p (c s) -> p c s", s=SC),
                                                 ACT.Copy).then_inc(h_ev, 1)
            with act.Fori(1, NCK // NS) as r:
                for s in range(NS):
                    act.wait_ge(mod_mm, NS * r + s + 1)
                    nc.scalar.activation(K.MOD[:, bass.ds(r * (NS * HALF) + s * HALF, HALF)], K.bank[s % 2][:],
                                         ACT.Copy).then_inc(mod_ev, 1)

        @block.vector
        def _(dve):
            dve.wait_ge(c_act, 1)
            nc.vector.tensor_copy(cb[:], cols[:].unsqueeze(3).to_broadcast([P, 2, KT, P])).then_inc(c_bc, 1)
            dve.wait_ge(ctx_ev, NCX)
            dve.wait_ge(mod_ev, NCX)
            for i in range(tiles):
                m = MODC if i < NCT else K.MOD
                dve.wait_ge(x_in[i % 3], 16 * (i // 3 + 1))
                if i >= 2:
                    dve.wait_ge(h_tr, i - 1)
                nc.vector.scalar_tensor_tensor(out=hb[i % 2][:], in0=m[:, D:2 * D], scalar=1.0, in1=xr[i % 3][:],
                                               op0=ALU.add, op1=ALU.mult).then_inc(h_mul, 1)
                dve.wait_ge(h_mul, i + 1)
                nc.vector.tensor_tensor(hb[i % 2][:], hb[i % 2][:], m[:, 0:D], ALU.add).then_inc(h_rdy, 1)

        @block.tensor
        def _(pe):
            pe.wait_ge(c_bc, 1)
            pe.wait_ge(consts, 3)

            def product(bank, which, s, done):
                for k in range(KT):
                    nc.tensor.matmul(bank[:], cb[:, which, k, :], ring[s][:, k, :], start=(k == 0), stop=False)
                nc.tensor.matmul(bank[:], K.ones[0:1, :], brow[:, s, :], start=False, stop=True).then_inc(done, 1)

            for j in range(NCX):
                pe.wait_ge(w_in[j], 32)
                if j >= 2:
                    pe.wait_ge(ctx_ev, j - 1)
                    pe.wait_ge(mod_ev, j - 1)
                product(K.bank[2 + j % 2], 1, j, ctx_mm)
                product(K.bank[j % 2], 0, j, mod_mm)
            for i in range(tiles):
                pe.wait_ge(h_rdy, i + 1)
                if i >= 2:
                    pe.wait_ge(h_ev, 2 * (i - 1) + 8 * min(i - 1, NCT))
                for k in range(KT):
                    tr = nc.tensor.transpose(K.bank[4 + 2 * (i % 2) + k // 4][:, (k % 4) * P:(k % 4 + 1) * P],
                                             hb[i % 2][:, k * P:(k + 1) * P], K.ident[:])
                tr.then_inc(h_tr, 1)
            with pe.Fori(1, NCK // NS) as r:
                for s in range(NS):
                    pe.wait_ge(w_in[s], 32 * r + 32)
                    pe.wait_ge(mod_ev, NS * r + s - 1)
                    product(K.bank[s % 2], 0, s, mod_mm)


def cmul(nc, link, out_r, out_i, a_r, a_i, b_r, b_i, t, u, conj=False):
    v = link.eng
    v.tensor_tensor(t, a_r, b_i, ALU.mult)
    link(v.tensor_tensor(u, a_i, b_i, ALU.mult))
    v.tensor_tensor(out_r, a_r, b_r, ALU.mult)
    link(v.tensor_tensor(out_i, a_i, b_r, ALU.mult))
    v.tensor_tensor(out_r, out_r, u, ALU.add if conj else ALU.subtract)
    link(v.tensor_tensor(out_i, out_i, t, ALU.subtract if conj else ALU.add))


def exp_exact(nc, link, dst, x, k, r, ki):
    v = nc.vector
    link(v.tensor_scalar(x, x, -87.0, 88.0, ALU.max, ALU.min))
    link(v.tensor_scalar(k, x, LOG2E, MAGIC, ALU.mult, ALU.add))
    link(v.tensor_scalar(k, k, MAGIC, None, ALU.subtract))
    link(v.scalar_tensor_tensor(out=r, in0=k, scalar=-LN2_HI, in1=x, op0=ALU.mult, op1=ALU.add))
    link(v.scalar_tensor_tensor(out=r, in0=k, scalar=-LN2_LO, in1=r, op0=ALU.mult, op1=ALU.add))
    link(v.tensor_scalar(dst, r, 1.0 / 5040, None, ALU.mult))
    for c in (1.0 / 720, 1.0 / 120, 1.0 / 24, 1.0 / 6, 0.5, 1.0):
        link(v.scalar_tensor_tensor(out=dst, in0=dst, scalar=c, in1=r, op0=ALU.add, op1=ALU.mult))
    link(v.tensor_scalar(k, k, 127.0, None, ALU.add))
    link(v.tensor_copy(ki, k))
    link(v.tensor_scalar(ki, ki, 23, None, ALU.logical_shift_left))
    link(v.scalar_tensor_tensor(out=dst, in0=dst, scalar=1.0, in1=ki.bitcast(F32), op0=ALU.add, op1=ALU.mult))


def reduce_angle(nc, link, r, quarter, x, k):
    v = nc.vector
    link(v.tensor_scalar(k, x, INV_2PI, MAGIC, ALU.mult, ALU.add))
    link(v.tensor_scalar(k, k, MAGIC, None, ALU.subtract))
    link(v.scalar_tensor_tensor(out=r, in0=k, scalar=-TWO_PI_1, in1=x, op0=ALU.mult, op1=ALU.add))
    for c in (TWO_PI_2, TWO_PI_3):
        link(v.scalar_tensor_tensor(out=r, in0=k, scalar=-c, in1=r, op0=ALU.mult, op1=ALU.add))
    link(v.tensor_scalar(r, r, -PI_IN, PI_IN, ALU.max, ALU.min))
    link(v.scalar_tensor_tensor(out=quarter, in0=r, scalar=-1.0, in1=r, op0=ALU.mult, op1=ALU.max))
    link(v.tensor_scalar(quarter, quarter, -1.0, math.pi / 2, ALU.mult, ALU.add))


def stage_s5(K):
    nc, I = K.nc, K.I
    wd = K.at("s5_wd", 72, [P, KT, W])
    d8 = K.at("s5_d8", 80, [P, G16, SC, SP])
    d8c = K.at("s5_d8c", 166, [NCC, SC, W])
    d8g = K.at("s5_d8g", 88, [NCC, G16, SC, SP])
    HB = K.at("s5_HB", 154, [P, 2, GP, NCH])
    ys = K.at("s5_ys", 146, [P, SC, W])
    dcx = K.at("s5_dcx", 96, [P, 2, W])
    glu = K.at("s5_glu", 96, [P, 2, W])
    U8 = K.at("s5_U8", 98, [P, G16, NCA])
    CA = K.at("s5_CA", 108, [P, 2, 2, GP, 9, SP])
    AB = K.at("s5_AB", 126, [P, 2, 2, GP, SC, SP])
    X = K.at("s5_X", 126, [P, 2, 2 * GP, NCA])
    scr = K.at("s5_scr", 146, [P, 2, GP * 9 * SP])
    TAB = K.at("s5_TAB", 146, [P, 2, 2 * GP, NCA])
    ABT = K.at("s5_ABT", 166, [P, 2, GP, 2, P])
    tmp = K.at("s5_tmp", 166, [P, 2, 2 * GP, NCA])
    ptmp = K.at("s5_ptmp", 186, [P, 2, 2 * GP, NCA // 2 - 16])
    yDT = K.at("s5_yDT", 166, [P, 2, T])
    sg = K.at("s5_sg", 174, [P, 2, T])
    Tz = K.at("s5_T", 186, [P, G16, P])
    Cn = K.at("s5_Cn", 186, [P, 2, 2, 2, SN])
    KL = K.at("s5_KL", 64, [SP, G16, 15 * SP])
    Bm = K.at("s5_B", 194, [P, 2, GP, SP])
    Cm = K.at("s5_C", 195, [P, 2, GP, SP])
    BB = K.at("s5_BB", 196, [P, 2, 2, GP, SP])
    Dr = K.at("s5_D", 198, [P, W])
    araw = K.prm[0:2 * GP, 0:3 * P].rearrange("p (a n) -> p a n", a=3)
    used = [3 * P]

    def columns(n, dt=F32):
        used[0] += n
        c = K.prm[:, used[0] - n:used[0]]
        return c if dt == F32 else c.bitcast(dt)

    N2 = 2 * GP
    par = columns(3 * N2).rearrange("p (a j) -> p a j", a=3)
    ang = columns(2 * N2).rearrange("p (a j) -> p a j", a=2)
    red, quar, kk, sn, cs = (columns(2 * N2).rearrange("p (a j) -> p a j", a=2) for _ in range(5))
    dt_c, er, k1, r1, fr, fi, den, tc, uc = (columns(N2) for _ in range(9))
    ki = columns(N2, I32)
    pw = columns(2 * 9 * N2).rearrange("p (c e j) -> p c e j", c=2, e=9)
    rot = columns(2 * N2).rearrange("p (c j) -> p c j", c=2)
    gb = columns(2)
    ldt = columns(2)
    pt = columns(2 * N2).rearrange("p (c j) -> p c j", c=2)
    s5_in, d_in, g_in = K.sem("s5_in"), K.sem("s5_d_in"), K.sem("s5_glu_in")
    mm, ev = K.sem("s5_mm"), K.sem("s5_ev")
    dg_rdy = K.sem("s5_dg")
    ldt_x, par_t, prm_rdy, c_rdy, sin_in, sin_out = (K.sem(f"s5_{n}") for n in ("ldtx", "part", "prm", "crdy", "sinin", "sinout"))
    ab_rdy, tab_rdy, t_in, h_rdy, y_mm, y_ev, y_act = (K.sem(f"s5_{n}") for n in ("ab", "tab", "tin", "h", "ymm", "yev", "yact"))
    yt_mm, yt_ev, g_mm, g_sg, chain, pchain = (K.sem(f"s5_{n}") for n in ("ytmm", "ytev", "gmm", "gsg", "chain", "pchain"))
    N_D, N_U, N_AB, N_X, N_KL = 5, 8, 8, 16, 8
    at_u, at_ab, at_x, at_kl, at_end = (int(v) for v in np.cumsum([N_D, N_U, N_AB, N_X, N_KL]))
    NB = 6

    def bank(n):
        return K.bank[2 + n % NB]

    with nc.Block() as block:
        @block.sync
        def _(sp):
            sp.dma_start(wd[:], I["w_in"][0].rearrange("(k p) n -> p k n", p=P)[:, :, OFF_D:OFF_D + W]).then_inc(s5_in, 16)
            for a, name in enumerate(("s5_a_re", "s5_a_im")):
                sp.dma_start(araw[:, a, :], I[name][0].rearrange("d (j h) n -> (d j) (h n)", h=2)).then_inc(s5_in, 16)
            sp.dma_start(ldt[0:N2, :], I["s5_log_dt"][0].rearrange("d (j h) -> (d j) h", h=2)).then_inc(s5_in, 16)
            for a, name in enumerate(("s5_b_re", "s5_b_im")):
                sp.dma_start(Bm[:, a], I[name][0].rearrange("(j h) n p -> (h n) j p", h=2)).then_inc(s5_in, 16)
            for a, name in enumerate(("s5_c_re", "s5_c_im")):
                for dup in range(2):
                    sp.dma_start(Cn[:, a, :, dup, :], I[name][0].rearrange("(t g) p n -> (g p) t n", t=2)).then_inc(s5_in, 16)
            sp.dma_start(Dr[:], I["s5_d"].to_broadcast([P, W])).then_inc(s5_in, 16)
            with nc.allow_non_contiguous_dma(reason="a bias as a column"):
                sp.dma_start(gb[:], I["s5_glu_b"][0].rearrange("(k p) -> p k", p=P)).then_inc(s5_in, 16)
            sp.wait_ge(ev, N_D)
            for s in range(SC):
                sp.dma_start(d8c[:, s, :], dcx[(s % 4) * NCC:(s % 4 + 1) * NCC, s // 4, :]).then_inc(d_in, 16)
            sp.wait_ge(d_in, 16 * SC)
            sp.dma_start(glu[:], I["s5_glu_w"][0].rearrange("(k p) n -> p k n", p=P)).then_inc(g_in, 16)
            sp.wait_ge(ev, at_end)
            sp.wait_ge(tab_rdy, 1)
            for s in range(SC):
                sp.dma_start(Tz[s * SP:(s + 1) * SP, :, :], KL[:, :, (7 - s) * SP:(15 - s) * SP]).then_inc(t_in, 16)

        @block.tensor
        def _(pe):
            n = 0

            def load(n):
                if n >= NB:
                    pe.wait_ge(ev, n - NB + 1)

            pe.wait_ge(s5_in, 16 * 12)
            for q in range(4):
                load(n)
                for s in (2 * q, 2 * q + 1):
                    for k in range(KT):
                        last = nc.tensor.matmul(bank(n)[:, (s % 2) * W:(s % 2 + 1) * W], K.HT[:, k, TC + s::SC], wd[:, k, :],
                                                start=(k == 0), stop=(k == KT - 1))
                last.then_inc(mm, 1)
                n += 1
            for h in range(2):
                for k in range(KT):
                    last = nc.tensor.matmul(bank(n)[:, h * W:(h + 1) * W],
                                            K.HTP[:, k, h * P:(h + 1) * P],
                                            wd[:, k, :], start=(k == 0), stop=(k == KT - 1))
            last.then_inc(mm, 1)
            n += 1
            pe.wait_ge(ldt_x, 1)
            for a in range(3):
                last = nc.tensor.transpose(K.bank[0][:, a * N2:(a + 1) * N2], araw[:, a, :], K.ident[0:N2, 0:N2])
            for a in range(2):
                for h in range(2):
                    last = nc.tensor.transpose(K.bank[1][:, (2 * a + h) * P:(2 * a + h + 1) * P],
                                               Cn[:, a, h, :, :], K.ident[:])
            last.then_inc(par_t, 1)
            pe.wait_ge(ev, N_D)
            pe.wait_ge(dg_rdy, 1)
            for q in range(N_U):
                load(n)
                for j in range(2):
                    g = 2 * q + j
                    nc.tensor.transpose(bank(n)[:, j * NCA:j * NCA + NCC], d8g[:, g, :, :], K.ident[0:NCC, 0:NCC])
                    last = nc.tensor.transpose(bank(n)[:, j * NCA + NCC:(j + 1) * NCA], d8[:, g, :, :], K.ident[:])
                last.then_inc(mm, 1)
                n += 1
            pe.wait_ge(ab_rdy, 1)
            for q in range(N_AB):
                load(n)
                for r in range(4):
                    d, j, c = (4 * q + r) // (2 * GP), (4 * q + r) // 2 % GP, r % 2
                    last = nc.tensor.transpose(bank(n)[:, r * P:(r + 1) * P], AB[:, d, c, j, :, :], K.ident[:])
                last.then_inc(mm, 1)
                n += 1
            for q in range(N_X):
                if q == 0:
                    pe.wait_ge(ev, at_ab)
                load(n)
                d, j = q // GP, q % GP
                for c in range(2):
                    for h in range(2):
                        last = nc.tensor.matmul(bank(n)[h * SN:(h + 1) * SN, c * NCA:(c + 1) * NCA],
                                                ABT[:, d, j, c, h * SN:(h + 1) * SN], U8[:, 2 * j + h, :], start=True, stop=True)
                last.then_inc(mm, 1)
                n += 1
            for q in range(N_KL):
                load(n)
                h, row = q % 2, slice(q % 2 * SN, (q % 2 + 1) * SN)
                for i2 in range(2):
                    j = q // 2 * 2 + i2
                    o = bank(n)[0:SP, i2 * 15 * SP:(i2 + 1) * 15 * SP]
                    parts = [(o[:, 7 * SP:8 * SP], [(0, 0), (1, 8)], 1), (o[:, 8 * SP:], [(0, 1)], 7), (o[:, :7 * SP], [(1, 1)], 7)]
                    for dst, terms, ne in parts:
                        for i, (d, e) in enumerate(terms):
                            for c in range(2):
                                last = nc.tensor.matmul(dst, BB[row, d, c, j, :], CA[row, d, c, j, e:e + ne, :],
                                                        start=(i == 0 and c == 0), stop=(i == len(terms) - 1 and c == 1))
                last.then_inc(mm, 1)
                n += 1
            pe.wait_ge(t_in, 16 * SC)
            pe.wait_ge(h_rdy, 1)
            for q in range(4):
                for r in range(4):
                    j, h = q // 2 * 4 + r, q % 2
                    g, row = 2 * j + h, slice(h * SN, (h + 1) * SN)
                    o = K.bank[2 + q][:, r * P:(r + 1) * P]
                    nc.tensor.matmul(o, U8[:, g, NCC:], Tz[:, g, :], start=True, stop=False)
                    for d in range(2):
                        for c in range(2):
                            st = X[row, c, d * GP + j, NCC - 1:NCA - 1] if d == 0 else HB[row, c, j, :]
                            last = nc.tensor.matmul(o, st, CA[row, d, c, j, 1 - d:9 - d, :], start=False, stop=(d == 1 and c == 1))
                last.then_inc(y_mm, 1)
            pe.wait_ge(y_act, 1)
            for q in range(4):
                if q >= 2:
                    pe.wait_ge(yt_ev, q - 1)
                for r in range(4):
                    last = nc.tensor.transpose(K.bank[6 + q % 2][:, r * P:(r + 1) * P],
                                               ys[:, 4 * (q % 2) + r, (q // 2) * P:(q // 2 + 1) * P], K.ident[:])
                last.then_inc(yt_mm, 1)
            pe.wait_ge(yt_ev, 4)
            pe.wait_ge(g_in, 16)
            for m in range(2):
                for h in range(2):
                    for k in range(2):
                        last = nc.tensor.matmul(K.bank[2 + 2 * m + h][:], glu[:, k, m * P:(m + 1) * P], yDT[:, k, h * HALF:(h + 1) * HALF],
                                                start=(k == 0), stop=(k == 1))
                    last.then_inc(g_mm, 1)

        @block.scalar
        def _(act):
            n = 0

            def take(dst, src, last=True):
                ins = nc.scalar.activation(dst, src, ACT.Copy)
                if last:
                    ins.then_inc(ev, 1)

            for q in range(4):
                act.wait_ge(mm, n + 1)
                for s in range(2):
                    take(d8[:, :, 2 * q + s, :], bank(n)[:, s * W:(s + 1) * W].rearrange("p (g o) -> p g o", g=G16), last=(s == 1))
                n += 1
            act.wait_ge(mm, n + 1)
            take(dcx[:], bank(n)[:].rearrange("p (h n) -> p h n", h=2))
            n += 1
            for q in range(N_U):
                act.wait_ge(mm, n + 1)
                take(U8[:, 2 * q:2 * q + 2, :], bank(n)[:, 0:2 * NCA].rearrange("p (g c) -> p g c", g=2))
                n += 1
            act.wait_ge(sin_in, 1)
            nc.scalar.activation(sn[:], red[:], ACT.Sin).then_inc(sin_out, 1)
            nc.scalar.activation(cs[:], quar[:], ACT.Sin).then_inc(sin_out, 1)
            for q in range(N_AB):
                act.wait_ge(mm, n + 1)
                d, j = 4 * q // (2 * GP), 2 * q % GP
                take(ABT[:, d, j:j + 2, :, :], bank(n)[:].rearrange("p (j c n) -> p j c n", j=2, c=2))
                n += 1
            for q in range(N_X):
                act.wait_ge(mm, n + 1)
                src = bank(n)[:, 0:2 * NCA].rearrange("p (c n) -> p c n", c=2)
                if q < GP:
                    take(X[:, :, q, :], src)
                else:
                    take(X[:, :, q, 0:NCC], src[:, :, NCC - 1::-1], last=False)
                    take(X[:, :, q, NCC:], src[:, :, :NCC - 1:-1])
                n += 1
            for q in range(N_KL):
                act.wait_ge(mm, n + 1)
                take(KL[:, q // 2 * 4 + q % 2:q // 2 * 4 + 4:2, :], bank(n)[0:SP, 0:30 * SP].rearrange("p (h l) -> p h l", h=2))
                n += 1
            act.wait_ge(y_ev, 4)
            nc.scalar.activation(ys[:], ys[:], ACT.Gelu_apprx_tanh).then_inc(y_act, 1)
            for q in range(4):
                act.wait_ge(yt_mm, q + 1)
                nc.scalar.activation(yDT[:, q // 2, :].rearrange("p (c s) -> p s c", s=SC)[:, 4 * (q % 2):4 * (q % 2) + 4, :],
                                     K.bank[6 + q % 2][:].rearrange("p (s c) -> p s c", s=4), ACT.Copy).then_inc(yt_ev, 1)
            for q in range(4):
                act.wait_ge(g_mm, q + 1)
                nc.scalar.activation(sg[:, q // 2, (q % 2) * HALF:(q % 2 + 1) * HALF], K.bank[2 + q][:], ACT.Sigmoid,
                                     bias=gb[:, q // 2:q // 2 + 1]).then_inc(g_sg, 1)

        @block.gpsimd
        def _(pool):
            pool.wait_ge(d_in, 16 * SC)
            nc.gpsimd.tensor_copy(d8g[:].rearrange("c g s o -> c s g o"), d8c[:].rearrange("c s (g o) -> c s g o", g=G16)).then_inc(dg_rdy, 1)
            link = Link(nc.gpsimd, pchain)
            pool.wait_ge(ab_rdy, 1)
            link(nc.gpsimd.memset(TAB[:, 0, :, 0:1], 1.0))
            link(nc.gpsimd.memset(TAB[:, 1, :, 0:1], 0.0))
            n = 1
            while n < NCA:
                m = min(n, NCA - n)
                turn = [rot[:, c, :].unsqueeze(2).to_broadcast([P, N2, m]) for c in range(2)]
                t, u = ptmp[:, 0, :, 0:m], ptmp[:, 1, :, 0:m]
                cmul(nc, link, TAB[:, 0, :, n:n + m], TAB[:, 1, :, n:n + m], TAB[:, 0, :, 0:m], TAB[:, 1, :, 0:m],
                     turn[0], turn[1], t, u)
                n += m
                if n < NCA:
                    cmul(nc, link, pt[:, 0, :], pt[:, 1, :], rot[:, 0, :], rot[:, 1, :], rot[:, 0, :], rot[:, 1, :], tc[:], uc[:])
                    link(nc.gpsimd.tensor_copy(rot[:], pt[:]))
            pool.sem_inc(tab_rdy, 1)

        @block.vector
        def _(dve):
            link = Link(nc.vector, chain)
            v = nc.vector
            dve.wait_ge(s5_in, 16 * 12)
            v.tensor_copy(araw[:, 2, :].rearrange("p (h n) -> p h n", h=2),
                          ldt[0:N2, :].unsqueeze(2).to_broadcast([N2, 2, SN])).then_inc(ldt_x, 1)
            dve.wait_ge(par_t, 1)
            link(v.tensor_copy(par[:], K.bank[0][:, 0:3 * N2].rearrange("p (a j) -> p a j", a=3)))
            for h in range(2):
                link(v.tensor_copy(Cm[h * SN:(h + 1) * SN].rearrange("p c (t g) o -> p (c t) g o", t=2),
                                   K.bank[1][h * SN:(h + 1) * SN, :].rearrange("p (a g h o) -> p a g h o", a=4, g=4, h=2)[:, :, :, h, :]))
            a_re, a_im = par[:, 0, :], par[:, 1, :]
            exp_exact(nc, link, dt_c[:], par[:, 2, :], k1[:], r1[:], ki[:])
            link(v.tensor_tensor(ang[:, 0, :], a_im, dt_c[:], ALU.mult))
            link(v.tensor_scalar(ang[:, 1, :], ang[:, 0, :], float(SC), None, ALU.mult))
            reduce_angle(nc, link, red[:], quar[:], ang[:], kk[:])
            link(v.tensor_tensor(dt_c[:], a_re, dt_c[:], ALU.mult))
            dve.sem_inc(sin_in, 1)
            exp_exact(nc, link, er[:], dt_c[:], k1[:], r1[:], ki[:])
            dve.wait_ge(sin_out, 2)
            link(v.memset(pw[:, 0, 0, :], 1.0))
            link(v.memset(pw[:, 1, 0, :], 0.0))
            link(v.tensor_tensor(pw[:, 0, 1, :], er[:], cs[:, 0, :], ALU.mult))
            link(v.tensor_tensor(pw[:, 1, 1, :], er[:], sn[:, 0, :], ALU.mult))
            for lo, n, by in ((2, 1, 1), (3, 2, 2), (5, 4, 4)):
                q = [pw[:, c, by, :].unsqueeze(1).to_broadcast([P, n, N2]) for c in range(2)]
                t, u = (scr[:, i, 0:n * N2].rearrange("p (e j) -> p e j", e=n) for i in range(2))
                cmul(nc, link, pw[:, 0, lo:lo + n, :], pw[:, 1, lo:lo + n, :], pw[:, 0, 1:1 + n, :], pw[:, 1, 1:1 + n, :],
                     q[0], q[1], t, u)
            for _ in range(3):
                link(v.tensor_tensor(er[:], er[:], er[:], ALU.mult))
            link(v.tensor_copy(rot[:, 0, :], cs[:, 1, :]))
            link(v.tensor_copy(rot[:, 1, :], sn[:, 1, :]))
            link(v.tensor_scalar(r1[:], pw[:, 0, 1, :], 1.0, None, ALU.subtract))
            link(v.tensor_tensor(den[:], a_re, a_re, ALU.mult))
            link(v.tensor_tensor(k1[:], a_im, a_im, ALU.mult))
            link(v.tensor_tensor(den[:], den[:], k1[:], ALU.add))
            link(v.reciprocal(den[:], den[:]))
            cmul(nc, link, fr[:], fi[:], r1[:], pw[:, 1, 1, :], a_re, a_im, tc[:], uc[:], conj=True)
            link(v.tensor_tensor(fr[:], fr[:], den[:], ALU.mult))
            link(v.tensor_tensor(fi[:], fi[:], den[:], ALU.mult))
            for d in range(2):
                s = slice(d * GP, (d + 1) * GP)
                f = [c[:, s].unsqueeze(2).to_broadcast([P, GP, SP]) for c in (fr, fi)]
                t, u = (scr[:, i, 0:GP * SP].rearrange("p (j o) -> p j o", j=GP) for i in range(2))
                cmul(nc, link, BB[:, d, 0], BB[:, d, 1], Bm[:, 0], Bm[:, 1], f[0], f[1], t, u)

                def powers(c, exps):
                    p = pw[:, c, exps, s]
                    return p.rearrange("p e j -> p j e").unsqueeze(3).to_broadcast([P, GP, p.shape[1], SP])

                e = slice(7, None, -1) if d == 0 else slice(0, SC)
                b = [BB[:, d, c].unsqueeze(2).to_broadcast([P, GP, SC, SP]) for c in range(2)]
                t, u = (scr[:, i, 0:GP * SC * SP].rearrange("p (j e o) -> p j e o", j=GP, e=SC) for i in range(2))
                cmul(nc, link, AB[:, d, 0], AB[:, d, 1], powers(0, e), powers(1, e), b[0], b[1], t, u)
                e = slice(0, 9) if d == 0 else slice(8, None, -1)
                cm = [Cm[:, c].unsqueeze(2).to_broadcast([P, GP, 9, SP]) for c in range(2)]
                t, u = (scr[:, i, :].rearrange("p (j e o) -> p j e o", j=GP, e=9) for i in range(2))
                cmul(nc, link, CA[:, d, 0], CA[:, d, 1], powers(0, e), powers(1, e), cm[0], cm[1], t, u)
                link(v.tensor_scalar(CA[:, d, 1], CA[:, d, 1], -1.0, None, ALU.mult))
            dve.sem_inc(ab_rdy, 1)
            dve.wait_ge(ev, at_u + N_U)
            for s in range(SC):
                link(v.tensor_tensor(d8[:, :, s, :], d8[:, :, s, :], Dr[:].rearrange("p (g o) -> p g o", g=G16), ALU.mult))
            dve.wait_ge(ev, at_x + N_X)
            dve.wait_ge(tab_rdy, 1)
            xr, xi = X[:, 0], X[:, 1]
            t, u = tmp[:, 0], tmp[:, 1]
            cmul(nc, link, xr, xi, xr, xi, TAB[:, 0], TAB[:, 1], t, u, conj=True)
            link(v.tensor_copy(t, er[:].unsqueeze(2).to_broadcast([P, N2, NCA])))
            link(v.memset(tmp[:, 0, :, 0:1], 0.0))
            for c in range(2):
                flat = X[:, c].rearrange("p j n -> p (j n)")
                link(v.tensor_tensor_scan(flat, tmp[:, 0].rearrange("p j n -> p (j n)"), flat, 0.0, ALU.mult, ALU.add))
            cmul(nc, link, xr, xi, xr, xi, TAB[:, 0], TAB[:, 1], t, u)
            for c in range(2):
                link(v.tensor_copy(HB[:, c], X[:, c, GP:, NCA - 2:NCC - 2:-1]))
            dve.sem_inc(h_rdy, 1)
            for q in range(4):
                dve.wait_ge(y_mm, q + 1)
                for r in range(4):
                    g = 2 * (q // 2 * 4 + r) + q % 2
                    last = v.tensor_tensor(ys[:, :, g * SP:(g + 1) * SP], K.bank[2 + q][:, r * P:(r + 1) * P].rearrange("p (s o) -> p s o", s=SC),
                                           d8[:, g], ALU.add)
                last.then_inc(y_ev, 1)
            for q in range(4):
                dve.wait_ge(g_sg, q + 1)
                o = (slice(None), q // 2, slice((q % 2) * HALF, (q % 2 + 1) * HALF))
                v.tensor_tensor(K.ydT[o], yDT[o], sg[o], ALU.mult).then_inc(chain, 1)


def stage_mixers(K):
    nc, I = K.nc, K.I
    NL = NCT + NT
    qkT = K.at("mx_qkT", 72, [P, 4, T])
    kn = K.at("mx_kn", 88, [P, NL, W])
    vx = K.at("mx_vx", 98, [P, NL, HEADS, HD + 1])
    so = K.at("mx_so", 109, [P, NT, W])
    GT = K.at("mx_GT", 117, [P, NL, 2, 2, HEADS])
    zb = K.at("mx_zb", 118, [P, NT, 2 * W])
    cT = K.at("mx_cT", 134, [P, 4, T])
    acc = K.at("mx_acc", 142, [P, 2, T])
    yc = K.at("mx_yc", 134, [P, NT, W])
    H = K.at("mx_H", 142, [P, NT, HEADS, HD])
    ring = [K.at(f"mx_w{s}", 150 + 16 * s, [P, KT, HALF]) for s in range(2)]
    apad = K.at("mx_apad", 182, [P, 2, ROWS, GRID + 2 * PAD])
    rows = K.at("mx_rows", 194, [P, 5, W])
    wsn = K.at("mx_wsn", 88, [P, 4, P])
    wcn = K.at("mx_wcn", 90, [CONV + 1, W])
    QR = 36
    ig, lf, bc, win, ee, d0m, d0a = (K.at(f"mx_g{n}", 150 + 5 * n + (2 if n == 6 else 0), [QR, NL * P]) for n in range(7))
    COL = K.at("mx_COL", 187, [P, 2, 4, NL, HEADS])
    CS = K.at("mx_CS", 188.5, [P, 2, 2, HD + 1])
    selp = K.at("mx_selp", 189.75, [QR, 2, 2, HD])
    mask = K.at("mx_mask", 190.75, [P, 2, P])
    sel = K.at("mx_sel", 191.75, [QR, HEADS, P])
    arg = [K.at(f"mx_arg{d}", 48 + 2 * d, [P, HEADS, P]) for d in range(2)]
    PT = [K.at(f"mx_PT{d}", 52 + 2 * d, [P, HEADS, P]) for d in range(2)]
    num = [K.at(f"mx_num{d}", 56 + 1.25 * d, [P, HEADS, HD + 1]) for d in range(2)]
    ke = [K.at(f"mx_ke{d}", 58.5 + d, [P, HEADS, HD]) for d in range(2)]
    used = [0]

    def columns(n):
        used[0] += n
        return K.prm[:, used[0] - n:used[0]]

    wcol = columns(2 * (CONV + 1)).rearrange("p (c k) -> p c k", c=2)
    bs = columns(4)
    gbias = columns(16)
    st6 = columns(6)
    mv = columns(2 * NT).rearrange("p (i a) -> p i a", a=2)
    rstd = columns(NT)
    mvc = columns(2 * NT).rearrange("p (i a) -> p i a", a=2)
    rstdc = columns(NT)
    BE, ME, BM, MPc, MEc, DEC = (columns(NL) for _ in range(6))
    MP = columns(NL + 1)
    dcol = columns(2 * 2 * NL).rearrange("p (d j c) -> p d j c", d=2, j=2)
    nd = [columns(HEADS) for _ in range(2)]
    sums = columns(NT * HEADS).rearrange("p (i h) -> p i h", h=HEADS)
    sqs = columns(NT * HEADS).rearrange("p (i h) -> p i h", h=HEADS)
    gt = columns(NL * 2 * HEADS).rearrange("p (i d h) -> p i d h", i=NL, d=2)
    ge = columns(NL * 2 * HEADS).rearrange("p (i d h) -> p i d h", i=NL, d=2)

    w_in = [K.sem(f"mx_win{s}") for s in range(2)]
    names = ("prm mm ev cons sel conv ctmm sgn wst bmm bdone ycn yc_tr yc_ev yb_tr yb_ev "
             "g1 g2 g3 gx gmm gev ga gb colmm colev st argmm argr pr ptr qmm pvmm nr ker umm hr yam yae eps1 eps2 chain pchain").split()
    S = {n: K.sem("mx_" + n) for n in names}
    slabs = [(OFF_C, 512), (OFF_B, 512), (3 * W, W + 16), (0, 512), (W, 512)]
    loads = [8, 8, NL, 8, NL]
    first = np.cumsum([0] + loads)
    total = int(first[-1])
    order = [list(range(NL)), [1, 0] + list(range(NL - 1, NCT - 1, -1))]

    with nc.Block() as block:
        @block.sync
        def _(sp):
            w = I["w_in"][0].rearrange("(k p) n -> p k n", p=P)
            for j, (col, n) in enumerate(slabs):
                if j >= 2:
                    sp.wait_ge(S["mm"], int(first[j - 1]))
                sp.dma_start(ring[j % 2][:, :, 0:n], w[:, :, col:col + n]).then_inc(w_in[j % 2], 16)
                if j == 1:
                    sp.dma_start(wcn[0:CONV, :], I["conv_w"][0]).then_inc(S["prm"], 16)
                    sp.dma_start(wcn[CONV:CONV + 1, :], I["conv_b"]).then_inc(S["prm"], 16)
                    sp.dma_start(wsn[:], I["sgu_w"][0].rearrange("g t s -> t g s")).then_inc(S["prm"], 16)
                    with nc.allow_non_contiguous_dma(reason="a bias as columns"):
                        sp.dma_start(bs[:], I["sgu_b"][0].rearrange("g t -> t g")).then_inc(S["prm"], 16)
                    sp.dma_start(gbias[:], I["mlstm_gate_bias"].to_broadcast([P, 16])).then_inc(S["prm"], 16)
                    for r, name in enumerate(("conv_ln_w", "conv_ln_b", "sgu_ln_w", "sgu_ln_b", "mlstm_norm_w")):
                        sp.dma_start(rows[:, r, :], I[name].to_broadcast([P, W])).then_inc(S["prm"], 16)

        @block.gpsimd
        def _(pool):
            g = nc.gpsimd
            g.memset(apad[:], 0.0).then_inc(S["cons"], 1)
            g.memset(vx[:, :, :, HD:], 1.0).then_inc(S["cons"], 1)
            pool.wait_ge(S["conv"], 1)
            pool.wait_ge(S["mm"], total)
            link = Link(g, S["pchain"])
            for t in (selp, mask, sel, CS, ig, lf, bc, win, ee, d0a):
                link(g.memset(t[:], 0.0))
            link(g.memset(d0m[:], 1.0))
            for r in (0, 32):
                link(g.affine_select(out=selp[r:r + 4], in_=selp[r:r + 4], compare_op=ALU.not_equal, fill=1.0, base=0,
                                     pattern=[[-2, 2], [-1, 2], [0, HD]], channel_multiplier=1))
                link(g.affine_select(out=sel[r:r + 4], in_=sel[r:r + 4], compare_op=ALU.not_equal, fill=-1.0, base=0,
                                     pattern=[[-1, HEADS], [0, P]], channel_multiplier=1))
                start = slice(0, None, P) if r == 0 else slice(P - 1, None, P)
                link(g.memset(d0m[r:r + 4, start], 0.0))
                link(g.memset(d0a[r:r + 4, start], LOW))
            link(g.affine_select(out=mask[:, 0, :], in_=mask[:, 0, :], compare_op=ALU.is_ge, fill=LOW, base=0,
                                 pattern=[[1, P]], channel_multiplier=-1))
            link(g.affine_select(out=mask[:, 1, :], in_=mask[:, 1, :], compare_op=ALU.is_ge, fill=LOW, base=0,
                                 pattern=[[-1, P]], channel_multiplier=1))
            pool.sem_inc(S["sel"], 1)

        @block.tensor
        def _(pe):
            n = 0

            def group(bank, cols, pairs, last):
                for k, (lhs, rhs) in enumerate(pairs):
                    mm = nc.tensor.matmul(bank[:, 0:cols], lhs, rhs, start=(k == 0), stop=(k == KT - 1))
                if last:
                    mm.then_inc(S["mm"], 1)

            for j, (col, cols) in enumerate(slabs):
                pe.wait_ge(w_in[j % 2], 16 * (j // 2 + 1))
                w = ring[j % 2]
                for r in range(loads[j]):
                    if n >= 8:
                        pe.wait_ge(S["ev"], n - 7)
                    if j in (0, 3):
                        m, h = r // 2, r % 2
                        group(K.bank[n % 8], HALF, [(w[:, k, m * P:(m + 1) * P], K.HT[:, k, TC + h * HALF:TC + (h + 1) * HALF]) for k in range(KT)], True)
                    else:
                        i = r + NCT if j == 1 else r
                        group(K.bank[n % 8], cols, [(K.HT[:, k, i * P:(i + 1) * P], w[:, k, 0:cols]) for k in range(KT)], True)
                    n += 1
                if j == 0:
                    pe.wait_ge(S["prm"], 16 * 10)
                    pe.wait_ge(S["ev"], 8)
                    for g in range(4):
                        nc.tensor.transpose(K.bank[1][:, g * P:(g + 1) * P], wsn[:, g, :], K.ident[:])
                    for c in range(2):
                        last = nc.tensor.transpose(K.bank[0][:, c * (CONV + 1):(c + 1) * (CONV + 1)], wcn[:, c * P:(c + 1) * P],
                                                   K.ident[0:CONV + 1, 0:CONV + 1])
                    last.then_inc(S["wst"], 1)
                    pe.wait_ge(S["g1"], 1)

            pe.wait_ge(S["ev"], total)
            pe.wait_ge(S["conv"], 1)
            for q in range(4):
                for r in range(4):
                    i, c = 2 * q + r // 2, r % 2
                    last = nc.tensor.transpose(K.bank[q][:, r * P:(r + 1) * P], acc[:, c, i * P:(i + 1) * P], K.ident[:])
                last.then_inc(S["ctmm"], 1)
            pe.wait_ge(S["sgn"], 1)
            for g in range(4):
                nc.tensor.matmul(K.bank[4 + g][:].rearrange("p (i n) -> p i n", i=NT), K.wsT[:, g, :],
                                 zb[:, :, W + g * HD:W + (g + 1) * HD], start=True, stop=True).then_inc(S["bmm"], 1)
            pe.wait_ge(S["ycn"], 1)
            for q in range(4):
                for r in range(4):
                    last = nc.tensor.transpose(K.bank[q][:, r * P:(r + 1) * P], yc[:, 4 * (q % 2) + r, (q // 2) * P:(q // 2 + 1) * P], K.ident[:])
                last.then_inc(S["yc_tr"], 1)
            pe.wait_ge(S["bdone"], 4)
            for q in range(4):
                for r in range(4):
                    last = nc.tensor.transpose(K.bank[4 + q][:, r * P:(r + 1) * P], zb[:, 4 * (q % 2) + r, (q // 2) * P:(q // 2 + 1) * P], K.ident[:])
                last.then_inc(S["yb_tr"], 1)
            pe.wait_ge(S["yc_ev"], 4)
            pe.wait_ge(S["yb_ev"], 4)
            pe.wait_ge(S["g3"], 1)
            for a in range(2):
                for c in range(NL):
                    for d in range(2):
                        last = nc.tensor.matmul(K.bank[4 * a + c // 4][32 * d:32 * d + HEADS, (c % 4) * P:(c % 4 + 1) * P],
                                                GT[:, c, d, a, :], K.ident[:], start=True, stop=True)
            last.then_inc(S["gmm"], 1)
            pe.wait_ge(S["gb"], 1)
            for d in range(2):
                r = slice(32 * d, 32 * d + HEADS)
                for a, t in enumerate((ig, win, bc, ee)):
                    for c in range(NL):
                        o = (a * NL + c) * HEADS
                        nc.tensor.matmul(K.bank[3 + 4 * d][:, o:o + HEADS], t[r, c * P:(c + 1) * P], K.ident[r, r], start=True, stop=True)
                for j in range(2):
                    o = 4 * NL * HEADS + j * NL
                    last = nc.tensor.matmul(K.bank[3 + 4 * d][:, o:o + NL], selp[r, j, :, :], DEC[r, :], start=True, stop=True)
            last.then_inc(S["colmm"], 1)
            pe.wait_ge(S["colev"], 1)
            nq = 0
            for step in range(NL):
                for d in range(2):
                    c = order[d][step]
                    r = slice(32 * d, 32 * d + HEADS)
                    b = [K.bank[4 * d + m] for m in range(4)]
                    tok = slice((c - NCT) * P, (c - NCT + 1) * P)
                    if c >= NCT:
                        if step > NCT:
                            pe.wait_ge(S["nr"], 2 * (step - NCT) - 1 + d)
                        pe.wait_ge(S["st"], 2 * step - 1 + d)
                        for h in range(HEADS):
                            last = nc.tensor.matmul(b[0][:, h * P:(h + 1) * P], sel[r, h, :], lf[r, c * P:(c + 1) * P], start=True, stop=True)
                        last.then_inc(S["argmm"], 1)
                        for h in range(HEADS):
                            hr = slice((h % 2) * HD, (h % 2 + 1) * HD)
                            last = nc.tensor.matmul(b[1 + h % 2][:, (h // 2) * P:(h // 2 + 1) * P], qkT[hr, 2 + h // 2, tok],
                                                    qkT[hr, h // 2, tok], start=True, stop=True)
                        for h in range(HEADS):
                            hr = slice((h % 2) * HD, (h % 2 + 1) * HD)
                            o = 2 * P + (h // 2) * (HD + 1)
                            last = nc.tensor.matmul(b[1 + h % 2][:, o:o + HD + 1], qkT[hr, h // 2, tok], CS[hr, d, h // 2, :], start=True, stop=True)
                        last.then_inc(S["qmm"], 1)
                    if step < NL - 1:
                        pe.wait_ge(S["ker"], 2 * step + 1 + d)
                        for h in range(HEADS):
                            o = (h // 2) * (HD + 1)
                            last = nc.tensor.matmul(b[0][(h % 2) * HD:(h % 2 + 1) * HD, o:o + HD + 1], ke[d][:, h, :], vx[:, c, h, :],
                                                    start=True, stop=True)
                        last.then_inc(S["umm"], 1)
                    if c >= NCT:
                        pe.wait_ge(S["ptr"], 2 * (step - NCT) + 1 + d)
                        for h in range(HEADS):
                            last = nc.tensor.matmul(b[3][:, h * (HD + 1):(h + 1) * (HD + 1)], PT[d][:, h, :], vx[:, c, h, :], start=True, stop=True)
                        last.then_inc(S["pvmm"], 1)
            pe.wait_ge(S["hr"], 1)
            for q in range(4):
                for r in range(4):
                    last = nc.tensor.transpose(K.bank[q][:, r * P:(r + 1) * P],
                                               H[:, 4 * (q % 2) + r, 2 * (q // 2):2 * (q // 2) + 2, :], K.ident[:])
                last.then_inc(S["yam"], 1)

        @block.scalar
        def _(act):
            n = 0

            def take(dst, src, func=ACT.Copy, last=True):
                ins = nc.scalar.activation(dst, src, func)
                if last:
                    ins.then_inc(S["ev"], 1)

            for j in range(5):
                if j == 4:
                    act.wait_ge(S["cons"], 2)
                for r in range(loads[j]):
                    act.wait_ge(S["mm"], n + 1)
                    b = K.bank[n % 8]
                    if j == 0:
                        take(cT[:, r // 2, (r % 2) * HALF:(r % 2 + 1) * HALF], b[:], ACT.Copy if r < 4 else ACT.Sigmoid)
                    elif j == 1:
                        take(zb[:, r, :], b[:], ACT.Gelu_apprx_tanh)
                    elif j == 2:
                        if r >= NCT:
                            take(so[:, r - NCT, :], b[:, 0:W], ACT.Sigmoid, last=False)
                        take(GT[:, r], b[:, W:W + 16].rearrange("p (d a h) -> p d a h", d=2, a=2))
                    elif j == 3:
                        take(qkT[:, r // 2, (r % 2) * HALF:(r % 2 + 1) * HALF], b[:])
                    else:
                        take(kn[:, r, :], b[:, 0:W], last=False)
                        take(vx[:, r, :, 0:HD], b[:, W:].rearrange("p (h e) -> p h e", h=HEADS))
                    n += 1
            act.wait_ge(S["g2"], 1)
            nc.scalar.activation(ge[:], gt[:], ACT.Exp).then_inc(S["gx"], 1)
            act.wait_ge(S["gx"], 1)
            nc.scalar.activation(ge[:], ge[:], ACT.Ln, bias=1.0).then_inc(S["gx"], 1)
            act.wait_ge(S["eps1"], 1)
            nc.scalar.activation(rstd[:], rstd[:], ACT.Sqrt).then_inc(S["eps1"], 1)
            act.wait_ge(S["eps2"], 1)
            nc.scalar.activation(rstdc[:], rstdc[:], ACT.Sqrt).then_inc(S["eps2"], 1)
            act.wait_ge(S["eps2"], 3)
            nc.scalar.activation(yc[:], yc[:], ACT.Silu).then_inc(S["ycn"], 1)
            for q in range(4):
                act.wait_ge(S["yc_tr"], q + 1)
                nc.scalar.activation(K.yT[4 + q // 2][:, (q % 2) * HALF:(q % 2 + 1) * HALF], K.bank[q][:], ACT.Copy).then_inc(S["yc_ev"], 1)
            for q in range(4):
                act.wait_ge(S["yb_tr"], q + 1)
                nc.scalar.activation(K.yT[2 + q // 2][:, (q % 2) * HALF:(q % 2 + 1) * HALF], K.bank[4 + q][:], ACT.Copy).then_inc(S["yb_ev"], 1)
            act.wait_ge(S["ga"], 1)
            for t in (win[:], ee[:], DEC[0:QR, :]):
                nc.scalar.activation(t, t, ACT.Exp)
            nc.scalar.activation(bc[:], bc[:], ACT.Exp, scale=-1.0).then_inc(S["gb"], 1)
            for m in range(2 * NT):
                act.wait_ge(S["argr"], m + 1)
                nc.scalar.activation(arg[m % 2][:], arg[m % 2][:], ACT.Exp).then_inc(S["pr"], 1)
            act.wait_ge(S["nr"], 2 * NT + 1)
            nc.scalar.activation(sqs[:], sqs[:], ACT.Sqrt).then_inc(S["nr"], 1)
            for q in range(4):
                act.wait_ge(S["yam"], q + 1)
                nc.scalar.activation(K.yT[q // 2][:, (q % 2) * HALF:(q % 2 + 1) * HALF], K.bank[q][:], ACT.Copy).then_inc(S["yae"], 1)

        @block.vector
        def _(dve):
            v = nc.vector
            link = Link(v, S["chain"])
            dve.wait_ge(S["wst"], 1)
            link(v.tensor_copy(K.wsT[:], K.bank[1][:].rearrange("p (g t) -> p g t", g=4)))
            v.tensor_copy(wcol[:], K.bank[0][:, 0:2 * (CONV + 1)].rearrange("p (c k) -> p c k", c=2)).then_inc(S["g1"], 1)
            dve.wait_ge(S["g1"], 1)
            dve.wait_ge(S["cons"], 2)
            dve.wait_ge(S["ev"], 8)
            for c in range(2):
                link(v.tensor_tensor(apad[:, c, :, PAD:PAD + GRID], cT[:, c, :].rearrange("p (r t) -> p r t", r=ROWS),
                                     cT[:, 2 + c, :].rearrange("p (r t) -> p r t", r=ROWS), ALU.mult))
            out = [acc[:, c, :].rearrange("p (r t) -> p r t", r=ROWS) for c in range(2)]
            for c in range(2):
                link(v.tensor_scalar(out[c], apad[:, c, :, 0:GRID], wcol[:, c, 0:1], wcol[:, c, CONV:CONV + 1], ALU.mult, ALU.add))
            for k in range(1, CONV):
                for c in range(2):
                    link(v.scalar_tensor_tensor(out=out[c], in0=apad[:, c, :, k:k + GRID], scalar=wcol[:, c, k:k + 1], in1=out[c],
                                                op0=ALU.mult, op1=ALU.add))
            dve.sem_inc(S["conv"], 1)

            def norm(x, mean_var, inv, i):
                link(v.bn_stats(st6[:], x))
                link(v.bn_aggr(mean_var[:, i, :], st6[:]))

            dve.wait_ge(S["ev"], int(first[2]))
            dve.wait_ge(S["prm"], 16 * 10)
            for i in range(NT):
                norm(zb[:, i, W:], mv, rstd, i)
            link(v.tensor_scalar(rstd[:], mv[:, :, 1], LN_EPS, None, ALU.add))
            dve.sem_inc(S["eps1"], 1)
            dve.wait_ge(S["ev"], int(first[3]))
            flat = GT[:].rearrange("p i d a h -> p i (d a h)")
            link(v.tensor_tensor(flat, flat, gbias[:].unsqueeze(1).to_broadcast([P, NL, 16]), ALU.add))
            for d in range(2):
                link(v.scalar_tensor_tensor(out=gt[:, :, d, :], in0=GT[:, :, d, 1, :], scalar=-1.0, in1=GT[:, :, d, 1, :], op0=ALU.mult, op1=ALU.min))
            dve.sem_inc(S["g2"], 1)
            dve.wait_ge(S["gx"], 2)
            for d in range(2):
                link(v.scalar_tensor_tensor(out=GT[:, :, d, 1, :], in0=GT[:, :, d, 1, :], scalar=0.0, in1=ge[:, :, d, :], op0=ALU.min, op1=ALU.subtract))
            dve.sem_inc(S["g3"], 1)
            dve.wait_ge(S["eps1"], 2)
            link(v.reciprocal(rstd[:], rstd[:]))
            for i in range(NT):
                link(v.tensor_scalar(zb[:, i, W:], zb[:, i, W:], mv[:, i, 0:1], rstd[:, i:i + 1], ALU.subtract, ALU.mult))
            for r, op in ((2, ALU.mult), (3, ALU.add)):
                link(v.tensor_tensor(zb[:, :, W:], zb[:, :, W:], rows[:, r, :].unsqueeze(1).to_broadcast([P, NT, W]), op))
            dve.sem_inc(S["sgn"], 1)
            for i in range(NT):
                dve.wait_ge(S["ctmm"], i // 2 + 1)
                x = K.bank[i // 2][:, (i % 2) * W:(i % 2 + 1) * W]
                norm(x, mvc, rstdc, i)
            link(v.tensor_scalar(rstdc[:], mvc[:, :, 1], LN_EPS, None, ALU.add))
            dve.sem_inc(S["eps2"], 1)
            dve.wait_ge(S["eps2"], 2)
            link(v.reciprocal(rstdc[:], rstdc[:]))
            for i in range(NT):
                x = K.bank[i // 2][:, (i % 2) * W:(i % 2 + 1) * W]
                link(v.tensor_scalar(yc[:, i, :], x, mvc[:, i, 0:1], rstdc[:, i:i + 1], ALU.subtract, ALU.mult))
            for r, op in ((0, ALU.mult), (1, ALU.add)):
                link(v.tensor_tensor(yc[:], yc[:], rows[:, r, :].unsqueeze(1).to_broadcast([P, NT, W]), op))
            dve.sem_inc(S["eps2"], 1)
            for g in range(4):
                dve.wait_ge(S["bmm"], g + 1)
                o = zb[:, :, g * HD:(g + 1) * HD]
                v.scalar_tensor_tensor(out=o, in0=K.bank[4 + g][:].rearrange("p (i n) -> p i n", i=NT), scalar=bs[:, g:g + 1], in1=o,
                                       op0=ALU.add, op1=ALU.mult).then_inc(S["bdone"], 1)
            dve.wait_ge(S["sel"], 1)
            dve.wait_ge(S["gmm"], 1)
            for a, t in enumerate((ig, lf)):
                for d in range(2):
                    r = slice(32 * d, 32 * d + HEADS)
                    for q in range(3):
                        n = min(HALF, NL * P - q * HALF)
                        link(v.tensor_copy(t[r, q * HALF:q * HALF + n], K.bank[4 * a + q][r, 0:n]))
            way = [slice(None), slice(None, None, -1)]
            for d in range(2):
                r = slice(32 * d, 32 * d + HEADS)
                link(v.tensor_tensor_scan(bc[r, way[d]], d0m[r, way[d]], lf[r, way[d]], 0.0, ALU.mult, ALU.add))
            link(v.tensor_tensor(ig[:], ig[:], bc[:], ALU.subtract))
            for d in range(2):
                r = slice(32 * d, 32 * d + HEADS)
                link(v.tensor_tensor_scan(lf[r, way[d]], d0a[r, way[d]], ig[r, way[d]], LOW, ALU.add, ALU.max))
            link(v.memset(BE[0:QR, :], 0.0))
            link(v.memset(ME[0:QR, :], 0.0))
            link(v.memset(MEc[0:QR, :], 0.0))
            link(v.memset(MPc[0:QR, :], 0.0))
            link(v.memset(MP[0:QR, :], LOW))
            for d in range(2):
                r = slice(32 * d, 32 * d + HEADS)
                for dst, src in ((BE, bc), (ME, lf)):
                    e = src[r, P - 1::P] if d == 0 else src[r, 0::P]
                    if d == 0:
                        link(v.tensor_copy(dst[r, :], e))
                    else:
                        link(v.tensor_copy(dst[r, 0:NCT], e[:, NCT - 1::-1]))
                        link(v.tensor_copy(dst[r, NCT:], e[:, :NCT - 1:-1]))
                link(v.tensor_copy(MEc[r, :], lf[r, P - 1::P] if d == 0 else lf[r, 0::P]))
            link(v.tensor_tensor(BM[0:QR, :], BE[0:QR, :], ME[0:QR, :], ALU.add))
            link(v.tensor_tensor_scan(MP[0:QR, 1:], BE[0:QR, :], BM[0:QR, :], LOW, ALU.add, ALU.max))
            link(v.tensor_copy(MPc[0:HEADS, :], MP[0:HEADS, 0:NL]))
            r = slice(32, 32 + HEADS)
            link(v.tensor_copy(MPc[r, 0:NCT], MP[r, NCT - 1::-1]))
            link(v.tensor_copy(MPc[r, NCT:], MP[r, NL - 1:NCT - 1:-1]))
            link(v.tensor_tensor(MEc[0:QR, :], MEc[0:QR, :], MPc[0:QR, :], ALU.max))

            def chunked(t):
                return t[:].rearrange("p (c t) -> p c t", c=NL)

            before, after = (t[0:QR, :].unsqueeze(2).to_broadcast([QR, NL, P]) for t in (MPc, MEc))
            link(v.tensor_tensor(chunked(lf), chunked(lf), before, ALU.max))
            link(v.tensor_tensor(chunked(win), before, chunked(lf), ALU.subtract))
            link(v.tensor_tensor(chunked(ee), chunked(ig), after, ALU.subtract))
            link(v.tensor_tensor(bc[:], bc[:], lf[:], ALU.add))
            link(v.tensor_tensor(DEC[0:QR, :], MPc[0:QR, :], MEc[0:QR, :], ALU.subtract))
            dve.sem_inc(S["ga"], 1)
            link(v.memset(H[:], 0.0))
            dve.wait_ge(S["colmm"], 1)
            for d in range(2):
                n = 4 * NL * HEADS
                link(v.tensor_copy(COL[:, d].rearrange("p a c h -> p (a c h)"), K.bank[3 + 4 * d][:, 0:n]))
                link(v.tensor_copy(dcol[:, d].rearrange("p j c -> p (j c)"), K.bank[3 + 4 * d][:, n:n + 2 * NL]))
            dve.sem_inc(S["colev"], 1)
            lat = 0
            for step in range(NL):
                for d in range(2):
                    c = order[d][step]
                    b = [K.bank[4 * d + m] for m in range(4)]
                    if c >= NCT:
                        dve.wait_ge(S["argmm"], lat + 1)
                        for h in range(HEADS):
                            last = v.scalar_tensor_tensor(out=arg[d][:, h, :], in0=b[0][:, h * P:(h + 1) * P], scalar=COL[:, d, 0, c, h:h + 1],
                                                          in1=mask[:, d, :], op0=ALU.add, op1=ALU.min)
                        last.then_inc(S["argr"], 1)
                    if step < NL - 1:
                        v.scalar_tensor_tensor(out=ke[d][:], in0=kn[:, c, :].rearrange("p (h e) -> p h e", h=HEADS), scalar=HD ** -0.5,
                                               in1=COL[:, d, 3, c, :].unsqueeze(2).to_broadcast([P, HEADS, HD]),
                                               op0=ALU.mult, op1=ALU.mult).then_inc(S["ker"], 1)
                    if c >= NCT:
                        dve.wait_ge(S["pr"], lat + 1)
                        dve.wait_ge(S["qmm"], lat + 1)
                        for m in range(2):
                            last = v.scalar_tensor_tensor(out=PT[d][:, m::2, :], in0=b[1 + m][:, 0:2 * P].rearrange("p (j t) -> p j t", j=2),
                                                          scalar=HD ** -0.5, in1=arg[d][:, m::2, :], op0=ALU.mult, op1=ALU.mult)
                        last.then_inc(S["ptr"], 1)
                        for m in range(2):
                            link(v.tensor_tensor(num[d][:, m::2, :], b[1 + m][:, 2 * P:2 * P + 2 * (HD + 1)].rearrange("p (j e) -> p j e", j=2),
                                                 COL[:, d, 1, c, m::2].unsqueeze(2).to_broadcast([P, 2, HD + 1]), ALU.mult))
                    if step < NL - 1:
                        dve.wait_ge(S["umm"], 2 * step + 1 + d)
                        for j in range(2):
                            o = j * (HD + 1)
                            last = v.scalar_tensor_tensor(out=CS[:, d, j, :], in0=CS[:, d, j, :], scalar=dcol[:, d, j, c:c + 1],
                                                          in1=b[0][:, o:o + HD + 1], op0=ALU.mult, op1=ALU.add)
                        last.then_inc(S["st"], 1)
                    if c >= NCT:
                        dve.wait_ge(S["pvmm"], lat + 1)
                        v.tensor_tensor(num[d][:], num[d][:], b[3][:, 0:HEADS * (HD + 1)].rearrange("p (h e) -> p h e", h=HEADS), ALU.add).then_inc(S["nr"], 1)
                        dve.wait_ge(S["nr"], lat + 1)
                        den = num[d][:, :, HD]
                        link(v.scalar_tensor_tensor(out=nd[d][:], in0=den, scalar=-1.0, in1=den, op0=ALU.mult, op1=ALU.max))
                        link(v.tensor_tensor(nd[d][:], nd[d][:], COL[:, d, 2, c, :], ALU.max))
                        link(v.reciprocal(nd[d][:], nd[d][:]))
                        x = num[d][:, :, 0:HD]
                        link(v.tensor_tensor(x, x, nd[d][:].unsqueeze(2).to_broadcast([P, HEADS, HD]), ALU.mult))
                        link(v.tensor_tensor(H[:, c - NCT], H[:, c - NCT], x, ALU.add))
                        lat += 1
            flat = H[:].rearrange("p i h e -> p (i h) e")
            mean, var = sums[:].rearrange("p i h -> p (i h)"), sqs[:].rearrange("p i h -> p (i h)")
            spare = kn[:, 0:NT, :].rearrange("p i (h e) -> p (i h) e", h=HEADS)
            link(v.tensor_reduce(mean, flat, AX.X, ALU.add))
            link(v.tensor_scalar(mean, mean, 1.0 / HD, None, ALU.mult))
            link(v.tensor_tensor(flat, flat, mean.unsqueeze(2).to_broadcast([P, NT * HEADS, HD]), ALU.subtract))
            link(v.tensor_tensor(spare, flat, flat, ALU.mult))
            link(v.tensor_reduce(var, spare, AX.X, ALU.add))
            v.tensor_scalar(var, var, 1.0 / HD, LN_EPS, ALU.mult, ALU.add).then_inc(S["nr"], 1)
            dve.wait_ge(S["nr"], 2 * NT + 2)
            link(v.reciprocal(var, var))
            link(v.tensor_tensor(flat, flat, var.unsqueeze(2).to_broadcast([P, NT * HEADS, HD]), ALU.mult))
            wide = H[:].rearrange("p i h e -> p i (h e)")
            link(v.tensor_tensor(wide, wide, rows[:, 4, :].unsqueeze(1).to_broadcast([P, NT, W]), ALU.mult))
            v.tensor_tensor(wide, wide, so[:], ALU.mult).then_inc(S["hr"], 1)


def stage_join(K):
    nc, I = K.nc, K.I
    wo = K.at("jn_w", 72, [P, KT, D])
    xr = [K.at(f"jn_x{s}", 104 + 4 * s, [P, D]) for s in range(3)]
    rows = K.at("jn_rows", 116, [P, 2, D])
    t = [K.at(f"jn_t{s}", 124 + 4 * s, [P, D]) for s in range(2)]
    h = [K.at(f"jn_h{s}", 48 + 4 * s, [P, D]) for s in range(2)]
    K.h2 = [K.at(f"h2{n}", 132 + 32 * n, [P, 2, KT, HALF], FR) for n in range(2)]
    st, mv, rs = K.prm[:, 0:12].rearrange("p (a b) -> p a b", a=2), K.prm[:, 12:14], K.prm[:, 14:15]
    K.x1 = nc.dram_tensor("x1", (T, D), F32, kind="Internal").ap()
    w_in, x_in, r_in = K.sem("jn_win"), [K.sem(f"jn_xin{s}") for s in range(3)], K.sem("jn_rin")
    mm, mev, sq, x1r, hr, tr, thi, tev, chain = (K.sem("jn_" + n) for n in "mm mev sq x1r hr tr thi tev chain".split())
    stored = [K.sem(f"jn_st{s}") for s in range(2)]
    with nc.Block() as block:
        @block.sync
        def _(sp):
            w = I["w_out"][0].rearrange("(k p) n -> p k n", p=P)
            for k in range(0, KT, 4):
                sp.dma_start(wo[:, k:k + 4, :], w[:, k:k + 4, :]).then_inc(w_in, 16)
            for r, name in enumerate(("ln1_w", "ln1_b")):
                sp.dma_start(rows[:, r, :], I[name].to_broadcast([P, D])).then_inc(r_in, 16)
            for i in range(NT):
                if i >= 3:
                    sp.wait_ge(x1r, i - 2)
                sp.dma_start(xr[i % 3][:], I["x"][0][i * P:(i + 1) * P, :]).then_inc(x_in[i % 3], 16)

        @block.gpsimd
        def _(pool):
            for i in range(NT):
                pool.wait_ge(x1r, i + 1)
                pool.dma_start(K.x1[i * P:(i + 1) * P, :], t[i % 2][:]).then_inc(stored[i % 2], 16)
            for s in range(2):
                pool.wait_ge(stored[s], 16 * NT // 2)

        @block.tensor
        def _(pe):
            def turn(i):
                pe.wait_ge(hr, i + 1)
                if i >= 2:
                    pe.wait_ge(tev, 2 * (i - 1))
                for k in range(KT):
                    last = nc.tensor.transpose(K.bank[4 + 2 * (i % 2) + k // 4][:, (k % 4) * P:(k % 4 + 1) * P],
                                               h[i % 2][:, k * P:(k + 1) * P], K.ident[:])
                last.then_inc(tr, 1)

            pe.wait_ge(w_in, 32)
            for i in range(NT):
                if i >= 2:
                    pe.wait_ge(mev, i - 1)
                for b in range(2):
                    for k in range(KT):
                        last = nc.tensor.matmul(K.bank[2 * (i % 2) + b][:], K.yT[k][:, i * P:(i + 1) * P], wo[:, k, b * HALF:(b + 1) * HALF],
                                                start=(k == 0), stop=(k == KT - 1))
                last.then_inc(mm, 1)
                if i:
                    turn(i - 1)
            turn(NT - 1)

        @block.scalar
        def _(act):
            def take(i):
                act.wait_ge(tr, i + 1)
                for b in range(2):
                    nc.scalar.activation(K.h2[0][:, i // 4, 4 * b:4 * b + 4, (i % 4) * P:(i % 4 + 1) * P],
                                         K.bank[4 + 2 * (i % 2) + b][:].rearrange("p (k t) -> p k t", k=4), ACT.Copy).then_inc(thi, 1)

            for i in range(NT):
                act.wait_ge(sq, 2 * i + 1)
                nc.scalar.activation(rs, rs, ACT.Sqrt).then_inc(sq, 1)
                if i:
                    take(i - 1)
            take(NT - 1)

        @block.vector
        def _(dve):
            v = nc.vector
            link = Link(v, chain)

            def low(i):
                for b in range(2):
                    dve.wait_ge(thi, 2 * i + b + 1)
                    at = (slice(None), i // 4, slice(4 * b, 4 * b + 4), slice((i % 4) * P, (i % 4 + 1) * P))
                    v.tensor_tensor(K.h2[1][at], K.bank[4 + 2 * (i % 2) + b][:].rearrange("p (k t) -> p k t", k=4), K.h2[0][at].bitcast(F32),
                                    ALU.subtract).then_inc(tev, 1)

            dve.wait_ge(r_in, 32)
            for i in range(NT):
                x, y = xr[i % 3], t[i % 2]
                dve.wait_ge(mm, i + 1)
                if i >= 2:
                    dve.wait_ge(stored[i % 2], 16 * (i // 2))
                for b in range(2):
                    s = slice(b * HALF, (b + 1) * HALF)
                    last = v.tensor_tensor(y[:, s], K.bank[2 * (i % 2) + b][:], K.MOD[:, 2 * D + b * HALF:2 * D + (b + 1) * HALF], ALU.mult)
                last.then_inc(mev, 1)
                dve.wait_ge(mev, i + 1)
                dve.wait_ge(x_in[i % 3], 16 * (i // 3 + 1))
                link(v.scalar_tensor_tensor(out=y[:], in0=x[:], scalar=ALPHA, in1=y[:], op0=ALU.mult, op1=ALU.add))
                norm_rows(K, dve, link, y, st, mv, rs, sq, i, rows[:, 0, :], rows[:, 1, :]).then_inc(x1r, 1)
                dve.wait_ge(x1r, i + 1)
                if i >= 2:
                    dve.wait_ge(tr, i - 1)
                link(v.scalar_tensor_tensor(out=h[i % 2][:], in0=K.MOD[:, 4 * D:5 * D], scalar=1.0, in1=y[:], op0=ALU.add, op1=ALU.mult))
                v.tensor_tensor(h[i % 2][:], h[i % 2][:], K.MOD[:, 3 * D:4 * D], ALU.add).then_inc(hr, 1)
                if i:
                    low(i - 1)
            low(NT - 1)


def norm_rows(K, dve, link, y, st, mv, rs, sq, i, w, b):
    v = K.nc.vector
    for h in range(2):
        link(v.bn_stats(st[:, h, :], y[:, h * HALF:(h + 1) * HALF]))
    link(v.bn_aggr(mv, st))
    v.tensor_scalar(rs, mv[:, 1:2], LN_EPS, None, ALU.add).then_inc(sq, 1)
    link(v.scalar_tensor_tensor(out=y[:], in0=y[:], scalar=mv[:, 0:1], in1=w, op0=ALU.subtract, op1=ALU.mult))
    dve.wait_ge(sq, 2 * i + 2)
    link(v.reciprocal(rs, rs))
    return v.scalar_tensor_tensor(out=y[:], in0=y[:], scalar=rs, in1=b, op0=ALU.mult, op1=ALU.add)


def rms_root(K, act, x, junk, ss, sem, i):
    K.nc.scalar.activation(junk, x, ACT.Square, accum_out=ss).then_inc(sem, 1)
    act.wait_ge(sem, 2 * i + 1)
    K.nc.scalar.activation(ss, ss, ACT.Sqrt, scale=1.0 / D, bias=K.eps[:]).then_inc(sem, 1)


def product(nc, out, w, x, first, last):
    nc.tensor.matmul(out, w[0], x[0], start=first, stop=False)
    nc.tensor.matmul(out, w[0], x[1], start=False, stop=False)
    return nc.tensor.matmul(out, w[1], x[0], start=False, stop=last)


def stage_ffn(K):
    nc, I = K.nc, K.I
    NR, FT = 4, 2
    QUART = (0, 6, 12, 17, NF)
    UH, UO = 2 * NF, 4 * KT
    hid = [K.at(f"ff_hid{n}", 24 + 44 * n, [P, NF, HALF], FR) for n in range(2)]
    raw = [K.at(f"ff_raw{s}", 112 + 4 * s, [P, KT, P]) for s in range(NR)]
    part = [[K.at(f"ff_part{s}{n}", 8 * s + 4 * n, [P, KT, P], FR) for n in range(2)] for s in range(2)]
    sil = [K.at(f"ff_sil{s}", 16 + 2 * s, [P, HALF]) for s in range(2)]
    hv = [K.at(f"ff_hv{s}", 128 + 2 * s, [P, HALF]) for s in range(2)]
    K.ynT = K.at("ynT", 164, [P, 2, KT, HALF])
    raw_in = [K.sem(f"ff_raw_in{s}") for s in range(NR)]
    hi, lo, mm, sr, hr, hhi, hlo, oev = (K.sem("ff_" + n) for n in "hi lo mm sr hr hhi hlo oev".split())
    w1 = I["w_ffn_in"][0].rearrange("(k p) (a f) -> p k a f", p=P, a=2)
    w2 = I["w_ffn_out"][0].rearrange("(f p) n -> p f n", p=P)

    def loop(eng, body, count):
        body(0)
        with eng.Fori(1, count) as r:
            body(r)

    def unit(h, r, c):
        return (UH + UO) * h + r * c

    with nc.Block() as block:
        @block.sync
        def _(sp):
            for h in range(2):
                def hidden(r):
                    for s in range(NR):
                        if h or not isinstance(r, int):
                            sp.wait_ge(lo, unit(h, r, NR) + s - (NR - 1))
                        sp.dma_start(raw[s][:], w1[:, :, s % 2, bass.ds(r * (FT * P) + (s // 2) * P, P)]).then_inc(raw_in[s], 16)

                def output(r):
                    for m in range(2):
                        for s in range(NR):
                            f = slice(QUART[s], QUART[s + 1])
                            sp.wait_ge(lo, unit(h, r, 2 * NR) + UH + NR * m + s - (NR - 1))
                            sp.dma_start(raw[s][:, 0:f.stop - f.start, :], w2[:, f, bass.ds(r * (2 * P) + m * P, P)]).then_inc(raw_in[s], 16)

                loop(sp, hidden, NF // FT)
                loop(sp, output, KT // 2)

        def arrivals(h, phase, r, m=0):
            return ((UH + UO) // NR) * h + (r if phase == 0 else UH // NR + r * 2 + m) + 1

        @block.scalar
        def _(act):
            def split(u, s, n, count):
                act.wait_ge(raw_in[s], count * 16)
                if not isinstance(u, int) or u >= 2:
                    act.wait_ge(mm, u - 1)
                nc.scalar.activation(part[s % 2][0][:, 0:n, :], raw[s][:, 0:n, :], ACT.Copy).then_inc(hi, 1)

            def silu(h, u, f, s):
                act.wait_ge(mm, u + 1)
                if not isinstance(f, int) or h or f >= 2:
                    act.wait_ge(hr, NF * h + f - 1)
                nc.scalar.activation(sil[s][:], K.bank[2 * s][:], ACT.Silu).then_inc(sr, 1)
                act.wait_ge(hr, NF * h + f + 1)
                nc.scalar.activation(hid[0][:, bass.ds(f, 1), :], hv[s][:].unsqueeze(1), ACT.Copy).then_inc(hhi, 1)

            def take(h, u, m, s):
                act.wait_ge(mm, u + 1)
                nc.scalar.activation(K.ynT[:, h, bass.ds(m, 1), :], K.bank[4 + s][:].unsqueeze(1), ACT.Copy).then_inc(oev, 1)

            for h in range(2):
                def hidden(r):
                    for j in range(FT):
                        u = unit(h, r, NR) + 2 * j
                        for a in range(2):
                            split(u + a, 2 * j + a, KT, arrivals(h, 0, r))
                        if j or not isinstance(r, int):
                            silu(h, u - 2, r * FT + (j - 1), 1 - j)
                        elif h:
                            take(0, u - 1, KT - 1, 1)

                def output(r):
                    for m in range(2):
                        u = unit(h, r, 2 * NR) + UH + NR * m
                        for s in range(NR):
                            split(u + s, s, QUART[s + 1] - QUART[s], arrivals(h, 1, r, m))
                            if s == 1:
                                if m or not isinstance(r, int):
                                    take(h, u - 1, r * 2 + (m - 1), 1 - m)
                                else:
                                    silu(h, u - 2, NF - 1, 1)

                loop(act, hidden, NF // FT)
                loop(act, output, KT // 2)
            take(1, 2 * (UH + UO) - 1, KT - 1, 1)

        @block.vector
        def _(dve):
            v = nc.vector

            def split(u, s, n):
                dve.wait_ge(hi, u + 1)
                v.tensor_tensor(part[s % 2][1][:, 0:n, :], raw[s][:, 0:n, :], part[s % 2][0][:, 0:n, :].bitcast(F32), ALU.subtract).then_inc(lo, 1)

            def multiply(h, u, f, s):
                dve.wait_ge(mm, u + 1)
                dve.wait_ge(sr, NF * h + f + 1)
                if not isinstance(f, int) or h or f >= 2:
                    dve.wait_ge(hlo, NF * h + f - 1)
                v.tensor_tensor(hv[s][:], sil[s][:], K.bank[2 * s + 1][:], ALU.mult).then_inc(hr, 1)
                dve.wait_ge(hhi, NF * h + f + 1)
                v.tensor_tensor(hid[1][:, bass.ds(f, 1), :], hv[s][:].unsqueeze(1), hid[0][:, bass.ds(f, 1), :].bitcast(F32), ALU.subtract).then_inc(hlo, 1)

            for h in range(2):
                def hidden(r):
                    for j in range(FT):
                        u = unit(h, r, NR) + 2 * j
                        for a in range(2):
                            split(u + a, 2 * j + a, KT)
                        if j or not isinstance(r, int):
                            multiply(h, u - 1, r * FT + (j - 1), 1 - j)

                def output(r):
                    for m in range(2):
                        u = unit(h, r, 2 * NR) + UH + NR * m
                        for s in range(NR):
                            split(u + s, s, QUART[s + 1] - QUART[s])
                            if s == 1 and m == 0 and isinstance(r, int):
                                multiply(h, u - 1, NF - 1, 1)

                loop(dve, hidden, NF // FT)
                loop(dve, output, KT // 2)

        @block.tensor
        def _(pe):
            for h in range(2):
                def hidden(r):
                    for j in range(FT):
                        for a in range(2):
                            u, s = unit(h, r, NR) + 2 * j + a, 2 * j + a
                            if a == 0 and (h or not isinstance(r, int)):
                                pe.wait_ge(hr, NF * h + r * FT + (j - 1))
                            pe.wait_ge(lo, u + 1)
                            for k in range(KT):
                                last = product(nc, K.bank[2 * j + a][:], [w[:, k, :] for w in part[s % 2]], [x[:, h, k, :] for x in K.h2],
                                               k == 0, k == KT - 1)
                            last.then_inc(mm, 1)

                def output(r):
                    for m in range(2):
                        if h or not isinstance(r, int):
                            pe.wait_ge(oev, KT * h + r * 2 + (m - 1))
                        for s in range(NR):
                            if m == 0 and isinstance(r, int):
                                pe.wait_ge(hlo, NF * h + QUART[s + 1])
                            pe.wait_ge(lo, unit(h, r, 2 * NR) + UH + NR * m + s + 1)
                            for f in range(QUART[s], QUART[s + 1]):
                                last = product(nc, K.bank[4 + m][:], [w[:, f - QUART[s], :] for w in part[s % 2]], [x[:, f, :] for x in hid],
                                               f == 0, f == NF - 1)
                            last.then_inc(mm, 1)

                loop(pe, hidden, NF // FT)
                loop(pe, output, KT // 2)


def stage_first_end(K):
    nc, I = K.nc, K.I
    xr = [K.at(f"fe_x{s}", 88 + 4 * s, [P, D]) for s in range(3)]
    rows = K.at("fe_rows", 100, [P, 3, D])
    t = [K.at(f"fe_t{s}", 112 + 4 * s, [P, D]) for s in range(2)]
    h = [K.at(f"fe_h{s}", 120 + 4 * s, [P, D]) for s in range(2)]
    K.h3 = [K.at(f"h3{n}", 24 + 32 * n, [P, KT, T], FR) for n in range(2)]
    st, mv, rs = K.prm[:, 0:12].rearrange("p (a b) -> p a b", a=2), K.prm[:, 12:14], K.prm[:, 14:15]
    ss = K.prm[:, 16:24]
    K.x2 = nc.dram_tensor("x2", (T, D), F32, kind="Internal").ap()
    x_in, r_in = [K.sem(f"fe_xin{s}") for s in range(3)], K.sem("fe_rin")
    mm, mev, sq, x2r, ssr, hr, tr, thi, tev, chain = (K.sem("fe_" + n) for n in "mm mev sq x2r ssr hr tr thi tev chain".split())
    stored = [K.sem(f"fe_st{s}") for s in range(2)]
    with nc.Block() as block:
        @block.sync
        def _(sp):
            for r, name in enumerate(("ln2_w", "ln2_b", "norm_mix_2")):
                sp.dma_start(rows[:, r, :], I[name].to_broadcast([P, D])).then_inc(r_in, 16)
            for i in range(NT):
                if i >= 3:
                    sp.wait_ge(x2r, i - 2)
                sp.dma_start(xr[i % 3][:], K.x1[i * P:(i + 1) * P, :]).then_inc(x_in[i % 3], 16)

        @block.gpsimd
        def _(pool):
            for i in range(NT):
                pool.wait_ge(x2r, i + 1)
                pool.dma_start(K.x2[i * P:(i + 1) * P, :], t[i % 2][:]).then_inc(stored[i % 2], 16)
            for s in range(2):
                pool.wait_ge(stored[s], 16 * NT // 2)

        @block.tensor
        def _(pe):
            def back(i):
                if i >= 2:
                    pe.wait_ge(mev, i - 1)
                for k in range(KT):
                    last = nc.tensor.transpose(K.bank[2 * (i % 2) + k // 4][:, (k % 4) * P:(k % 4 + 1) * P],
                                               K.ynT[:, i // 4, k, (i % 4) * P:(i % 4 + 1) * P], K.ident[:])
                last.then_inc(mm, 1)

            def turn(i):
                pe.wait_ge(hr, i + 1)
                if i >= 2:
                    pe.wait_ge(tev, 2 * (i - 1))
                for k in range(KT):
                    last = nc.tensor.transpose(K.bank[4 + 2 * (i % 2) + k // 4][:, (k % 4) * P:(k % 4 + 1) * P],
                                               h[i % 2][:, k * P:(k + 1) * P], K.ident[:])
                last.then_inc(tr, 1)

            for i in range(NT):
                back(i)
                if i:
                    turn(i - 1)
            turn(NT - 1)

        @block.scalar
        def _(act):
            def take(i):
                act.wait_ge(tr, i + 1)
                for b in range(2):
                    nc.scalar.activation(K.h3[0][:, 4 * b:4 * b + 4, i * P:(i + 1) * P],
                                         K.bank[4 + 2 * (i % 2) + b][:].rearrange("p (k t) -> p k t", k=4), ACT.Copy).then_inc(thi, 1)

            for i in range(NT):
                act.wait_ge(sq, 2 * i + 1)
                nc.scalar.activation(rs, rs, ACT.Sqrt).then_inc(sq, 1)
                act.wait_ge(x2r, i + 1)
                if i >= 2:
                    act.wait_ge(tr, i - 1)
                rms_root(K, act, t[i % 2][:], h[i % 2][:], ss[:, i:i + 1], ssr, i)
                if i:
                    take(i - 1)
            take(NT - 1)

        @block.vector
        def _(dve):
            v = nc.vector
            link = Link(v, chain)

            def norm(i):
                x, y = xr[i % 3], t[i % 2]
                dve.wait_ge(mm, i + 1)
                if i >= 2:
                    dve.wait_ge(stored[i % 2], 16 * (i // 2))
                for b in range(2):
                    s = slice(b * HALF, (b + 1) * HALF)
                    last = v.tensor_tensor(y[:, s], K.bank[2 * (i % 2) + b][:], K.MOD[:, 5 * D + b * HALF:5 * D + (b + 1) * HALF], ALU.mult)
                last.then_inc(mev, 1)
                dve.wait_ge(mev, i + 1)
                dve.wait_ge(x_in[i % 3], 16 * (i // 3 + 1))
                link(v.scalar_tensor_tensor(out=y[:], in0=x[:], scalar=ALPHA, in1=y[:], op0=ALU.mult, op1=ALU.add))
                norm_rows(K, dve, link, y, st, mv, rs, sq, i, rows[:, 0, :], rows[:, 1, :]).then_inc(x2r, 1)

            def scale(i):
                dve.wait_ge(ssr, 2 * i + 2)
                link(v.reciprocal(ss[:, i:i + 1], ss[:, i:i + 1]))
                v.scalar_tensor_tensor(out=h[i % 2][:], in0=t[i % 2][:], scalar=ss[:, i:i + 1], in1=rows[:, 2, :],
                                       op0=ALU.mult, op1=ALU.mult).then_inc(hr, 1)

            def low(i):
                for b in range(2):
                    dve.wait_ge(thi, 2 * i + b + 1)
                    at = (slice(None), slice(4 * b, 4 * b + 4), slice(i * P, (i + 1) * P))
                    v.tensor_tensor(K.h3[1][at], K.bank[4 + 2 * (i % 2) + b][:].rearrange("p (k t) -> p k t", k=4), K.h3[0][at].bitcast(F32),
                                    ALU.subtract).then_inc(tev, 1)

            dve.wait_ge(r_in, 48)
            for i in range(NT):
                norm(i)
                if i:
                    scale(i - 1)
                if i >= 2:
                    low(i - 2)
            scale(NT - 1)
            low(NT - 2)
            low(NT - 1)


PJ_KB, FREE_KB, SMALL_KB = 88, 24, 18


def packed(i):
    return slice(P * i * (i + 1) // 2, P * (i + 1) * (i + 2) // 2)


def stage_project(K):
    nc, I = K.nc, K.I
    NR = 4
    K.PJ = K.at("PJ", PJ_KB, [P, 6, NT, HALF])
    K.MS = K.at("MS", 184, [P, NT, N_MIX])
    K.NM = K.at("NM", 0, [P, P * NT * (NT + 1) // 2])
    part = [[K.at(f"pj_part{s}{n}", PJ_KB + 80 + 4 * s + 2 * n, [P, HALF], FR) for n in range(2)] for s in range(NR)]
    raw = [K.at(f"pj_raw{s}", PJ_KB + 80 + 4 * s + 2, [P, HALF]) for s in range(NR)]
    iqT = K.at("pj_iqT", PJ_KB, [P, 2, T])
    ikT = K.at("pj_ikT", PJ_KB + 8, [P, T])
    ikd = K.at("pj_ikd", PJ_KB + 12, [P, NT, P])
    sqr = K.at("pj_sqr", PJ_KB + 16, [P, NT, LAT])
    kvr = K.at("pj_kvr", PJ_KB + 20, [P, LAT])
    scr = K.at("pj_scr", PJ_KB + 22, [P, 2, NT * IH * FREQ_I])
    ang, red, quar, kk = (K.at(f"pj_ang{n}", SMALL_KB + 1.375 * n, [P, NT, NFREQ]) for n in range(4))
    rel = [K.at(f"pj_rel{s}", SMALL_KB + 2 * s, [P, HALF]) for s in range(2)]
    run = K.at("pj_run", SMALL_KB, [P, T])
    flag = K.at("pj_flag", SMALL_KB + 4, [P, T], mybir.dt.uint8)
    junk = K.at("pj_junk", SMALL_KB, [P, P * NT * (NT + 1) // 2], mybir.dt.uint8)
    pscr = K.at("pj_pscr", 197.75, [P, 2, RH * FREQ_R])
    used = [0]

    def columns(n, dt=F32):
        used[0] += n
        c = K.prm[:, used[0] - n:used[0]]
        return c if dt == F32 else c.bitcast(dt)

    NB = NT - 2
    sin, cos = (columns(NT * NFREQ).rearrange("p (i f) -> p i f", i=NT) for _ in range(2))
    freq, pos = columns(NFREQ), columns(NT)
    posi = columns(NT, I32)
    wq = columns(NT * IH).rearrange("p (i h) -> p i h", i=NT)
    ss = columns(NT)
    key, bit, cand, sign, flip, keep = (columns(NB, I32) for _ in range(6))
    cnt, need = columns(NB), columns(NB)
    w_in = [K.sem(f"pj_win{s}") for s in range(NR)]
    names = "prm hi lo um tm ev angr tab rope rms kvr itr iev smm relr used zero key chain pchain".split()
    S = {n: K.sem("pj_" + n) for n in names}
    R_Q, R_K, R_V, R_G, D_Q, D_G = range(6)
    slabs = [None, R_Q, R_K, R_V, R_G, D_Q, D_G]
    pieces = [(i, h, c) for i in range(NT) for h in range(IH) for c in range(0, P * (i + 1), HALF)]

    def table(t, lo, n, heads):
        return t[:, :, lo:lo + n].unsqueeze(2).to_broadcast([P, NT, heads, n])

    with nc.Block() as block:
        @block.sync
        def _(sp):
            w = I["w_in_2"][0].rearrange("(k p) n -> p k n", p=P)
            def load(u, s, *cols):
                if not isinstance(u, int) or u >= NR:
                    sp.wait_ge(S["um"], u - (NR - 1))
                at = 0
                for c, n in cols:
                    sp.dma_start(raw[s % NR][:, at:at + n], w[:, s, c:c + n] if isinstance(c, int) else w[:, s, bass.ds(c, n)]).then_inc(w_in[s % NR], 16)
                    at += n

            for k in range(NR):
                load(k, k, (C_LAT, M_IQ), (C_IDX, N_IDX))
            with nc.allow_non_contiguous_dma(reason="positions as columns"):
                sp.dma_start(posi[:], I["positions_2"].rearrange("(i p) -> p i", p=P)).then_inc(S["prm"], 16)
            sp.dma_start(freq[:], I["freq"].to_broadcast([P, NFREQ])).then_inc(S["prm"], 16)
            sp.dma_start(kvr[:], I["kv_norm_2"].to_broadcast([P, LAT])).then_inc(S["prm"], 16)
            for k in range(NR, KT):
                load(k, k, (C_LAT, M_IQ), (C_IDX, N_IDX))
            with sp.Fori(1, len(slabs) - 1) as j:
                for k in range(KT):
                    load(j * KT + k, k, ((j - 1) * HALF, HALF))
            for k in range(KT):
                load((len(slabs) - 1) * KT + k, k, (C_GATE, HALF))

        @block.tensor
        def _(pe):
            def slab(j):
                cols = N_MIX if isinstance(j, int) and j == 0 else HALF
                for k in range(KT):
                    pe.wait_ge(S["lo"], j * KT + k + 1)
                    for i in range(NT):
                        if k == 0 and (not isinstance(j, int) or j):
                            pe.wait_ge(S["ev"], (j - 1) * NT + i + 1)
                        last = product(nc, K.bank[i][:, 0:cols], [x[:, k, i * P:(i + 1) * P] for x in K.h3], [w[:, 0:cols] for w in part[k % NR]],
                                       k == 0, k == KT - 1)
                        if k == KT - 1 and i < NT - 1:
                            last.then_inc(S["tm"], 1)
                    last.then_inc(S["um"], 1)

            slab(0)
            pe.wait_ge(S["ev"], NT)
            pe.wait_ge(S["rope"], 1)
            for i in range(NT):
                if i >= 4:
                    pe.wait_ge(S["iev"], i - 3)
                b = K.bank[4 + i % 4]
                for m in range(2):
                    nc.tensor.transpose(b[:, m * P:(m + 1) * P], K.MS[:, i, M_IQ + m * P:M_IQ + (m + 1) * P], K.ident[:])
                nc.tensor.transpose(b[:, 2 * P:3 * P], ikd[:, i, :], K.ident[:]).then_inc(S["itr"], 1)
            pe.wait_ge(S["iev"], NT)
            for m, (i, h, c) in enumerate(pieces):
                if m >= 4:
                    pe.wait_ge(S["relr"], m - 3)
                r = slice(IDIM * (h % 4), IDIM * (h % 4 + 1))
                e = min(c + HALF, P * (i + 1))
                nc.tensor.matmul(K.bank[4 + m % 4][:, 0:e - c], iqT[r, h // 4, i * P:(i + 1) * P], ikT[r, c:e],
                                 start=True, stop=True).then_inc(S["smm"], 1)
            pe.wait_ge(S["relr"], len(pieces))
            with pe.Fori(1, len(slabs)) as j:
                slab(j)

        @block.scalar
        def _(act):
            arrived = [0] * NR

            def split(j, ks):
                cols = N_MIX if j == 0 else HALF
                for k in ks:
                    arrived[k % NR] += 32 if j == 0 else 16
                    act.wait_ge(w_in[k % NR], arrived[k % NR])
                    nc.scalar.activation(part[k % NR][0][:, 0:cols], raw[k % NR][:, 0:cols], ACT.Copy).then_inc(S["hi"], 1)

            def take(j):
                if j == len(slabs) - 1:
                    act.wait_ge(S["um"], len(slabs) * KT)
                for i in range(NT):
                    if i < NT - 1:
                        act.wait_ge(S["tm"], j * (NT - 1) + i + 1)
                    else:
                        act.wait_ge(S["um"], (j + 1) * KT)
                    dst = K.MS[:, i, :] if j == 0 else K.PJ[:, slabs[j], i, :]
                    func = ACT.Silu if slabs[j] in (R_G, D_G) else ACT.Copy
                    nc.scalar.activation(dst, K.bank[i][:, 0:N_MIX if j == 0 else HALF], func).then_inc(S["ev"], 1)

            split(0, range(4))
            act.wait_ge(S["angr"], 1)
            nc.scalar.activation(sin[:], red[:], ACT.Sin).then_inc(S["tab"], 1)
            nc.scalar.activation(cos[:], quar[:], ACT.Sin).then_inc(S["tab"], 1)
            split(0, range(4, KT))
            split(1, range(3))
            take(0)
            split(1, range(3, 4))
            for i in range(NT):
                act.wait_ge(S["itr"], i + 1)
                b = K.bank[4 + i % 4]
                nc.scalar.activation(iqT[:, :, i * P:(i + 1) * P], b[:, 0:2 * P].rearrange("p (m t) -> p m t", m=2), ACT.Copy)
                nc.scalar.activation(ikT[:, i * P:(i + 1) * P], b[:, 2 * P:3 * P], ACT.Copy).then_inc(S["iev"], 1)
            act.wait_ge(S["rms"], 1)
            nc.scalar.activation(ss[:], ss[:], ACT.Sqrt).then_inc(S["rms"], 1)
            for m, (i, h, c) in enumerate(pieces):
                act.wait_ge(S["smm"], m + 1)
                if m >= 2:
                    act.wait_ge(S["used"], m - 1)
                e = min(c + HALF, P * (i + 1))
                nc.scalar.activation(rel[m % 2][:, 0:e - c], K.bank[4 + m % 4][:, 0:e - c], ACT.Relu, scale=IDIM ** -0.5).then_inc(S["relr"], 1)
            split(1, range(4, KT))
            for j in range(2, len(slabs)):
                split(j, range(3))
                take(j - 1)
                split(j, range(3, KT))
            take(len(slabs) - 1)

        @block.gpsimd
        def _(pool):
            g = nc.gpsimd
            link = Link(g, S["pchain"])

            def turn(j, lo, n, tiles):
                pool.wait_ge(S["ev"], NT * j + tiles.stop)
                x = K.PJ[:, slabs[j], tiles].rearrange("p i (h e) -> p i h e", h=RH)
                ni = tiles.stop - tiles.start
                t, u = (pscr[:, a, 0:ni * RH * n].rearrange("p (i h f) -> p i h f", i=ni, h=RH) for a in range(2))
                c, s = (x[:, tiles, lo:lo + n].unsqueeze(2).to_broadcast([P, ni, RH, n]) for x in (cos, sin))
                cmul(nc, link, x[:, :, :, 0:n], x[:, :, :, n:2 * n], x[:, :, :, 0:n], x[:, :, :, n:2 * n], c, s, t, u)

            for j in range(len(slabs)):
                cols = N_MIX if j == 0 else HALF
                for k in range(KT):
                    pool.wait_ge(S["hi"], j * KT + k + 1)
                    g.tensor_tensor(part[k % NR][1][:, 0:cols], raw[k % NR][:, 0:cols], part[k % NR][0][:, 0:cols].bitcast(F32), ALU.subtract).then_inc(S["lo"], 1)
                    if k == 0 and j == 1:
                        pool.wait_ge(S["tab"], 2)
                    if k >= 4 and slabs[j - 1] == D_Q:
                        turn(j - 1, FREQ_R, FREQ_A, slice(2 * (k - 4), 2 * (k - 3)))
                    elif k >= 4 and slabs[j - 1] in (R_Q, R_K):
                        for i in range(2 * (k - 4), 2 * (k - 3)):
                            turn(j - 1, 0, FREQ_R, slice(i, i + 1))

        @block.vector
        def _(dve):
            v = nc.vector
            link = Link(v, S["chain"])
            dve.wait_ge(S["prm"], 48)
            link(v.tensor_copy(pos[:], posi[:]))
            link(v.tensor_tensor(ang[:], pos[:].unsqueeze(2).to_broadcast([P, NT, NFREQ]), freq[:].unsqueeze(1).to_broadcast([P, NT, NFREQ]), ALU.mult))
            reduce_angle(nc, link, red[:], quar[:], ang[:], kk[:])
            dve.sem_inc(S["angr"], 1)
            dve.wait_ge(S["ev"], NT)
            dve.wait_ge(S["tab"], 2)
            for at, heads, width, lo, n in ((M_IK, 1, IDIM, FREQ_R + FREQ_A, FREQ_I), (M_IQ, IH, IDIM, FREQ_R + FREQ_A, FREQ_I),
                                            (M_PE, 1, PE_D, FREQ_R, FREQ_A)):
                if at == M_PE:
                    for m in range(4):
                        last = v.tensor_copy(ikd[:, :, m * IDIM:(m + 1) * IDIM], K.MS[:, :, M_IK:M_IK + IDIM])
                    last.then_inc(S["rope"], 1)
                x = K.MS[:, :, at:at + heads * width].rearrange("p i (h e) -> p i h e", h=heads)
                t, u = (scr[:, a, 0:NT * heads * n].rearrange("p (i h f) -> p i h f", i=NT, h=heads) for a in range(2))
                cmul(nc, link, x[:, :, :, 0:n], x[:, :, :, n:2 * n], x[:, :, :, 0:n], x[:, :, :, n:2 * n],
                     table(cos, lo, n, heads), table(sin, lo, n, heads), t, u)
            lat = K.MS[:, :, 0:LAT]
            link(v.tensor_tensor(sqr[:], lat, lat, ALU.mult))
            link(v.tensor_reduce(ss[:], sqr[:], AX.X, ALU.add))
            v.tensor_scalar(ss[:], ss[:], 1.0 / LAT, RMS_EPS, ALU.mult, ALU.add).then_inc(S["rms"], 1)
            link(v.tensor_scalar(wq[:], K.MS[:, :, M_IW:M_IW + IH], IH ** -0.5, None, ALU.mult))
            dve.wait_ge(S["rms"], 2)
            link(v.reciprocal(ss[:], ss[:]))
            link(v.tensor_tensor(lat, lat, ss[:].unsqueeze(2).to_broadcast([P, NT, LAT]), ALU.mult))
            link(v.tensor_tensor(lat, lat, kvr[:].unsqueeze(1).to_broadcast([P, NT, LAT]), ALU.mult))
            for m, (i, h, c) in enumerate(pieces):
                dve.wait_ge(S["relr"], m + 1)
                e = min(c + HALF, P * (i + 1))
                dst = K.NM[:, packed(i)][:, c:e]
                if h == 0:
                    ins = v.tensor_scalar(dst, rel[m % 2][:, 0:e - c], wq[:, i, h:h + 1], None, ALU.mult)
                else:
                    ins = v.scalar_tensor_tensor(out=dst, in0=rel[m % 2][:, 0:e - c], scalar=wq[:, i, h:h + 1], in1=dst, op0=ALU.mult, op1=ALU.add)
                ins.then_inc(S["used"], 1)
                dve.wait_ge(S["used"], m + 1)
            for i in range(2):
                link(v.memset(K.NM[:, packed(i)], 0.0))
            for i in range(NT):
                link(v.memset(K.NM[0:RCHUNK, packed(i)][:, P * (i + 1) - RCHUNK:], LOW))
            link(v.memset(key[:], 0))
            link(v.memset(bit[:], 1))
            link(v.tensor_scalar(bit[:], bit[:], 31, None, ALU.logical_shift_left))
            with dve.Fori(0, 32) as r:
                per = 8
                v.tensor_tensor(cand[:], key[:], bit[:], ALU.bitwise_or).then_inc(S["key"], 1)
                dve.wait_ge(S["key"], per * r + 1)
                v.tensor_scalar(sign[:], cand[:], 31, None, ALU.arith_shift_right).then_inc(S["key"], 1)
                dve.wait_ge(S["key"], per * r + 2)
                v.tensor_scalar(flip[:], sign[:], -1, -2147483648, ALU.bitwise_xor, ALU.bitwise_or).then_inc(S["key"], 1)
                dve.wait_ge(S["key"], per * r + 3)
                v.tensor_tensor(flip[:], cand[:], flip[:], ALU.bitwise_xor).then_inc(S["key"], 1)
                dve.wait_ge(S["key"], per * r + 4)
                for j in range(NB):
                    i = j + 2
                    last = v.tensor_scalar(junk[:, packed(i)], K.NM[:, packed(i)], flip[:, j:j + 1].bitcast(F32), 0.0, ALU.is_ge, ALU.add,
                                           accum_out=cnt[:, j:j + 1])
                last.then_inc(S["key"], 1)
                dve.wait_ge(S["key"], per * r + 5)
                v.tensor_scalar(keep[:], cnt[:], TOPK - 0.5, None, ALU.is_ge).then_inc(S["key"], 1)
                dve.wait_ge(S["key"], per * r + 6)
                v.tensor_scalar(bit[:], bit[:], 1, None, ALU.logical_shift_right).then_inc(S["key"], 1)
                v.copy_predicated(key[:], keep[:], cand[:]).then_inc(S["key"], 1)
                dve.wait_ge(S["key"], per * r + 8)
            link(v.tensor_scalar(sign[:], key[:], 31, None, ALU.arith_shift_right))
            link(v.tensor_scalar(flip[:], sign[:], -1, -2147483648, ALU.bitwise_xor, ALU.bitwise_or))
            link(v.tensor_tensor(flip[:], key[:], flip[:], ALU.bitwise_xor))
            for j in range(NB):
                i = j + 2
                n = P * (i + 1)
                thr, x = flip[:, j:j + 1].bitcast(F32), K.NM[:, packed(i)]
                link(v.tensor_scalar(flag[:, 0:n], x, thr, 0.0, ALU.is_gt, ALU.add, accum_out=cnt[:, j:j + 1]))
                link(v.tensor_scalar(need[:, j:j + 1], cnt[:, j:j + 1], -1.0, TOPK + 0.5, ALU.mult, ALU.add))
                link(v.tensor_scalar(flag[:, 0:n], x, thr, None, ALU.is_equal))
                link(v.tensor_tensor_scan(run[:, 0:n], flag[:, 0:n], flag[:, 0:n], 0.0, ALU.add, ALU.max))
                link(v.scalar_tensor_tensor(out=run[:, 0:n], in0=run[:, 0:n], scalar=need[:, j:j + 1], in1=flag[:, 0:n], op0=ALU.is_le, op1=ALU.mult))
                link(v.scalar_tensor_tensor(out=x, in0=x, scalar=thr, in1=run[:, 0:n], op0=ALU.is_gt, op1=ALU.add))
                link(v.tensor_scalar(x, x, 1.0, -LOW, ALU.subtract, ALU.mult))


def stage_retention(K):
    nc, I = K.nc, K.I
    J = RH // 2
    qT, kT, xq, rkz = ([K.at(f"rt_{n}{s}", kb + 2 * s, [P, J, P]) for s in range(2)]
                       for n, kb in (("qT", 24), ("kT", 28), ("xq", 32), ("kz", 44)))
    prob = [K.at(f"rt_prob{s}", 36 + 4 * s, [P, J, 2, P]) for s in range(2)]
    state = [K.at(f"rt_state{s}", 48 + s, [P, J, RD]) for s in range(2)]
    intra = K.at("rt_intra", 50, [P, J, 2, P])
    xi = K.at("rt_xi", 54, [P, J, P])
    row = K.at("rt_row", SMALL_KB, [P, HALF])
    sqr = K.at("rt_sqr", 72, [P, RH, RD])
    K.dqT = K.at("dqT", 56, [P, J, T])
    zeta, decay = K.prm[:, 0:RH], K.prm[:, 8:8 + J]
    mu, var = (K.prm[:, 16 + RH * n:16 + RH * (n + 1)] for n in range(2))
    names = "const tr qkr dqr smm prob xqr kzr out oev upd state var gate norm done chain".split()
    S = {n: K.sem("rt_" + n) for n in names}
    R_Q, R_K, R_V, R_G, D_Q, D_G = range(6)

    with nc.Block() as block:
        @block.sync
        def _(sp):
            sp.dma_start(intra[:], I["intra"].rearrange("p (j a) t -> p j a t", a=2)).then_inc(S["const"], 16)
            sp.dma_start(xi[:], I["xi"]).then_inc(S["const"], 16)
            sp.dma_start(zeta, I["zeta"]).then_inc(S["const"], 16)
            sp.dma_start(decay, I["decay"]).then_inc(S["const"], 16)
            sp.dma_start(row[:], I["ret_norm_2"].to_broadcast([P, HALF])).then_inc(S["const"], 16)

        @block.tensor
        def _(pe):
            def turn(i):
                if i:
                    pe.wait_ge(S["qkr"], 2 * i)
                    pe.wait_ge(S["dqr"], i)
                for b, slab in enumerate((R_Q, R_K, D_Q)):
                    for j in range(J):
                        tr = nc.tensor.transpose(K.bank[b][:, j * P:(j + 1) * P], K.PJ[:, slab, i, j * P:(j + 1) * P], K.ident[:])
                    tr.then_inc(S["tr"], 1)

            turn(0)
            for i in range(NT):
                s = i % 2
                pe.wait_ge(S["qkr"], 2 * (i + 1))
                if i:
                    pe.wait_ge(S["prob"], i)
                for h in range(RH):
                    d = slice(RD * (h % 2), RD * (h % 2 + 1))
                    mm = nc.tensor.matmul(K.bank[3 + h % 2][:, (h // 2) * P:(h // 2 + 1) * P], kT[s][d, h // 2, :], qT[s][d, h // 2, :],
                                          start=True, stop=True)
                mm.then_inc(S["smm"], 1)
                if i + 1 < NT:
                    turn(i + 1)
                    pe.wait_ge(S["kzr"], i + 1)
                    if i:
                        pe.wait_ge(S["state"], i)
                    for j in range(J):
                        mm = nc.tensor.matmul(K.bank[7][:, j * P:(j + 1) * P], rkz[s][:, j, :], K.PJ[:, R_V, i, j * P:(j + 1) * P],
                                              start=True, stop=True)
                    mm.then_inc(S["upd"], 1)
                pe.wait_ge(S["prob"], i + 1)
                if i:
                    pe.wait_ge(S["xqr"], i + 1)
                    pe.wait_ge(S["state"], i)
                    pe.wait_ge(S["oev"], i)
                for h in range(RH):
                    o = K.bank[5 + h % 2][:, (h // 2) * RD:(h // 2 + 1) * RD]
                    d = slice(RD * (h % 2), RD * (h % 2 + 1))
                    mm = nc.tensor.matmul(o, prob[s][:, h // 2, h % 2, :], K.PJ[:, R_V, i, h * RD:(h + 1) * RD], start=True, stop=(i == 0))
                    if i:
                        mm = nc.tensor.matmul(o, xq[s][d, h // 2, :], state[s][d, h // 2, :], start=False, stop=True)
                mm.then_inc(S["out"], 1)

        @block.scalar
        def _(act):
            def take(i):
                if i >= 2:
                    act.wait_ge(S["xqr"], i - 1)
                act.wait_ge(S["tr"], 3 * i + 3)
                for b, dst in enumerate((qT[i % 2], kT[i % 2])):
                    nc.scalar.activation(dst[:], K.bank[b][:].rearrange("p (j t) -> p j t", j=J), ACT.Copy).then_inc(S["qkr"], 1)
                nc.scalar.activation(K.dqT[:, :, i * P:(i + 1) * P], K.bank[2][:].rearrange("p (j t) -> p j t", j=J), ACT.Copy).then_inc(S["dqr"], 1)

            take(0)
            for i in range(NT):
                if i + 1 < NT:
                    take(i + 1)
                act.wait_ge(S["out"], i + 1)
                for b in range(2):
                    ev = nc.scalar.activation(K.PJ[:, R_Q, i, :].rearrange("p (j a d) -> p j a d", a=2, d=RD)[:, :, b, :],
                                              K.bank[5 + b][:, 0:J * RD].rearrange("p (j d) -> p j d", j=J), ACT.Copy)
                ev.then_inc(S["oev"], 1)
                act.wait_ge(S["var"], 2 * i + 1)
                nc.scalar.activation(var, var, ACT.Sqrt).then_inc(S["var"], 1)

        @block.gpsimd
        def _(pool):
            g = nc.gpsimd
            pool.wait_ge(S["const"], 80)
            for i in range(NT):
                s = i % 2
                if i + 1 < NT:
                    if i >= 2:
                        pool.wait_ge(S["upd"], i - 1)
                    g.tensor_tensor(rkz[s][:].rearrange("p j (a d) -> p (j a) d", a=2), K.PJ[:, R_K, i, :].rearrange("p (h d) -> p h d", h=RH),
                                    zeta.unsqueeze(2).to_broadcast([P, RH, RD]), ALU.mult).then_inc(S["kzr"], 1)
                pool.wait_ge(S["qkr"], 2 * i + 1)
                if i >= 2:
                    pool.wait_ge(S["out"], i - 1)
                g.tensor_tensor(xq[s][:], qT[s][:], xi[:], ALU.mult).then_inc(S["xqr"], 1)
                g.tensor_tensor(K.PJ[:, R_G, i, :], K.PJ[:, R_G, i, :], row[:], ALU.mult).then_inc(S["gate"], 1)
                if i:
                    pool.wait_ge(S["gate"], i)
                    pool.wait_ge(S["norm"], i)
                    g.tensor_tensor(K.PJ[:, R_Q, i - 1, :], K.PJ[:, R_Q, i - 1, :], K.PJ[:, R_G, i - 1, :], ALU.mult).then_inc(S["done"], 1)
            pool.wait_ge(S["norm"], NT)
            pool.wait_ge(S["gate"], NT)
            g.tensor_tensor(K.PJ[:, R_Q, NT - 1, :], K.PJ[:, R_Q, NT - 1, :], K.PJ[:, R_G, NT - 1, :], ALU.mult).then_inc(S["done"], 1)

        @block.vector
        def _(dve):
            v = nc.vector
            link = Link(v, S["chain"])

            def norm(i):
                o = K.PJ[:, R_Q, i, :].rearrange("p (h d) -> p h d", h=RH)
                dve.wait_ge(S["oev"], i + 1)
                link(v.tensor_reduce(mu, o, AX.X, ALU.add))
                link(v.tensor_scalar(mu, mu, 1.0 / RD, None, ALU.mult))
                link(v.tensor_tensor(o, o, mu.unsqueeze(2).to_broadcast([P, RH, RD]), ALU.subtract))
                link(v.tensor_tensor(sqr[:], o, o, ALU.mult))
                link(v.tensor_reduce(var, sqr[:], AX.X, ALU.add))
                v.tensor_scalar(var, var, 1.0 / RD, RMS_EPS, ALU.mult, ALU.add).then_inc(S["var"], 1)
                dve.wait_ge(S["var"], 2 * i + 2)
                link(v.reciprocal(var, var))
                v.tensor_tensor(o, o, var.unsqueeze(2).to_broadcast([P, RH, RD]), ALU.mult).then_inc(S["norm"], 1)

            dve.wait_ge(S["const"], 80)
            for i in range(NT):
                s = i % 2
                dve.wait_ge(S["smm"], i + 1)
                if i >= 2:
                    dve.wait_ge(S["out"], i - 1)
                for a in range(2):
                    pr = v.tensor_tensor(prob[s][:, :, a, :], K.bank[3 + a][:].rearrange("p (j t) -> p j t", j=J), intra[:, :, a, :], ALU.mult)
                pr.then_inc(S["prob"], 1)
                if i + 1 < NT:
                    new = state[1 - s]
                    if i:
                        link(v.tensor_tensor(new[:], state[s][:], decay.unsqueeze(2).to_broadcast([P, J, RD]), ALU.mult))
                    dve.wait_ge(S["upd"], i + 1)
                    b = K.bank[7][:].rearrange("p (j c) -> p j c", j=J)
                    for a in range(2):
                        d = slice(RD * a, RD * (a + 1))
                        if i:
                            up = v.tensor_tensor(new[d], new[d], b[d, :, d], ALU.add)
                        else:
                            up = v.tensor_copy(new[d], b[d, :, d])
                    up.then_inc(S["state"], 1)
                    dve.wait_ge(S["state"], i + 1)
                if i:
                    norm(i - 1)
            norm(NT - 1)


def stage_attention(K):
    nc, I = K.nc, K.I
    J = AH // 2
    kfT = K.at("at_kT", 24, [P, J, T])
    val = K.at("at_v", 40, [P, NT, AH * AD])
    prob = [K.at(f"at_prob{s}", 72 + 4 * s, [P, T]) for s in range(2)]
    probT = [K.at(f"at_probT{s}", 80 + 4 * s, [P, NT, P]) for s in range(2)]
    latT = K.at("at_latT", 80, [P, T])
    peT = K.at("at_peT", 84, [PE_D, T])
    ukT = K.at("at_ukT", SMALL_KB, [P, J, P])
    wuv = K.at("at_wuv", SMALL_KB + 2, [P, AH, AD])
    spread = K.at("at_spread", SMALL_KB + 4, [PE_D, 2, AD])
    uk = K.wsT
    den = K.prm[:, 0:NT * AH].rearrange("p (i h) -> p i h", i=NT)
    top = K.prm[:, 64:64 + 2]
    K.w_end = [[K.at(f"w_end{b}{n}", PJ_KB + 16 + 32 * b + 16 * n, [P, KT, HALF], FR) for n in range(2)] for b in range(2)]
    K.raw_end = [K.at(f"raw_end{b}", PJ_KB + 32 + 32 * b, [P, KT, HALF]) for b in range(2)]
    w_in = [K.sem(f"at_win{b}") for b in range(2)]
    names = "zero uk wuv spread whi wlo turn ukr latr pre prer lmm logit mx er tr pa pd pv done chain".split()
    S = {n: K.sem("at_" + n) for n in names}
    R_Q, R_K, R_V, R_G, D_Q, D_G = range(6)
    steps = [(i, h) for i in range(NT) for h in range(AH)]
    long_before = lambda n: sum(i >= 4 for i, h in steps[:n])
    n_pre = 2 * J + NT

    with nc.Block() as block:
        @block.sync
        def _(sp):
            sp.wait_ge(S["zero"], 2)
            for h in range(AH):
                sp.dma_start(uk[AD * (h % 2) + PE_D:AD * (h % 2 + 1), h // 2, :], I["w_uk_2"][0, h]).then_inc(S["uk"], 16)
            with nc.allow_non_contiguous_dma(reason="latent to partitions"):
                sp.dma_start(wuv[:], I["w_uv_2"][0].rearrange("h c d -> c h d")).then_inc(S["wuv"], 16)
            for b in range(2):
                sp.dma_start(K.raw_end[b][:], I["w_out_2"][0].rearrange("(k p) n -> p k n", p=P)[:, :, b * HALF:(b + 1) * HALF]).then_inc(w_in[b], 16)

        @block.gpsimd
        def _(pool):
            nc.gpsimd.memset(spread[:], 0.0).then_inc(S["zero"], 1)
            nc.gpsimd.memset(uk[:], 0.0).then_inc(S["zero"], 1)
            for m in range(2 * KT):
                pool.wait_ge(S["whi"], m + 1)
                b, k = m // KT, m % KT
                nc.gpsimd.tensor_tensor(K.w_end[b][1][:, k, :], K.raw_end[b][:, k, :], K.w_end[b][0][:, k, :].bitcast(F32), ALU.subtract).then_inc(S["wlo"], 1)

        @block.tensor
        def _(pe):
            for i in range(NT):
                if i >= 4:
                    pe.wait_ge(S["latr"], i - 3)
                b = K.bank[i % 4]
                nc.tensor.transpose(b[:, 0:P], K.MS[:, i, 0:LAT], K.ident[:])
                nc.tensor.transpose(b[0:PE_D, P:2 * P], K.MS[:, i, M_PE:M_PE + PE_D], K.ident[:]).then_inc(S["turn"], 1)
            pe.wait_ge(S["uk"], 16 * AH)
            for j in range(J):
                tr = nc.tensor.transpose(K.bank[4][:, j * P:(j + 1) * P], uk[:, j, :], K.ident[:])
            tr.then_inc(S["ukr"], 1)
            pe.wait_ge(S["latr"], NT)
            pe.wait_ge(S["wuv"], 16)
            n = 0
            for i in range(NT):
                if n >= 4:
                    pe.wait_ge(S["prer"], n - 3)
                nc.tensor.matmul(K.bank[n % 4][:], latT[:, i * P:(i + 1) * P], wuv[:].rearrange("p h d -> p (h d)"),
                                 start=True, stop=True).then_inc(S["pre"], 1)
                n += 1
            pe.wait_ge(S["ukr"], 2)
            pe.wait_ge(S["spread"], 2)
            for j in range(J):
                for c in range(0, T, HALF):
                    pe.wait_ge(S["prer"], n - 3)
                    nc.tensor.matmul(K.bank[n % 4][:], ukT[:, j, :], latT[:, c:c + HALF], start=True, stop=False)
                    nc.tensor.matmul(K.bank[n % 4][:], spread[:].rearrange("p a d -> p (a d)"), peT[:, c:c + HALF],
                                     start=False, stop=True).then_inc(S["pre"], 1)
                    n += 1
            pe.wait_ge(S["prer"], n_pre)

            def logits(n):
                i, h = steps[n]
                d = slice(AD * (h % 2), AD * (h % 2 + 1))
                if n >= 2:
                    pe.wait_ge(S["logit"], n - 1)
                for c in range(0, P * (i + 1), HALF):
                    e = min(c + HALF, P * (i + 1))
                    mm = nc.tensor.matmul(K.bank[2 * (h % 2) + c // HALF][:, 0:e - c], K.dqT[d, h // 2, i * P:(i + 1) * P], kfT[d, h // 2, c:e],
                                          start=True, stop=True)
                mm.then_inc(S["lmm"], 1)

            def turn(n):
                i, h = steps[n]
                pe.wait_ge(S["er"], n + 1)
                if n:
                    pe.wait_ge(S["pa"], n)
                    if long_before(n):
                        pe.wait_ge(S["pd"], long_before(n))
                for t in range(i + 1):
                    tr = nc.tensor.transpose(K.bank[4 + t // 4][:, (t % 4) * P:(t % 4 + 1) * P], prob[n % 2][:, t * P:(t + 1) * P], K.ident[:])
                tr.then_inc(S["tr"], 1)

            def values(n):
                i, h = steps[n]
                pe.wait_ge(S["pa"], n + 1)
                if i >= 4:
                    pe.wait_ge(S["pd"], long_before(n + 1))
                if h == 0 and i >= 2:
                    pe.wait_ge(S["done"], i - 1)
                for t in range(i + 1):
                    mm = nc.tensor.matmul(K.bank[6 + i % 2][:, h * AD:(h + 1) * AD], probT[n % 2][:, t, :], val[:, t, h * AD:(h + 1) * AD],
                                          start=(t == 0), stop=(t == i))
                mm.then_inc(S["pv"], 1)

            logits(0)
            for n in range(len(steps)):
                if n + 1 < len(steps):
                    logits(n + 1)
                turn(n)
                if n:
                    values(n - 1)
            values(len(steps) - 1)

        @block.scalar
        def _(act):
            for i in range(NT):
                act.wait_ge(S["turn"], i + 1)
                b = K.bank[i % 4]
                nc.scalar.activation(latT[:, i * P:(i + 1) * P], b[:, 0:P], ACT.Copy)
                nc.scalar.activation(peT[:, i * P:(i + 1) * P], b[0:PE_D, P:2 * P], ACT.Copy).then_inc(S["latr"], 1)
            act.wait_ge(S["ukr"], 1)
            nc.scalar.activation(ukT[:], K.bank[4][:].rearrange("p (j r) -> p j r", j=J), ACT.Copy).then_inc(S["ukr"], 1)
            for n in range(n_pre):
                act.wait_ge(S["pre"], n + 1)
                m = n - NT
                dst = val[:, n, :] if n < NT else kfT[:, m // 2, (m % 2) * HALF:(m % 2 + 1) * HALF]
                nc.scalar.activation(dst, K.bank[n % 4][:], ACT.Copy).then_inc(S["prer"], 1)

            def expo(n):
                i, h = steps[n]
                act.wait_ge(S["mx"], n + 1)
                x = prob[n % 2][:, 0:P * (i + 1)]
                nc.scalar.activation(x, x, ACT.Exp, bias=top[:, n % 2:n % 2 + 1], accum_out=den[:, i, h:h + 1]).then_inc(S["er"], 1)

            def take(n):
                i, h = steps[n]
                act.wait_ge(S["tr"], n + 1)
                if n >= 2:
                    act.wait_ge(S["pv"], n - 1)
                c = min(i + 1, 4)
                nc.scalar.activation(probT[n % 2][:, 0:c, :], K.bank[4][:, 0:c * P].rearrange("p (s t) -> p s t", s=c), ACT.Copy).then_inc(S["pa"], 1)

            expo(0)
            for n in range(len(steps)):
                if n + 1 < len(steps):
                    expo(n + 1)
                take(n)
                m = n - AH
                if 0 <= m < 2 * KT:
                    act.wait_ge(w_in[m // KT], 16)
                    nc.scalar.activation(K.w_end[m // KT][0][:, m % KT, :], K.raw_end[m // KT][:, m % KT, :], ACT.Copy).then_inc(S["whi"], 1)

        @block.vector
        def _(dve):
            v = nc.vector
            link = Link(v, S["chain"])
            dve.wait_ge(S["zero"], 1)
            for a in range(2):
                v.tensor_copy(spread[:, a, 0:PE_D], K.ident[0:PE_D, 0:PE_D]).then_inc(S["spread"], 1)

            def logit(n):
                i, h = steps[n]
                w = P * (i + 1)
                dve.wait_ge(S["lmm"], n + 1)
                if n >= 2:
                    dve.wait_ge(S["tr"], n - 1)
                b = K.ps[:, 2 * (h % 2):2 * (h % 2) + 2, :].rearrange("p b c -> p (b c)")
                mx = top[:, n % 2:n % 2 + 1]
                v.tensor_tensor_reduce(out=prob[n % 2][:, 0:w], in0=b[:, 0:w], in1=K.NM[:, packed(i)], scale=AD ** -0.5, scalar=LOW,
                                       op0=ALU.add, op1=ALU.max, accum_out=mx).then_inc(S["logit"], 1)
                dve.wait_ge(S["logit"], n + 1)
                v.tensor_scalar(mx, mx, -1.0, None, ALU.mult).then_inc(S["mx"], 1)

            def take(n):
                i, h = steps[n]
                if i < 4:
                    return
                dve.wait_ge(S["tr"], n + 1)
                dve.wait_ge(S["pv"], n - 1)
                c = i + 1 - 4
                v.tensor_copy(probT[n % 2][:, 4:4 + c, :], K.bank[5][:, 0:c * P].rearrange("p (s t) -> p s t", s=c)).then_inc(S["pd"], 1)

            def finish(i):
                dve.wait_ge(S["pv"], AH * (i + 1))
                g = K.PJ[:, D_G, i, :]
                v.tensor_tensor(g, K.bank[6 + i % 2][:], g, ALU.mult).then_inc(S["done"], 1)
                dve.wait_ge(S["done"], i + 1)
                link(v.reciprocal(den[:, i, :], den[:, i, :]))
                g = g.rearrange("p (h d) -> p h d", h=AH)
                link(v.tensor_tensor(g, g, den[:, i, :].unsqueeze(2).to_broadcast([P, AH, AD]), ALU.mult))

            dve.wait_ge(S["prer"], n_pre)
            logit(0)
            for n in range(len(steps)):
                if n + 1 < len(steps):
                    logit(n + 1)
                take(n)
                if n and steps[n][1] == 0:
                    finish(steps[n - 1][0])
            finish(NT - 1)


def stage_second_end(K):
    nc, I = K.nc, K.I
    MIX = (K.PJ[:, 0], K.PJ[:, 5])
    w = K.w_end
    hT = [K.at(f"se_hT{n}", FREE_KB + 32 * n, [P, KT, T], FR) for n in range(2)]
    X = [K.at(f"se_x{g}", PJ_KB + 80 * g, [P, NT // 2, D]) for g in range(2)]
    w_proj = K.at("w_proj", 0, [P, 2, D])
    pT = K.at("se_pT", 8, [P, 2, T])
    rows = K.at("se_rows", 16, [P, 2, D])
    pn = K.at("se_pn", 184, [P, NT, 2, P])
    h = [K.at(f"se_h{s}", 184 + 4 * s, [P, D]) for s in range(2)]
    gate = [K.at(f"se_gate{s}", 192 + 2 * s, [P, HALF]) for s in range(2)]
    ss, ss2 = K.prm[:, 0:NT], K.prm[:, NT:2 * NT]
    p_in, r_in, wp_in, stored = (K.sem("se_" + n) for n in ("pin", "rin", "wpin", "stored"))
    x_in, g_in = [K.sem(f"se_xin{q}") for q in range(4)], [K.sem(f"se_gin{q}") for q in range(4)]
    names = "mtr mhi mlo ptr ptev omm oev ssr hr htr hhi hlo ghi glo pmm gmm gr used x4 ssr2 outr chain".split()
    S = {n: K.sem("se_" + n) for n in names}

    def x3(i):
        return X[i // 4][:, i % 4, :]

    def tile_of(t, i, b):
        return t[:, 4 * b:4 * b + 4, i * P:(i + 1) * P]

    def wide(bank):
        return bank[:].rearrange("p (k t) -> p k t", k=4)

    with nc.Block() as block:
        @block.sync
        def _(sp):
            sp.dma_start(pn[:], I["p_2"][0, 0].rearrange("(i p) (k c) -> p i k c", p=P, k=2)).then_inc(p_in, 16)
            sp.dma_start(rows[:, 0, :], I["norm_ple_2"].to_broadcast([P, D])).then_inc(r_in, 16)
            sp.dma_start(rows[:, 1, :], I["norm_final_2"].unsqueeze(0).to_broadcast([P, D])).then_inc(r_in, 16)
            sp.wait_ge(S["mtr"], NT)
            for q in range(4):
                sp.dma_start(X[q // 2][:, 2 * (q % 2):2 * (q % 2) + 2, :],
                             K.x2[2 * q * P:2 * (q + 1) * P, :].rearrange("(i p) n -> p i n", p=P)).then_inc(x_in[q], 16)
            sp.dma_start(w_proj[:], I["w_ple_proj_2"][0].rearrange("(k p) n -> p k n", p=P)).then_inc(wp_in, 16)
            for q in range(4):
                b, k = q // 2, slice(4 * (q % 2), 4 * (q % 2) + 4)
                sp.wait_ge(S["omm"], NT * (b + 1))
                sp.dma_start(K.raw_end[b][:, k, :],
                             I["w_ple_gate_2"][0].rearrange("(k p) n -> p k n", p=P)[:, k, b * HALF:(b + 1) * HALF]).then_inc(g_in[q], 16)
            for i in range(NT):
                sp.wait_ge(S["outr"], i + 1)
                sp.dma_start(K.out[0, i * P:(i + 1) * P, :], x3(i)).then_inc(stored, 16)
            sp.wait_ge(stored, 16 * NT)

        @block.gpsimd
        def _(pool):
            for b in range(2):
                for k in range(KT):
                    pool.wait_ge(S["ghi"], KT * b + k + 1)
                    nc.gpsimd.tensor_tensor(w[b][1][:, k, :], K.raw_end[b][:, k, :], w[b][0][:, k, :].bitcast(F32), ALU.subtract).then_inc(S["glo"], 1)

        @block.tensor
        def _(pe):
            def output(b, i):
                n = NT * b + i
                if n >= 4:
                    pe.wait_ge(S["oev"], n - 3)
                for k in range(KT):
                    last = product(nc, K.bank[4 + n % 4][:], [x[:, k, i * P:(i + 1) * P] for x in hT], [x[:, k, :] for x in w[b]],
                                   k == 0, k == KT - 1)
                last.then_inc(S["omm"], 1)

            def turn(i):
                pe.wait_ge(S["hr"], i + 1)
                if i < 2:
                    pe.wait_ge(S["ptev"], 4)
                else:
                    pe.wait_ge(S["hlo"], 2 * (i - 1))
                for k in range(KT):
                    tr = nc.tensor.transpose(K.bank[2 * (i % 2) + k // 4][:, (k % 4) * P:(k % 4 + 1) * P], h[i % 2][:, k * P:(k + 1) * P], K.ident[:])
                tr.then_inc(S["htr"], 1)

            def gates(b, i):
                n = NT * b + i
                if n < 2:
                    pe.wait_ge(S["oev"], 2 * NT)
                else:
                    pe.wait_ge(S["used"], n - 1)
                for k in range(2):
                    mm = nc.tensor.matmul(K.bank[4 + n % 2][:], pT[:, k, i * P:(i + 1) * P], w_proj[:, k, b * HALF:(b + 1) * HALF], start=(k == 0), stop=(k == 1))
                mm.then_inc(S["pmm"], 1)
                if b == 0:
                    pe.wait_ge(S["hlo"], 2 * (i + 1))
                if n >= 2:
                    pe.wait_ge(S["gr"], n - 1)
                for k in range(KT):
                    if i == 0:
                        pe.wait_ge(S["glo"], KT * b + k + 1)
                    last = product(nc, K.bank[6 + n % 2][:], [x[:, k, i * P:(i + 1) * P] for x in hT], [x[:, k, :] for x in w[b]],
                                   k == 0, k == KT - 1)
                last.then_inc(S["gmm"], 1)

            for i in range(NT):
                if i >= 4:
                    pe.wait_ge(S["mlo"], 2 * (i - 3))
                for k in range(KT):
                    tr = nc.tensor.transpose(K.bank[2 * (i % 4) + k // 4][:, (k % 4) * P:(k % 4 + 1) * P], MIX[k // 4][:, i, (k % 4) * P:(k % 4 + 1) * P], K.ident[:])
                tr.then_inc(S["mtr"], 1)
            pe.wait_ge(p_in, 16)
            pe.wait_ge(S["mlo"], 2 * 6)
            for b in range(4):
                for m in range(2):
                    for k in range(2):
                        tr = nc.tensor.transpose(K.bank[b][:, (2 * k + m) * P:(2 * k + m + 1) * P], pn[:, 2 * b + m, k, :], K.ident[:])
                tr.then_inc(S["ptr"], 1)
            pe.wait_ge(S["mlo"], 2 * NT)
            for i in range(NT):
                output(0, i)
            for i in range(NT):
                output(1, i)
                if i >= 2:
                    turn(i - 2)
            pe.wait_ge(wp_in, 16)
            for i in range(NT):
                gates(0, i)
                if i < 2:
                    turn(NT - 2 + i)
            for i in range(NT):
                gates(1, i)

        @block.scalar
        def _(act):
            def high(done, i, banks, sem):
                act.wait_ge(done, i + 1)
                for b in range(2):
                    nc.scalar.activation(tile_of(hT[0], i, b), wide(K.bank[banks + b]), ACT.Copy).then_inc(sem, 1)

            def split(b, k):
                act.wait_ge(g_in[2 * b + k // 4], 16)
                nc.scalar.activation(w[b][0][:, k, :], K.raw_end[b][:, k, :], ACT.Copy).then_inc(S["ghi"], 1)

            def sigmoid(b, i):
                n = NT * b + i
                act.wait_ge(S["gmm"], n + 1)
                if n >= 2:
                    act.wait_ge(S["x4"], n - 1)
                nc.scalar.activation(gate[n % 2][:], K.bank[6 + n % 2][:], ACT.Sigmoid).then_inc(S["gr"], 1)

            for i in range(NT):
                high(S["mtr"], i, 2 * (i % 4), S["mhi"])
            for b in range(4):
                act.wait_ge(S["ptr"], b + 1)
                nc.scalar.activation(pT[:, :, 2 * b * P:2 * (b + 1) * P], K.bank[b][:].rearrange("p (k t) -> p k t", k=2), ACT.Copy).then_inc(S["ptev"], 1)
            for i in range(NT):
                act.wait_ge(S["oev"], NT + i + 1)
                if i >= 2:
                    act.wait_ge(S["htr"], i - 1)
                rms_root(K, act, x3(i), h[i % 2][:], ss[:, i:i + 1], S["ssr"], i)
                if i >= 2:
                    high(S["htr"], i - 2, 2 * (i % 2), S["hhi"])
                split(0, i)
            for i in range(NT):
                if i < 2:
                    high(S["htr"], NT - 2 + i, 2 * (i % 2), S["hhi"])
                split(1, i)
                sigmoid(0, i)
            for i in range(NT):
                sigmoid(1, i)
                act.wait_ge(S["x4"], NT + i + 1)
                rms_root(K, act, x3(i), h[i % 2][:], ss2[:, i:i + 1], S["ssr2"], i)

        @block.vector
        def _(dve):
            v = nc.vector
            link = Link(v, S["chain"])

            def low(done, i, banks, sem):
                for b in range(2):
                    dve.wait_ge(done, 2 * i + b + 1)
                    v.tensor_tensor(tile_of(hT[1], i, b), wide(K.bank[banks + b]), tile_of(hT[0], i, b).bitcast(F32), ALU.subtract).then_inc(sem, 1)

            def residual(b, i):
                n = NT * b + i
                x = x3(i)[:, b * HALF:(b + 1) * HALF]
                if b == 0 and i % 2 == 0:
                    dve.wait_ge(x_in[i // 2], 16)
                dve.wait_ge(S["omm"], n + 1)
                v.tensor_tensor(x, K.bank[4 + n % 4][:], x, ALU.add).then_inc(S["oev"], 1)

            def scale(i, dst, root, col, row, sem):
                dve.wait_ge(root, 2 * i + 2)
                link(v.reciprocal(col[:, i:i + 1], col[:, i:i + 1]))
                v.scalar_tensor_tensor(out=dst, in0=x3(i), scalar=col[:, i:i + 1], in1=rows[:, row, :], op0=ALU.mult, op1=ALU.mult).then_inc(sem, 1)

            def add_gated(b, i):
                n = NT * b + i
                g, x = gate[n % 2], x3(i)[:, b * HALF:(b + 1) * HALF]
                dve.wait_ge(S["gr"], n + 1)
                dve.wait_ge(S["pmm"], n + 1)
                v.tensor_tensor(g[:], K.bank[4 + n % 2][:], g[:], ALU.mult).then_inc(S["used"], 1)
                dve.wait_ge(S["used"], n + 1)
                v.tensor_tensor(x, x, g[:], ALU.add).then_inc(S["x4"], 1)

            for i in range(NT):
                low(S["mhi"], i, 2 * (i % 4), S["mlo"])
            for i in range(NT):
                residual(0, i)
            dve.wait_ge(r_in, 32)
            for i in range(NT):
                residual(1, i)
                if i:
                    scale(i - 1, h[(i - 1) % 2][:], S["ssr"], ss, 0, S["hr"])
                if i >= 2:
                    low(S["hhi"], i - 2, 2 * (i % 2), S["hlo"])
            scale(NT - 1, h[1][:], S["ssr"], ss, 0, S["hr"])
            for i in range(NT):
                if i < 2:
                    low(S["hhi"], NT - 2 + i, 2 * (i % 2), S["hlo"])
                add_gated(0, i)
            for i in range(NT):
                add_gated(1, i)
                if i:
                    scale(i - 1, x3(i - 1), S["ssr2"], ss2, 1, S["outr"])
            scale(NT - 1, x3(NT - 1), S["ssr2"], ss2, 1, S["outr"])


STAGES = (stage_modulate, stage_s5, stage_mixers, stage_join, stage_ffn, stage_first_end,
          stage_project, stage_retention, stage_attention, stage_second_end)


def build(nc, I, out):
    K = setup(nc, I, out)
    for stage in STAGES:
        stage(K)
        if stage is stage_first_end:
            nc.clear_and_free_semaphores(K.sems)
            nc.all_engine_barrier()


def kernel(**inputs):
    import concourse.bacc as bacc
    from concourse.bass_utils import run_bass_kernel_spmd

    nc = bacc.Bacc("TRN2", target_bir_lowering=False, num_devices=1)
    arrays = {f"in_{name}": np.ascontiguousarray(a) for name, a in {**inputs, **constants()}.items()}
    I = {name[3:]: nc.dram_tensor(name, a.shape, mybir.dt.from_np(a.dtype), kind="ExternalInput").ap() for name, a in arrays.items()}
    out = nc.dram_tensor("out", (1, T, D), F32, kind="ExternalOutput").ap()
    build(nc, I, out)
    return run_bass_kernel_spmd(nc, [arrays], core_ids=[0]).results[0]["out"]
```

```python
import math

import numpy as np

import concourse.bass as bass
from concourse import mybir

F32 = mybir.dt.float32
I32 = mybir.dt.int32
FR = mybir.dt.float32r
ALU = mybir.AluOpType
ACT = mybir.ActivationFunctionType
AX = mybir.AxisListType

P = 128
T = 1024
TC = 256
D = 1024
KT = D // P
NT = T // P
NCT = TC // P
W = 256
HALF = 512
HEADS, HD = 4, 64
LN_EPS = 1e-5
RMS_EPS = 1e-6
DFF = 2816
NF = DFF // P
ALPHA = 2.0 ** 0.25
OFF_B = 4 * W + 16
OFF_C = OFF_B + 2 * W
OFF_D = OFF_C + 2 * W
CONV, PAD, GRID = 31, 15, 64
ROWS = T // GRID
G16, SP, SN, SC = 16, 16, 64, 8
GP = G16 // 2
NCH, NCC = T // SC, TC // SC
NCA = NCH + NCC
N2 = 2 * GP
LOW = -1.0e30
MAGIC = 1.5 * 2.0 ** 23
LOG2E = 1.4426950408889634
LN2_HI, LN2_LO = 0.693359375, -2.12194440054690583e-4
INV_2PI = 1.0 / (2.0 * math.pi)
TWO_PI_1 = 6.28125
TWO_PI_2 = float(np.float32(round((2.0 * math.pi - TWO_PI_1) * 2 ** 20) / 2 ** 20))
TWO_PI_3 = 2.0 * math.pi - TWO_PI_1 - TWO_PI_2
PI_IN = 3.1415925


RH, RD = 8, 64
RCHUNK = 64
AH, AD = 8, 64
PE_D, NOPE, LAT = 16, 48, 128
IH, IDIM, IROT = 8, 32, 8
TOPK = 256
FREQ_R, FREQ_A, FREQ_I = RD // 2, PE_D // 2, IROT // 2
NFREQ = FREQ_R + FREQ_A + FREQ_I
C_LAT = 5 * HALF
C_GATE = C_LAT + LAT + PE_D
C_IDX = C_GATE + HALF
N_IDX = IH * IDIM + IDIM + IH
M_PE, M_IQ = LAT, LAT + PE_D
M_IK = M_IQ + IH * IDIM
M_IW = M_IK + IDIM
N_MIX = M_IW + IH


def constants():
    def freq(theta, r):
        return theta ** (-np.arange(0, r, 2, dtype=np.float64) / r)

    log_g = np.log1p(-np.exp2(-5.0 - np.arange(RH)))
    n = np.arange(P)
    gap, chunk = n[None, :] - n[:, None], n // RCHUNK
    seen = chunk[None, :] >= chunk[:, None]
    intra = np.exp(log_g[:, None, None] * np.abs(gap)) * seen * RD ** -0.5
    pair = np.repeat(np.arange(2), RD)
    head = 2 * np.arange(RH // 2)[None, :] + pair[:, None]
    return {
        "freq": np.concatenate([freq(10000.0, RD), freq(500000.0, PE_D), freq(500000.0, IROT)])[None].astype(np.float32),
        "intra": intra.transpose(1, 0, 2).astype(np.float32),
        "xi": (np.exp(log_g[head][:, :, None] * (n + 1.0)) * RD ** -0.5).astype(np.float32),
        "zeta": np.exp(log_g[None, :] * (P - 1.0 - n)[:, None]).astype(np.float32),
        "decay": np.exp(log_g[head] * P).astype(np.float32),
    }


class Kept:

    def __init__(self, nc, I, out):
        self.nc, self.I, self.out = nc, I, out


class Link:

    def __init__(self, eng, sem):
        self.eng, self.sem, self.n = eng, sem, 0

    def __call__(self, ins):
        self.n += 1
        ins.then_inc(self.sem, 1)
        self.eng.wait_ge(self.sem, self.n)


def setup(nc, I, out):
    K = Kept(nc, I, out)
    K.ps = nc.alloc_psum_tensor("ps", [P, 8, HALF], F32)
    K.bank = [K.ps[:, i, :] for i in range(8)]
    K.ident = nc.alloc_sbuf_tensor("ident", [P, P], F32)
    K.ones = nc.alloc_sbuf_tensor("ones", [P, P], F32)
    K.prm = nc.alloc_sbuf_tensor("prm", [P, 1168], F32)
    K.eps = nc.alloc_sbuf_tensor("eps", [P, 1], F32)
    K.wsT = nc.alloc_sbuf_tensor("wsT", [P, 4, P], F32)
    K.base = 24 * 1024
    K.sems = []

    def at(name, kb, shape, dt=F32):
        return nc.alloc_sbuf_tensor_at(name, shape, dt, offset=K.base + int(kb * 1024))

    def sem(name):
        K.sems.append(nc.alloc_semaphore(name))
        return K.sems[-1]

    K.at, K.sem = at, sem
    K.MOD = at("MOD", 0, [P, 6 * D])
    K.HT = at("HT", 24, [P, KT, TC + T])
    K.ydT = at("ydT", 64, [P, 2, T])
    K.HTP = at("HTP", 64, [P, KT, TC])
    K.yT = [at(f"yT{k}", 24 + 4 * k, [P, T]) for k in range(6)] + [K.ydT[:, k, :] for k in range(2)]
    return K


class Names:
    pass


def s5_names(K):
    Z = Names()
    Z.wd = K.at("s5_wd", 72, [P, KT, W])
    Z.d8 = K.at("s5_d8", 80, [P, G16, SC, SP])
    Z.d8c = K.at("s5_d8c", 64, [NCC, SC, W])
    Z.d8g = K.at("s5_d8g", 88, [NCC, G16, SC, SP])
    Z.HB = K.at("s5_HB", 154, [P, 2, GP, NCH])
    Z.ys = K.at("s5_ys", 146, [P, SC, W])
    Z.dcx = K.at("s5_dcx", 96, [P, 2, W])
    Z.glu = K.at("s5_glu", 96, [P, 2, W])
    Z.U8 = K.at("s5_U8", 98, [P, G16, NCA])
    Z.CA = K.at("s5_CA", 108, [P, 2, 2, GP, 9, SP])
    Z.AB = K.at("s5_AB", 126, [P, 2, 2, GP, SC, SP])
    Z.X = K.at("s5_X", 126, [P, 2, 2 * GP, NCA])
    Z.scr = K.at("s5_scr", 146, [P, 2, GP * 9 * SP])
    Z.TAB = K.at("s5_TAB", 146, [P, 2, 2 * GP, NCA])
    Z.ABT = K.at("s5_ABT", 166, [P, 2, GP, 2, P])
    Z.tmp = K.at("s5_tmp", 166, [P, 2, 2 * GP, NCA])
    Z.ptmp = K.at("s5_ptmp", 186, [P, 2, 2 * GP, NCA // 2 - 16])
    Z.yDT = K.at("s5_yDT", 166, [P, 2, T])
    Z.sg = K.at("s5_sg", 174, [P, 2, T])
    Z.Tz = K.at("s5_T", 186, [P, G16, P])
    Z.Cn = K.at("s5_Cn", 186, [P, 2, 2, 2, SN])
    Z.KL = K.at("s5_KL", 126, [SP, G16, 15 * SP])
    Z.Bm = K.at("s5_B", 194, [P, 2, GP, SP])
    Z.Cm = K.at("s5_C", 195, [P, 2, GP, SP])
    Z.BB = K.at("s5_BB", 196, [P, 2, 2, GP, SP])
    Z.Dr = K.at("s5_D", 198, [P, W])
    Z.araw = K.prm[0:2 * GP, 0:3 * P].rearrange("p (a n) -> p a n", a=3)
    used = [3 * P]

    def columns(n, dt=F32):
        used[0] += n
        c = K.prm[:, used[0] - n:used[0]]
        return c if dt == F32 else c.bitcast(dt)

    Z.par = columns(3 * N2).rearrange("p (a j) -> p a j", a=3)
    Z.ang = columns(2 * N2).rearrange("p (a j) -> p a j", a=2)
    Z.red, Z.quar, Z.kk, Z.sn, Z.cs = (columns(2 * N2).rearrange("p (a j) -> p a j", a=2) for _ in range(5))
    Z.dt_c, Z.er, Z.k1, Z.r1, Z.fr, Z.fi, Z.den, Z.tc, Z.uc = (columns(N2) for _ in range(9))
    Z.ki = columns(N2, I32)
    Z.pw = columns(2 * 9 * N2).rearrange("p (c e j) -> p c e j", c=2, e=9)
    Z.rot = columns(2 * N2).rearrange("p (c j) -> p c j", c=2)
    Z.gb = columns(2)
    Z.ldt = columns(2)
    Z.pt = columns(2 * N2).rearrange("p (c j) -> p c j", c=2)
    return Z


def stage_modulate(K):
    nc, I = K.nc, K.I
    NCK, NCX, KH = 12, 4, KT // 2
    Z = K.s5 = s5_names(K)
    ring = [K.at(f"mod_w{s}", 72 + 8 * s, [P, KH, HALF]) for s in range(4)]
    brow = K.at("mod_b", 104, [1, 2, HALF])
    cols = K.prm[:, 1152:1152 + 2 * KT].rearrange("p (w t) -> p w t", w=2)
    MODC = K.at("MODC", 166, [P, NCX * HALF])
    cb = K.at("mod_cb", 174, [P, 2, KT, P])
    xr = [K.at(f"mod_x{s}", kb, [P, D]) for s, kb in enumerate((8, 12, 182))]
    hb = [K.at(f"mod_h{s}", 16 + 4 * s, [P, D]) for s in range(2)]
    c_in, c_act, c_bc = K.sem("c_in"), K.sem("c_act"), K.sem("c_bc")
    consts = K.sem("consts")
    w_in, b_in = [K.sem(f"modw_in{s}") for s in range(4)], [K.sem(f"modb_in{s}") for s in range(2)]
    w_use, mod_mm, mod_ev, ctx_mm, ctx_ev = (K.sem("mod_" + n) for n in ("use", "mm", "ev", "cmm", "cev"))
    x_in = [K.sem(f"modx_in{s}") for s in range(3)]
    h_mul, h_rdy, h_tr, h_ev = K.sem("h_mul"), K.sem("h_rdy"), K.sem("h_tr"), K.sem("h_ev")
    S = {n: K.sem("s5p_" + n) for n in "in ldtx part sinin sinout ab chain pchain".split()}
    w_mod = I["w_mod"][0].rearrange("(p t) n -> p t n", t=KT)
    tiles = NCT + NT

    def src(i):
        return I["ctx"][0][i * P:(i + 1) * P, :] if i < NCT else I["x"][0][(i - NCT) * P:(i - NCT + 1) * P, :]

    with nc.Block() as block:
        @block.sync
        def _(sp):
            sp.dma_start(cols[:, 0, :], I["c"][0].rearrange("(p t) -> p t", t=KT)).then_inc(c_in, 16)
            sp.dma_start(cols[:, 1, :], I["c_ctx"].rearrange("(p t) -> p t", t=KT)).then_inc(c_in, 16)

            def weights(r, s):
                cols_of = slice((2 * r + s) * HALF, (2 * r + s + 1) * HALF) if isinstance(r, int) else bass.ds(r * (2 * HALF) + s * HALF, HALF)
                for h in range(2):
                    if not isinstance(r, int) or r:
                        sp.wait_ge(w_use, 4 * r + 2 * s + h - 3)
                    sp.dma_start(ring[2 * s + h][:], w_mod[:, KH * h:KH * (h + 1), cols_of]).then_inc(w_in[2 * s + h], 16)
                if not isinstance(r, int) or r:
                    sp.wait_ge(mod_mm, 2 * r + s - 1)
                sp.dma_start(brow[:, s, :], I["b_mod"][:, cols_of]).then_inc(b_in[s], 16)

            def tokens(i):
                if i >= 3:
                    sp.wait_ge(h_rdy, i - 2)
                sp.dma_start(xr[i % 3][:], src(i)).then_inc(x_in[i % 3], 16)

            weights(0, 0)
            weights(0, 1)
            for i in range(3):
                tokens(i)
            for r in (1, 2):
                weights(r, 0)
                weights(r, 1)
            for i in range(3, tiles):
                tokens(i)
            with sp.Fori(3, NCK // 2) as r:
                weights(r, 0)
                weights(r, 1)

        @block.gpsimd
        def _(pool):
            nc.gpsimd.memset(K.eps[:], RMS_EPS)
            nc.gpsimd.memset(K.ident[:], 0.0).then_inc(consts, 1)
            nc.gpsimd.memset(K.ones[:], 1.0).then_inc(consts, 1)
            pool.wait_ge(consts, 2)
            nc.gpsimd.affine_select(out=K.ident[:], in_=K.ident[:], compare_op=ALU.not_equal, fill=1.0, base=0,
                                    pattern=[[-1, P]], channel_multiplier=1).then_inc(consts, 1)
            s5_tables(K, pool, Link(nc.gpsimd, S["pchain"]), S)

        @block.scalar
        def _(act):
            act.wait_ge(c_in, 32)
            nc.scalar.activation(cols[:], cols[:], ACT.Silu).then_inc(c_act, 1)
            for a, name in enumerate(("s5_a_re", "s5_a_im")):
                act.dma_start(Z.araw[:, a, :], I[name][0].rearrange("d (j h) n -> (d j) (h n)", h=2)).then_inc(S["in"], 16)
            act.dma_start(Z.ldt[0:N2, :], I["s5_log_dt"][0].rearrange("d (j h) -> (d j) h", h=2)).then_inc(S["in"], 16)
            for a, name in enumerate(("s5_b_re", "s5_b_im")):
                act.dma_start(Z.Bm[:, a], I[name][0].rearrange("(j h) n p -> (h n) j p", h=2)).then_inc(S["in"], 16)
            for a, name in enumerate(("s5_c_re", "s5_c_im")):
                for dup in range(2):
                    act.dma_start(Z.Cn[:, a, :, dup, :], I[name][0].rearrange("(t g) p n -> (g p) t n", t=2)).then_inc(S["in"], 16)
            act.dma_start(Z.Dr[:], I["s5_d"].to_broadcast([P, W])).then_inc(S["in"], 16)
            with nc.allow_non_contiguous_dma(reason="a bias as a column"):
                act.dma_start(Z.gb[:], I["s5_glu_b"][0].rearrange("(k p) -> p k", p=P)).then_inc(S["in"], 16)

            def evacuate(j, col):
                act.wait_ge(mod_mm, j + 1)
                nc.scalar.activation(K.MOD[:, col], K.bank[j % 2][:], ACT.Copy).then_inc(mod_ev, 1)

            for j in range(NCX):
                act.wait_ge(ctx_mm, j + 1)
                nc.scalar.activation(MODC[:, j * HALF:(j + 1) * HALF], K.bank[2 + j % 2][:], ACT.Copy).then_inc(ctx_ev, 1)
                evacuate(j, slice(j * HALF, (j + 1) * HALF))
                if j == 1:
                    act.wait_ge(S["sinin"], 1)
                    nc.scalar.activation(Z.sn[:], Z.red[:], ACT.Sin).then_inc(S["sinout"], 1)
                    nc.scalar.activation(Z.cs[:], Z.quar[:], ACT.Sin).then_inc(S["sinout"], 1)
            for i in range(tiles):
                act.wait_ge(h_tr, i + 1)
                for b in range(2):
                    nc.scalar.activation(K.HT[:, 4 * b:4 * b + 4, i * P:(i + 1) * P],
                                         K.bank[4 + 2 * (i % 2) + b][:].rearrange("p (k t) -> p k t", k=4),
                                         ACT.Copy).then_inc(h_ev, 1)
                    if i < NCT:
                        nk = P // SC
                        for k in range(4):
                            nc.scalar.activation(K.HTP[:, 4 * b + k, :].rearrange("p (s c) -> p c s", s=SC)[:, i * nk:(i + 1) * nk, :],
                                                 K.bank[4 + 2 * (i % 2) + b][:, k * P:(k + 1) * P].rearrange("p (c s) -> p c s", s=SC),
                                                 ACT.Copy).then_inc(h_ev, 1)
            with act.Fori(NCX // 2, NCK // 2) as r:
                for s in range(2):
                    act.wait_ge(mod_mm, 2 * r + s + 1)
                    nc.scalar.activation(K.MOD[:, bass.ds(r * (2 * HALF) + s * HALF, HALF)], K.bank[s][:], ACT.Copy).then_inc(mod_ev, 1)

        @block.vector
        def _(dve):
            dve.wait_ge(c_act, 1)
            nc.vector.tensor_copy(cb[:], cols[:].unsqueeze(3).to_broadcast([P, 2, KT, P])).then_inc(c_bc, 1)
            s5_parameters(K, dve, Link(nc.vector, S["chain"]), S)
            dve.wait_ge(ctx_ev, NCX)
            dve.wait_ge(mod_ev, NCX)
            for i in range(tiles):
                m = MODC if i < NCT else K.MOD
                dve.wait_ge(x_in[i % 3], 16 * (i // 3 + 1))
                if i >= 2:
                    dve.wait_ge(h_tr, i - 1)
                nc.vector.scalar_tensor_tensor(out=hb[i % 2][:], in0=m[:, D:2 * D], scalar=1.0, in1=xr[i % 3][:],
                                               op0=ALU.add, op1=ALU.mult).then_inc(h_mul, 1)
                dve.wait_ge(h_mul, i + 1)
                nc.vector.tensor_tensor(hb[i % 2][:], hb[i % 2][:], m[:, 0:D], ALU.add).then_inc(h_rdy, 1)

        @block.tensor
        def _(pe):
            pe.wait_ge(c_bc, 1)
            pe.wait_ge(consts, 3)

            def product(bank, which, r, s, done):
                for k in range(KT):
                    if k % KH == 0:
                        pe.wait_ge(w_in[2 * s + k // KH], 16 * r + 16)
                    last = nc.tensor.matmul(bank[:], cb[:, which, k, :], ring[2 * s + k // KH][:, k % KH, :], start=(k == 0), stop=False)
                    if which == 0 and k % KH == KH - 1:
                        last.then_inc(w_use, 1)
                pe.wait_ge(b_in[s], 16 * r + 16)
                nc.tensor.matmul(bank[:], K.ones[0:1, :], brow[:, s, :], start=False, stop=True).then_inc(done, 1)

            for j in range(NCX):
                if j >= 2:
                    pe.wait_ge(ctx_ev, j - 1)
                    pe.wait_ge(mod_ev, j - 1)
                product(K.bank[2 + j % 2], 1, j // 2, j % 2, ctx_mm)
                product(K.bank[j % 2], 0, j // 2, j % 2, mod_mm)
                if j == 0:
                    pe.wait_ge(S["ldtx"], 1)
                    for a in range(3):
                        nc.tensor.transpose(K.bank[4][:, a * N2:(a + 1) * N2], Z.araw[:, a, :], K.ident[0:N2, 0:N2])
                    for a in range(2):
                        for h in range(2):
                            last = nc.tensor.transpose(K.bank[5][:, (2 * a + h) * P:(2 * a + h + 1) * P], Z.Cn[:, a, h, :, :], K.ident[:])
                    last.then_inc(S["part"], 1)
            for i in range(tiles):
                pe.wait_ge(h_rdy, i + 1)
                if i >= 2:
                    pe.wait_ge(h_ev, 2 * (i - 1) + 8 * min(i - 1, NCT))
                for k in range(KT):
                    tr = nc.tensor.transpose(K.bank[4 + 2 * (i % 2) + k // 4][:, (k % 4) * P:(k % 4 + 1) * P],
                                             hb[i % 2][:, k * P:(k + 1) * P], K.ident[:])
                tr.then_inc(h_tr, 1)
            with pe.Fori(NCX // 2, NCK // 2) as r:
                for s in range(2):
                    pe.wait_ge(mod_ev, 2 * r + s - 1)
                    product(K.bank[s], 0, r, s, mod_mm)


def cmul(nc, link, out_r, out_i, a_r, a_i, b_r, b_i, t, u, conj=False):
    v = link.eng
    v.tensor_tensor(t, a_r, b_i, ALU.mult)
    link(v.tensor_tensor(u, a_i, b_i, ALU.mult))
    v.tensor_tensor(out_r, a_r, b_r, ALU.mult)
    link(v.tensor_tensor(out_i, a_i, b_r, ALU.mult))
    v.tensor_tensor(out_r, out_r, u, ALU.add if conj else ALU.subtract)
    link(v.tensor_tensor(out_i, out_i, t, ALU.subtract if conj else ALU.add))


def exp_exact(nc, link, dst, x, k, r, ki):
    v = nc.vector
    link(v.tensor_scalar(x, x, -87.0, 88.0, ALU.max, ALU.min))
    link(v.tensor_scalar(k, x, LOG2E, MAGIC, ALU.mult, ALU.add))
    link(v.tensor_scalar(k, k, MAGIC, None, ALU.subtract))
    link(v.scalar_tensor_tensor(out=r, in0=k, scalar=-LN2_HI, in1=x, op0=ALU.mult, op1=ALU.add))
    link(v.scalar_tensor_tensor(out=r, in0=k, scalar=-LN2_LO, in1=r, op0=ALU.mult, op1=ALU.add))
    link(v.tensor_scalar(dst, r, 1.0 / 5040, None, ALU.mult))
    for c in (1.0 / 720, 1.0 / 120, 1.0 / 24, 1.0 / 6, 0.5, 1.0):
        link(v.scalar_tensor_tensor(out=dst, in0=dst, scalar=c, in1=r, op0=ALU.add, op1=ALU.mult))
    link(v.tensor_scalar(k, k, 127.0, None, ALU.add))
    link(v.tensor_copy(ki, k))
    link(v.tensor_scalar(ki, ki, 23, None, ALU.logical_shift_left))
    link(v.scalar_tensor_tensor(out=dst, in0=dst, scalar=1.0, in1=ki.bitcast(F32), op0=ALU.add, op1=ALU.mult))


def reduce_angle(nc, link, r, quarter, x, k):
    v = nc.vector
    link(v.tensor_scalar(k, x, INV_2PI, MAGIC, ALU.mult, ALU.add))
    link(v.tensor_scalar(k, k, MAGIC, None, ALU.subtract))
    link(v.scalar_tensor_tensor(out=r, in0=k, scalar=-TWO_PI_1, in1=x, op0=ALU.mult, op1=ALU.add))
    for c in (TWO_PI_2, TWO_PI_3):
        link(v.scalar_tensor_tensor(out=r, in0=k, scalar=-c, in1=r, op0=ALU.mult, op1=ALU.add))
    link(v.tensor_scalar(r, r, -PI_IN, PI_IN, ALU.max, ALU.min))
    link(v.scalar_tensor_tensor(out=quarter, in0=r, scalar=-1.0, in1=r, op0=ALU.mult, op1=ALU.max))
    link(v.tensor_scalar(quarter, quarter, -1.0, math.pi / 2, ALU.mult, ALU.add))


def s5_parameters(K, dve, link, S):
    nc, Z, v = K.nc, K.s5, K.nc.vector
    dve.wait_ge(S["in"], 16 * 11)
    v.tensor_copy(Z.araw[:, 2, :].rearrange("p (h n) -> p h n", h=2),
                  Z.ldt[0:N2, :].unsqueeze(2).to_broadcast([N2, 2, SN])).then_inc(S["ldtx"], 1)
    dve.wait_ge(S["part"], 1)
    link(v.tensor_copy(Z.par[:], K.bank[4][:, 0:3 * N2].rearrange("p (a j) -> p a j", a=3)))
    for h in range(2):
        link(v.tensor_copy(Z.Cm[h * SN:(h + 1) * SN].rearrange("p c (t g) o -> p (c t) g o", t=2),
                           K.bank[5][h * SN:(h + 1) * SN, :].rearrange("p (a g h o) -> p a g h o", a=4, g=4, h=2)[:, :, :, h, :]))
    a_re, a_im = Z.par[:, 0, :], Z.par[:, 1, :]
    exp_exact(nc, link, Z.dt_c[:], Z.par[:, 2, :], Z.k1[:], Z.r1[:], Z.ki[:])
    link(v.tensor_tensor(Z.ang[:, 0, :], a_im, Z.dt_c[:], ALU.mult))
    link(v.tensor_scalar(Z.ang[:, 1, :], Z.ang[:, 0, :], float(SC), None, ALU.mult))
    reduce_angle(nc, link, Z.red[:], Z.quar[:], Z.ang[:], Z.kk[:])
    link(v.tensor_tensor(Z.dt_c[:], a_re, Z.dt_c[:], ALU.mult))
    dve.sem_inc(S["sinin"], 1)
    exp_exact(nc, link, Z.er[:], Z.dt_c[:], Z.k1[:], Z.r1[:], Z.ki[:])
    dve.wait_ge(S["sinout"], 2)
    link(v.memset(Z.pw[:, 0, 0, :], 1.0))
    link(v.memset(Z.pw[:, 1, 0, :], 0.0))
    link(v.tensor_tensor(Z.pw[:, 0, 1, :], Z.er[:], Z.cs[:, 0, :], ALU.mult))
    link(v.tensor_tensor(Z.pw[:, 1, 1, :], Z.er[:], Z.sn[:, 0, :], ALU.mult))
    for lo, n, by in ((2, 1, 1), (3, 2, 2), (5, 4, 4)):
        q = [Z.pw[:, c, by, :].unsqueeze(1).to_broadcast([P, n, N2]) for c in range(2)]
        t, u = (Z.scr[:, i, 0:n * N2].rearrange("p (e j) -> p e j", e=n) for i in range(2))
        cmul(nc, link, Z.pw[:, 0, lo:lo + n, :], Z.pw[:, 1, lo:lo + n, :], Z.pw[:, 0, 1:1 + n, :], Z.pw[:, 1, 1:1 + n, :],
             q[0], q[1], t, u)
    for _ in range(3):
        link(v.tensor_tensor(Z.er[:], Z.er[:], Z.er[:], ALU.mult))
    link(v.tensor_copy(Z.rot[:, 0, :], Z.cs[:, 1, :]))
    link(v.tensor_copy(Z.rot[:, 1, :], Z.sn[:, 1, :]))
    link(v.tensor_scalar(Z.r1[:], Z.pw[:, 0, 1, :], 1.0, None, ALU.subtract))
    link(v.tensor_tensor(Z.den[:], a_re, a_re, ALU.mult))
    link(v.tensor_tensor(Z.k1[:], a_im, a_im, ALU.mult))
    link(v.tensor_tensor(Z.den[:], Z.den[:], Z.k1[:], ALU.add))
    link(v.reciprocal(Z.den[:], Z.den[:]))
    cmul(nc, link, Z.fr[:], Z.fi[:], Z.r1[:], Z.pw[:, 1, 1, :], a_re, a_im, Z.tc[:], Z.uc[:], conj=True)
    link(v.tensor_tensor(Z.fr[:], Z.fr[:], Z.den[:], ALU.mult))
    link(v.tensor_tensor(Z.fi[:], Z.fi[:], Z.den[:], ALU.mult))
    for d in range(2):
        s = slice(d * GP, (d + 1) * GP)
        f = [c[:, s].unsqueeze(2).to_broadcast([P, GP, SP]) for c in (Z.fr, Z.fi)]
        t, u = (Z.scr[:, i, 0:GP * SP].rearrange("p (j o) -> p j o", j=GP) for i in range(2))
        cmul(nc, link, Z.BB[:, d, 0], Z.BB[:, d, 1], Z.Bm[:, 0], Z.Bm[:, 1], f[0], f[1], t, u)

        def powers(c, exps):
            p = Z.pw[:, c, exps, s]
            return p.rearrange("p e j -> p j e").unsqueeze(3).to_broadcast([P, GP, p.shape[1], SP])

        e = slice(7, None, -1) if d == 0 else slice(0, SC)
        b = [Z.BB[:, d, c].unsqueeze(2).to_broadcast([P, GP, SC, SP]) for c in range(2)]
        t, u = (Z.scr[:, i, 0:GP * SC * SP].rearrange("p (j e o) -> p j e o", j=GP, e=SC) for i in range(2))
        cmul(nc, link, Z.AB[:, d, 0], Z.AB[:, d, 1], powers(0, e), powers(1, e), b[0], b[1], t, u)
        e = slice(0, 9) if d == 0 else slice(8, None, -1)
        cm = [Z.Cm[:, c].unsqueeze(2).to_broadcast([P, GP, 9, SP]) for c in range(2)]
        t, u = (Z.scr[:, i, :].rearrange("p (j e o) -> p j e o", j=GP, e=9) for i in range(2))
        cmul(nc, link, Z.CA[:, d, 0], Z.CA[:, d, 1], powers(0, e), powers(1, e), cm[0], cm[1], t, u)
        link(v.tensor_scalar(Z.CA[:, d, 1], Z.CA[:, d, 1], -1.0, None, ALU.mult))
    dve.sem_inc(S["ab"], 1)


def s5_tables(K, pool, link, S):
    nc, Z = K.nc, K.s5
    pool.wait_ge(S["ab"], 1)
    link(nc.gpsimd.memset(Z.TAB[:, 0, :, 0:1], 1.0))
    link(nc.gpsimd.memset(Z.TAB[:, 1, :, 0:1], 0.0))
    n = 1
    while n < NCA:
        m = min(n, NCA - n)
        turn = [Z.rot[:, c, :].unsqueeze(2).to_broadcast([P, N2, m]) for c in range(2)]
        t, u = Z.ptmp[:, 0, :, 0:m], Z.ptmp[:, 1, :, 0:m]
        cmul(nc, link, Z.TAB[:, 0, :, n:n + m], Z.TAB[:, 1, :, n:n + m], Z.TAB[:, 0, :, 0:m], Z.TAB[:, 1, :, 0:m],
             turn[0], turn[1], t, u)
        n += m
        if n < NCA:
            cmul(nc, link, Z.pt[:, 0, :], Z.pt[:, 1, :], Z.rot[:, 0, :], Z.rot[:, 1, :], Z.rot[:, 0, :], Z.rot[:, 1, :], Z.tc[:], Z.uc[:])
            link(nc.gpsimd.tensor_copy(Z.rot[:], Z.pt[:]))


def stage_s5(K):
    nc, I = K.nc, K.I
    Z = K.s5
    wc = K.at("s5_wc", 64, [P, KT, HALF])
    K.cT = [K.at(f"cT{n}", 88 * n, [P, 2, T]) for n in range(2)]
    s5_in, d_in, g_in = K.sem("s5_in"), K.sem("s5_d_in"), K.sem("s5_glu_in")
    mm, ev = K.sem("s5_mm"), K.sem("s5_ev")
    dg_rdy = K.sem("s5_dg")
    t_in, c_in, h_rdy, y_mm, y_ev, y_act = (K.sem(f"s5_{n}") for n in ("tin", "cin", "h", "ymm", "yev", "yact"))
    yt_mm, yt_ev, g_mm, g_sg, chain = (K.sem(f"s5_{n}") for n in ("ytmm", "ytev", "gmm", "gsg", "chain"))
    N_AB, N_KL, N_D, N_U, N_X, N_C = 8, 8, 5, 8, 16, 8
    at_kl, at_d, at_u, at_x, at_c, at_end = (int(v) for v in np.cumsum([N_AB, N_KL, N_D, N_U, N_X, N_C]))
    NB = 6

    def bank(n):
        return K.bank[2 + n % NB]

    with nc.Block() as block:
        @block.sync
        def _(sp):
            sp.dma_start(Z.wd[:], I["w_in"][0].rearrange("(k p) n -> p k n", p=P)[:, :, OFF_D:OFF_D + W]).then_inc(s5_in, 16)
            sp.wait_ge(ev, at_d)
            for s in range(SC):
                sp.dma_start(Z.Tz[s * SP:(s + 1) * SP, :, :], Z.KL[:, :, (7 - s) * SP:(15 - s) * SP]).then_inc(t_in, 16)
            sp.wait_ge(ev, at_d + 1)
            for s in range(SC):
                sp.dma_start(Z.d8c[:, s, :], Z.dcx[(s % 4) * NCC:(s % 4 + 1) * NCC, s // 4, :]).then_inc(d_in, 16)
            sp.wait_ge(d_in, 16 * SC)
            sp.dma_start(Z.glu[:], I["s5_glu_w"][0].rearrange("(k p) n -> p k n", p=P)).then_inc(g_in, 16)
            sp.wait_ge(dg_rdy, 1)
            sp.wait_ge(ev, at_u)
            sp.dma_start(wc[:], I["w_in"][0].rearrange("(k p) n -> p k n", p=P)[:, :, OFF_C:OFF_C + HALF]).then_inc(c_in, 16)

        @block.tensor
        def _(pe):
            n = 0

            def load(n):
                if n >= NB:
                    pe.wait_ge(ev, n - NB + 1)

            for q in range(N_AB):
                load(n)
                for r in range(4):
                    d, j, c = (4 * q + r) // (2 * GP), (4 * q + r) // 2 % GP, r % 2
                    last = nc.tensor.transpose(bank(n)[:, r * P:(r + 1) * P], Z.AB[:, d, c, j, :, :], K.ident[:])
                last.then_inc(mm, 1)
                n += 1
            for q in range(N_KL):
                load(n)
                h, row = q % 2, slice(q % 2 * SN, (q % 2 + 1) * SN)
                for i2 in range(2):
                    j = q // 2 * 2 + i2
                    o = bank(n)[0:SP, i2 * 15 * SP:(i2 + 1) * 15 * SP]
                    parts = [(o[:, 7 * SP:8 * SP], [(0, 0), (1, 8)], 1), (o[:, 8 * SP:], [(0, 1)], 7), (o[:, :7 * SP], [(1, 1)], 7)]
                    for dst, terms, ne in parts:
                        for i, (d, e) in enumerate(terms):
                            for c in range(2):
                                last = nc.tensor.matmul(dst, Z.BB[row, d, c, j, :], Z.CA[row, d, c, j, e:e + ne, :],
                                                        start=(i == 0 and c == 0), stop=(i == len(terms) - 1 and c == 1))
                last.then_inc(mm, 1)
                n += 1
            pe.wait_ge(s5_in, 16)
            load(n)
            for h in range(2):
                for k in range(KT):
                    last = nc.tensor.matmul(bank(n)[:, h * W:(h + 1) * W],
                                            K.HTP[:, k, h * P:(h + 1) * P],
                                            Z.wd[:, k, :], start=(k == 0), stop=(k == KT - 1))
            last.then_inc(mm, 1)
            n += 1
            for q in range(4):
                load(n)
                for s in (2 * q, 2 * q + 1):
                    for k in range(KT):
                        last = nc.tensor.matmul(bank(n)[:, (s % 2) * W:(s % 2 + 1) * W], K.HT[:, k, TC + s::SC], Z.wd[:, k, :],
                                                start=(k == 0), stop=(k == KT - 1))
                last.then_inc(mm, 1)
                n += 1
            pe.wait_ge(ev, at_u)
            pe.wait_ge(dg_rdy, 1)
            for q in range(N_U):
                load(n)
                for j in range(2):
                    g = 2 * q + j
                    nc.tensor.transpose(bank(n)[:, j * NCA:j * NCA + NCC], Z.d8g[:, g, :, :], K.ident[0:NCC, 0:NCC])
                    last = nc.tensor.transpose(bank(n)[:, j * NCA + NCC:(j + 1) * NCA], Z.d8[:, g, :, :], K.ident[:])
                last.then_inc(mm, 1)
                n += 1
            for q in range(N_X):
                if q == 0:
                    pe.wait_ge(ev, at_x)
                load(n)
                d, j = q // GP, q % GP
                for c in range(2):
                    for h in range(2):
                        last = nc.tensor.matmul(bank(n)[h * SN:(h + 1) * SN, c * NCA:(c + 1) * NCA],
                                                Z.ABT[:, d, j, c, h * SN:(h + 1) * SN], Z.U8[:, 2 * j + h, :], start=True, stop=True)
                last.then_inc(mm, 1)
                n += 1
            pe.wait_ge(c_in, 16)
            for q in range(N_C):
                load(n)
                m, h = q // 2, q % 2
                for k in range(KT):
                    last = nc.tensor.matmul(bank(n)[:], wc[:, k, m * P:(m + 1) * P], K.HT[:, k, TC + h * HALF:TC + (h + 1) * HALF],
                                            start=(k == 0), stop=(k == KT - 1))
                last.then_inc(mm, 1)
                n += 1
            pe.wait_ge(ev, at_end)
            pe.wait_ge(t_in, 16 * SC)
            pe.wait_ge(h_rdy, 1)
            for q in range(4):
                for r in range(4):
                    j, h = q // 2 * 4 + r, q % 2
                    g, row = 2 * j + h, slice(h * SN, (h + 1) * SN)
                    o = K.bank[2 + q][:, r * P:(r + 1) * P]
                    nc.tensor.matmul(o, Z.U8[:, g, NCC:], Z.Tz[:, g, :], start=True, stop=False)
                    for d in range(2):
                        for c in range(2):
                            st = Z.X[row, c, d * GP + j, NCC - 1:NCA - 1] if d == 0 else Z.HB[row, c, j, :]
                            last = nc.tensor.matmul(o, st, Z.CA[row, d, c, j, 1 - d:9 - d, :], start=False, stop=(d == 1 and c == 1))
                last.then_inc(y_mm, 1)
            pe.wait_ge(y_act, 1)
            for q in range(4):
                if q >= 2:
                    pe.wait_ge(yt_ev, q - 1)
                for r in range(4):
                    last = nc.tensor.transpose(K.bank[6 + q % 2][:, r * P:(r + 1) * P],
                                               Z.ys[:, 4 * (q % 2) + r, (q // 2) * P:(q // 2 + 1) * P], K.ident[:])
                last.then_inc(yt_mm, 1)
            pe.wait_ge(yt_ev, 4)
            pe.wait_ge(g_in, 16)
            for m in range(2):
                for h in range(2):
                    for k in range(2):
                        last = nc.tensor.matmul(K.bank[2 + 2 * m + h][:], Z.glu[:, k, m * P:(m + 1) * P], Z.yDT[:, k, h * HALF:(h + 1) * HALF],
                                                start=(k == 0), stop=(k == 1))
                    last.then_inc(g_mm, 1)

        @block.scalar
        def _(act):
            n = 0

            def take(dst, src, last=True):
                ins = nc.scalar.activation(dst, src, ACT.Copy)
                if last:
                    ins.then_inc(ev, 1)

            for q in range(N_AB):
                act.wait_ge(mm, n + 1)
                d, j = 4 * q // (2 * GP), 2 * q % GP
                take(Z.ABT[:, d, j:j + 2, :, :], bank(n)[:].rearrange("p (j c n) -> p j c n", j=2, c=2))
                n += 1
            for q in range(N_KL):
                act.wait_ge(mm, n + 1)
                take(Z.KL[:, q // 2 * 4 + q % 2:q // 2 * 4 + 4:2, :], bank(n)[0:SP, 0:30 * SP].rearrange("p (h l) -> p h l", h=2))
                n += 1
            act.wait_ge(mm, n + 1)
            take(Z.dcx[:], bank(n)[:].rearrange("p (h n) -> p h n", h=2))
            n += 1
            for q in range(4):
                act.wait_ge(mm, n + 1)
                for s in range(2):
                    take(Z.d8[:, :, 2 * q + s, :], bank(n)[:, s * W:(s + 1) * W].rearrange("p (g o) -> p g o", g=G16), last=(s == 1))
                n += 1
            for q in range(N_U):
                act.wait_ge(mm, n + 1)
                take(Z.U8[:, 2 * q:2 * q + 2, :], bank(n)[:, 0:2 * NCA].rearrange("p (g c) -> p g c", g=2))
                n += 1
            act.wait_ge(t_in, 16 * SC)
            for q in range(N_X):
                act.wait_ge(mm, n + 1)
                src = bank(n)[:, 0:2 * NCA].rearrange("p (c n) -> p c n", c=2)
                if q < GP:
                    take(Z.X[:, :, q, :], src)
                else:
                    take(Z.X[:, :, q, 0:NCC], src[:, :, NCC - 1::-1], last=False)
                    take(Z.X[:, :, q, NCC:], src[:, :, :NCC - 1:-1])
                n += 1
            for q in range(N_C):
                act.wait_ge(mm, n + 1)
                ins = nc.scalar.activation(K.cT[q // 4][:, q // 2 % 2, (q % 2) * HALF:(q % 2 + 1) * HALF], bank(n)[:], ACT.Copy if q < 4 else ACT.Sigmoid)
                ins.then_inc(ev, 1)
                n += 1
            act.wait_ge(y_ev, 4)
            nc.scalar.activation(Z.ys[:], Z.ys[:], ACT.Gelu_apprx_tanh).then_inc(y_act, 1)
            for q in range(4):
                act.wait_ge(yt_mm, q + 1)
                nc.scalar.activation(Z.yDT[:, q // 2, :].rearrange("p (c s) -> p s c", s=SC)[:, 4 * (q % 2):4 * (q % 2) + 4, :],
                                     K.bank[6 + q % 2][:].rearrange("p (s c) -> p s c", s=4), ACT.Copy).then_inc(yt_ev, 1)
            for q in range(4):
                act.wait_ge(g_mm, q + 1)
                nc.scalar.activation(Z.sg[:, q // 2, (q % 2) * HALF:(q % 2 + 1) * HALF], K.bank[2 + q][:], ACT.Sigmoid,
                                     bias=Z.gb[:, q // 2:q // 2 + 1]).then_inc(g_sg, 1)

        @block.gpsimd
        def _(pool):
            pool.wait_ge(d_in, 16 * SC)
            nc.gpsimd.tensor_copy(Z.d8g[:].rearrange("c g s o -> c s g o"), Z.d8c[:].rearrange("c s (g o) -> c s g o", g=G16)).then_inc(dg_rdy, 1)

        @block.vector
        def _(dve):
            link = Link(nc.vector, chain)
            v = nc.vector
            dve.wait_ge(ev, at_x)
            for s in range(SC):
                link(v.tensor_tensor(Z.d8[:, :, s, :], Z.d8[:, :, s, :], Z.Dr[:].rearrange("p (g o) -> p g o", g=G16), ALU.mult))
            dve.wait_ge(ev, at_c)
            xr, xi = Z.X[:, 0], Z.X[:, 1]
            t, u = Z.tmp[:, 0], Z.tmp[:, 1]
            cmul(nc, link, xr, xi, xr, xi, Z.TAB[:, 0], Z.TAB[:, 1], t, u, conj=True)
            link(v.tensor_copy(t, Z.er[:].unsqueeze(2).to_broadcast([P, N2, NCA])))
            link(v.memset(Z.tmp[:, 0, :, 0:1], 0.0))
            for c in range(2):
                flat = Z.X[:, c].rearrange("p j n -> p (j n)")
                link(v.tensor_tensor_scan(flat, Z.tmp[:, 0].rearrange("p j n -> p (j n)"), flat, 0.0, ALU.mult, ALU.add))
            cmul(nc, link, xr, xi, xr, xi, Z.TAB[:, 0], Z.TAB[:, 1], t, u)
            for c in range(2):
                link(v.tensor_copy(Z.HB[:, c], Z.X[:, c, GP:, NCA - 2:NCC - 2:-1]))
            dve.sem_inc(h_rdy, 1)
            for q in range(4):
                dve.wait_ge(y_mm, q + 1)
                for r in range(4):
                    g = 2 * (q // 2 * 4 + r) + q % 2
                    last = v.tensor_tensor(Z.ys[:, :, g * SP:(g + 1) * SP], K.bank[2 + q][:, r * P:(r + 1) * P].rearrange("p (s o) -> p s o", s=SC),
                                           Z.d8[:, g], ALU.add)
                last.then_inc(y_ev, 1)
            for q in range(4):
                dve.wait_ge(g_sg, q + 1)
                o = (slice(None), q // 2, slice((q % 2) * HALF, (q % 2 + 1) * HALF))
                v.tensor_tensor(K.ydT[o], Z.yDT[o], Z.sg[o], ALU.mult).then_inc(chain, 1)


def stage_mixers(K):
    nc, I = K.nc, K.I
    NL = NCT + NT
    qkT = K.at("mx_qkT", 72, [P, 4, T])
    kn = K.at("mx_kn", 88, [P, NL, W])
    HX = HD + 1
    vflat = K.at("mx_vx", 98, [P, NL * HEADS * HX + P - HX])
    vx = vflat[:, 0:NL * HEADS * HX].rearrange("p (c h e) -> p c h e", c=NL, h=HEADS)
    so = K.at("mx_so", 109, [P, NT, W])
    GT = K.at("mx_GT", 117, [P, NL, 2, 2, HEADS])
    zb = K.at("mx_zb", 118, [P, NT, 2 * W])
    acc = K.at("mx_acc", 142, [P, 2, T])
    yc = K.at("mx_yc", 134, [P, NT, W])
    H = K.at("mx_H", 142, [P, NT, HEADS, HD])
    spares = K.at("mx_spares", 118, [P, NT, W])
    K.wo = K.at("w_out", 72, [P, KT, D])
    K.wo_in = K.sem("mx_woin")
    ring = [K.at(f"mx_w{s}", 150 + 16 * s, [P, KT, HALF]) for s in range(2)]
    apad = K.at("mx_apad", 182, [P, 2, ROWS, GRID + 2 * PAD])
    rows = K.at("mx_rows", 194, [P, 5, W])
    wsn = K.at("mx_wsn", 134, [P, 4, P])
    wcn = K.at("mx_wcn", 136, [CONV + 1, W])
    QR = 36
    ig, d0 = (K.at(f"mx_g{n}", kb, [QR, NL * P]) for n, kb in enumerate((150, 142)))
    lrows = K.at("mx_lf", 155, [P, NL * P])
    lf = lrows[0:QR]
    QS = 64 + QR
    pair_rows = [K.at(f"mx_rows{k}", kb, [QS, NL * P]) for k, kb in enumerate((182, 160))]
    win, ee, bc, acopy = (t[r] for t in pair_rows for r in (slice(0, QR), slice(64, QS)))
    COL = K.at("mx_COL", 187, [P, 2, NL, 2, 2, HEADS])
    CF = K.at("mx_CS", 0, [P, 2, 2 * HX + P - HX])
    CS = CF[:, :, 0:2 * HX].rearrange("p d (j e) -> p d j e", j=2)
    selp = K.at("mx_selp", 189.75, [QR, 2, 2, HD])
    mask = K.at("mx_mask", 190.75, [P, 2, P])
    sel = [K.at(f"mx_sel{d}", kb, [P, HEADS, P]) for d, kb in enumerate((191.75, 6))]
    qp = [K.at(f"mx_qp{d}", 2 + 2 * d, [P, HEADS, P]) for d in range(2)]
    arg = [K.at(f"mx_arg{d}", 48 + 2 * d, [P, HEADS, P]) for d in range(2)]
    PT = [K.at(f"mx_PT{d}", 52 + 2 * d, [P, HEADS, P]) for d in range(2)]
    num = [K.at(f"mx_num{d}", 56 + 1.25 * d, [P, HEADS, HX]) for d in range(2)]
    ke = [K.at(f"mx_ke{d}", 58.5 + d, [P, HEADS, HD]) for d in range(2)]
    used = [0]

    def columns(n):
        used[0] += n
        return K.prm[:, used[0] - n:used[0]]

    wcol = columns(2 * (CONV + 1)).rearrange("p (c k) -> p c k", c=2)
    bs = columns(4)
    gbias = columns(16)
    st6 = columns(6)
    mv = columns(2 * NT).rearrange("p (i a) -> p i a", a=2)
    rstd = columns(NT)
    mvc = columns(2 * NT).rearrange("p (i a) -> p i a", a=2)
    rstdc = columns(NT)
    BE, ME, BM, MPc, MEc, DEC = (columns(NL) for _ in range(6))
    MP = columns(NL + 1)
    dcol = columns(2 * 2 * NL).rearrange("p (d j c) -> p d j c", d=2, j=2)
    nd = [columns(HEADS) for _ in range(2)]
    sums = columns(NT * HEADS).rearrange("p (i h) -> p i h", h=HEADS)
    sqs = columns(NT * HEADS).rearrange("p (i h) -> p i h", h=HEADS)
    gt = columns(NL * 2 * HEADS).rearrange("p (i d h) -> p i d h", i=NL, d=2)
    ge = columns(NL * 2 * HEADS).rearrange("p (i d h) -> p i d h", i=NL, d=2)

    w_in = [K.sem(f"mx_win{s}") for s in range(2)]
    names = ("prm rows mm ev qp sor xr hadd readout cons apr gcp ycp sel conv ctmm sgn wst bmm bdone ycn yc_tr yc_ev yb_tr yb_ev "
             "g1 g2 g3 gx gmm gev ga gb colmm colev st argmm argr pr ptr smm qmm pvmm nr ker umm hr yam yae eps1 eps2 chain pchain").split()
    S = {n: K.sem("mx_" + n) for n in names}
    slabs = [(OFF_B, 512), (3 * W, W + 16), (0, 512), (W, 512)]
    loads = [8, NL, 8, NL]
    first = np.cumsum([0] + loads)
    total = int(first[-1])
    order = [list(range(NL)), [1, 0] + list(range(NL - 1, NCT - 1, -1))]
    steps = [(step, d) for step in range(NL) for d in range(2)]

    with nc.Block() as block:
        @block.sync
        def _(sp):
            w = I["w_in"][0].rearrange("(k p) n -> p k n", p=P)

            def load(j):
                col, n = slabs[j]
                if j >= 2:
                    sp.wait_ge(S["mm"], int(first[j - 1]))
                sp.dma_start(ring[j % 2][:, :, 0:n], w[:, :, col:col + n]).then_inc(w_in[j % 2], 16)

            load(0)
            sp.dma_start(wcn[0:CONV, :], I["conv_w"][0]).then_inc(S["prm"], 16)
            sp.dma_start(wcn[CONV:CONV + 1, :], I["conv_b"]).then_inc(S["prm"], 16)
            sp.dma_start(wsn[:], I["sgu_w"][0].rearrange("g t s -> t g s")).then_inc(S["prm"], 16)
            load(1)
            with nc.allow_non_contiguous_dma(reason="a bias as columns"):
                sp.dma_start(bs[:], I["sgu_b"][0].rearrange("g t -> t g")).then_inc(S["rows"], 16)
            sp.dma_start(gbias[:], I["mlstm_gate_bias"].to_broadcast([P, 16])).then_inc(S["rows"], 16)
            for r, name in enumerate(("conv_ln_w", "conv_ln_b", "sgu_ln_w", "sgu_ln_b", "mlstm_norm_w")):
                sp.dma_start(rows[:, r, :], I[name].to_broadcast([P, W])).then_inc(S["rows"], 16)
            load(2)
            load(3)
            sp.wait_ge(S["pvmm"], 2 * NT)
            wo = I["w_out"][0].rearrange("(k p) n -> p k n", p=P)
            for k in range(0, KT, 2):
                sp.dma_start(K.wo[:, k:k + 2, :], wo[:, k:k + 2, :]).then_inc(K.wo_in, 16)

        @block.gpsimd
        def _(pool):
            g = nc.gpsimd
            g.memset(apad[:], 0.0).then_inc(S["cons"], 1)
            g.memset(vx[:, :, :, HD:], 1.0)
            g.memset(vflat[:, NL * HEADS * HX:], 0.0).then_inc(S["cons"], 1)
            pool.wait_ge(S["ctmm"], 4)
            pool.wait_ge(S["mm"], int(first[3]))
            link = Link(g, S["pchain"])
            for t in (selp, mask, *sel, CF, *qp, ig, lrows, *pair_rows):
                link(g.memset(t[:], 0.0))
            link(g.memset(d0[:], 1.0))
            for r in (0, 32):
                link(g.affine_select(out=selp[r:r + 4], in_=selp[r:r + 4], compare_op=ALU.not_equal, fill=1.0, base=0,
                                     pattern=[[-2, 2], [-1, 2], [0, HD]], channel_multiplier=1))
                s = sel[r // 32][r:r + 4]
                link(g.affine_select(out=s, in_=s, compare_op=ALU.not_equal, fill=-1.0, base=0,
                                     pattern=[[-1, HEADS], [0, P]], channel_multiplier=1))
                start = slice(0, None, P) if r == 0 else slice(P - 1, None, P)
                link(g.memset(d0[r:r + 4, start], 0.0))
            link(g.affine_select(out=mask[:, 0, :], in_=mask[:, 0, :], compare_op=ALU.is_ge, fill=LOW, base=0,
                                 pattern=[[1, P]], channel_multiplier=-1))
            link(g.affine_select(out=mask[:, 1, :], in_=mask[:, 1, :], compare_op=ALU.is_ge, fill=LOW, base=0,
                                 pattern=[[-1, P]], channel_multiplier=1))
            pool.sem_inc(S["sel"], 1)
            pool.wait_ge(S["rows"], 16 * 7)
            pool.wait_ge(S["ev"], int(first[2]))
            g.tensor_tensor(so[:], so[:], rows[:, 4, :].unsqueeze(1).to_broadcast([P, NT, W]), ALU.mult).then_inc(S["sor"], 1)
            pool.wait_ge(S["sor"], 1)
            pool.wait_ge(S["ev"], total)
            pool.wait_ge(S["colev"], 1)

            def keys(n):
                step, d = steps[n]
                if step == NL - 1:
                    return
                if n >= 2:
                    pool.wait_ge(S["umm"], n - 1)
                c = order[d][step]
                g.tensor_tensor(ke[d][:], kn[:, c, :].rearrange("p (h e) -> p h e", h=HEADS),
                                COL[:, 0, c, 1, d, :].unsqueeze(2).to_broadcast([P, HEADS, HD]), ALU.mult).then_inc(S["ker"], 1)
                pool.wait_ge(S["ker"], n + 1)

            def queries(n):
                step, d = steps[n]
                lat = n - 2 * NCT
                if lat < 0:
                    return
                if lat >= 2:
                    pool.wait_ge(S["qmm"], lat - 1)
                tok = slice((order[d][step] - NCT) * P, (order[d][step] - NCT + 1) * P)
                for a in range(2):
                    hr = slice(a * HD, (a + 1) * HD)
                    g.tensor_copy(qp[d][hr, a::2, :], qkT[hr, 0:2, tok]).then_inc(S["qp"], 1)
                pool.wait_ge(S["qp"], 2 * (lat + 1))

            keys(0)
            keys(1)
            for n, (step, d) in enumerate(steps):
                lat = n - 2 * NCT
                if n + 2 < len(steps):
                    queries(n + 2)
                    keys(n + 2)
                if lat >= 0:
                    c = order[d][step] - NCT
                    pool.wait_ge(S["xr"], lat + 1)
                    g.tensor_tensor(H[:, c], H[:, c], num[d][:, :, 0:HD], ALU.add).then_inc(S["hadd"], 1)
                    pool.wait_ge(S["hadd"], lat + 1)

        @block.tensor
        def _(pe):
            def group(bank, cols, pairs, last):
                for k, (lhs, rhs) in enumerate(pairs):
                    mm = nc.tensor.matmul(bank[:, 0:cols], lhs, rhs, start=(k == 0), stop=(k == KT - 1))
                if last:
                    mm.then_inc(S["mm"], 1)

            def slab(j, n, rs):
                w, cols = ring[j % 2], slabs[j][1]
                pe.wait_ge(w_in[j % 2], 16 * (j // 2 + 1))
                for r in rs:
                    if n >= 4:
                        pe.wait_ge(S["ev"], n - 3)
                    b = K.bank[4 + n % 4]
                    if j == 2:
                        m, h = r // 2, r % 2
                        group(b, HALF, [(w[:, k, m * P:(m + 1) * P], K.HT[:, k, TC + h * HALF:TC + (h + 1) * HALF]) for k in range(KT)], True)
                    else:
                        i = r + NCT if j == 0 else r
                        group(b, cols, [(K.HT[:, k, i * P:(i + 1) * P], w[:, k, 0:cols]) for k in range(KT)], True)
                    n += 1
                return n

            pe.wait_ge(S["prm"], 16 * 3)
            for g in range(4):
                nc.tensor.transpose(K.bank[1][:, g * P:(g + 1) * P], wsn[:, g, :], K.ident[:])
            for c in range(2):
                last = nc.tensor.transpose(K.bank[0][:, c * (CONV + 1):(c + 1) * (CONV + 1)], wcn[:, c * P:(c + 1) * P],
                                           K.ident[0:CONV + 1, 0:CONV + 1])
            last.then_inc(S["wst"], 1)
            n = slab(0, 0, range(loads[0]))
            n = slab(1, n, range(loads[1]))
            pe.wait_ge(S["conv"], 1)
            for q in range(4):
                for r in range(4):
                    i, c = 2 * q + r // 2, r % 2
                    last = nc.tensor.transpose(K.bank[q][:, r * P:(r + 1) * P], acc[:, c, i * P:(i + 1) * P], K.ident[:])
                last.then_inc(S["ctmm"], 1)
            n = slab(2, n, range(loads[2]))
            pe.wait_ge(S["ev"], int(first[3]))
            pe.wait_ge(S["ycp"], 1)
            pe.wait_ge(S["g3"], 1)
            for a in range(2):
                for c in range(NL):
                    for d in range(2):
                        last = nc.tensor.matmul(K.bank[4 * a + c // 4][32 * d:32 * d + HEADS, (c % 4) * P:(c % 4 + 1) * P],
                                                GT[:, c, d, a, :], K.ident[:], start=True, stop=True)
            last.then_inc(S["gmm"], 1)
            pe.wait_ge(S["gcp"], 1)
            n = slab(3, n, range(4))
            pe.wait_ge(S["sgn"], 1)
            for g in range(4):
                nc.tensor.matmul(K.bank[g][:].rearrange("p (i n) -> p i n", i=NT), K.wsT[:, g, :],
                                 zb[:, :, W + g * HD:W + (g + 1) * HD], start=True, stop=True).then_inc(S["bmm"], 1)
            n = slab(3, n, range(4, loads[3]))
            pe.wait_ge(S["ev"], total)
            pe.wait_ge(S["ycn"], 1)
            for q in range(4):
                for r in range(4):
                    last = nc.tensor.transpose(K.bank[4 + q][:, r * P:(r + 1) * P], yc[:, 4 * (q % 2) + r, (q // 2) * P:(q // 2 + 1) * P], K.ident[:])
                last.then_inc(S["yc_tr"], 1)
            pe.wait_ge(S["bdone"], 4)
            for q in range(4):
                for r in range(4):
                    last = nc.tensor.transpose(K.bank[q][:, r * P:(r + 1) * P], zb[:, 4 * (q % 2) + r, (q // 2) * P:(q // 2 + 1) * P], K.ident[:])
                last.then_inc(S["yb_tr"], 1)
            pe.wait_ge(S["yc_ev"], 4)
            pe.wait_ge(S["yb_ev"], 4)
            pe.wait_ge(S["gb"], 1)
            for n in range(2 * NL):
                k, c = n // NL, n % NL
                nc.tensor.matmul(K.bank[n // 4][:, n % 4 * P:(n % 4 + 1) * P], pair_rows[k][:, c * P:(c + 1) * P], K.ident[0:QS, :],
                                 start=True, stop=True)
            for d in range(2):
                r = slice(32 * d, 32 * d + HEADS)
                for j in range(2):
                    o = j * NL
                    last = nc.tensor.matmul(K.bank[6 + d][:, o:o + NL], selp[r, j, :, :], DEC[r, :], start=True, stop=True)
            last.then_inc(S["colmm"], 1)
            pe.wait_ge(S["colev"], 1)
            def argument(n):
                step, d = steps[n]
                c = order[d][step]
                if c < NCT:
                    return
                pe.wait_ge(S["st"], n - 1)
                for h in range(HEADS):
                    last = nc.tensor.matmul(K.bank[4 * d][:, h * P:(h + 1) * P], sel[d][:, h, :], lrows[:, c * P:(c + 1) * P], start=True, stop=True)
                last.then_inc(S["argmm"], 1)

            for n, (step, d) in enumerate(steps):
                c, lat = order[d][step], n - 2 * NCT
                b = [K.bank[4 * d + m] for m in range(4)]
                tok = slice((c - NCT) * P, (c - NCT + 1) * P)
                if lat >= 0:
                    if lat >= 2:
                        pe.wait_ge(S["nr"], lat - 1)
                    pe.wait_ge(S["st"], n - 1)
                    pe.wait_ge(S["qp"], 2 * (lat + 1))
                    for j in range(2):
                        last = nc.tensor.matmul(b[1].rearrange("p (h t) -> p h t", h=HEADS)[:, 2 * j:2 * j + 2, :], qkT[:, 2 + j, tok],
                                                qp[d][:, 2 * j:2 * j + 2, :], start=True, stop=True)
                    last.then_inc(S["smm"], 1)
                    for h in range(HEADS):
                        last = nc.tensor.matmul(b[2][:, h * P:(h + 1) * P], qp[d][:, h, :], CF[:, d, h // 2 * HX:h // 2 * HX + P],
                                                start=True, stop=True)
                    last.then_inc(S["qmm"], 1)
                if n + 1 < len(steps):
                    argument(n + 1)
                if step < NL - 1:
                    pe.wait_ge(S["ker"], n + 1)
                    if lat >= 0:
                        pe.wait_ge(S["argr"], lat + 1)
                    elif n >= 2:
                        pe.wait_ge(S["st"], n - 1)
                    for h in range(HEADS):
                        o = (h // 2) * HX
                        last = nc.tensor.matmul(b[0][(h % 2) * HD:(h % 2 + 1) * HD, o:o + HX], ke[d][:, h, :], vx[:, c, h, :],
                                                start=True, stop=True)
                    last.then_inc(S["umm"], 1)
                if lat >= 0:
                    pe.wait_ge(S["ptr"], lat + 1)
                    for h in range(HEADS):
                        o = (c * HEADS + h) * HX
                        last = nc.tensor.matmul(b[3][:, h * P:(h + 1) * P], PT[d][:, h, :], vflat[:, o:o + P], start=True, stop=True)
                    last.then_inc(S["pvmm"], 1)
            for q in (0, 2, 1, 3):
                pe.wait_ge(S["hr"], q % 2 + 1)
                for r in range(4):
                    last = nc.tensor.transpose(K.bank[q][:, r * P:(r + 1) * P],
                                               H[:, 4 * (q % 2) + r, 2 * (q // 2):2 * (q // 2) + 2, :], K.ident[:])
                last.then_inc(S["yam"], 1)

        @block.scalar
        def _(act):
            def take(dst, src, func=ACT.Copy, last=True):
                ins = nc.scalar.activation(dst, src, func)
                if last:
                    ins.then_inc(S["ev"], 1)

            def slab(j, n, rs):
                for r in rs:
                    act.wait_ge(S["mm"], n + 1)
                    b = K.bank[4 + n % 4]
                    if j == 0:
                        take(zb[:, r, :], b[:], ACT.Gelu_apprx_tanh)
                    elif j == 1:
                        if r >= NCT:
                            take(so[:, r - NCT, :], b[:, 0:W], ACT.Sigmoid, last=False)
                        take(GT[:, r], b[:, W:W + 16].rearrange("p (d a h) -> p d a h", d=2, a=2))
                    elif j == 2:
                        take(qkT[:, r // 2, (r % 2) * HALF:(r % 2 + 1) * HALF], b[:])
                    else:
                        take(kn[:, r, :], b[:, 0:W], last=False)
                        take(vx[:, r, :, 0:HD], b[:, W:].rearrange("p (h e) -> p h e", h=HEADS))
                    n += 1
                return n

            n = slab(0, 0, range(loads[0]))
            n = slab(1, n, range(loads[1]))
            act.wait_ge(S["g2"], 1)
            nc.scalar.activation(ge[:], gt[:], ACT.Exp).then_inc(S["gx"], 1)
            act.wait_ge(S["gx"], 1)
            nc.scalar.activation(ge[:], ge[:], ACT.Ln, bias=1.0).then_inc(S["gx"], 1)
            act.wait_ge(S["eps1"], 1)
            nc.scalar.activation(rstd[:], rstd[:], ACT.Sqrt).then_inc(S["eps1"], 1)
            n = slab(2, n, range(2))
            act.wait_ge(S["eps2"], 1)
            nc.scalar.activation(rstdc[:], rstdc[:], ACT.Sqrt).then_inc(S["eps2"], 1)
            n = slab(2, n, range(2, loads[2]))
            act.wait_ge(S["eps2"], 3)
            nc.scalar.activation(yc[:], yc[:], ACT.Silu).then_inc(S["ycn"], 1)
            act.wait_ge(S["cons"], 2)
            act.wait_ge(S["apr"], 1)
            n = slab(3, n, range(loads[3]))
            for q in range(4):
                act.wait_ge(S["yc_tr"], q + 1)
                nc.scalar.activation(K.yT[4 + q // 2][:, (q % 2) * HALF:(q % 2 + 1) * HALF], K.bank[4 + q][:], ACT.Copy).then_inc(S["yc_ev"], 1)
            for q in range(4):
                act.wait_ge(S["yb_tr"], q + 1)
                nc.scalar.activation(K.yT[2 + q // 2][:, (q % 2) * HALF:(q % 2 + 1) * HALF], K.bank[q][:], ACT.Copy).then_inc(S["yb_ev"], 1)
            act.wait_ge(S["ga"], 1)
            for t in (pair_rows[0][:], DEC[0:QR, :]):
                nc.scalar.activation(t, t, ACT.Exp)
            nc.scalar.activation(bc, bc, ACT.Exp, scale=-1.0).then_inc(S["gb"], 1)
            for m in range(2 * NT):
                act.wait_ge(S["argr"], m + 1)
                nc.scalar.activation(arg[m % 2][:], arg[m % 2][:], ACT.Exp).then_inc(S["pr"], 1)
            for half in range(2):
                act.wait_ge(S["readout"], 2 * half + 1)
                t = slice(half * NT // 2, (half + 1) * NT // 2)
                nc.scalar.activation(sqs[:, t], sqs[:, t], ACT.Sqrt).then_inc(S["readout"], 1)
            for m, q in enumerate((0, 2, 1, 3)):
                act.wait_ge(S["yam"], m + 1)
                nc.scalar.activation(K.yT[q // 2][:, (q % 2) * HALF:(q % 2 + 1) * HALF], K.bank[q][:], ACT.Copy).then_inc(S["yae"], 1)

        @block.vector
        def _(dve):
            v = nc.vector
            link = Link(v, S["chain"])
            dve.wait_ge(S["wst"], 1)
            link(v.tensor_copy(K.wsT[:], K.bank[1][:].rearrange("p (g t) -> p g t", g=4)))
            v.tensor_copy(wcol[:], K.bank[0][:, 0:2 * (CONV + 1)].rearrange("p (c k) -> p c k", c=2)).then_inc(S["g1"], 1)
            dve.wait_ge(S["g1"], 1)
            dve.wait_ge(S["cons"], 2)
            for c in range(2):
                link(v.tensor_tensor(apad[:, c, :, PAD:PAD + GRID], K.cT[0][:, c, :].rearrange("p (r t) -> p r t", r=ROWS),
                                     K.cT[1][:, c, :].rearrange("p (r t) -> p r t", r=ROWS), ALU.mult))
            dve.sem_inc(S["apr"], 1)
            out = [acc[:, c, :].rearrange("p (r t) -> p r t", r=ROWS) for c in range(2)]
            for c in range(2):
                link(v.tensor_scalar(out[c], apad[:, c, :, 0:GRID], wcol[:, c, 0:1], wcol[:, c, CONV:CONV + 1], ALU.mult, ALU.add))
            for k in range(1, CONV):
                for c in range(2):
                    link(v.scalar_tensor_tensor(out=out[c], in0=apad[:, c, :, k:k + GRID], scalar=wcol[:, c, k:k + 1], in1=out[c],
                                                op0=ALU.mult, op1=ALU.add))
            dve.sem_inc(S["conv"], 1)

            def norm(x, mean_var, inv, i):
                link(v.bn_stats(st6[:], x))
                link(v.bn_aggr(mean_var[:, i, :], st6[:]))

            dve.wait_ge(S["ev"], int(first[1]))
            dve.wait_ge(S["rows"], 16 * 7)
            for i in range(NT):
                norm(zb[:, i, W:], mv, rstd, i)
            link(v.tensor_scalar(rstd[:], mv[:, :, 1], LN_EPS, None, ALU.add))
            dve.sem_inc(S["eps1"], 1)
            dve.wait_ge(S["ev"], int(first[2]))
            flat = GT[:].rearrange("p i d a h -> p i (d a h)")
            link(v.tensor_tensor(flat, flat, gbias[:].unsqueeze(1).to_broadcast([P, NL, 16]), ALU.add))
            for d in range(2):
                link(v.scalar_tensor_tensor(out=gt[:, :, d, :], in0=GT[:, :, d, 1, :], scalar=-1.0, in1=GT[:, :, d, 1, :], op0=ALU.mult, op1=ALU.min))
            dve.sem_inc(S["g2"], 1)
            for i in range(NT):
                dve.wait_ge(S["ctmm"], i // 2 + 1)
                x = K.bank[i // 2][:, (i % 2) * W:(i % 2 + 1) * W]
                norm(x, mvc, rstdc, i)
            link(v.tensor_scalar(rstdc[:], mvc[:, :, 1], LN_EPS, None, ALU.add))
            dve.sem_inc(S["eps2"], 1)
            dve.wait_ge(S["gx"], 2)
            for d in range(2):
                link(v.scalar_tensor_tensor(out=GT[:, :, d, 1, :], in0=GT[:, :, d, 1, :], scalar=0.0, in1=ge[:, :, d, :], op0=ALU.min, op1=ALU.subtract))
            dve.sem_inc(S["g3"], 1)
            dve.wait_ge(S["eps1"], 2)
            link(v.reciprocal(rstd[:], rstd[:]))
            for i in range(NT):
                link(v.tensor_scalar(zb[:, i, W:], zb[:, i, W:], mv[:, i, 0:1], rstd[:, i:i + 1], ALU.subtract, ALU.mult))
            for r, op in ((2, ALU.mult), (3, ALU.add)):
                link(v.tensor_tensor(zb[:, :, W:], zb[:, :, W:], rows[:, r, :].unsqueeze(1).to_broadcast([P, NT, W]), op))
            dve.sem_inc(S["sgn"], 1)
            dve.wait_ge(S["eps2"], 2)
            link(v.reciprocal(rstdc[:], rstdc[:]))
            for i in range(NT):
                x = K.bank[i // 2][:, (i % 2) * W:(i % 2 + 1) * W]
                link(v.tensor_scalar(yc[:, i, :], x, mvc[:, i, 0:1], rstdc[:, i:i + 1], ALU.subtract, ALU.mult))
            dve.sem_inc(S["ycp"], 1)
            for r, op in ((0, ALU.mult), (1, ALU.add)):
                link(v.tensor_tensor(yc[:], yc[:], rows[:, r, :].unsqueeze(1).to_broadcast([P, NT, W]), op))
            dve.sem_inc(S["eps2"], 1)
            dve.wait_ge(S["sel"], 1)
            dve.wait_ge(S["gmm"], 1)
            for a, t in enumerate((ig, lf)):
                for d in range(2):
                    r = slice(32 * d, 32 * d + HEADS)
                    for q in range(3):
                        n = min(HALF, NL * P - q * HALF)
                        link(v.tensor_copy(t[r, q * HALF:q * HALF + n], K.bank[4 * a + q][r, 0:n]))
            dve.sem_inc(S["gcp"], 1)
            way = [slice(None), slice(None, None, -1)]
            for d in range(2):
                r = slice(32 * d, 32 * d + HEADS)
                link(v.tensor_tensor_scan(bc[r, way[d]], d0[r, way[d]], lf[r, way[d]], 0.0, ALU.mult, ALU.add))
            link(v.tensor_tensor(ig[:], ig[:], bc, ALU.subtract))
            link(v.tensor_copy(acopy, ig[:]))
            link(v.tensor_scalar(d0[:], d0[:], 1.0, -LOW, ALU.subtract, ALU.mult))
            for d in range(2):
                r = slice(32 * d, 32 * d + HEADS)
                link(v.tensor_tensor_scan(lf[r, way[d]], d0[r, way[d]], ig[r, way[d]], LOW, ALU.add, ALU.max))
            for g in range(4):
                dve.wait_ge(S["bmm"], g + 1)
                o = zb[:, :, g * HD:(g + 1) * HD]
                v.scalar_tensor_tensor(out=o, in0=K.bank[g][:].rearrange("p (i n) -> p i n", i=NT), scalar=bs[:, g:g + 1], in1=o,
                                       op0=ALU.add, op1=ALU.mult).then_inc(S["bdone"], 1)
            link(v.memset(BE[0:QR, :], 0.0))
            link(v.memset(ME[0:QR, :], 0.0))
            link(v.memset(MEc[0:QR, :], 0.0))
            link(v.memset(MPc[0:QR, :], 0.0))
            link(v.memset(MP[0:QR, :], LOW))
            for d in range(2):
                r = slice(32 * d, 32 * d + HEADS)
                for dst, src in ((BE, bc), (ME, lf)):
                    e = src[r, P - 1::P] if d == 0 else src[r, 0::P]
                    if d == 0:
                        link(v.tensor_copy(dst[r, :], e))
                    else:
                        link(v.tensor_copy(dst[r, 0:NCT], e[:, NCT - 1::-1]))
                        link(v.tensor_copy(dst[r, NCT:], e[:, :NCT - 1:-1]))
                link(v.tensor_copy(MEc[r, :], lf[r, P - 1::P] if d == 0 else lf[r, 0::P]))
            link(v.tensor_tensor(BM[0:QR, :], BE[0:QR, :], ME[0:QR, :], ALU.add))
            link(v.tensor_tensor_scan(MP[0:QR, 1:], BE[0:QR, :], BM[0:QR, :], LOW, ALU.add, ALU.max))
            link(v.tensor_copy(MPc[0:HEADS, :], MP[0:HEADS, 0:NL]))
            r = slice(32, 32 + HEADS)
            link(v.tensor_copy(MPc[r, 0:NCT], MP[r, NCT - 1::-1]))
            link(v.tensor_copy(MPc[r, NCT:], MP[r, NL - 1:NCT - 1:-1]))
            link(v.tensor_tensor(MEc[0:QR, :], MEc[0:QR, :], MPc[0:QR, :], ALU.max))

            def chunked(t):
                return t[0:].rearrange("p (c t) -> p c t", c=NL)

            before, after = (t[0:QR, :].unsqueeze(2).to_broadcast([QR, NL, P]) for t in (MPc, MEc))
            link(v.tensor_tensor(chunked(lf), chunked(lf), before, ALU.max))
            link(v.tensor_tensor(chunked(win), before, chunked(lf), ALU.subtract))
            link(v.tensor_tensor(chunked(ee), chunked(ig), after, ALU.subtract))
            link(v.tensor_tensor(bc, bc, lf[:], ALU.add))
            link(v.tensor_tensor(DEC[0:QR, :], MPc[0:QR, :], MEc[0:QR, :], ALU.subtract))
            dve.sem_inc(S["ga"], 1)
            link(v.memset(H[:], 0.0))
            dve.wait_ge(S["colmm"], 1)
            for q in range(2 * NL // 4):
                link(v.tensor_copy(COL[:].rearrange("p k c s d h -> p (k c) (s d) h")[:, 4 * q:4 * q + 4],
                                   K.bank[q][:].rearrange("p (c y x) -> p c y x", c=4, x=32)[:, :, :, 0:HEADS]))
            for d in range(2):
                link(v.tensor_copy(dcol[:, d].rearrange("p j c -> p (j c)"), K.bank[6 + d][:, 0:2 * NL]))
            link(v.tensor_scalar(COL[:, 0, :, 1], COL[:, 0, :, 1], HD ** -0.5, None, ALU.mult))
            dve.sem_inc(S["colev"], 1)
            def argument(n):
                step, d = steps[n]
                c = order[d][step]
                if c < NCT:
                    return
                dve.wait_ge(S["argmm"], n - 2 * NCT + 1)
                for h in range(HEADS):
                    last = v.scalar_tensor_tensor(out=arg[d][:, h, :], in0=K.bank[4 * d][:, h * P:(h + 1) * P], scalar=COL[:, 1, c, 1, d, h:h + 1],
                                                  in1=mask[:, d, :], op0=ALU.add, op1=ALU.min)
                last.then_inc(S["argr"], 1)

            for n, (step, d) in enumerate(steps):
                c, lat = order[d][step], n - 2 * NCT
                b = [K.bank[4 * d + m] for m in range(4)]
                if lat >= 0:
                    dve.wait_ge(S["pr"], lat + 1)
                    dve.wait_ge(S["smm"], lat + 1)
                    v.scalar_tensor_tensor(out=PT[d][:], in0=b[1].rearrange("p (h t) -> p h t", h=HEADS), scalar=HD ** -0.5, in1=arg[d][:],
                                           op0=ALU.mult, op1=ALU.mult).then_inc(S["ptr"], 1)
                if n + 1 < len(steps):
                    argument(n + 1)
                if lat >= 0:
                    if lat >= 2:
                        dve.wait_ge(S["hadd"], lat - 1)
                    dve.wait_ge(S["qmm"], lat + 1)
                    link(v.tensor_tensor(num[d][:], b[2].rearrange("p (h e) -> p h e", h=HEADS)[:, :, 0:HX],
                                         COL[:, 0, c, 0, d, :].unsqueeze(2).to_broadcast([P, HEADS, HX]), ALU.mult))
                if step < NL - 1:
                    dve.wait_ge(S["umm"], n + 1)
                    for j in range(2):
                        o = j * HX
                        last = v.scalar_tensor_tensor(out=CS[:, d, j, :], in0=CS[:, d, j, :], scalar=dcol[:, d, j, c:c + 1],
                                                      in1=b[0][:, o:o + HX], op0=ALU.mult, op1=ALU.add)
                    last.then_inc(S["st"], 1)
                if lat >= 0:
                    dve.wait_ge(S["pvmm"], lat + 1)
                    v.tensor_tensor(num[d][:], num[d][:], b[3][:].rearrange("p (h e) -> p h e", h=HEADS)[:, :, 0:HX], ALU.add).then_inc(S["nr"], 1)
                    dve.wait_ge(S["nr"], lat + 1)
                    den = num[d][:, :, HD]
                    link(v.scalar_tensor_tensor(out=nd[d][:], in0=den, scalar=-1.0, in1=den, op0=ALU.mult, op1=ALU.max))
                    link(v.tensor_tensor(nd[d][:], nd[d][:], COL[:, 1, c, 0, d, :], ALU.max))
                    link(v.reciprocal(nd[d][:], nd[d][:]))
                    x = num[d][:, :, 0:HD]
                    v.tensor_tensor(x, x, nd[d][:].unsqueeze(2).to_broadcast([P, HEADS, HD]), ALU.mult).then_inc(S["xr"], 1)
            dve.wait_ge(S["hadd"], 2 * NT)
            dve.wait_ge(S["sor"], 1)
            for half in range(2):
                t = slice(half * NT // 2, (half + 1) * NT // 2)
                n = NT // 2 * HEADS
                x, spare = H[:, t].rearrange("p i h e -> p (i h) e"), spares[:, t].rearrange("p i (h e) -> p (i h) e", h=HEADS)
                mean, var = sums[:, t].rearrange("p i h -> p (i h)"), sqs[:, t].rearrange("p i h -> p (i h)")
                link(v.tensor_reduce(mean, x, AX.X, ALU.add))
                link(v.tensor_scalar(mean, mean, 1.0 / HD, None, ALU.mult))
                link(v.tensor_tensor(x, x, mean.unsqueeze(2).to_broadcast([P, n, HD]), ALU.subtract))
                link(v.tensor_tensor(spare, x, x, ALU.mult))
                link(v.tensor_reduce(var, spare, AX.X, ALU.add))
                v.tensor_scalar(var, var, 1.0 / HD, LN_EPS, ALU.mult, ALU.add).then_inc(S["readout"], 1)
                dve.wait_ge(S["readout"], 2 * half + 2)
                link(v.reciprocal(var, var))
                link(v.tensor_tensor(x, x, var.unsqueeze(2).to_broadcast([P, n, HD]), ALU.mult))
                wide = H[:, t].rearrange("p i h e -> p i (h e)")
                v.tensor_tensor(wide, wide, so[:, t, :], ALU.mult).then_inc(S["hr"], 1)


def stage_join(K):
    nc, I = K.nc, K.I
    wo = K.wo
    xr = [K.at(f"jn_x{s}", 104 + 4 * s, [P, D]) for s in range(3)]
    rows = K.at("jn_rows", 116, [P, 2, D])
    t = [K.at(f"jn_t{s}", 124 + 4 * s, [P, D]) for s in range(2)]
    h = [K.at(f"jn_h{s}", 48 + 4 * s, [P, D]) for s in range(2)]
    K.h2 = [K.at(f"h2{n}", 132 + 32 * n, [P, 2, KT, HALF], FR) for n in range(2)]
    st, mv, rs = K.prm[:, 0:12].rearrange("p (a b) -> p a b", a=2), K.prm[:, 12:14], K.prm[:, 14:15]
    K.x1 = nc.dram_tensor("x1", (T, D), F32, kind="Internal").ap()
    x_in, r_in = [K.sem(f"jn_xin{s}") for s in range(3)], K.sem("jn_rin")
    mm, mev, sq, x1r, hr, tr, thi, tev, chain = (K.sem("jn_" + n) for n in "mm mev sq x1r hr tr thi tev chain".split())
    stored = [K.sem(f"jn_st{s}") for s in range(2)]
    with nc.Block() as block:
        @block.sync
        def _(sp):
            for r, name in enumerate(("ln1_w", "ln1_b")):
                sp.dma_start(rows[:, r, :], I[name].to_broadcast([P, D])).then_inc(r_in, 16)
            for i in range(NT):
                if i >= 3:
                    sp.wait_ge(x1r, i - 2)
                sp.dma_start(xr[i % 3][:], I["x"][0][i * P:(i + 1) * P, :]).then_inc(x_in[i % 3], 16)

        @block.gpsimd
        def _(pool):
            for i in range(NT):
                pool.wait_ge(x1r, i + 1)
                pool.dma_start(K.x1[i * P:(i + 1) * P, :], t[i % 2][:]).then_inc(stored[i % 2], 16)
            for s in range(2):
                pool.wait_ge(stored[s], 16 * NT // 2)

        @block.tensor
        def _(pe):
            def turn(i):
                pe.wait_ge(hr, i + 1)
                if i >= 2:
                    pe.wait_ge(tev, 2 * (i - 1))
                for k in range(KT):
                    last = nc.tensor.transpose(K.bank[4 + 2 * (i % 2) + k // 4][:, (k % 4) * P:(k % 4 + 1) * P],
                                               h[i % 2][:, k * P:(k + 1) * P], K.ident[:])
                last.then_inc(tr, 1)

            pe.wait_ge(K.wo_in, 16 * KT // 2)
            for i in range(NT):
                if i >= 2:
                    pe.wait_ge(mev, i - 1)
                for b in range(2):
                    for k in range(KT):
                        last = nc.tensor.matmul(K.bank[2 * (i % 2) + b][:], K.yT[k][:, i * P:(i + 1) * P], wo[:, k, b * HALF:(b + 1) * HALF],
                                                start=(k == 0), stop=(k == KT - 1))
                last.then_inc(mm, 1)
                if i:
                    turn(i - 1)
            turn(NT - 1)

        @block.scalar
        def _(act):
            def take(i):
                act.wait_ge(tr, i + 1)
                for b in range(2):
                    nc.scalar.activation(K.h2[0][:, i // 4, 4 * b:4 * b + 4, (i % 4) * P:(i % 4 + 1) * P],
                                         K.bank[4 + 2 * (i % 2) + b][:].rearrange("p (k t) -> p k t", k=4), ACT.Copy).then_inc(thi, 1)

            for i in range(NT):
                act.wait_ge(sq, 2 * i + 1)
                nc.scalar.activation(rs, rs, ACT.Sqrt).then_inc(sq, 1)
                if i:
                    take(i - 1)
            take(NT - 1)

        @block.vector
        def _(dve):
            v = nc.vector
            link = Link(v, chain)

            def low(i):
                for b in range(2):
                    dve.wait_ge(thi, 2 * i + b + 1)
                    at = (slice(None), i // 4, slice(4 * b, 4 * b + 4), slice((i % 4) * P, (i % 4 + 1) * P))
                    v.tensor_tensor(K.h2[1][at], K.bank[4 + 2 * (i % 2) + b][:].rearrange("p (k t) -> p k t", k=4), K.h2[0][at].bitcast(F32),
                                    ALU.subtract).then_inc(tev, 1)

            dve.wait_ge(r_in, 32)
            for i in range(NT):
                x, y = xr[i % 3], t[i % 2]
                dve.wait_ge(mm, i + 1)
                if i >= 2:
                    dve.wait_ge(stored[i % 2], 16 * (i // 2))
                for b in range(2):
                    s = slice(b * HALF, (b + 1) * HALF)
                    last = v.tensor_tensor(y[:, s], K.bank[2 * (i % 2) + b][:], K.MOD[:, 2 * D + b * HALF:2 * D + (b + 1) * HALF], ALU.mult)
                last.then_inc(mev, 1)
                dve.wait_ge(mev, i + 1)
                dve.wait_ge(x_in[i % 3], 16 * (i // 3 + 1))
                link(v.scalar_tensor_tensor(out=y[:], in0=x[:], scalar=ALPHA, in1=y[:], op0=ALU.mult, op1=ALU.add))
                norm_rows(K, dve, link, y, st, mv, rs, sq, i, rows[:, 0, :], rows[:, 1, :]).then_inc(x1r, 1)
                dve.wait_ge(x1r, i + 1)
                if i >= 2:
                    dve.wait_ge(tr, i - 1)
                link(v.scalar_tensor_tensor(out=h[i % 2][:], in0=K.MOD[:, 4 * D:5 * D], scalar=1.0, in1=y[:], op0=ALU.add, op1=ALU.mult))
                v.tensor_tensor(h[i % 2][:], h[i % 2][:], K.MOD[:, 3 * D:4 * D], ALU.add).then_inc(hr, 1)
                if i:
                    low(i - 1)
            low(NT - 1)


def norm_rows(K, dve, link, y, st, mv, rs, sq, i, w, b):
    v = K.nc.vector
    for h in range(2):
        link(v.bn_stats(st[:, h, :], y[:, h * HALF:(h + 1) * HALF]))
    link(v.bn_aggr(mv, st))
    v.tensor_scalar(rs, mv[:, 1:2], LN_EPS, None, ALU.add).then_inc(sq, 1)
    link(v.scalar_tensor_tensor(out=y[:], in0=y[:], scalar=mv[:, 0:1], in1=w, op0=ALU.subtract, op1=ALU.mult))
    dve.wait_ge(sq, 2 * i + 2)
    link(v.reciprocal(rs, rs))
    return v.scalar_tensor_tensor(out=y[:], in0=y[:], scalar=rs, in1=b, op0=ALU.mult, op1=ALU.add)


def rms_root(K, act, x, junk, ss, sem, i):
    K.nc.scalar.activation(junk, x, ACT.Square, accum_out=ss).then_inc(sem, 1)
    act.wait_ge(sem, 2 * i + 1)
    K.nc.scalar.activation(ss, ss, ACT.Sqrt, scale=1.0 / D, bias=K.eps[:]).then_inc(sem, 1)


def product(nc, out, w, x, first, last):
    nc.tensor.matmul(out, w[0], x[0], start=first, stop=False)
    nc.tensor.matmul(out, w[0], x[1], start=False, stop=False)
    return nc.tensor.matmul(out, w[1], x[0], start=False, stop=last)


def stage_ffn(K):
    nc, I = K.nc, K.I
    NR, FT = 4, 2
    QUART = (0, 6, 12, 17, NF)
    UH, UO = 2 * NF, 4 * KT
    hid = [K.at(f"ff_hid{n}", 24 + 44 * n, [P, NF, HALF], FR) for n in range(2)]
    raw = [K.at(f"ff_raw{s}", 112 + 4 * s, [P, KT, P]) for s in range(NR)]
    part = [[K.at(f"ff_part{s}{n}", 8 * s + 4 * n, [P, KT, P], FR) for n in range(2)] for s in range(2)]
    sil = [K.at(f"ff_sil{s}", 16 + 2 * s, [P, HALF]) for s in range(2)]
    hv = [K.at(f"ff_hv{s}", 128 + 2 * s, [P, HALF]) for s in range(2)]
    K.ynT = K.at("ynT", 164, [P, 2, KT, HALF])
    raw_in = [K.sem(f"ff_raw_in{s}") for s in range(NR)]
    hi, lo, mm, sr, hr, hhi, hlo, oev = (K.sem("ff_" + n) for n in "hi lo mm sr hr hhi hlo oev".split())
    w1 = I["w_ffn_in"][0].rearrange("(k p) (a f) -> p k a f", p=P, a=2)
    w2 = I["w_ffn_out"][0].rearrange("(f p) n -> p f n", p=P)

    def loop(eng, body, count):
        body(0)
        with eng.Fori(1, count) as r:
            body(r)

    def unit(h, r, c):
        return (UH + UO) * h + r * c

    with nc.Block() as block:
        @block.sync
        def _(sp):
            for h in range(2):
                def hidden(r):
                    for s in range(NR):
                        if h or not isinstance(r, int):
                            sp.wait_ge(lo, unit(h, r, NR) + s - (NR - 1))
                        sp.dma_start(raw[s][:], w1[:, :, s % 2, bass.ds(r * (FT * P) + (s // 2) * P, P)]).then_inc(raw_in[s], 16)

                def output(r):
                    for m in range(2):
                        for s in range(NR):
                            f = slice(QUART[s], QUART[s + 1])
                            sp.wait_ge(lo, unit(h, r, 2 * NR) + UH + NR * m + s - (NR - 1))
                            sp.dma_start(raw[s][:, 0:f.stop - f.start, :], w2[:, f, bass.ds(r * (2 * P) + m * P, P)]).then_inc(raw_in[s], 16)

                loop(sp, hidden, NF // FT)
                loop(sp, output, KT // 2)

        def arrivals(h, phase, r, m=0):
            return ((UH + UO) // NR) * h + (r if phase == 0 else UH // NR + r * 2 + m) + 1

        @block.scalar
        def _(act):
            def split(u, s, n, count):
                act.wait_ge(raw_in[s], count * 16)
                if not isinstance(u, int) or u >= 2:
                    act.wait_ge(mm, u - 1)
                nc.scalar.activation(part[s % 2][0][:, 0:n, :], raw[s][:, 0:n, :], ACT.Copy).then_inc(hi, 1)

            def silu(h, u, f, s):
                act.wait_ge(mm, u + 1)
                if not isinstance(f, int) or h or f >= 2:
                    act.wait_ge(hr, NF * h + f - 1)
                nc.scalar.activation(sil[s][:], K.bank[2 * s][:], ACT.Silu).then_inc(sr, 1)
                act.wait_ge(hr, NF * h + f + 1)
                nc.scalar.activation(hid[0][:, bass.ds(f, 1), :], hv[s][:].unsqueeze(1), ACT.Copy).then_inc(hhi, 1)

            def take(h, u, m, s):
                act.wait_ge(mm, u + 1)
                nc.scalar.activation(K.ynT[:, h, bass.ds(m, 1), :], K.bank[4 + s][:].unsqueeze(1), ACT.Copy).then_inc(oev, 1)

            for h in range(2):
                def hidden(r):
                    for j in range(FT):
                        u = unit(h, r, NR) + 2 * j
                        for a in range(2):
                            split(u + a, 2 * j + a, KT, arrivals(h, 0, r))
                        if j or not isinstance(r, int):
                            silu(h, u - 2, r * FT + (j - 1), 1 - j)
                        elif h:
                            take(0, u - 1, KT - 1, 1)

                def output(r):
                    for m in range(2):
                        u = unit(h, r, 2 * NR) + UH + NR * m
                        for s in range(NR):
                            split(u + s, s, QUART[s + 1] - QUART[s], arrivals(h, 1, r, m))
                            if s == 1:
                                if m or not isinstance(r, int):
                                    take(h, u - 1, r * 2 + (m - 1), 1 - m)
                                else:
                                    silu(h, u - 2, NF - 1, 1)

                loop(act, hidden, NF // FT)
                loop(act, output, KT // 2)
            take(1, 2 * (UH + UO) - 1, KT - 1, 1)

        @block.vector
        def _(dve):
            v = nc.vector

            def split(u, s, n):
                dve.wait_ge(hi, u + 1)
                v.tensor_tensor(part[s % 2][1][:, 0:n, :], raw[s][:, 0:n, :], part[s % 2][0][:, 0:n, :].bitcast(F32), ALU.subtract).then_inc(lo, 1)

            def multiply(h, u, f, s):
                dve.wait_ge(mm, u + 1)
                dve.wait_ge(sr, NF * h + f + 1)
                if not isinstance(f, int) or h or f >= 2:
                    dve.wait_ge(hlo, NF * h + f - 1)
                v.tensor_tensor(hv[s][:], sil[s][:], K.bank[2 * s + 1][:], ALU.mult).then_inc(hr, 1)
                dve.wait_ge(hhi, NF * h + f + 1)
                v.tensor_tensor(hid[1][:, bass.ds(f, 1), :], hv[s][:].unsqueeze(1), hid[0][:, bass.ds(f, 1), :].bitcast(F32), ALU.subtract).then_inc(hlo, 1)

            for h in range(2):
                def hidden(r):
                    for j in range(FT):
                        u = unit(h, r, NR) + 2 * j
                        for a in range(2):
                            split(u + a, 2 * j + a, KT)
                        if j or not isinstance(r, int):
                            multiply(h, u - 1, r * FT + (j - 1), 1 - j)

                def output(r):
                    for m in range(2):
                        u = unit(h, r, 2 * NR) + UH + NR * m
                        for s in range(NR):
                            split(u + s, s, QUART[s + 1] - QUART[s])
                            if s == 1 and m == 0 and isinstance(r, int):
                                multiply(h, u - 1, NF - 1, 1)

                loop(dve, hidden, NF // FT)
                loop(dve, output, KT // 2)

        @block.tensor
        def _(pe):
            for h in range(2):
                def hidden(r):
                    for j in range(FT):
                        for a in range(2):
                            u, s = unit(h, r, NR) + 2 * j + a, 2 * j + a
                            if a == 0 and (h or not isinstance(r, int)):
                                pe.wait_ge(hr, NF * h + r * FT + (j - 1))
                            pe.wait_ge(lo, u + 1)
                            for k in range(KT):
                                last = product(nc, K.bank[2 * j + a][:], [w[:, k, :] for w in part[s % 2]], [x[:, h, k, :] for x in K.h2],
                                               k == 0, k == KT - 1)
                            last.then_inc(mm, 1)

                def output(r):
                    for m in range(2):
                        if h or not isinstance(r, int):
                            pe.wait_ge(oev, KT * h + r * 2 + (m - 1))
                        for s in range(NR):
                            if m == 0 and isinstance(r, int):
                                pe.wait_ge(hlo, NF * h + QUART[s + 1])
                            pe.wait_ge(lo, unit(h, r, 2 * NR) + UH + NR * m + s + 1)
                            for f in range(QUART[s], QUART[s + 1]):
                                last = product(nc, K.bank[4 + m][:], [w[:, f - QUART[s], :] for w in part[s % 2]], [x[:, f, :] for x in hid],
                                               f == 0, f == NF - 1)
                            last.then_inc(mm, 1)

                loop(pe, hidden, NF // FT)
                loop(pe, output, KT // 2)


def stage_first_end(K):
    nc, I = K.nc, K.I
    xr = [K.at(f"fe_x{s}", 88 + 4 * s, [P, D]) for s in range(3)]
    rows = K.at("fe_rows", 100, [P, 3, D])
    t = [K.at(f"fe_t{s}", 112 + 4 * s, [P, D]) for s in range(2)]
    h = [K.at(f"fe_h{s}", 120 + 4 * s, [P, D]) for s in range(2)]
    K.h3 = [K.at(f"h3{n}", 24 + 32 * n, [P, KT, T], FR) for n in range(2)]
    st, mv, rs = K.prm[:, 0:12].rearrange("p (a b) -> p a b", a=2), K.prm[:, 12:14], K.prm[:, 14:15]
    ss = K.prm[:, 16:24]
    K.x2 = nc.dram_tensor("x2", (T, D), F32, kind="Internal").ap()
    x_in, r_in = [K.sem(f"fe_xin{s}") for s in range(3)], K.sem("fe_rin")
    mm, mev, sq, x2r, ssr, hr, tr, thi, tev, chain = (K.sem("fe_" + n) for n in "mm mev sq x2r ssr hr tr thi tev chain".split())
    stored = [K.sem(f"fe_st{s}") for s in range(2)]
    with nc.Block() as block:
        @block.sync
        def _(sp):
            for r, name in enumerate(("ln2_w", "ln2_b", "norm_mix_2")):
                sp.dma_start(rows[:, r, :], I[name].to_broadcast([P, D])).then_inc(r_in, 16)
            for i in range(NT):
                if i >= 3:
                    sp.wait_ge(x2r, i - 2)
                sp.dma_start(xr[i % 3][:], K.x1[i * P:(i + 1) * P, :]).then_inc(x_in[i % 3], 16)

        @block.gpsimd
        def _(pool):
            for i in range(NT):
                pool.wait_ge(x2r, i + 1)
                pool.dma_start(K.x2[i * P:(i + 1) * P, :], t[i % 2][:]).then_inc(stored[i % 2], 16)
            for s in range(2):
                pool.wait_ge(stored[s], 16 * NT // 2)

        @block.tensor
        def _(pe):
            def back(i):
                if i >= 2:
                    pe.wait_ge(mev, i - 1)
                for k in range(KT):
                    last = nc.tensor.transpose(K.bank[2 * (i % 2) + k // 4][:, (k % 4) * P:(k % 4 + 1) * P],
                                               K.ynT[:, i // 4, k, (i % 4) * P:(i % 4 + 1) * P], K.ident[:])
                last.then_inc(mm, 1)

            def turn(i):
                pe.wait_ge(hr, i + 1)
                if i >= 2:
                    pe.wait_ge(tev, 2 * (i - 1))
                for k in range(KT):
                    last = nc.tensor.transpose(K.bank[4 + 2 * (i % 2) + k // 4][:, (k % 4) * P:(k % 4 + 1) * P],
                                               h[i % 2][:, k * P:(k + 1) * P], K.ident[:])
                last.then_inc(tr, 1)

            for i in range(NT):
                back(i)
                if i:
                    turn(i - 1)
            turn(NT - 1)

        @block.scalar
        def _(act):
            def take(i):
                act.wait_ge(tr, i + 1)
                for b in range(2):
                    nc.scalar.activation(K.h3[0][:, 4 * b:4 * b + 4, i * P:(i + 1) * P],
                                         K.bank[4 + 2 * (i % 2) + b][:].rearrange("p (k t) -> p k t", k=4), ACT.Copy).then_inc(thi, 1)

            for i in range(NT):
                act.wait_ge(sq, 2 * i + 1)
                nc.scalar.activation(rs, rs, ACT.Sqrt).then_inc(sq, 1)
                act.wait_ge(x2r, i + 1)
                if i >= 2:
                    act.wait_ge(tr, i - 1)
                rms_root(K, act, t[i % 2][:], h[i % 2][:], ss[:, i:i + 1], ssr, i)
                if i:
                    take(i - 1)
            take(NT - 1)

        @block.vector
        def _(dve):
            v = nc.vector
            link = Link(v, chain)

            def norm(i):
                x, y = xr[i % 3], t[i % 2]
                dve.wait_ge(mm, i + 1)
                if i >= 2:
                    dve.wait_ge(stored[i % 2], 16 * (i // 2))
                for b in range(2):
                    s = slice(b * HALF, (b + 1) * HALF)
                    last = v.tensor_tensor(y[:, s], K.bank[2 * (i % 2) + b][:], K.MOD[:, 5 * D + b * HALF:5 * D + (b + 1) * HALF], ALU.mult)
                last.then_inc(mev, 1)
                dve.wait_ge(mev, i + 1)
                dve.wait_ge(x_in[i % 3], 16 * (i // 3 + 1))
                link(v.scalar_tensor_tensor(out=y[:], in0=x[:], scalar=ALPHA, in1=y[:], op0=ALU.mult, op1=ALU.add))
                norm_rows(K, dve, link, y, st, mv, rs, sq, i, rows[:, 0, :], rows[:, 1, :]).then_inc(x2r, 1)

            def scale(i):
                dve.wait_ge(ssr, 2 * i + 2)
                link(v.reciprocal(ss[:, i:i + 1], ss[:, i:i + 1]))
                v.scalar_tensor_tensor(out=h[i % 2][:], in0=t[i % 2][:], scalar=ss[:, i:i + 1], in1=rows[:, 2, :],
                                       op0=ALU.mult, op1=ALU.mult).then_inc(hr, 1)

            def low(i):
                for b in range(2):
                    dve.wait_ge(thi, 2 * i + b + 1)
                    at = (slice(None), slice(4 * b, 4 * b + 4), slice(i * P, (i + 1) * P))
                    v.tensor_tensor(K.h3[1][at], K.bank[4 + 2 * (i % 2) + b][:].rearrange("p (k t) -> p k t", k=4), K.h3[0][at].bitcast(F32),
                                    ALU.subtract).then_inc(tev, 1)

            dve.wait_ge(r_in, 48)
            for i in range(NT):
                norm(i)
                if i:
                    scale(i - 1)
                if i >= 2:
                    low(i - 2)
            scale(NT - 1)
            low(NT - 2)
            low(NT - 1)


PJ_KB, FREE_KB, SMALL_KB = 88, 24, 18


def packed(i):
    return slice(P * i * (i + 1) // 2, P * (i + 1) * (i + 2) // 2)


def stage_project(K):
    nc, I = K.nc, K.I
    NR = 4
    K.PJ = K.at("PJ", PJ_KB, [P, 6, NT, HALF])
    K.MS = K.at("MS", 184, [P, NT, N_MIX])
    K.NM = K.at("NM", 0, [P, P * NT * (NT + 1) // 2])
    part = [[K.at(f"pj_part{s}{n}", PJ_KB + 80 + 4 * s + 2 * n, [P, HALF], FR) for n in range(2)] for s in range(NR)]
    raw = [K.at(f"pj_raw{s}", PJ_KB + 80 + 4 * s + 2, [P, HALF]) for s in range(NR)]
    iqT = K.at("pj_iqT", PJ_KB + 32, [P, IH, T])
    ikT = K.at("pj_ikT", PJ_KB + 8, [P, T])
    ikd = K.at("pj_ikd", PJ_KB + 12, [P, NT, P])
    sqr = K.at("pj_sqr", PJ_KB + 16, [P, NT, LAT])
    kvr = K.at("pj_kvr", PJ_KB + 20, [P, LAT])
    scr = K.at("pj_scr", PJ_KB + 22, [P, 2, NT * IH * FREQ_I])
    ang, red, quar, kk = (K.at(f"pj_ang{n}", SMALL_KB + 1.375 * n, [P, NT, NFREQ]) for n in range(4))
    rel = [K.at(f"pj_rel{s}", SMALL_KB + 2 * s, [P, HALF]) for s in range(2)]
    run = K.at("pj_run", SMALL_KB, [P, T])
    flag = K.at("pj_flag", SMALL_KB + 4, [P, T], mybir.dt.uint8)
    junk = K.at("pj_junk", SMALL_KB, [P, P * NT * (NT + 1) // 2], mybir.dt.uint8)
    pscr = K.at("pj_pscr", 197.75, [P, 2, RH * FREQ_R])
    used = [0]

    def columns(n, dt=F32):
        used[0] += n
        c = K.prm[:, used[0] - n:used[0]]
        return c if dt == F32 else c.bitcast(dt)

    NB = NT - 2
    sin, cos = (columns(NT * NFREQ).rearrange("p (i f) -> p i f", i=NT) for _ in range(2))
    freq, pos = columns(NFREQ), columns(NT)
    posi = columns(NT, I32)
    wq = columns(NT * IH).rearrange("p (i h) -> p i h", i=NT)
    ss = columns(NT)
    key, bit, cand, sign, flip, keep = (columns(NB, I32) for _ in range(6))
    cnt, need = columns(NB), columns(NB)
    w_in = [K.sem(f"pj_win{s}") for s in range(NR)]
    names = "prm hi lo um tm ev angr tab rope rms kvr itr iev smm relr used zero key chain pchain".split()
    S = {n: K.sem("pj_" + n) for n in names}
    R_Q, R_K, R_V, R_G, D_Q, D_G = range(6)
    slabs = [None, R_Q, R_K, R_V, R_G, D_Q, D_G]
    pieces = [(i, h, c) for i in range(NT) for h in range(IH) for c in range(0, P * (i + 1), HALF)]

    def table(t, lo, n, heads):
        return t[:, :, lo:lo + n].unsqueeze(2).to_broadcast([P, NT, heads, n])

    with nc.Block() as block:
        @block.sync
        def _(sp):
            w = I["w_in_2"][0].rearrange("(k p) n -> p k n", p=P)
            def load(u, s, *cols):
                if not isinstance(u, int) or u >= NR:
                    sp.wait_ge(S["um"], u - (NR - 1))
                at = 0
                for c, n in cols:
                    sp.dma_start(raw[s % NR][:, at:at + n], w[:, s, c:c + n] if isinstance(c, int) else w[:, s, bass.ds(c, n)]).then_inc(w_in[s % NR], 16)
                    at += n

            for k in range(NR):
                load(k, k, (C_LAT, M_IQ), (C_IDX, N_IDX))
            with nc.allow_non_contiguous_dma(reason="positions as columns"):
                sp.dma_start(posi[:], I["positions_2"].rearrange("(i p) -> p i", p=P)).then_inc(S["prm"], 16)
            sp.dma_start(freq[:], I["freq"].to_broadcast([P, NFREQ])).then_inc(S["prm"], 16)
            sp.dma_start(kvr[:], I["kv_norm_2"].to_broadcast([P, LAT])).then_inc(S["prm"], 16)
            for k in range(NR, KT):
                load(k, k, (C_LAT, M_IQ), (C_IDX, N_IDX))
            with sp.Fori(1, len(slabs) - 1) as j:
                for k in range(KT):
                    load(j * KT + k, k, ((j - 1) * HALF, HALF))
            for k in range(KT):
                load((len(slabs) - 1) * KT + k, k, (C_GATE, HALF))

        @block.tensor
        def _(pe):
            def slab(j):
                cols = N_MIX if isinstance(j, int) and j == 0 else HALF
                for k in range(KT):
                    pe.wait_ge(S["lo"], j * KT + k + 1)
                    for i in range(NT):
                        if k == 0 and (not isinstance(j, int) or j):
                            pe.wait_ge(S["ev"], (j - 1) * NT + i + 1)
                        last = product(nc, K.bank[i][:, 0:cols], [x[:, k, i * P:(i + 1) * P] for x in K.h3], [w[:, 0:cols] for w in part[k % NR]],
                                       k == 0, k == KT - 1)
                        if k == KT - 1 and i < NT - 1:
                            last.then_inc(S["tm"], 1)
                    last.then_inc(S["um"], 1)

            slab(0)
            pe.wait_ge(S["ev"], NT)
            pe.wait_ge(S["rope"], 1)
            for i in range(NT):
                if i >= 4:
                    pe.wait_ge(S["iev"], i - 3)
                b = K.bank[4 + i % 4]
                for m in range(2):
                    nc.tensor.transpose(b[:, m * P:(m + 1) * P], K.MS[:, i, M_IQ + m * P:M_IQ + (m + 1) * P], K.ident[:])
                nc.tensor.transpose(b[:, 2 * P:3 * P], ikd[:, i, :], K.ident[:]).then_inc(S["itr"], 1)
            pe.wait_ge(S["iev"], NT)
            for m, (i, h, c) in enumerate(pieces):
                if m >= 4:
                    pe.wait_ge(S["relr"], m - 3)
                e = min(c + HALF, P * (i + 1))
                nc.tensor.matmul(K.bank[4 + m % 4][:, 0:e - c], iqT[:, h, i * P:(i + 1) * P], ikT[:, c:e],
                                 start=True, stop=True).then_inc(S["smm"], 1)
            pe.wait_ge(S["relr"], len(pieces))
            with pe.Fori(1, len(slabs)) as j:
                slab(j)

        @block.scalar
        def _(act):
            arrived = [0] * NR

            def split(j, ks):
                cols = N_MIX if j == 0 else HALF
                for k in ks:
                    arrived[k % NR] += 32 if j == 0 else 16
                    act.wait_ge(w_in[k % NR], arrived[k % NR])
                    nc.scalar.activation(part[k % NR][0][:, 0:cols], raw[k % NR][:, 0:cols], ACT.Copy).then_inc(S["hi"], 1)

            def take(j):
                if j == len(slabs) - 1:
                    act.wait_ge(S["um"], len(slabs) * KT)
                for i in range(NT):
                    if i < NT - 1:
                        act.wait_ge(S["tm"], j * (NT - 1) + i + 1)
                    else:
                        act.wait_ge(S["um"], (j + 1) * KT)
                    dst = K.MS[:, i, :] if j == 0 else K.PJ[:, slabs[j], i, :]
                    func = ACT.Silu if slabs[j] in (R_G, D_G) else ACT.Copy
                    nc.scalar.activation(dst, K.bank[i][:, 0:N_MIX if j == 0 else HALF], func).then_inc(S["ev"], 1)

            split(0, range(4))
            act.wait_ge(S["angr"], 1)
            nc.scalar.activation(sin[:], red[:], ACT.Sin).then_inc(S["tab"], 1)
            nc.scalar.activation(cos[:], quar[:], ACT.Sin).then_inc(S["tab"], 1)
            split(0, range(4, KT))
            split(1, range(3))
            take(0)
            split(1, range(3, 4))
            act.wait_ge(S["zero"], 1)
            for i in range(NT):
                act.wait_ge(S["itr"], i + 1)
                b = K.bank[4 + i % 4]
                for h in range(4):
                    r = slice(IDIM * h, IDIM * (h + 1))
                    nc.scalar.activation(iqT[r, h::4, i * P:(i + 1) * P], b[r, 0:2 * P].rearrange("p (m t) -> p m t", m=2), ACT.Copy)
                nc.scalar.activation(ikT[:, i * P:(i + 1) * P], b[:, 2 * P:3 * P], ACT.Copy).then_inc(S["iev"], 1)
            act.wait_ge(S["rms"], 1)
            nc.scalar.activation(ss[:], ss[:], ACT.Sqrt).then_inc(S["rms"], 1)
            for m, (i, h, c) in enumerate(pieces):
                act.wait_ge(S["smm"], m + 1)
                if m >= 2:
                    act.wait_ge(S["used"], m - 1)
                e = min(c + HALF, P * (i + 1))
                nc.scalar.activation(rel[m % 2][:, 0:e - c], K.bank[4 + m % 4][:, 0:e - c], ACT.Relu, scale=IDIM ** -0.5).then_inc(S["relr"], 1)
            split(1, range(4, KT))
            for j in range(2, len(slabs)):
                split(j, range(3))
                take(j - 1)
                split(j, range(3, KT))
            take(len(slabs) - 1)

        @block.gpsimd
        def _(pool):
            g = nc.gpsimd
            link = Link(g, S["pchain"])

            def turn(j, lo, n, tiles):
                pool.wait_ge(S["ev"], NT * j + tiles.stop)
                x = K.PJ[:, slabs[j], tiles].rearrange("p i (h e) -> p i h e", h=RH)
                ni = tiles.stop - tiles.start
                t, u = (pscr[:, a, 0:ni * RH * n].rearrange("p (i h f) -> p i h f", i=ni, h=RH) for a in range(2))
                c, s = (x[:, tiles, lo:lo + n].unsqueeze(2).to_broadcast([P, ni, RH, n]) for x in (cos, sin))
                cmul(nc, link, x[:, :, :, 0:n], x[:, :, :, n:2 * n], x[:, :, :, 0:n], x[:, :, :, n:2 * n], c, s, t, u)

            for j in range(len(slabs)):
                cols = N_MIX if j == 0 else HALF
                for k in range(KT):
                    pool.wait_ge(S["hi"], j * KT + k + 1)
                    g.tensor_tensor(part[k % NR][1][:, 0:cols], raw[k % NR][:, 0:cols], part[k % NR][0][:, 0:cols].bitcast(F32), ALU.subtract).then_inc(S["lo"], 1)
                    if k == 0 and j == 1:
                        pool.wait_ge(S["tab"], 2)
                    if k >= 4 and slabs[j - 1] == D_Q:
                        turn(j - 1, FREQ_R, FREQ_A, slice(2 * (k - 4), 2 * (k - 3)))
                    elif k >= 4 and slabs[j - 1] in (R_Q, R_K):
                        for i in range(2 * (k - 4), 2 * (k - 3)):
                            turn(j - 1, 0, FREQ_R, slice(i, i + 1))

        @block.vector
        def _(dve):
            v = nc.vector
            link = Link(v, S["chain"])
            dve.wait_ge(S["prm"], 48)
            link(v.tensor_copy(pos[:], posi[:]))
            link(v.tensor_tensor(ang[:], pos[:].unsqueeze(2).to_broadcast([P, NT, NFREQ]), freq[:].unsqueeze(1).to_broadcast([P, NT, NFREQ]), ALU.mult))
            reduce_angle(nc, link, red[:], quar[:], ang[:], kk[:])
            dve.sem_inc(S["angr"], 1)
            v.memset(iqT[:], 0.0).then_inc(S["zero"], 1)
            dve.wait_ge(S["ev"], NT)
            dve.wait_ge(S["tab"], 2)
            for at, heads, width, lo, n in ((M_IK, 1, IDIM, FREQ_R + FREQ_A, FREQ_I), (M_IQ, IH, IDIM, FREQ_R + FREQ_A, FREQ_I),
                                            (M_PE, 1, PE_D, FREQ_R, FREQ_A)):
                if at == M_PE:
                    for m in range(4):
                        last = v.tensor_copy(ikd[:, :, m * IDIM:(m + 1) * IDIM], K.MS[:, :, M_IK:M_IK + IDIM])
                    last.then_inc(S["rope"], 1)
                x = K.MS[:, :, at:at + heads * width].rearrange("p i (h e) -> p i h e", h=heads)
                t, u = (scr[:, a, 0:NT * heads * n].rearrange("p (i h f) -> p i h f", i=NT, h=heads) for a in range(2))
                cmul(nc, link, x[:, :, :, 0:n], x[:, :, :, n:2 * n], x[:, :, :, 0:n], x[:, :, :, n:2 * n],
                     table(cos, lo, n, heads), table(sin, lo, n, heads), t, u)
            lat = K.MS[:, :, 0:LAT]
            link(v.tensor_tensor(sqr[:], lat, lat, ALU.mult))
            link(v.tensor_reduce(ss[:], sqr[:], AX.X, ALU.add))
            v.tensor_scalar(ss[:], ss[:], 1.0 / LAT, RMS_EPS, ALU.mult, ALU.add).then_inc(S["rms"], 1)
            link(v.tensor_scalar(wq[:], K.MS[:, :, M_IW:M_IW + IH], IH ** -0.5, None, ALU.mult))
            dve.wait_ge(S["rms"], 2)
            link(v.reciprocal(ss[:], ss[:]))
            link(v.tensor_tensor(lat, lat, ss[:].unsqueeze(2).to_broadcast([P, NT, LAT]), ALU.mult))
            link(v.tensor_tensor(lat, lat, kvr[:].unsqueeze(1).to_broadcast([P, NT, LAT]), ALU.mult))
            for m, (i, h, c) in enumerate(pieces):
                dve.wait_ge(S["relr"], m + 1)
                e = min(c + HALF, P * (i + 1))
                dst = K.NM[:, packed(i)][:, c:e]
                if h == 0:
                    ins = v.tensor_scalar(dst, rel[m % 2][:, 0:e - c], wq[:, i, h:h + 1], None, ALU.mult)
                else:
                    ins = v.scalar_tensor_tensor(out=dst, in0=rel[m % 2][:, 0:e - c], scalar=wq[:, i, h:h + 1], in1=dst, op0=ALU.mult, op1=ALU.add)
                ins.then_inc(S["used"], 1)
                dve.wait_ge(S["used"], m + 1)
            for i in range(2):
                link(v.memset(K.NM[:, packed(i)], 0.0))
            for i in range(NT):
                link(v.memset(K.NM[0:RCHUNK, packed(i)][:, P * (i + 1) - RCHUNK:], LOW))
            link(v.memset(key[:], 0))
            link(v.memset(bit[:], 1))
            link(v.tensor_scalar(bit[:], bit[:], 31, None, ALU.logical_shift_left))
            with dve.Fori(0, 32) as r:
                per = 8
                v.tensor_tensor(cand[:], key[:], bit[:], ALU.bitwise_or).then_inc(S["key"], 1)
                dve.wait_ge(S["key"], per * r + 1)
                v.tensor_scalar(sign[:], cand[:], 31, None, ALU.arith_shift_right).then_inc(S["key"], 1)
                dve.wait_ge(S["key"], per * r + 2)
                v.tensor_scalar(flip[:], sign[:], -1, -2147483648, ALU.bitwise_xor, ALU.bitwise_or).then_inc(S["key"], 1)
                dve.wait_ge(S["key"], per * r + 3)
                v.tensor_tensor(flip[:], cand[:], flip[:], ALU.bitwise_xor).then_inc(S["key"], 1)
                dve.wait_ge(S["key"], per * r + 4)
                for j in range(NB):
                    i = j + 2
                    last = v.tensor_scalar(junk[:, packed(i)], K.NM[:, packed(i)], flip[:, j:j + 1].bitcast(F32), 0.0, ALU.is_ge, ALU.add,
                                           accum_out=cnt[:, j:j + 1])
                last.then_inc(S["key"], 1)
                dve.wait_ge(S["key"], per * r + 5)
                v.tensor_scalar(keep[:], cnt[:], TOPK - 0.5, None, ALU.is_ge).then_inc(S["key"], 1)
                dve.wait_ge(S["key"], per * r + 6)
                v.tensor_scalar(bit[:], bit[:], 1, None, ALU.logical_shift_right).then_inc(S["key"], 1)
                v.copy_predicated(key[:], keep[:], cand[:]).then_inc(S["key"], 1)
                dve.wait_ge(S["key"], per * r + 8)
            link(v.tensor_scalar(sign[:], key[:], 31, None, ALU.arith_shift_right))
            link(v.tensor_scalar(flip[:], sign[:], -1, -2147483648, ALU.bitwise_xor, ALU.bitwise_or))
            link(v.tensor_tensor(flip[:], key[:], flip[:], ALU.bitwise_xor))
            for j in range(NB):
                i = j + 2
                n = P * (i + 1)
                thr, x = flip[:, j:j + 1].bitcast(F32), K.NM[:, packed(i)]
                link(v.tensor_scalar(flag[:, 0:n], x, thr, 0.0, ALU.is_gt, ALU.add, accum_out=cnt[:, j:j + 1]))
                link(v.tensor_scalar(need[:, j:j + 1], cnt[:, j:j + 1], -1.0, TOPK + 0.5, ALU.mult, ALU.add))
                link(v.tensor_scalar(flag[:, 0:n], x, thr, None, ALU.is_equal))
                link(v.tensor_tensor_scan(run[:, 0:n], flag[:, 0:n], flag[:, 0:n], 0.0, ALU.add, ALU.max))
                link(v.scalar_tensor_tensor(out=run[:, 0:n], in0=run[:, 0:n], scalar=need[:, j:j + 1], in1=flag[:, 0:n], op0=ALU.is_le, op1=ALU.mult))
                link(v.scalar_tensor_tensor(out=x, in0=x, scalar=thr, in1=run[:, 0:n], op0=ALU.is_gt, op1=ALU.add))
                link(v.tensor_scalar(x, x, 1.0, -LOW, ALU.subtract, ALU.mult))


def stage_retention(K):
    nc, I = K.nc, K.I
    J = RH // 2
    qT, kT, xq, rkz = ([K.at(f"rt_{n}{s}", kb + 2 * s, [P, J, P]) for s in range(2)]
                       for n, kb in (("qT", 24), ("kT", 28), ("xq", 32), ("kz", 44)))
    prob = [K.at(f"rt_prob{s}", 36 + 4 * s, [P, J, 2, P]) for s in range(2)]
    state = [K.at(f"rt_state{s}", 48 + s, [P, J, RD]) for s in range(2)]
    intra = K.at("rt_intra", 50, [P, J, 2, P])
    xi = K.at("rt_xi", 54, [P, J, P])
    row = K.at("rt_row", SMALL_KB, [P, HALF])
    sqr = K.at("rt_sqr", 72, [P, RH, RD])
    K.dqT = K.at("dqT", 56, [P, J, T])
    zeta, decay = K.prm[:, 0:RH], K.prm[:, 8:8 + J]
    mu, var = (K.prm[:, 16 + RH * n:16 + RH * (n + 1)] for n in range(2))
    names = "const tr qkr dqr smm prob xqr kzr out oev upd state var gate norm done chain".split()
    S = {n: K.sem("rt_" + n) for n in names}
    R_Q, R_K, R_V, R_G, D_Q, D_G = range(6)

    with nc.Block() as block:
        @block.sync
        def _(sp):
            sp.dma_start(intra[:], I["intra"].rearrange("p (j a) t -> p j a t", a=2)).then_inc(S["const"], 16)
            sp.dma_start(xi[:], I["xi"]).then_inc(S["const"], 16)
            sp.dma_start(zeta, I["zeta"]).then_inc(S["const"], 16)
            sp.dma_start(decay, I["decay"]).then_inc(S["const"], 16)
            sp.dma_start(row[:], I["ret_norm_2"].to_broadcast([P, HALF])).then_inc(S["const"], 16)

        @block.tensor
        def _(pe):
            def turn(i):
                if i:
                    pe.wait_ge(S["qkr"], 2 * i)
                    pe.wait_ge(S["dqr"], i)
                for b, slab in enumerate((R_Q, R_K, D_Q)):
                    for j in range(J):
                        tr = nc.tensor.transpose(K.bank[b][:, j * P:(j + 1) * P], K.PJ[:, slab, i, j * P:(j + 1) * P], K.ident[:])
                    tr.then_inc(S["tr"], 1)

            turn(0)
            for i in range(NT):
                s = i % 2
                pe.wait_ge(S["qkr"], 2 * (i + 1))
                if i:
                    pe.wait_ge(S["prob"], i)
                for h in range(RH):
                    d = slice(RD * (h % 2), RD * (h % 2 + 1))
                    mm = nc.tensor.matmul(K.bank[3 + h % 2][:, (h // 2) * P:(h // 2 + 1) * P], kT[s][d, h // 2, :], qT[s][d, h // 2, :],
                                          start=True, stop=True)
                mm.then_inc(S["smm"], 1)
                if i + 1 < NT:
                    turn(i + 1)
                    pe.wait_ge(S["kzr"], i + 1)
                    if i:
                        pe.wait_ge(S["state"], i)
                    for j in range(J):
                        mm = nc.tensor.matmul(K.bank[7][:, j * P:(j + 1) * P], rkz[s][:, j, :], K.PJ[:, R_V, i, j * P:(j + 1) * P],
                                              start=True, stop=True)
                    mm.then_inc(S["upd"], 1)
                pe.wait_ge(S["prob"], i + 1)
                if i:
                    pe.wait_ge(S["xqr"], i + 1)
                    pe.wait_ge(S["state"], i)
                    pe.wait_ge(S["oev"], i)
                for h in range(RH):
                    o = K.bank[5 + h % 2][:, (h // 2) * RD:(h // 2 + 1) * RD]
                    d = slice(RD * (h % 2), RD * (h % 2 + 1))
                    mm = nc.tensor.matmul(o, prob[s][:, h // 2, h % 2, :], K.PJ[:, R_V, i, h * RD:(h + 1) * RD], start=True, stop=(i == 0))
                    if i:
                        mm = nc.tensor.matmul(o, xq[s][d, h // 2, :], state[s][d, h // 2, :], start=False, stop=True)
                mm.then_inc(S["out"], 1)

        @block.scalar
        def _(act):
            def take(i):
                if i >= 2:
                    act.wait_ge(S["xqr"], i - 1)
                act.wait_ge(S["tr"], 3 * i + 3)
                for b, dst in enumerate((qT[i % 2], kT[i % 2])):
                    nc.scalar.activation(dst[:], K.bank[b][:].rearrange("p (j t) -> p j t", j=J), ACT.Copy).then_inc(S["qkr"], 1)
                nc.scalar.activation(K.dqT[:, :, i * P:(i + 1) * P], K.bank[2][:].rearrange("p (j t) -> p j t", j=J), ACT.Copy).then_inc(S["dqr"], 1)

            take(0)
            for i in range(NT):
                if i + 1 < NT:
                    take(i + 1)
                act.wait_ge(S["out"], i + 1)
                for b in range(2):
                    ev = nc.scalar.activation(K.PJ[:, R_Q, i, :].rearrange("p (j a d) -> p j a d", a=2, d=RD)[:, :, b, :],
                                              K.bank[5 + b][:, 0:J * RD].rearrange("p (j d) -> p j d", j=J), ACT.Copy)
                ev.then_inc(S["oev"], 1)
                act.wait_ge(S["var"], 2 * i + 1)
                nc.scalar.activation(var, var, ACT.Sqrt).then_inc(S["var"], 1)

        @block.gpsimd
        def _(pool):
            g = nc.gpsimd
            pool.wait_ge(S["const"], 80)
            for i in range(NT):
                s = i % 2
                if i + 1 < NT:
                    if i >= 2:
                        pool.wait_ge(S["upd"], i - 1)
                    g.tensor_tensor(rkz[s][:].rearrange("p j (a d) -> p (j a) d", a=2), K.PJ[:, R_K, i, :].rearrange("p (h d) -> p h d", h=RH),
                                    zeta.unsqueeze(2).to_broadcast([P, RH, RD]), ALU.mult).then_inc(S["kzr"], 1)
                pool.wait_ge(S["qkr"], 2 * i + 1)
                if i >= 2:
                    pool.wait_ge(S["out"], i - 1)
                g.tensor_tensor(xq[s][:], qT[s][:], xi[:], ALU.mult).then_inc(S["xqr"], 1)
                g.tensor_tensor(K.PJ[:, R_G, i, :], K.PJ[:, R_G, i, :], row[:], ALU.mult).then_inc(S["gate"], 1)
                if i:
                    pool.wait_ge(S["gate"], i)
                    pool.wait_ge(S["norm"], i)
                    g.tensor_tensor(K.PJ[:, R_Q, i - 1, :], K.PJ[:, R_Q, i - 1, :], K.PJ[:, R_G, i - 1, :], ALU.mult).then_inc(S["done"], 1)
            pool.wait_ge(S["norm"], NT)
            pool.wait_ge(S["gate"], NT)
            g.tensor_tensor(K.PJ[:, R_Q, NT - 1, :], K.PJ[:, R_Q, NT - 1, :], K.PJ[:, R_G, NT - 1, :], ALU.mult).then_inc(S["done"], 1)

        @block.vector
        def _(dve):
            v = nc.vector
            link = Link(v, S["chain"])

            def norm(i):
                o = K.PJ[:, R_Q, i, :].rearrange("p (h d) -> p h d", h=RH)
                dve.wait_ge(S["oev"], i + 1)
                link(v.tensor_reduce(mu, o, AX.X, ALU.add))
                link(v.tensor_scalar(mu, mu, 1.0 / RD, None, ALU.mult))
                link(v.tensor_tensor(o, o, mu.unsqueeze(2).to_broadcast([P, RH, RD]), ALU.subtract))
                link(v.tensor_tensor(sqr[:], o, o, ALU.mult))
                link(v.tensor_reduce(var, sqr[:], AX.X, ALU.add))
                v.tensor_scalar(var, var, 1.0 / RD, RMS_EPS, ALU.mult, ALU.add).then_inc(S["var"], 1)
                dve.wait_ge(S["var"], 2 * i + 2)
                link(v.reciprocal(var, var))
                v.tensor_tensor(o, o, var.unsqueeze(2).to_broadcast([P, RH, RD]), ALU.mult).then_inc(S["norm"], 1)

            dve.wait_ge(S["const"], 80)
            for i in range(NT):
                s = i % 2
                dve.wait_ge(S["smm"], i + 1)
                if i >= 2:
                    dve.wait_ge(S["out"], i - 1)
                for a in range(2):
                    pr = v.tensor_tensor(prob[s][:, :, a, :], K.bank[3 + a][:].rearrange("p (j t) -> p j t", j=J), intra[:, :, a, :], ALU.mult)
                pr.then_inc(S["prob"], 1)
                if i + 1 < NT:
                    new = state[1 - s]
                    if i:
                        link(v.tensor_tensor(new[:], state[s][:], decay.unsqueeze(2).to_broadcast([P, J, RD]), ALU.mult))
                    dve.wait_ge(S["upd"], i + 1)
                    b = K.bank[7][:].rearrange("p (j c) -> p j c", j=J)
                    for a in range(2):
                        d = slice(RD * a, RD * (a + 1))
                        if i:
                            up = v.tensor_tensor(new[d], new[d], b[d, :, d], ALU.add)
                        else:
                            up = v.tensor_copy(new[d], b[d, :, d])
                    up.then_inc(S["state"], 1)
                    dve.wait_ge(S["state"], i + 1)
                if i:
                    norm(i - 1)
            norm(NT - 1)


def stage_attention(K):
    nc, I = K.nc, K.I
    J = AH // 2
    kfT = K.at("at_kT", 24, [P, J, T])
    val = K.at("at_v", 40, [P, NT, AH * AD])
    prob = [K.at(f"at_prob{s}", 72 + 4 * s, [P, T]) for s in range(2)]
    probT = [K.at(f"at_probT{s}", 80 + 4 * s, [P, NT, P]) for s in range(2)]
    latT = K.at("at_latT", 80, [P, T])
    peT = K.at("at_peT", 84, [P, T])
    ukT = K.at("at_ukT", SMALL_KB, [P, J, P])
    wuv = K.at("at_wuv", SMALL_KB + 2, [P, AH, AD])
    spread = K.at("at_spread", SMALL_KB + 4, [P, 2, AD])
    qpad = [K.at(f"at_qpad{s}", 184 + 4 * s, [P, AH, P]) for s in range(2)]
    outT = [K.at(f"at_outT{s}", SMALL_KB + 4.5 + 0.5 * s, [P, P]) for s in range(2)]
    uk = K.wsT
    den = K.prm[:, 0:NT * AH].rearrange("p (i h) -> p i h", i=NT)
    top = K.prm[:, 64:64 + 2]
    K.w_end = [[K.at(f"w_end{b}{n}", PJ_KB + 16 + 32 * b + 16 * n, [P, KT, HALF], FR) for n in range(2)] for b in range(2)]
    K.raw_end = [K.at(f"raw_end{b}", PJ_KB + 32 + 32 * b, [P, KT, HALF]) for b in range(2)]
    w_in = [K.sem(f"at_win{b}") for b in range(2)]
    names = "zero uk wuv spread qzero qpad whi wlo turn ukr latr pre prer lmm logit mx er tr pa pd pv ot back done chain".split()
    S = {n: K.sem("at_" + n) for n in names}
    R_Q, R_K, R_V, R_G, D_Q, D_G = range(6)
    steps = [(i, h) for i in range(NT) for h in range(AH)]
    long_before = lambda n: sum(i >= 4 for i, h in steps[:n])
    n_pre = 2 * J + NT

    with nc.Block() as block:
        @block.sync
        def _(sp):
            sp.wait_ge(S["zero"], 2)
            for h in range(AH):
                sp.dma_start(uk[AD * (h % 2) + PE_D:AD * (h % 2 + 1), h // 2, :], I["w_uk_2"][0, h]).then_inc(S["uk"], 16)
            with nc.allow_non_contiguous_dma(reason="latent to partitions"):
                sp.dma_start(wuv[:], I["w_uv_2"][0].rearrange("h c d -> c h d")).then_inc(S["wuv"], 16)
            for b in range(2):
                sp.dma_start(K.raw_end[b][:], I["w_out_2"][0].rearrange("(k p) n -> p k n", p=P)[:, :, b * HALF:(b + 1) * HALF]).then_inc(w_in[b], 16)

        @block.gpsimd
        def _(pool):
            nc.gpsimd.memset(spread[:], 0.0).then_inc(S["zero"], 1)
            nc.gpsimd.memset(uk[:], 0.0).then_inc(S["zero"], 1)
            pool.wait_ge(S["turn"], NT)
            for q in qpad:
                nc.gpsimd.memset(q[:], 0.0).then_inc(S["qzero"], 1)
            pool.wait_ge(S["qzero"], 2)

            def pad(i):
                if i >= 2:
                    pool.wait_ge(S["lmm"], AH * (i - 1))
                for a in range(2):
                    d = slice(AD * a, AD * (a + 1))
                    nc.gpsimd.tensor_copy(qpad[i % 2][d, a::2, :], K.dqT[d, :, i * P:(i + 1) * P]).then_inc(S["qpad"], 1)
                pool.wait_ge(S["qpad"], 2 * (i + 1))

            pad(0)
            pad(1)
            for m in range((NT - 2) * AH):
                if m % AH == 0:
                    if m:
                        pool.wait_ge(S["wlo"], min(m, 2 * KT))
                    pad(m // AH + 2)
                if m >= 2 * KT:
                    continue
                pool.wait_ge(S["whi"], m + 1)
                b, k = m // KT, m % KT
                nc.gpsimd.tensor_tensor(K.w_end[b][1][:, k, :], K.raw_end[b][:, k, :], K.w_end[b][0][:, k, :].bitcast(F32), ALU.subtract).then_inc(S["wlo"], 1)

        @block.tensor
        def _(pe):
            for i in range(NT):
                if i >= 4:
                    pe.wait_ge(S["latr"], i - 3)
                b = K.bank[i % 4]
                nc.tensor.transpose(b[:, 0:P], K.MS[:, i, 0:LAT], K.ident[:])
                nc.tensor.transpose(b[:, P:2 * P], K.MS[:, i, M_PE:M_PE + P], K.ident[:]).then_inc(S["turn"], 1)
            pe.wait_ge(S["uk"], 16 * AH)
            for j in range(J):
                tr = nc.tensor.transpose(K.bank[4][:, j * P:(j + 1) * P], uk[:, j, :], K.ident[:])
            tr.then_inc(S["ukr"], 1)
            pe.wait_ge(S["latr"], NT)
            pe.wait_ge(S["wuv"], 16)
            n = 0
            for i in range(NT):
                if n >= 4:
                    pe.wait_ge(S["prer"], n - 3)
                nc.tensor.matmul(K.bank[n % 4][:], latT[:, i * P:(i + 1) * P], wuv[:].rearrange("p h d -> p (h d)"),
                                 start=True, stop=True).then_inc(S["pre"], 1)
                n += 1
            pe.wait_ge(S["ukr"], 2)
            pe.wait_ge(S["spread"], 2)
            for j in range(J):
                for c in range(0, T, HALF):
                    pe.wait_ge(S["prer"], n - 3)
                    nc.tensor.matmul(K.bank[n % 4][:], ukT[:, j, :], latT[:, c:c + HALF], start=True, stop=False)
                    nc.tensor.matmul(K.bank[n % 4][:], spread[:].rearrange("p a d -> p (a d)"), peT[:, c:c + HALF],
                                     start=False, stop=True).then_inc(S["pre"], 1)
                    n += 1
            pe.wait_ge(S["prer"], n_pre)

            def logits(n):
                i, h = steps[n]
                if h == 0:
                    pe.wait_ge(S["qpad"], 2 * (i + 1))
                if n >= 2:
                    pe.wait_ge(S["logit"], n - 1)
                for c in range(0, P * (i + 1), HALF):
                    e = min(c + HALF, P * (i + 1))
                    mm = nc.tensor.matmul(K.bank[2 * (h % 2) + c // HALF][:, 0:e - c], qpad[i % 2][:, h, :], kfT[:, h // 2, c:e],
                                          start=True, stop=True)
                mm.then_inc(S["lmm"], 1)

            def turn(n):
                i, h = steps[n]
                pe.wait_ge(S["er"], n + 1)
                if n:
                    pe.wait_ge(S["pa"], n)
                    if long_before(n):
                        pe.wait_ge(S["pd"], long_before(n))
                for t in range(i + 1):
                    tr = nc.tensor.transpose(K.bank[4 + t // 4][:, (t % 4) * P:(t % 4 + 1) * P], prob[n % 2][:, t * P:(t + 1) * P], K.ident[:])
                tr.then_inc(S["tr"], 1)

            def values(n):
                i, h = steps[n]
                pe.wait_ge(S["pa"], n + 1)
                if i >= 4:
                    pe.wait_ge(S["pd"], long_before(n + 1))
                pair = n // 2
                if h % 2 == 0 and pair:
                    pe.wait_ge(S["ot"], pair)
                d = slice(AD * (h % 2), AD * (h % 2 + 1))
                for t in range(i + 1):
                    mm = nc.tensor.matmul(K.bank[6][d, 0:P], val[:, t, h * AD:(h + 1) * AD], probT[n % 2][:, t, :],
                                          start=(t == 0), stop=(t == i))
                mm.then_inc(S["pv"], 1)

            def back(pair):
                i, j = pair // J, pair % J
                pe.wait_ge(S["ot"], pair + 1)
                if j == 0 and i:
                    pe.wait_ge(S["done"], i)
                nc.tensor.transpose(K.bank[7][:, j * P:(j + 1) * P], outT[pair % 2][:], K.ident[:]).then_inc(S["back"], 1)

            logits(0)
            for n in range(len(steps)):
                if n + 1 < len(steps):
                    logits(n + 1)
                turn(n)
                if n:
                    values(n - 1)
                if n >= 4 and n % 2 == 0:
                    back(n // 2 - 2)
            values(len(steps) - 1)
            back(len(steps) // 2 - 2)
            back(len(steps) // 2 - 1)

        @block.scalar
        def _(act):
            for i in range(NT):
                act.wait_ge(S["turn"], i + 1)
                b = K.bank[i % 4]
                nc.scalar.activation(latT[:, i * P:(i + 1) * P], b[:, 0:P], ACT.Copy)
                nc.scalar.activation(peT[:, i * P:(i + 1) * P], b[:, P:2 * P], ACT.Copy).then_inc(S["latr"], 1)
            act.wait_ge(S["ukr"], 1)
            nc.scalar.activation(ukT[:], K.bank[4][:].rearrange("p (j r) -> p j r", j=J), ACT.Copy).then_inc(S["ukr"], 1)
            for n in range(n_pre):
                act.wait_ge(S["pre"], n + 1)
                m = n - NT
                dst = val[:, n, :] if n < NT else kfT[:, m // 2, (m % 2) * HALF:(m % 2 + 1) * HALF]
                nc.scalar.activation(dst, K.bank[n % 4][:], ACT.Copy).then_inc(S["prer"], 1)

            def expo(n):
                i, h = steps[n]
                act.wait_ge(S["mx"], n + 1)
                x = prob[n % 2][:, 0:P * (i + 1)]
                nc.scalar.activation(x, x, ACT.Exp, bias=top[:, n % 2:n % 2 + 1], accum_out=den[:, i, h:h + 1]).then_inc(S["er"], 1)

            def take(n):
                i, h = steps[n]
                act.wait_ge(S["tr"], n + 1)
                if n >= 2:
                    act.wait_ge(S["pv"], n - 1)
                c = min(i + 1, 4)
                nc.scalar.activation(probT[n % 2][:, 0:c, :], K.bank[4][:, 0:c * P].rearrange("p (s t) -> p s t", s=c), ACT.Copy).then_inc(S["pa"], 1)

            expo(0)
            for n in range(len(steps)):
                if n + 1 < len(steps):
                    expo(n + 1)
                take(n)
                m = n - AH
                if 0 <= m < 2 * KT:
                    act.wait_ge(w_in[m // KT], 16)
                    nc.scalar.activation(K.w_end[m // KT][0][:, m % KT, :], K.raw_end[m // KT][:, m % KT, :], ACT.Copy).then_inc(S["whi"], 1)

        @block.vector
        def _(dve):
            v = nc.vector
            link = Link(v, S["chain"])
            dve.wait_ge(S["zero"], 1)
            for a in range(2):
                v.tensor_copy(spread[0:PE_D, a, 0:PE_D], K.ident[0:PE_D, 0:PE_D]).then_inc(S["spread"], 1)

            def logit(n):
                i, h = steps[n]
                w = P * (i + 1)
                dve.wait_ge(S["lmm"], n + 1)
                if n >= 2:
                    dve.wait_ge(S["tr"], n - 1)
                b = K.ps[:, 2 * (h % 2):2 * (h % 2) + 2, :].rearrange("p b c -> p (b c)")
                mx = top[:, n % 2:n % 2 + 1]
                v.tensor_tensor_reduce(out=prob[n % 2][:, 0:w], in0=b[:, 0:w], in1=K.NM[:, packed(i)], scale=AD ** -0.5, scalar=LOW,
                                       op0=ALU.add, op1=ALU.max, accum_out=mx).then_inc(S["logit"], 1)
                dve.wait_ge(S["logit"], n + 1)
                v.tensor_scalar(mx, mx, -1.0, None, ALU.mult).then_inc(S["mx"], 1)

            def take(n):
                i, h = steps[n]
                if i < 4:
                    return
                dve.wait_ge(S["tr"], n + 1)
                dve.wait_ge(S["pv"], n - 1)
                c = i + 1 - 4
                v.tensor_copy(probT[n % 2][:, 4:4 + c, :], K.bank[5][:, 0:c * P].rearrange("p (s t) -> p s t", s=c)).then_inc(S["pd"], 1)

            def pair_out(pair):
                dve.wait_ge(S["pv"], 2 * (pair + 1))
                if pair >= 2:
                    dve.wait_ge(S["back"], pair - 1)
                v.tensor_copy(outT[pair % 2][:], K.bank[6][:, 0:P]).then_inc(S["ot"], 1)

            def finish(i):
                dve.wait_ge(S["back"], J * (i + 1))
                g = K.PJ[:, D_G, i, :]
                v.tensor_tensor(g, K.bank[7][:], g, ALU.mult).then_inc(S["done"], 1)
                dve.wait_ge(S["done"], i + 1)
                link(v.reciprocal(den[:, i, :], den[:, i, :]))
                g = g.rearrange("p (h d) -> p h d", h=AH)
                link(v.tensor_tensor(g, g, den[:, i, :].unsqueeze(2).to_broadcast([P, AH, AD]), ALU.mult))

            dve.wait_ge(S["prer"], n_pre)
            logit(0)
            for n in range(len(steps)):
                if n + 1 < len(steps):
                    logit(n + 1)
                take(n)
                if n >= 2 and n % 2 == 0:
                    pair_out(n // 2 - 1)
                if n >= AH and n % AH == AH // 2:
                    finish(n // AH - 1)
            pair_out(len(steps) // 2 - 1)
            finish(NT - 1)


def stage_second_end(K):
    nc, I = K.nc, K.I
    MIX = (K.PJ[:, 0], K.PJ[:, 5])
    w = K.w_end
    hT = [K.at(f"se_hT{n}", FREE_KB + 32 * n, [P, KT, T], FR) for n in range(2)]
    X = [K.at(f"se_x{g}", PJ_KB + 80 * g, [P, NT // 2, D]) for g in range(2)]
    w_proj = K.at("w_proj", 0, [P, 2, D])
    pT = K.at("se_pT", 8, [P, 2, T])
    rows = K.at("se_rows", 16, [P, 2, D])
    pn = K.at("se_pn", 184, [P, NT, 2, P])
    h = [K.at(f"se_h{s}", 184 + 4 * s, [P, D]) for s in range(2)]
    gate = [K.at(f"se_gate{s}", 192 + 2 * s, [P, HALF]) for s in range(2)]
    ss, ss2 = K.prm[:, 0:NT], K.prm[:, NT:2 * NT]
    p_in, r_in, wp_in, stored = (K.sem("se_" + n) for n in ("pin", "rin", "wpin", "stored"))
    x_in, g_in = [K.sem(f"se_xin{q}") for q in range(4)], [K.sem(f"se_gin{q}") for q in range(4)]
    names = "mtr mhi mlo ptr ptev omm oev ssr hr htr hhi hlo ghi glo pmm gmm gr used x4 ssr2 outr chain".split()
    S = {n: K.sem("se_" + n) for n in names}

    def x3(i):
        return X[i // 4][:, i % 4, :]

    def tile_of(t, i, b):
        return t[:, 4 * b:4 * b + 4, i * P:(i + 1) * P]

    def wide(bank):
        return bank[:].rearrange("p (k t) -> p k t", k=4)

    with nc.Block() as block:
        @block.sync
        def _(sp):
            sp.dma_start(pn[:], I["p_2"][0, 0].rearrange("(i p) (k c) -> p i k c", p=P, k=2)).then_inc(p_in, 16)
            sp.dma_start(rows[:, 0, :], I["norm_ple_2"].to_broadcast([P, D])).then_inc(r_in, 16)
            sp.dma_start(rows[:, 1, :], I["norm_final_2"].unsqueeze(0).to_broadcast([P, D])).then_inc(r_in, 16)
            sp.wait_ge(S["mtr"], NT)
            for q in range(4):
                sp.dma_start(X[q // 2][:, 2 * (q % 2):2 * (q % 2) + 2, :],
                             K.x2[2 * q * P:2 * (q + 1) * P, :].rearrange("(i p) n -> p i n", p=P)).then_inc(x_in[q], 16)
            sp.dma_start(w_proj[:], I["w_ple_proj_2"][0].rearrange("(k p) n -> p k n", p=P)).then_inc(wp_in, 16)
            for q in range(4):
                b, k = q // 2, slice(4 * (q % 2), 4 * (q % 2) + 4)
                sp.wait_ge(S["omm"], NT * (b + 1))
                sp.dma_start(K.raw_end[b][:, k, :],
                             I["w_ple_gate_2"][0].rearrange("(k p) n -> p k n", p=P)[:, k, b * HALF:(b + 1) * HALF]).then_inc(g_in[q], 16)
            for i in range(NT):
                sp.wait_ge(S["outr"], i + 1)
                sp.dma_start(K.out[0, i * P:(i + 1) * P, :], x3(i)).then_inc(stored, 16)
            sp.wait_ge(stored, 16 * NT)

        @block.gpsimd
        def _(pool):
            for b in range(2):
                for k in range(KT):
                    pool.wait_ge(S["ghi"], KT * b + k + 1)
                    nc.gpsimd.tensor_tensor(w[b][1][:, k, :], K.raw_end[b][:, k, :], w[b][0][:, k, :].bitcast(F32), ALU.subtract).then_inc(S["glo"], 1)

        @block.tensor
        def _(pe):
            def output(b, i):
                n = NT * b + i
                if n >= 4:
                    pe.wait_ge(S["oev"], n - 3)
                for k in range(KT):
                    last = product(nc, K.bank[4 + n % 4][:], [x[:, k, i * P:(i + 1) * P] for x in hT], [x[:, k, :] for x in w[b]],
                                   k == 0, k == KT - 1)
                last.then_inc(S["omm"], 1)

            def turn(i):
                pe.wait_ge(S["hr"], i + 1)
                if i < 2:
                    pe.wait_ge(S["ptev"], 4)
                else:
                    pe.wait_ge(S["hlo"], 2 * (i - 1))
                for k in range(KT):
                    tr = nc.tensor.transpose(K.bank[2 * (i % 2) + k // 4][:, (k % 4) * P:(k % 4 + 1) * P], h[i % 2][:, k * P:(k + 1) * P], K.ident[:])
                tr.then_inc(S["htr"], 1)

            def gates(b, i):
                n = NT * b + i
                if n < 2:
                    pe.wait_ge(S["oev"], 2 * NT)
                else:
                    pe.wait_ge(S["used"], n - 1)
                for k in range(2):
                    mm = nc.tensor.matmul(K.bank[4 + n % 2][:], pT[:, k, i * P:(i + 1) * P], w_proj[:, k, b * HALF:(b + 1) * HALF], start=(k == 0), stop=(k == 1))
                mm.then_inc(S["pmm"], 1)
                if b == 0:
                    pe.wait_ge(S["hlo"], 2 * (i + 1))
                if n >= 2:
                    pe.wait_ge(S["gr"], n - 1)
                for k in range(KT):
                    if i == 0:
                        pe.wait_ge(S["glo"], KT * b + k + 1)
                    last = product(nc, K.bank[6 + n % 2][:], [x[:, k, i * P:(i + 1) * P] for x in hT], [x[:, k, :] for x in w[b]],
                                   k == 0, k == KT - 1)
                last.then_inc(S["gmm"], 1)

            for i in range(NT):
                if i >= 4:
                    pe.wait_ge(S["mlo"], 2 * (i - 3))
                for k in range(KT):
                    tr = nc.tensor.transpose(K.bank[2 * (i % 4) + k // 4][:, (k % 4) * P:(k % 4 + 1) * P], MIX[k // 4][:, i, (k % 4) * P:(k % 4 + 1) * P], K.ident[:])
                tr.then_inc(S["mtr"], 1)
            pe.wait_ge(p_in, 16)
            pe.wait_ge(S["mlo"], 2 * 6)
            for b in range(4):
                for m in range(2):
                    for k in range(2):
                        tr = nc.tensor.transpose(K.bank[b][:, (2 * k + m) * P:(2 * k + m + 1) * P], pn[:, 2 * b + m, k, :], K.ident[:])
                tr.then_inc(S["ptr"], 1)
            pe.wait_ge(S["mlo"], 2 * NT)
            for i in range(NT):
                output(0, i)
            for i in range(NT):
                output(1, i)
                if i >= 2:
                    turn(i - 2)
            pe.wait_ge(wp_in, 16)
            for i in range(NT):
                gates(0, i)
                if i < 2:
                    turn(NT - 2 + i)
            for i in range(NT):
                gates(1, i)

        @block.scalar
        def _(act):
            def high(done, i, banks, sem):
                act.wait_ge(done, i + 1)
                for b in range(2):
                    nc.scalar.activation(tile_of(hT[0], i, b), wide(K.bank[banks + b]), ACT.Copy).then_inc(sem, 1)

            def split(b, k):
                act.wait_ge(g_in[2 * b + k // 4], 16)
                nc.scalar.activation(w[b][0][:, k, :], K.raw_end[b][:, k, :], ACT.Copy).then_inc(S["ghi"], 1)

            def sigmoid(b, i):
                n = NT * b + i
                act.wait_ge(S["gmm"], n + 1)
                if n >= 2:
                    act.wait_ge(S["x4"], n - 1)
                nc.scalar.activation(gate[n % 2][:], K.bank[6 + n % 2][:], ACT.Sigmoid).then_inc(S["gr"], 1)

            for i in range(NT):
                high(S["mtr"], i, 2 * (i % 4), S["mhi"])
            for b in range(4):
                act.wait_ge(S["ptr"], b + 1)
                nc.scalar.activation(pT[:, :, 2 * b * P:2 * (b + 1) * P], K.bank[b][:].rearrange("p (k t) -> p k t", k=2), ACT.Copy).then_inc(S["ptev"], 1)
            for i in range(NT):
                act.wait_ge(S["oev"], NT + i + 1)
                if i >= 2:
                    act.wait_ge(S["htr"], i - 1)
                rms_root(K, act, x3(i), h[i % 2][:], ss[:, i:i + 1], S["ssr"], i)
                if i >= 2:
                    high(S["htr"], i - 2, 2 * (i % 2), S["hhi"])
                split(0, i)
            for i in range(NT):
                if i < 2:
                    high(S["htr"], NT - 2 + i, 2 * (i % 2), S["hhi"])
                split(1, i)
                sigmoid(0, i)
            for i in range(NT):
                sigmoid(1, i)
                act.wait_ge(S["x4"], NT + i + 1)
                rms_root(K, act, x3(i), h[i % 2][:], ss2[:, i:i + 1], S["ssr2"], i)

        @block.vector
        def _(dve):
            v = nc.vector
            link = Link(v, S["chain"])

            def low(done, i, banks, sem):
                for b in range(2):
                    dve.wait_ge(done, 2 * i + b + 1)
                    v.tensor_tensor(tile_of(hT[1], i, b), wide(K.bank[banks + b]), tile_of(hT[0], i, b).bitcast(F32), ALU.subtract).then_inc(sem, 1)

            def residual(b, i):
                n = NT * b + i
                x = x3(i)[:, b * HALF:(b + 1) * HALF]
                if b == 0 and i % 2 == 0:
                    dve.wait_ge(x_in[i // 2], 16)
                dve.wait_ge(S["omm"], n + 1)
                v.tensor_tensor(x, K.bank[4 + n % 4][:], x, ALU.add).then_inc(S["oev"], 1)

            def scale(i, dst, root, col, row, sem):
                dve.wait_ge(root, 2 * i + 2)
                link(v.reciprocal(col[:, i:i + 1], col[:, i:i + 1]))
                v.scalar_tensor_tensor(out=dst, in0=x3(i), scalar=col[:, i:i + 1], in1=rows[:, row, :], op0=ALU.mult, op1=ALU.mult).then_inc(sem, 1)

            def add_gated(b, i):
                n = NT * b + i
                g, x = gate[n % 2], x3(i)[:, b * HALF:(b + 1) * HALF]
                dve.wait_ge(S["gr"], n + 1)
                dve.wait_ge(S["pmm"], n + 1)
                v.tensor_tensor(g[:], K.bank[4 + n % 2][:], g[:], ALU.mult).then_inc(S["used"], 1)
                dve.wait_ge(S["used"], n + 1)
                v.tensor_tensor(x, x, g[:], ALU.add).then_inc(S["x4"], 1)

            for i in range(NT):
                low(S["mhi"], i, 2 * (i % 4), S["mlo"])
            for i in range(NT):
                residual(0, i)
            dve.wait_ge(r_in, 32)
            for i in range(NT):
                residual(1, i)
                if i:
                    scale(i - 1, h[(i - 1) % 2][:], S["ssr"], ss, 0, S["hr"])
                if i >= 2:
                    low(S["hhi"], i - 2, 2 * (i % 2), S["hlo"])
            scale(NT - 1, h[1][:], S["ssr"], ss, 0, S["hr"])
            for i in range(NT):
                if i < 2:
                    low(S["hhi"], NT - 2 + i, 2 * (i % 2), S["hlo"])
                add_gated(0, i)
            for i in range(NT):
                add_gated(1, i)
                if i:
                    scale(i - 1, x3(i - 1), S["ssr2"], ss2, 1, S["outr"])
            scale(NT - 1, x3(NT - 1), S["ssr2"], ss2, 1, S["outr"])


STAGES = (stage_modulate, stage_s5, stage_mixers, stage_join, stage_ffn, stage_first_end,
          stage_project, stage_retention, stage_attention, stage_second_end)


def build(nc, I, out):
    K = setup(nc, I, out)
    for stage in STAGES:
        stage(K)
        if stage is stage_first_end:
            nc.clear_and_free_semaphores(K.sems)
            nc.all_engine_barrier()


def kernel(**inputs):
    import concourse.bacc as bacc
    from concourse.bass_utils import run_bass_kernel_spmd

    nc = bacc.Bacc("TRN2", target_bir_lowering=False, num_devices=1)
    arrays = {f"in_{name}": np.ascontiguousarray(a) for name, a in {**inputs, **constants()}.items()}
    I = {name[3:]: nc.dram_tensor(name, a.shape, mybir.dt.from_np(a.dtype), kind="ExternalInput").ap() for name, a in arrays.items()}
    out = nc.dram_tensor("out", (1, T, D), F32, kind="ExternalOutput").ap()
    build(nc, I, out)
    return run_bass_kernel_spmd(nc, [arrays], core_ids=[0]).results[0]["out"]
```
